# Optimizing a Trainium2 kernel written in Bass

```python
import jax
import jax.numpy as jnp
from jax import lax
import numpy as np
import jax, jax.numpy as jnp

D_MODEL = 1024
BATCH = 1
SEQ = 1024
DEPTH = 1

GRID_W = 64
CTX_LEN = 256
HEAD_DIM = 64
ATTN_WIDTH = D_MODEL // 2
N_Q_HEADS = ATTN_WIDTH // HEAD_DIM
N_KV_HEADS = N_Q_HEADS // 4
Q_PER_KV = N_Q_HEADS // N_KV_HEADS
KV_WIDTH = N_KV_HEADS * HEAD_DIM
WINDOW = 128
BLOCK = 128
ROPE_BASE = 10000.0
RWKV_WIDTH = D_MODEL // 2
RWKV_HEAD_DIM = 64
RWKV_HEADS = RWKV_WIDTH // RWKV_HEAD_DIM
DECAY_LORA = 32
ICLR_LORA = 32
GATE_LORA = 96
RWKV_IN_WIDTH = 3 * RWKV_WIDTH + DECAY_LORA + ICLR_LORA + GATE_LORA
SHORT_CONV = 3
N_BRANCHES = 2
IN_WIDTH = ATTN_WIDTH + 2 * KV_WIDTH + RWKV_IN_WIDTH + N_BRANCHES * D_MODEL
D_FF = 4 * D_MODEL
N_MOD = 6
NORM_EPS = 1e-6
LNX_EPS = 1e-5 * RWKV_HEAD_DIM
IN_SPLITS = [ATTN_WIDTH, ATTN_WIDTH + KV_WIDTH, ATTN_WIDTH + 2 * KV_WIDTH,
             ATTN_WIDTH + 2 * KV_WIDTH + RWKV_IN_WIDTH]
RW_SPLITS = [RWKV_WIDTH, 2 * RWKV_WIDTH, 3 * RWKV_WIDTH,
             3 * RWKV_WIDTH + DECAY_LORA, 3 * RWKV_WIDTH + DECAY_LORA + ICLR_LORA]


def rmsnorm(x, g):
    xf = x.astype(jnp.float32)
    y = xf * lax.rsqrt(jnp.mean(xf * xf, axis=-1, keepdims=True) + NORM_EPS)
    return (y * g.astype(jnp.float32)).astype(x.dtype)

def modulate(h, shift, scale):
    return h * (1 + scale) + shift

def axial_rope_tables(rows):
    n_freq = HEAD_DIM // 4
    inv_freq = jnp.power(ROPE_BASE, -jnp.arange(n_freq, dtype=jnp.float32) / n_freq)
    row = jnp.repeat(jnp.arange(rows, dtype=jnp.float32), GRID_W)
    col = jnp.tile(jnp.arange(GRID_W, dtype=jnp.float32), rows)
    ang = jnp.concatenate([row[:, None] * inv_freq, col[:, None] * inv_freq], axis=-1)
    return jnp.cos(ang), jnp.sin(ang)

def apply_rope(x, cos, sin):
    half = x.shape[-1] // 2
    x1, x2 = x[..., :half], x[..., half:]
    c = cos[:, None, :].astype(x.dtype)
    s = sin[:, None, :].astype(x.dtype)
    return jnp.concatenate([x1 * c - x2 * s, x1 * s + x2 * c], axis=-1)

def sink_column(sink, lead_shape):
    s = sink.astype(jnp.float32).reshape(N_KV_HEADS, Q_PER_KV)
    return jnp.broadcast_to(s[:, :, None, None], lead_shape + (1,))

def latent_window_attention(q, k, v, kc, vc, sink):
    B, L, _, dh = q.shape
    Lc = kc.shape[1]
    nb = L // BLOCK
    scale = dh ** -0.5
    qb = q.reshape(B, nb, BLOCK, N_KV_HEADS, Q_PER_KV, dh)
    pad = ((0, 0), (BLOCK, BLOCK), (0, 0), (0, 0))

    def band(t):
        tb = jnp.pad(t, pad).reshape(B, nb + 2, BLOCK, N_KV_HEADS, dh)
        return jnp.concatenate([tb[:, :-2], tb[:, 1:-1], tb[:, 2:]], axis=2)

    kb, vb = band(k), band(v)
    s_loc = jnp.einsum('bnqgrd,bnkgd->bngrqk', qb, kb).astype(jnp.float32) * scale
    s_ctx = jnp.einsum('bnqgrd,bcgd->bngrqc', qb, kc).astype(jnp.float32) * scale
    blk = jnp.arange(nb)[:, None, None]
    qi = jnp.arange(BLOCK)[None, :, None]
    kj = jnp.arange(3 * BLOCK)[None, None, :]
    i_pos = blk * BLOCK + qi
    j_pos = blk * BLOCK - BLOCK + kj
    valid = (jnp.abs(i_pos - j_pos) <= WINDOW) & (j_pos >= 0) & (j_pos < L)
    s_loc = jnp.where(valid[None, :, None, None], s_loc, -jnp.inf)
    s_sink = jnp.broadcast_to(sink.astype(jnp.float32).reshape(N_KV_HEADS, Q_PER_KV)[None, None, :, :, None, None],
                              s_loc.shape[:-1] + (1,))
    p = jax.nn.softmax(jnp.concatenate([s_loc, s_ctx, s_sink], axis=-1), axis=-1)
    p_loc = p[..., :3 * BLOCK].astype(v.dtype)
    p_ctx = p[..., 3 * BLOCK:3 * BLOCK + Lc].astype(v.dtype)
    o = (jnp.einsum('bngrqk,bnkgd->bnqgrd', p_loc, vb)
         + jnp.einsum('bngrqc,bcgd->bnqgrd', p_ctx, vc))
    return o.reshape(B, L, N_Q_HEADS * dh)

def context_attention(qc, kc, vc, sink):
    B, Lc, _, dh = qc.shape
    qg = qc.reshape(B, Lc, N_KV_HEADS, Q_PER_KV, dh)
    s = jnp.einsum('bqgrd,bkgd->bgrqk', qg, kc).astype(jnp.float32) * dh ** -0.5
    s_sink = sink_column(sink, s.shape[1:-1])[None]
    s_sink = jnp.broadcast_to(s_sink, s.shape[:-1] + (1,))
    p = jax.nn.softmax(jnp.concatenate([s, s_sink], axis=-1), axis=-1)
    o = jnp.einsum('bgrqk,bkgd->bqgrd', p[..., :Lc].astype(vc.dtype), vc)
    return o.reshape(B, Lc, N_Q_HEADS * dh)

def short_conv(u, w):
    L = u.shape[1]
    half = SHORT_CONV // 2
    up = jnp.pad(u, ((0, 0), (half, half), (0, 0)))
    return sum(up[:, t:t + L] * w[t] for t in range(SHORT_CONV))

def rwkv_prepare(u, decay_w0, decay_w2, iclr_a0, iclr_a2, k_k, k_a):
    B, L, _ = u.shape
    r, k, v, hw, ha, hg = jnp.split(u, RW_SPLITS, axis=-1)

    def heads(t):
        return t.astype(jnp.float32).reshape(B, L, RWKV_HEADS, RWKV_HEAD_DIM)

    kk = heads(k * k_k)
    kk = kk * lax.rsqrt(jnp.maximum(jnp.sum(kk * kk, axis=-1, keepdims=True), 1e-24))
    dirs = []
    for d in range(2):
        w_log = -jax.nn.softplus(-(decay_w0[d] + jnp.tanh(hw) @ decay_w2[d])) - 0.5
        a = jax.nn.sigmoid(iclr_a0[d] + ha @ iclr_a2[d])
        decay = jnp.exp(-jnp.exp(heads(w_log)))
        k_d = heads(k * (1 + (a - 1) * k_a))
        dirs.append((decay, kk * heads(a), k_d))
    return heads(r), heads(v), hg, kk, dirs

def wkv7_scan(S0, r, decay, kk, b, k, v, reverse, emit):
    xs = tuple(jnp.moveaxis(t, 1, 0) for t in (r, decay, kk, b, k, v))

    def step(S, inp):
        r_t, w_t, kk_t, b_t, k_t, v_t = inp
        sa = jnp.einsum('bhvk,bhk->bhv', S, -kk_t)
        S = S * w_t[:, :, None, :] + sa[..., None] * b_t[:, :, None, :] + v_t[..., None] * k_t[:, :, None, :]
        y = jnp.einsum('bhvk,bhk->bhv', S, r_t) if emit else None
        return S, y

    S, ys = lax.scan(step, S0, xs, reverse=reverse)
    return S, (jnp.moveaxis(ys, 0, 1) if emit else None)

def rwkv_output(y, r, v, hg, dirs, gate_g2, r_k, lnx_w, lnx_b):
    B, L = y.shape[:2]
    mu = jnp.mean(y, axis=-1, keepdims=True)
    var = jnp.mean(jnp.square(y - mu), axis=-1, keepdims=True)
    yn = (y - mu) * lax.rsqrt(var + LNX_EPS)
    k_sum = dirs[0][2] + dirs[1][2]
    bonus = jnp.sum(r * k_sum * r_k.astype(jnp.float32), axis=-1, keepdims=True) * v
    out = (yn.reshape(B, L, RWKV_WIDTH) * lnx_w + lnx_b + bonus.reshape(B, L, RWKV_WIDTH)).astype(hg.dtype)
    g = jax.nn.sigmoid(hg) @ gate_g2
    return out * g

def merge_branches(ya, yr, gate_logits, w_branch_attn, w_branch_rwkv, w_out):
    ga, gr = jnp.split(jax.nn.sigmoid(gate_logits), N_BRANCHES, axis=-1)
    return (ga * (ya @ w_branch_attn) + gr * (yr @ w_branch_rwkv)) @ w_out

def sq_relu_mlp(h, w_up, w_down):
    return jnp.square(jax.nn.relu(h @ w_up)) @ w_down

def trunk_layer(x, xc, c, c_ctx, cos, sin, w_ada, b_ada, norm1_g, w_in, sink, conv_w,
                decay_w0, decay_w2, iclr_a0, iclr_a2, gate_g2, k_k, k_a, r_k, lnx_w, lnx_b,
                w_branch_attn, w_branch_rwkv, w_out, norm2_g, w_mlp_up, w_mlp_down, update_ctx):
    B, L, D = x.shape
    Lc = xc.shape[1]
    mod = (jax.nn.silu(c) @ w_ada + b_ada).reshape(B, 1, N_MOD, D)
    shift1, scale1, gate1, shift2, scale2, gate2 = [mod[:, :, i] for i in range(N_MOD)]
    modc = (jax.nn.silu(c_ctx) @ w_ada + b_ada).reshape(N_MOD, D)

    h = modulate(rmsnorm(x, norm1_g), shift1, scale1)
    hc = modulate(rmsnorm(xc, norm1_g), modc[0], modc[1])
    q, k, v, rw, gl = jnp.split(h @ w_in, IN_SPLITS, axis=-1)
    qc, kc, vc, rwc, glc = jnp.split(hc @ w_in, IN_SPLITS, axis=-1)

    q = apply_rope(q.reshape(B, L, N_Q_HEADS, HEAD_DIM), cos, sin)
    k = apply_rope(k.reshape(B, L, N_KV_HEADS, HEAD_DIM), cos, sin)
    v = v.reshape(B, L, N_KV_HEADS, HEAD_DIM)
    kc = kc.reshape(B, Lc, N_KV_HEADS, HEAD_DIM)
    vc = vc.reshape(B, Lc, N_KV_HEADS, HEAD_DIM)
    ya = latent_window_attention(q, k, v, kc, vc, sink)

    r_l, v_l, hg_l, kk_l, dirs_l = rwkv_prepare(short_conv(rw, conv_w), decay_w0, decay_w2,
                                               iclr_a0, iclr_a2, k_k, k_a)
    r_c, v_c, hg_c, kk_c, dirs_c = rwkv_prepare(short_conv(rwc, conv_w), decay_w0, decay_w2,
                                               iclr_a0, iclr_a2, k_k, k_a)
    S0 = jnp.zeros((B, RWKV_HEADS, RWKV_HEAD_DIM, RWKV_HEAD_DIM), jnp.float32)
    y_lat = []
    y_ctx = []
    for d, rev in enumerate((False, True)):
        dec_c, b_c, k_c = dirs_c[d]
        S_ctx, yc_d = wkv7_scan(S0, r_c, dec_c, kk_c, b_c, k_c, v_c, rev, update_ctx)
        dec_l, b_l, k_l = dirs_l[d]
        _, y_d = wkv7_scan(S_ctx, r_l, dec_l, kk_l, b_l, k_l, v_l, rev, True)
        y_lat.append(y_d)
        y_ctx.append(yc_d)
    yr = rwkv_output(y_lat[0] + y_lat[1], r_l, v_l, hg_l, dirs_l, gate_g2, r_k, lnx_w, lnx_b)

    x = x + gate1 * merge_branches(ya, yr, gl, w_branch_attn, w_branch_rwkv, w_out)
    x = x + gate2 * sq_relu_mlp(modulate(rmsnorm(x, norm2_g), shift2, scale2), w_mlp_up, w_mlp_down)

    if update_ctx:
        yac = context_attention(qc.reshape(B, Lc, N_Q_HEADS, HEAD_DIM), kc, vc, sink)
        yrc = rwkv_output(y_ctx[0] + y_ctx[1], r_c, v_c, hg_c, dirs_c, gate_g2, r_k, lnx_w, lnx_b)
        xc = xc + modc[2] * merge_branches(yac, yrc, glc, w_branch_attn, w_branch_rwkv, w_out)
        xc = xc + modc[5] * sq_relu_mlp(modulate(rmsnorm(xc, norm2_g), modc[3], modc[4]), w_mlp_up, w_mlp_down)
    return x, xc

def first_inputs(seed: int = 0) -> dict:
    key = jax.random.key(seed)
    ks = iter(jax.random.split(key, 32))

    def nrm(shape, s):
        return jax.random.normal(next(ks), shape, jnp.float32) * s

    D = D_MODEL
    L = DEPTH
    conv_base = jnp.asarray([0.25, 1.0, 0.25], jnp.float32)[None, :, None]
    return {
        "x": nrm((BATCH, SEQ, D), 1.0),
        "c": nrm((BATCH, D), 1.0),
        "ctx": nrm((BATCH, CTX_LEN, D), 1.0),
        "c_ctx": nrm((D,), 1.0),
        "w_ada": nrm((L, D, N_MOD * D), 0.5 * D ** -0.5),
        "b_ada": nrm((L, N_MOD * D), 0.02),
        "norm1_g": 1.0 + nrm((L, D), 0.05),
        "w_in": nrm((L, D, IN_WIDTH), D ** -0.5),
        "sink": nrm((L, N_Q_HEADS), 0.5),
        "conv_w": conv_base + nrm((L, SHORT_CONV, RWKV_IN_WIDTH), 0.05),
        "decay_w0": nrm((L, 2, RWKV_WIDTH), 0.5),
        "decay_w2": nrm((L, 2, DECAY_LORA, RWKV_WIDTH), DECAY_LORA ** -0.5),
        "iclr_a0": nrm((L, 2, RWKV_WIDTH), 0.5),
        "iclr_a2": nrm((L, 2, ICLR_LORA, RWKV_WIDTH), ICLR_LORA ** -0.5),
        "gate_g2": nrm((L, GATE_LORA, RWKV_WIDTH), GATE_LORA ** -0.5),
        "k_k": 1.0 + nrm((L, RWKV_WIDTH), 0.1),
        "k_a": 1.0 + nrm((L, RWKV_WIDTH), 0.1),
        "r_k": nrm((L, RWKV_HEADS, RWKV_HEAD_DIM), 0.1),
        "lnx_w": 1.0 + nrm((L, RWKV_WIDTH), 0.05),
        "lnx_b": nrm((L, RWKV_WIDTH), 0.02),
        "w_branch_attn": nrm((L, ATTN_WIDTH, D), ATTN_WIDTH ** -0.5),
        "w_branch_rwkv": nrm((L, RWKV_WIDTH, D), RWKV_WIDTH ** -0.5),
        "w_out": nrm((L, D, D), D ** -0.5),
        "norm2_g": 1.0 + nrm((L, D), 0.05),
        "w_mlp_up": nrm((L, D, D_FF), D ** -0.5),
        "w_mlp_down": nrm((L, D_FF, D), D_FF ** -0.5),
        "norm_f_g": 1.0 + nrm((D,), 0.05),
    }

def first_block(x, c, ctx, c_ctx, w_ada, b_ada, norm1_g, w_in, sink, conv_w, decay_w0, decay_w2,
              iclr_a0, iclr_a2, gate_g2, k_k, k_a, r_k, lnx_w, lnx_b, w_branch_attn, w_branch_rwkv,
              w_out, norm2_g, w_mlp_up, w_mlp_down, norm_f_g):
    rows = x.shape[1] // GRID_W
    cos, sin = axial_rope_tables(rows)
    xc = ctx
    for l in range(DEPTH):
        x, xc = trunk_layer(x, xc, c, c_ctx, cos, sin, w_ada[l], b_ada[l], norm1_g[l], w_in[l], sink[l],
                            conv_w[l], decay_w0[l], decay_w2[l], iclr_a0[l], iclr_a2[l], gate_g2[l],
                            k_k[l], k_a[l], r_k[l], lnx_w[l], lnx_b[l], w_branch_attn[l], w_branch_rwkv[l],
                            w_out[l], norm2_g[l], w_mlp_up[l], w_mlp_down[l], update_ctx=(l < DEPTH - 1))
    return rmsnorm(x, norm_f_g)


DEPTH_2 = 2


SGU_HEADS = 4
SGU_HEAD_DIM = 64
SGU_W = SGU_HEADS * SGU_HEAD_DIM
CHUNK = 128
FNET_GROUPS = 4
FNET_GROUP_DIM = 64
FNET_W = FNET_GROUPS * FNET_GROUP_DIM
MLA_HEADS = 4
QK_NOPE_DIM = 128
QK_ROPE_DIM = 64
QK_DIM = QK_NOPE_DIM + QK_ROPE_DIM
V_DIM = 128
Q_LORA = 256
KV_LORA = 128
MLA_W = MLA_HEADS * V_DIM
Q_BLOCK = 128
ROPE_THETA = 10000.0
OFF_U = 0
OFF_V = OFF_U + SGU_W
OFF_F = OFF_V + SGU_W
OFF_Q = OFF_F + FNET_W
OFF_KV = OFF_Q + Q_LORA
OFF_KR = OFF_KV + KV_LORA
IN_W = OFF_KR + QK_ROPE_DIM
MIX_W = SGU_W + FNET_W + MLA_W
N_EXPERTS = 16
EC_FACTOR = 2
D_EXPERT = 512
EPS = 1e-6


def rms_norm(x):
    xf = x.astype(jnp.float32)
    return (xf * lax.rsqrt(jnp.mean(xf * xf, axis=-1, keepdims=True) + EPS)).astype(x.dtype)

def ada_modulation(cond, w_ada, b_ada):
    m = (jax.nn.silu(cond) @ w_ada + b_ada)[:, None, :]
    return jnp.split(m, 6, axis=-1)

def modulate_2(x, shift, scale):
    return rms_norm(x) * (1 + scale) + shift

def rope_1d(x, pos):
    half = x.shape[-1] // 2
    freqs = ROPE_THETA ** (-jnp.arange(half, dtype=jnp.float32) / half)
    ang = pos.astype(jnp.float32)[:, None] * freqs
    cos = jnp.cos(ang)[:, None, :]
    sin = jnp.sin(ang)[:, None, :]
    xf = x.astype(jnp.float32)
    x1, x2 = xf[..., :half], xf[..., half:]
    return jnp.concatenate([x1 * cos - x2 * sin, x1 * sin + x2 * cos], axis=-1).astype(x.dtype)

def rope_2d(x, pos_row, pos_col):
    half = x.shape[-1] // 2
    return jnp.concatenate([rope_1d(x[..., :half], pos_row), rope_1d(x[..., half:], pos_col)], axis=-1)

def with_rope(t, pos_row, pos_col):
    return jnp.concatenate([t[..., :QK_NOPE_DIM], rope_2d(t[..., QK_NOPE_DIM:], pos_row, pos_col)], axis=-1)

def chunk_mlp(pu, pv, sgu_norm, w_sgu, b_sgu):
    b, n, _ = pu.shape
    u = jax.nn.gelu(pu)
    v = rms_norm(jax.nn.gelu(pv)) * sgu_norm
    v = v.reshape(b, n // CHUNK, CHUNK, SGU_HEADS, SGU_HEAD_DIM)
    z = jnp.einsum('hpq,bcqhd->bcphd', w_sgu, v) + b_sgu.T[:, :, None]
    return u * z.reshape(b, n, SGU_W)

def fourier_mix(pf):
    b, n, _ = pf.shape
    f = pf.reshape(b, n, FNET_GROUPS, FNET_GROUP_DIM).astype(jnp.float32)
    y = jnp.fft.fft2(f, axes=(1, 3), norm="ortho").real
    return y.reshape(b, n, FNET_W).astype(pf.dtype)

def mla_queries(pq, q_lora_norm, w_uq, q_norm):
    b, n, _ = pq.shape
    cq = rms_norm(pq) * q_lora_norm
    q = (cq @ w_uq).reshape(b, n, MLA_HEADS, QK_DIM)
    return rms_norm(q) * q_norm

def mla_keys_values(pkv, pkr, kv_lora_norm, w_ukv, k_norm):
    b, n, _ = pkv.shape
    ckv = rms_norm(pkv) * kv_lora_norm
    kv = (ckv @ w_ukv).reshape(b, n, MLA_HEADS, QK_NOPE_DIM + V_DIM)
    k_nope, v = kv[..., :QK_NOPE_DIM], kv[..., QK_NOPE_DIM:]
    k_rope = jnp.broadcast_to(pkr[:, :, None, :], (b, n, MLA_HEADS, QK_ROPE_DIM))
    k = rms_norm(jnp.concatenate([k_nope, k_rope], axis=-1)) * k_norm
    return k, v

def block_attention(q, k, v):
    b, n, h, _ = q.shape
    scale = QK_DIM ** -0.5
    qb = jnp.moveaxis(q.reshape(b, n // Q_BLOCK, Q_BLOCK, h, QK_DIM), 1, 0)

    def one_block(qblk):
        s = jnp.einsum('bqhd,bkhd->bhqk', qblk, k).astype(jnp.float32) * scale
        p = jax.nn.softmax(s, axis=-1).astype(v.dtype)
        return jnp.einsum('bhqk,bkhv->bqhv', p, v)

    o = lax.map(one_block, qb)
    return jnp.moveaxis(o, 0, 1).reshape(b, n, h * V_DIM)

def local_head_groups(p, sgu_norm, w_sgu, b_sgu, q_lora_norm, w_uq, q_norm):
    ya = chunk_mlp(p[..., OFF_U:OFF_V], p[..., OFF_V:OFF_F], sgu_norm, w_sgu, b_sgu)
    yb = fourier_mix(p[..., OFF_F:OFF_Q])
    q = mla_queries(p[..., OFF_Q:OFF_KV], q_lora_norm, w_uq, q_norm)
    return ya, yb, q

def expert_choice_moe(h, w_router, w_gate, w_up, w_down):
    b, n, d = h.shape
    cap = EC_FACTOR * n // N_EXPERTS
    aff = jax.nn.softmax(jnp.einsum('bnd,de->bne', h, w_router).astype(jnp.float32), axis=-1)
    g, idx = lax.top_k(jnp.swapaxes(aff, 1, 2), cap)
    xs = jax.vmap(lambda hb, ib: hb[ib])(h, idx)
    hid = jax.nn.silu(jnp.einsum('becd,edf->becf', xs, w_gate)) * jnp.einsum('becd,edf->becf', xs, w_up)
    y = jnp.einsum('becf,efd->becd', hid, w_down) * g[..., None].astype(h.dtype)
    return jax.vmap(lambda yb, ib: jnp.zeros((n, d), h.dtype).at[ib.reshape(-1)].add(yb.reshape(-1, d)))(y, idx)

def second_inputs(seed: int = 0) -> dict:
    key = jax.random.key(seed)
    ks = jax.random.split(key, 22)

    def nrm(k, shape, scale):
        return jax.random.normal(k, shape, jnp.float32) * scale

    return {
        "x": nrm(ks[0], (BATCH, SEQ, D_MODEL), 1.0),
        "c": nrm(ks[1], (BATCH, D_MODEL), 1.0),
        "ctx": nrm(ks[2], (BATCH, CTX_LEN, D_MODEL), 1.0),
        "c_ctx": nrm(ks[3], (D_MODEL,), 1.0),
        "w_ada": nrm(ks[4], (DEPTH_2, D_MODEL, 6 * D_MODEL), 0.5 * D_MODEL ** -0.5),
        "b_ada": nrm(ks[5], (DEPTH_2, 6 * D_MODEL), 0.01),
        "w_in": nrm(ks[6], (DEPTH_2, D_MODEL, IN_W), D_MODEL ** -0.5),
        "sgu_norm": 1.0 + nrm(ks[7], (DEPTH_2, SGU_W), 0.01),
        "w_sgu": nrm(ks[8], (DEPTH_2, SGU_HEADS, CHUNK, CHUNK), CHUNK ** -0.5),
        "b_sgu": 1.0 + nrm(ks[9], (DEPTH_2, SGU_HEADS, CHUNK), 0.01),
        "q_lora_norm": 1.0 + nrm(ks[10], (DEPTH_2, Q_LORA), 0.01),
        "w_uq": nrm(ks[11], (DEPTH_2, Q_LORA, MLA_HEADS * QK_DIM), Q_LORA ** -0.5),
        "kv_lora_norm": 1.0 + nrm(ks[12], (DEPTH_2, KV_LORA), 0.01),
        "w_ukv": nrm(ks[13], (DEPTH_2, KV_LORA, MLA_HEADS * (QK_NOPE_DIM + V_DIM)), KV_LORA ** -0.5),
        "q_norm": 1.0 + nrm(ks[14], (DEPTH_2, QK_DIM), 0.01),
        "k_norm": 1.0 + nrm(ks[15], (DEPTH_2, QK_DIM), 0.01),
        "w_out": nrm(ks[16], (DEPTH_2, MIX_W, D_MODEL), MIX_W ** -0.5),
        "w_router": nrm(ks[17], (DEPTH_2, D_MODEL, N_EXPERTS), D_MODEL ** -0.5),
        "w_gate": nrm(ks[18], (DEPTH_2, N_EXPERTS, D_MODEL, D_EXPERT), D_MODEL ** -0.5),
        "w_up": nrm(ks[19], (DEPTH_2, N_EXPERTS, D_MODEL, D_EXPERT), D_MODEL ** -0.5),
        "w_down": nrm(ks[20], (DEPTH_2, N_EXPERTS, D_EXPERT, D_MODEL), D_EXPERT ** -0.5),
    }

def second_block(x, c, ctx, c_ctx, w_ada, b_ada, w_in, sgu_norm, w_sgu, b_sgu, q_lora_norm, w_uq,
              kv_lora_norm, w_ukv, q_norm, k_norm, w_out, w_router, w_gate, w_up, w_down):
    n = x.shape[1]
    rows = n // GRID_W
    pos_row = jnp.repeat(jnp.arange(rows, dtype=jnp.int32), GRID_W)
    pos_col = jnp.tile(jnp.arange(GRID_W, dtype=jnp.int32), rows)
    xc = ctx
    for l in range(DEPTH_2):
        last = l == DEPTH_2 - 1
        sh1, sc1, g1, sh2, sc2, g2 = ada_modulation(c, w_ada[l], b_ada[l])
        csh1, csc1, cg1, csh2, csc2, cg2 = ada_modulation(c_ctx[None], w_ada[l], b_ada[l])

        hx = modulate_2(x, sh1, sc1)
        hc = modulate_2(xc, csh1, csc1)
        col0 = OFF_KV if last else 0
        pc = hc @ w_in[l][:, col0:]
        k_ctx, v_ctx = mla_keys_values(pc[..., OFF_KV - col0:OFF_KR - col0], pc[..., OFF_KR - col0:],
                                       kv_lora_norm[l], w_ukv[l], k_norm[l])

        px = hx @ w_in[l]
        ya, yb, q = local_head_groups(px, sgu_norm[l], w_sgu[l], b_sgu[l], q_lora_norm[l], w_uq[l], q_norm[l])
        k, v = mla_keys_values(px[..., OFF_KV:OFF_KR], px[..., OFF_KR:], kv_lora_norm[l], w_ukv[l], k_norm[l])
        q = with_rope(q, pos_row, pos_col)
        k = with_rope(k, pos_row, pos_col)
        yc = block_attention(q, jnp.concatenate([k_ctx, k], axis=1), jnp.concatenate([v_ctx, v], axis=1))
        x = x + g1 * (jnp.concatenate([ya, yb, yc], axis=-1) @ w_out[l])

        if not last:
            ya_c, yb_c, q_c = local_head_groups(pc, sgu_norm[l], w_sgu[l], b_sgu[l], q_lora_norm[l], w_uq[l], q_norm[l])
            yc_c = block_attention(q_c, k_ctx, v_ctx)
            xc = xc + cg1 * (jnp.concatenate([ya_c, yb_c, yc_c], axis=-1) @ w_out[l])

        x = x + g2 * expert_choice_moe(modulate_2(x, sh2, sc2), w_router[l], w_gate[l], w_up[l], w_down[l])
        if not last:
            xc = xc + cg2 * expert_choice_moe(modulate_2(xc, csh2, csc2), w_router[l], w_gate[l], w_up[l], w_down[l])
    return x


def setup_inputs(seed=0):
    out = dict(first_inputs(seed))
    for name, value in second_inputs(seed + 1).items():
        if name != "x":
            out[name + "_2"] = value
    return out


def reference(
    x, c, ctx, c_ctx, w_ada, b_ada, norm1_g, w_in, sink, conv_w, decay_w0, decay_w2, iclr_a0,
    iclr_a2, gate_g2, k_k, k_a, r_k, lnx_w, lnx_b, w_branch_attn, w_branch_rwkv, w_out, norm2_g,
    w_mlp_up, w_mlp_down, norm_f_g, c_2, ctx_2, c_ctx_2, w_ada_2, b_ada_2, w_in_2, sgu_norm_2,
    w_sgu_2, b_sgu_2, q_lora_norm_2, w_uq_2, kv_lora_norm_2, w_ukv_2, q_norm_2, k_norm_2,
    w_out_2, w_router_2, w_gate_2, w_up_2, w_down_2,
):
    x = first_block(
        x, c, ctx, c_ctx, w_ada, b_ada, norm1_g, w_in, sink, conv_w, decay_w0, decay_w2,
        iclr_a0, iclr_a2, gate_g2, k_k, k_a, r_k, lnx_w, lnx_b, w_branch_attn, w_branch_rwkv,
        w_out, norm2_g, w_mlp_up, w_mlp_down, norm_f_g,
    )
    return second_block(
        x, c_2, ctx_2, c_ctx_2, w_ada_2, b_ada_2, w_in_2, sgu_norm_2, w_sgu_2, b_sgu_2,
        q_lora_norm_2, w_uq_2, kv_lora_norm_2, w_ukv_2, q_norm_2, k_norm_2, w_out_2, w_router_2,
        w_gate_2, w_up_2, w_down_2,
    )


_drawn_inputs = setup_inputs


def setup_inputs(seed=0):
    import zlib

    import numpy as np

    out = dict(_drawn_inputs(seed))
    spreads = {}
    factors = {'ctx': 4.329,
     'norm1_g': 3.337,
     'sink': 64.0,
     'decay_w0': 3.139,
     'decay_w2': 3.361,
     'k_k': 8.0,
     'k_a': 2.74,
     'lnx_w': 8.0,
     'lnx_b': 8.0,
     'ctx_2': 7.539,
     'c_ctx_2': 3.0,
     'b_ada_2': 4.355,
     'sgu_norm_2': 8.0,
     'b_sgu_2': 8.0,
     'q_lora_norm_2': 8.0,
     'kv_lora_norm_2': 8.0,
     'q_norm_2': 8.0,
     'k_norm_2': 8.0}
    for name, (base, spread) in spreads.items():
        noise = np.random.default_rng([zlib.crc32(name.encode()), seed]).standard_normal(out[name].shape)
        drawn = base * np.exp(spread * noise) if base else spread * noise
        out[name] = jnp.asarray(drawn.astype(out[name].dtype))
    for name, factor in factors.items():
        out[name] = (out[name] * factor).astype(out[name].dtype)
    return out
```

```python
from contextlib import ExitStack

import numpy as np
import concourse.bass as bass
from concourse import mybir

F32 = mybir.dt.float32
I32 = mybir.dt.int32
U32 = mybir.dt.uint32
ALU = mybir.AluOpType
ACT = mybir.ActivationFunctionType
AX = mybir.AxisListType

P = 128
D = 1024
KT = D // P
L = 1024
C = 256
T = L + C
CHUNKS = [(0, 512), (512, 512), (1024, 256)]
LAT = CHUNKS[:2]
HD = 64
NQ = 8
WQ, WKV, WRW = 512, 128, 1696
EPS = 1e-6
NEG = -1.0e30


class Stage:

    def __init__(self, nc, name):
        self.nc, self.name, self.sems, self.stack = nc, name, [], ExitStack()

    def __enter__(self):
        self.stack.__enter__()
        return self

    def sb(self, name, shape, dt=F32):
        return self.stack.enter_context(self.nc.sbuf_tensor(f"{self.name}_{name}", shape, dt))

    def ps(self, name, shape, dt=F32):
        return self.stack.enter_context(self.nc.psum_tensor(f"{self.name}_{name}", shape, dt))

    def sem(self, name):
        self.sems.append(self.nc.alloc_semaphore(name=f"{self.name}_{name}"))
        return self.sems[-1]

    def slots(self, name, n=2):
        return [self.sem(f"{name}{b}") for b in range(n)]

    def __exit__(self, *e):
        if e[0] is None:
            self.nc.clear_and_free_semaphores(self.sems)
            self.nc.all_engine_barrier()
        return self.stack.__exit__(*e)


class Chain:

    def __init__(self, eng, sem, i=None, per=0):
        self.eng, self.sem, self.i, self.per, self.n = eng, sem, i, per, 0

    def __call__(self, ins):
        self.n += 1
        ins.then_inc(self.sem, 1)
        self.eng.wait_ge(self.sem, self.n if self.i is None else self.i * self.per + self.n)

    def close(self):
        assert self.i is None or self.n == self.per, f"{self.n} links, not {self.per}"


def by_tiles(ap):
    return ap.rearrange("(k p) m -> p k m", p=P)


def load_weights(sp, turns, source, w, w_full, ps_full, spans, first=0):
    with sp.Fori(0, turns) as i:
        for b in range(2):
            sp.wait_ge(ps_full[b], i * spans)
            sp.dma_start(w[:, b], source(i * 2 + b)).then_inc(w_full[b], 16)


def multiply_tiles(nc, pe, turns, w, rhs, kt, spans, ps, w_full, ps_free, ps_full):
    with pe.Fori(0, turns) as i:
        for b in range(2):
            pe.wait_ge(w_full[b], i * 16 + 16)
            pe.wait_ge(ps_free[b], i)
            for c, (t0, n) in enumerate(spans):
                for k in range(kt):
                    mm = nc.tensor.matmul(ps[:, b, c, 0:n], w[:, b, k], rhs[:, k, t0:t0 + n],
                                          start=(k == 0), stop=(k == kt - 1))
                mm.then_inc(ps_full[b], 1)



def modulation(nc, name, cond, cond_ctx, w_ada, b_ada, mod):
    NF = 6 * KT
    G = 4
    TURNS = NF // G // 2
    with Stage(nc, name) as s:
        cond_sb = s.sb("cond", [P, KT, 2])
        silu_sb = s.sb("silu", [P, KT, 2])
        bias = s.sb("bias", [P, NF, 2])
        w = s.sb("w", [P, 2, KT, G * P])
        ps = s.ps("ps", [P, 2, 512])
        small_loaded, silu_done = s.sem("small"), s.sem("silu")
        w_full, ps_full, ps_free = s.slots("w_full"), s.slots("ps_full"), s.slots("ps_free")
        with nc.Block() as block:
            @block.sync
            def _(sp):
                with nc.allow_non_contiguous_dma("vectors into columns"):
                    for j, v in enumerate((cond, cond_ctx)):
                        sp.dma_start(cond_sb[:, :, j], v.rearrange("(k p) -> p k", p=P)).then_inc(small_loaded, 16)
                        sp.dma_start(bias[:, :, j], b_ada.rearrange("(k p) -> p k", p=P)).then_inc(small_loaded, 16)
                with sp.Fori(0, TURNS) as i:
                    for b in range(2):
                        sp.wait_ge(ps_full[b], i)
                        sp.dma_start(w[:, b], by_tiles(w_ada)[:, :, bass.ds((i * 2 + b) * (G * P), G * P)]
                                     ).then_inc(w_full[b], 16)

            @block.scalar
            def _(act):
                act.wait_ge(small_loaded, 64)
                nc.scalar.activation(silu_sb[:], cond_sb[:], ACT.Silu).then_inc(silu_done, 1)

            @block.tensor
            def _(pe):
                pe.wait_ge(silu_done, 1)
                with pe.Fori(0, TURNS) as i:
                    for b in range(2):
                        pe.wait_ge(w_full[b], i * 16 + 16)
                        pe.wait_ge(ps_free[b], i)
                        for g in range(G):
                            for k in range(KT):
                                mm = nc.tensor.matmul(ps[:, b, 2 * g:2 * g + 2], w[:, b, k, g * P:(g + 1) * P],
                                                      silu_sb[:, k], start=(k == 0), stop=(k == KT - 1))
                        mm.then_inc(ps_full[b], 1)

            @block.vector
            def _(dve):
                dve.wait_ge(small_loaded, 64)
                with dve.Fori(0, TURNS) as i:
                    for b in range(2):
                        dve.wait_ge(ps_full[b], i + 1)
                        f = bass.ds((i * 2 + b) * G, G)
                        nc.vector.tensor_tensor(mod[:, f, :], ps[:, b, 0:2 * G].rearrange("p (g j) -> p g j", j=2),
                                                bias[:, f, :], ALU.add).then_inc(ps_free[b], 1)



def load_transposed(nc, name, ident, src, dst, tokens):
    TURNS = tokens // P // 2
    with Stage(nc, name) as s:
        rows = s.sb("rows", [P, 2, D])
        ps = s.ps("ps", [P, 2, KT, P])
        full, turned, free = s.slots("full"), s.slots("turned"), s.slots("free")
        with nc.Block() as block:
            @block.sync
            def _(sp):
                with sp.Fori(0, TURNS) as i:
                    for b in range(2):
                        sp.wait_ge(turned[b], i)
                        sp.dma_start(rows[:, b], src[bass.ds((i * 2 + b) * P, P), :]).then_inc(full[b], 16)

            @block.tensor
            def _(pe):
                with pe.Fori(0, TURNS) as i:
                    for b in range(2):
                        pe.wait_ge(full[b], i * 16 + 16)
                        pe.wait_ge(free[b], i)
                        for k in range(KT):
                            tr = nc.tensor.transpose(ps[:, b, k], rows[:, b, k * P:(k + 1) * P], ident)
                        tr.then_inc(turned[b], 1)

            @block.scalar
            def _(act):
                with act.Fori(0, TURNS) as i:
                    act.wait_ge(turned[0], i + 1)
                    nc.scalar.activation(dst[:, :, bass.ds(i * 2 * P, P)], ps[:, 0], ACT.Copy).then_inc(free[0], 1)

            @block.vector
            def _(dve):
                with dve.Fori(0, TURNS) as i:
                    dve.wait_ge(turned[1], i + 1)
                    nc.vector.tensor_copy(dst[:, :, bass.ds(i * 2 * P + P, P)], ps[:, 1]).then_inc(free[1], 1)



def norm_modulate(nc, name, ones, groups, g_vec=None):
    spans = [(n, c0, min(512, gr[2] - c0)) for n, gr in enumerate(groups) for c0 in range(0, gr[2], 512)]
    with Stage(nc, name) as s:
        g = s.sb("g", [P, KT])
        gain = s.sb("gain", [P, len(groups), KT])
        sq = s.sb("sq", [P, 2, 512])
        rstd = s.sb("rstd", [P, len(spans), 512])
        scaled = s.sb("scaled", [P, 2, 512])
        ps = s.ps("ps", [P, len(spans), 512])
        g_loaded, squared, summed, mean_done = s.sem("g"), s.sem("squared"), s.sem("summed"), s.sem("mean")
        rooted, gain_done = s.sem("rooted"), s.sem("gain")
        inv_done, scaled_done, out_done, chain_sem = s.sem("inv"), s.sem("scaled"), s.sem("out"), s.sem("chain")
        with nc.Block() as block:
            @block.sync
            def _(sp):
                if g_vec is not None:
                    with nc.allow_non_contiguous_dma("a vector into columns"):
                        sp.dma_start(g[:], g_vec.rearrange("(k p) -> p k", p=P)).then_inc(g_loaded, 16)

            @block.scalar
            def _(act):
                for m, (n, c0, w) in enumerate(spans):
                    for k in range(KT):
                        q = m * KT + k
                        if q >= 2:
                            act.wait_ge(summed, q - 1)
                        nc.scalar.activation(sq[:, q % 2, 0:w], groups[n][0][:, k, c0:c0 + w], ACT.Square
                                             ).then_inc(squared, 1)
                for m, (n, c0, w) in enumerate(spans):
                    act.wait_ge(mean_done, m + 1)
                    nc.scalar.activation(rstd[:, m, 0:w], rstd[:, m, 0:w], ACT.Sqrt).then_inc(rooted, 1)
                act.wait_ge(gain_done, len(groups))
                for m, (n, c0, w) in enumerate(spans):
                    _, t0, _, dst, shift, _ = groups[n]
                    for k in range(KT):
                        q = m * KT + k
                        act.wait_ge(scaled_done, q + 1)
                        nc.scalar.activation(dst[:, k, t0 + c0:t0 + c0 + w], scaled[:, q % 2, 0:w], ACT.Identity,
                                             scale=gain[:, n, k:k + 1],
                                             bias=0.0 if shift is None else shift[:, k:k + 1]).then_inc(out_done, 1)

            @block.tensor
            def _(pe):
                for m, (n, c0, w) in enumerate(spans):
                    for k in range(KT):
                        pe.wait_ge(squared, m * KT + k + 1)
                        nc.tensor.matmul(ps[:, m, 0:w], ones, sq[:, (m * KT + k) % 2, 0:w], start=(k == 0),
                                         stop=(k == KT - 1)).then_inc(summed, 1)

            @block.vector
            def _(dve):
                chain = Chain(dve, chain_sem)
                if g_vec is not None:
                    dve.wait_ge(g_loaded, 16)
                else:
                    chain(nc.vector.memset(g[:], 1.0))
                for n, gr in enumerate(groups):
                    if gr[5] is None:
                        nc.vector.tensor_copy(gain[:, n], g[:]).then_inc(gain_done, 1)
                    else:
                        nc.vector.scalar_tensor_tensor(gain[:, n], gr[5], 1.0, g[:], ALU.add, ALU.mult
                                                       ).then_inc(gain_done, 1)
                for m, (n, c0, w) in enumerate(spans):
                    dve.wait_ge(summed, (m + 1) * KT)
                    nc.vector.tensor_scalar(rstd[:, m, 0:w], ps[:, m, 0:w], 1.0 / D, EPS, ALU.mult, ALU.add
                                            ).then_inc(mean_done, 1)
                for m, (n, c0, w) in enumerate(spans):
                    dve.wait_ge(rooted, m + 1)
                    nc.vector.reciprocal(rstd[:, m, 0:w], rstd[:, m, 0:w]).then_inc(inv_done, 1)
                    dve.wait_ge(inv_done, m + 1)
                    for k in range(KT):
                        q = m * KT + k
                        if q >= 2:
                            dve.wait_ge(out_done, q - 1)
                        nc.vector.tensor_tensor(scaled[:, q % 2, 0:w], groups[n][0][:, k, c0:c0 + w],
                                                rstd[:, m, 0:w], ALU.mult).then_inc(scaled_done, 1)



def store_columns(nc, name, src, dram):
    with Stage(nc, name) as s:
        stored = s.sem("stored")
        with nc.Block() as block:
            @block.sync
            def _(sp):
                sp.dma_start(by_tiles(dram), src).then_inc(stored, 16)
                sp.wait_ge(stored, 16)


def load_columns(nc, name, dram, dst):
    with Stage(nc, name) as s:
        loaded = s.sem("loaded")
        with nc.Block() as block:
            @block.sync
            def _(sp):
                sp.dma_start(dst[:], by_tiles(dram)).then_inc(loaded, 16)
                sp.wait_ge(loaded, 16)


def load_matrix(nc, name, dram, dst):
    with Stage(nc, name) as s:
        loaded = s.sem("loaded")
        with nc.Block() as block:
            @block.sync
            def _(sp):
                sp.dma_start(dst[:], dram).then_inc(loaded, 16)
                sp.wait_ge(loaded, 16)



def project_qkv(nc, name, cst, hT, w_in, qT, kT, v):
    NT = 5
    with Stage(nc, name) as s:
        w = s.sb("w", [P, 2, KT, P])
        wv = s.sb("wv", [P, KT, WKV])
        cos, sin = s.sb("cos", [P, L]), s.sb("sin", [P, L])
        rot = s.sb("rot", [P, P])
        raw = s.sb("raw", [P, 2, T])
        part = s.sb("part", [P, 2, 512])
        ps = s.ps("ps", [P, 3, 512])
        pr = s.ps("pr", [P, 2, 512])
        pv = s.ps("pv", [P, 2, 512])
        loaded, w_full = s.sem("loaded"), s.slots("w_full")
        mul_done, raw_done, rot_done, rot_read = s.sem("mul"), s.sem("raw"), s.sem("rot"), s.sem("rot_read")
        cos_done, v_done, v_read, chain_sem = s.sem("cos"), s.sem("v"), s.sem("v_read"), s.sem("chain")
        halves = [(0, 512), (512, 512)]
        with nc.Block() as block:
            @block.sync
            def _(sp):
                sp.dma_start(cos[:], cst["cos1"]).then_inc(loaded, 16)
                sp.dma_start(sin[:], cst["sin1"]).then_inc(loaded, 16)
                sp.dma_start(rot[:], cst["rot1"]).then_inc(loaded, 16)
                sp.dma_start(wv[:], by_tiles(w_in)[:, :, WQ + WKV:WQ + 2 * WKV]).then_inc(loaded, 16)
                for m in range(NT):
                    if m >= 2:
                        sp.wait_ge(mul_done, m - 1)
                    if m < 4:
                        for h in range(2):
                            c0 = (m + 4 * h) * HD
                            sp.dma_start(w[:, m % 2, :, h * HD:(h + 1) * HD], by_tiles(w_in)[:, :, c0:c0 + HD]
                                         ).then_inc(w_full[m % 2], 16)
                    else:
                        sp.dma_start(w[:, m % 2], by_tiles(w_in)[:, :, WQ:WQ + WKV]).then_inc(w_full[m % 2], 16)

            @block.tensor
            def _(pe):
                need = [0, 0]

                def rotate(m):
                    pe.wait_ge(raw_done, m + 1)
                    for c, (t0, n) in enumerate(halves):
                        if 2 * m + c >= 2:
                            pe.wait_ge(rot_read, 2 * m + c - 1)
                        nc.tensor.matmul(pr[:, c], rot[:], raw[:, m % 2, t0:t0 + n], start=True, stop=True
                                         ).then_inc(rot_done, 1)

                pe.wait_ge(loaded, 64)
                for m in range(NT):
                    need[m % 2] += 32 if m < 4 else 16
                    pe.wait_ge(w_full[m % 2], need[m % 2])
                    if m:
                        pe.wait_ge(raw_done, m)
                    spans = LAT if m < 4 else CHUNKS
                    for c, (t0, n) in enumerate(spans):
                        for k in range(KT):
                            mm = nc.tensor.matmul(ps[:, c, 0:n], w[:, m % 2, k], hT[:, k, t0:t0 + n],
                                                  start=(k == 0), stop=(k == KT - 1))
                    mm.then_inc(mul_done, 1)
                    if m:
                        rotate(m - 1)
                rotate(NT - 1)
                for t in range(T // P):
                    if t >= 2:
                        pe.wait_ge(v_read, t - 1)
                    for k in range(KT):
                        mm = nc.tensor.matmul(pv[:, t % 2, 0:WKV], hT[:, k, t * P:(t + 1) * P], wv[:, k],
                                              start=(k == 0), stop=(k == KT - 1))
                    mm.then_inc(v_done, 1)

            @block.scalar
            def _(act):
                for m in range(NT):
                    act.wait_ge(mul_done, m + 1)
                    if m >= 2:
                        act.wait_ge(cos_done, 2 * (m - 1))
                    spans = LAT if m < 4 else CHUNKS
                    for t0, n in spans:
                        ev = nc.scalar.activation(raw[:, m % 2, t0:t0 + n], ps[:, t0 // 512, 0:n], ACT.Copy)
                    ev.then_inc(raw_done, 1)
                for t in range(T // P):
                    act.wait_ge(v_done, t + 1)
                    nc.scalar.activation(v[:, t], pv[:, t % 2, 0:WKV], ACT.Copy).then_inc(v_read, 1)

            @block.vector
            def _(dve):
                chain = Chain(dve, chain_sem)
                dve.wait_ge(loaded, 64)
                for m in range(NT):
                    dve.wait_ge(raw_done, m + 1)
                    for c, (t0, n) in enumerate(halves):
                        dst = qT[:, m, t0:t0 + n] if m < 4 else kT[:, t0:t0 + n]
                        dve.wait_ge(rot_done, 2 * m + c + 1)
                        chain(nc.vector.tensor_tensor(part[:, c], pr[:, c], sin[:, t0:t0 + n], ALU.mult))
                        nc.vector.sem_inc(rot_read, 1)
                        chain(nc.vector.tensor_tensor(dst, raw[:, m % 2, t0:t0 + n], cos[:, t0:t0 + n], ALU.mult))
                        nc.vector.tensor_tensor(dst, dst, part[:, c], ALU.add).then_inc(cos_done, 1)
                dve.wait_ge(cos_done, 2 * NT)
                nc.vector.tensor_copy(kT[:, L:T], raw[:, (NT - 1) % 2, L:T])


def project_gates(nc, name, hT, w_gl, gates_dram):
    NT = 2 * KT
    with Stage(nc, name) as s:
        w = s.sb("w", [P, 2, KT, P])
        out = s.sb("out", [P, 2, L])
        ps = s.ps("ps", [P, 2, 2, 512])
        w_full, ps_full, ps_free = s.slots("w_full"), s.slots("ps_full"), s.slots("ps_free")
        stored = s.slots("stored")
        with nc.Block() as block:
            @block.sync
            def _(sp):
                load_weights(sp, NT // 2, lambda m: by_tiles(w_gl)[:, :, bass.ds(m * P, P)], w, w_full, ps_full, 2)

            @block.tensor
            def _(pe):
                multiply_tiles(nc, pe, NT // 2, w, hT, KT, LAT, ps, w_full, ps_free, ps_full)

            @block.scalar
            def _(act):
                with act.Fori(0, NT // 2) as i:
                    for b in range(2):
                        act.wait_ge(ps_full[b], i * 2 + 2)
                        act.wait_ge(stored[b], i * 16)
                        nc.scalar.activation(out[:, b], ps[:, b].rearrange("p c t -> p (c t)"), ACT.Sigmoid
                                             ).then_inc(ps_free[b], 1)
                        act.wait_ge(ps_free[b], i + 1)
                        act.dma_start(gates_dram[bass.ds((i * 2 + b) * P, P), :], out[:, b]).then_inc(stored[b], 16)
                for b in range(2):
                    act.wait_ge(stored[b], NT // 2 * 16)


def project_rwkv(nc, name, hT, w_rw, conv_w, rkv, lora_a, lora_b):
    NT = 14
    with Stage(nc, name) as s:
        w = s.sb("w", [P, 2, KT, P])
        cw = s.sb("cw", [P, 3, NT])
        raw = s.sb("raw", [P, 2, T + 4])
        ps = s.ps("ps", [P, 2, 3, 512])
        cw_loaded, zeroed, tail_conv = s.sem("cw"), s.sem("zeroed"), s.sem("tail")
        w_full, ps_full, ps_free, conv_done = (s.slots("w_full"), s.slots("ps_full"), s.slots("ps_free"),
                                               s.slots("conv"))
        chain_sem = s.sem("chain")
        SEQS = [(1, 0, L), (L + 3, L, C)]
        with nc.Block() as block:
            @block.sync
            def _(sp):
                with nc.allow_non_contiguous_dma("vectors into columns"):
                    for j in range(3):
                        sp.dma_start(cw[:, j, 0:13], conv_w[j, 0:13 * P].rearrange("(k p) -> p k", p=P)
                                     ).then_inc(cw_loaded, 16)
                        sp.dma_start(cw[0:32, j, 13:14], conv_w[j, 13 * P:WRW].rearrange("(p k) -> p k", k=1)
                                     ).then_inc(cw_loaded, 16)
                load_weights(sp, 6, lambda m: by_tiles(w_rw)[:, :, bass.ds(m * P, P)], w, w_full, ps_full, 3)
                sp.wait_ge(ps_full[0], 18)
                sp.dma_start(w[:, 0], by_tiles(w_rw)[:, :, 12 * P:13 * P]).then_inc(w_full[0], 16)
                sp.wait_ge(ps_full[1], 18)
                sp.dma_start(w[:, 1, :, 0:32], by_tiles(w_rw)[:, :, 13 * P:WRW]).then_inc(w_full[1], 16)

            @block.tensor
            def _(pe):
                multiply_tiles(nc, pe, 6, w, hT, KT, CHUNKS, ps, w_full, ps_free, ps_full)
                for b, rows in ((0, P), (1, 32)):
                    pe.wait_ge(w_full[b], 7 * 16)
                    pe.wait_ge(ps_free[b], 6)
                    for c, (t0, n) in enumerate(CHUNKS):
                        for k in range(KT):
                            mm = nc.tensor.matmul(ps[0:rows, b, c, 0:n], w[:, b, k, 0:rows], hT[:, k, t0:t0 + n],
                                                  start=(k == 0), stop=(k == KT - 1))
                        mm.then_inc(ps_full[b], 1)

            def copy_out(act, b, rows):
                for (r0, t0, n) in ((1, 0, 512), (513, 512, 512), (L + 3, L, C)):
                    ev = nc.scalar.activation(raw[0:rows, b, r0:r0 + n], ps[0:rows, b, t0 // 512, 0:n], ACT.Copy)
                ev.then_inc(ps_free[b], 1)

            @block.scalar
            def _(act):
                act.wait_ge(zeroed, 1)
                with act.Fori(0, 6) as i:
                    for b in range(2):
                        act.wait_ge(ps_full[b], i * 3 + 3)
                        act.wait_ge(conv_done[b], i)
                        copy_out(act, b, P)
                for b, rows in ((0, P), (1, 32)):
                    act.wait_ge(ps_full[b], 21)
                    act.wait_ge(conv_done[b], 6)
                    copy_out(act, b, rows)

            def convolve(dve, chain, b, rows, dst, weight, done):
                for r0, t0, n in SEQS:
                    out = dst(t0, n)
                    chain(nc.vector.tensor_scalar(out, raw[0:rows, b, r0 - 1:r0 - 1 + n], weight(0), None, ALU.mult))
                    chain(nc.vector.scalar_tensor_tensor(out, raw[0:rows, b, r0:r0 + n], weight(1), out,
                                                         ALU.mult, ALU.add))
                    ins = nc.vector.scalar_tensor_tensor(out, raw[0:rows, b, r0 + 1:r0 + 1 + n], weight(2), out,
                                                         ALU.mult, ALU.add)
                ins.then_inc(done, 1)

            @block.vector
            def _(dve):
                nc.vector.memset(raw[:], 0.0).then_inc(zeroed, 1)
                dve.wait_ge(cw_loaded, 96)
                with dve.Fori(0, 6) as i:
                    chain = Chain(dve, chain_sem, i, 8)
                    for b in range(2):
                        dve.wait_ge(ps_free[b], i + 1)
                        m = i * 2 + b
                        convolve(dve, chain, b, P, lambda t0, n: rkv[:, bass.ds(m, 1), t0:t0 + n].rearrange(
                            "p a t -> p (a t)"), lambda j: cw[:, j, bass.ds(m, 1)], conv_done[b])
                    chain.close()
                chain = Chain(dve, chain_sem)
                chain.n = 48
                for b, rows, dst in ((0, P, lora_a), (1, 32, lora_b)):
                    dve.wait_ge(ps_free[b], 7)
                    convolve(dve, chain, b, rows, lambda t0, n: dst[0:rows, t0:t0 + n],
                             lambda j: cw[0:rows, j, 12 + b:13 + b], tail_conv)



def window_attention(nc, name, cst, ident, qT, kT, v, kpad, vpad, sink, yT):
    H = NQ
    SC = HD ** -0.5
    NK = C + 3 * P
    U = 2 * H
    TURNS = L // P // 2
    with Stage(nc, name) as s:
        qs, ks, vs = s.sb("qs", [P, 2, 4, P]), s.sb("ks", [P, 2, NK]), s.sb("vs", [P, 2, 3, WKV])
        window = s.sb("window", [P, L // P, 2, P])
        sk, nsk = s.sb("sk", [P, H]), s.sb("nsk", [P, H])
        prob, probT = s.sb("prob", [P, 2, NK]), s.sb("probT", [P, 2, 5, P])
        nmax, total, rest, inv = s.sb("nmax", [P, 2]), s.sb("total", [P, 2]), s.sb("rest", [P, 2]), s.sb("inv", [P, 2])
        nm = s.sb("nm", [P, 2])
        out = s.sb("out", [P, 2, H * HD])
        pS, pT = s.ps("pS", [P, 2, 1024]), s.ps("pT", [P, 8, P])
        pO, pY = s.ps("pO", [P, 512]), s.ps("pY", [P, 4, P])
        loaded, padded, ready = s.sem("loaded"), s.sem("padded"), s.sem("ready")
        staged = s.slots("staged")
        s_full, max_done = s.slots("s_full"), s.slots("max")
        t_done, t_copied, pv_done, sums = s.slots("t_done"), s.slots("t_copied"), s.slots("pv"), s.slots("sums")
        sums_read = s.slots("sums_read")
        o_done, y_turned, y_copied, chain_sem = s.slots("o"), s.slots("y_turned"), s.sem("y_copied"), s.sem("chain")

        def at(i, u):
            return i * (U // 2) + u // 2

        with nc.Block() as block:
            @block.sync
            def _(sp):
                sp.dma_start(window[:], cst["window"]).then_inc(loaded, 16)
                sp.dma_start(sk[:], sink.partition_broadcast(P)).then_inc(loaded, 16)

            @block.gpsimd
            def _(pool):
                for x in (kpad[:, 0:P], kpad[:, P + L:], vpad[:, 0], vpad[:, L // P + 1]):
                    nc.gpsimd.memset(x, 0.0).then_inc(padded, 1)
                nc.gpsimd.tensor_copy(kpad[:, P:P + L], kT[:, 0:L]).then_inc(padded, 1)
                nc.gpsimd.tensor_copy(vpad[:, 1:1 + L // P], v[:, 0:L // P]).then_inc(padded, 1)
                for b in range(2):
                    nc.gpsimd.tensor_copy(ks[:, b, 0:C], kT[:, L:T]).then_inc(padded, 1)
                pool.wait_ge(padded, 8)
                with pool.Fori(0, TURNS) as i:
                    for b in range(2):
                        n = i * 2 + b
                        pool.wait_ge(y_turned[b], i)
                        nc.gpsimd.tensor_copy(qs[:, b], qT[:, :, bass.ds(n * P, P)]).then_inc(staged[b], 1)
                        nc.gpsimd.tensor_copy(ks[:, b, C:NK], kpad[:, bass.ds(n * P, 3 * P)]).then_inc(staged[b], 1)
                        nc.gpsimd.tensor_copy(vs[:, b], vpad[:, bass.ds(n, 3)]).then_inc(staged[b], 1)

            @block.tensor
            def _(pe):
                with pe.Fori(0, TURNS) as i:
                    def scores(u):
                        b, h, p = u // H, u % H, u % 2
                        if h == 0:
                            pe.wait_ge(staged[b], i * 3 + 3)
                        pe.wait_ge(sums[p], at(i, u))
                        r = slice(h // 4 * 64, h // 4 * 64 + 64)
                        nc.tensor.matmul(pS[:, p, 0:512], qs[r, b, h % 4], ks[r, b, 0:512], start=True, stop=True)
                        nc.tensor.matmul(pS[:, p, 512:NK], qs[r, b, h % 4], ks[r, b, 512:NK], start=True, stop=True
                                         ).then_inc(s_full[p], 1)

                    def turn(u):
                        p = u % 2
                        pe.wait_ge(sums[p], at(i, u) + 1)
                        if u:
                            pe.wait_ge(t_copied[1 - p], at(i, u - 1) + 1)
                        else:
                            pe.wait_ge(t_copied[1], i * (U // 2))
                        for j in range(5):
                            tr = nc.tensor.transpose(pT[:, j], prob[:, p, j * P:(j + 1) * P], ident)
                        tr.then_inc(t_done[p], 1)

                    def values(u):
                        b, h, p = u // H, u % H, u % 2
                        pe.wait_ge(t_copied[p], at(i, u) + 1)
                        if u:
                            pe.wait_ge(o_done[1 - p], at(i, u - 1) + 1)
                        else:
                            pe.wait_ge(o_done[1], i * (U // 2))
                        g = h // 4 * 64
                        for j in range(5):
                            val = v[:, L // P + j, g:g + 64] if j < 2 else vs[:, b, j - 2, g:g + 64]
                            mm = nc.tensor.matmul(pO[:, 0:HD], probT[:, p, j], val, start=(j == 0), stop=(j == 4))
                        mm.then_inc(pv_done[p], 1)

                    def turn_out(b):
                        pe.wait_ge(o_done[0], at(i, b * H + H - 2) + 1)
                        pe.wait_ge(o_done[1], at(i, b * H + H - 1) + 1)
                        pe.wait_ge(y_copied, i * 2 + b)
                        for m in range(4):
                            tr = nc.tensor.transpose(pY[:, m], out[:, b, m * P:(m + 1) * P], ident)
                        tr.then_inc(y_turned[b], 1)

                    scores(0)
                    for u in range(U):
                        if u + 1 < U:
                            scores(u + 1)
                        turn(u)
                        if u:
                            values(u - 1)
                        if u == H + 1:
                            turn_out(0)
                    values(U - 1)
                    turn_out(1)

            @block.scalar
            def _(act):
                act.wait_ge(ready, 1)
                with act.Fori(0, TURNS) as i:
                    def exps(u):
                        h, p = u % H, u % 2
                        act.wait_ge(max_done[p], at(i, u) + 1)
                        act.wait_ge(t_done[p], at(i, u))
                        act.wait_ge(sums_read[p], at(i, u))
                        nc.scalar.activation(rest[:, p:p + 1], sk[:, h:h + 1], ACT.Exp, bias=nm[:, p:p + 1])
                        nc.scalar.activation(prob[:, p], pS[:, p, 0:NK], ACT.Exp, bias=nm[:, p:p + 1], scale=SC,
                                             accum_out=total[:, p:p + 1]).then_inc(sums[p], 1)

                    def copy(u):
                        p = u % 2
                        act.wait_ge(t_done[p], at(i, u) + 1)
                        act.wait_ge(pv_done[p], at(i, u))
                        nc.scalar.activation(probT[:, p], pT[:, 0:5], ACT.Copy).then_inc(t_copied[p], 1)

                    exps(0)
                    for u in range(U):
                        if u + 1 < U:
                            exps(u + 1)
                        copy(u)

            @block.vector
            def _(dve):
                dve.wait_ge(loaded, 32)
                nc.vector.tensor_scalar(nsk[:], sk[:], -1.0, None, ALU.mult).then_inc(ready, 1)
                dve.wait_ge(ready, 1)
                with dve.Fori(0, TURNS) as i:
                    chain = Chain(dve, chain_sem, i, 4 * U)

                    def maxima(u):
                        b, h, p = u // H, u % H, u % 2
                        dve.wait_ge(s_full[p], at(i, u) + 1)
                        sides = pS[:, p, C:C + 512].rearrange("p (a k) -> p a k", k=256)[:, :, 0:P]
                        chain(nc.vector.tensor_tensor(sides, sides, window[:, bass.ds(i * 2 + b, 1)].rearrange(
                            "p o a k -> p (o a) k"), ALU.add))
                        chain(nc.vector.tensor_reduce(nmax[:, p:p + 1], pS[:, p, 0:NK], AX.X, ALU.max, negate=True))
                        nc.vector.tensor_scalar(nm[:, p:p + 1], nmax[:, p:p + 1], SC, nsk[:, h:h + 1],
                                                ALU.mult, ALU.min).then_inc(max_done[p], 1)

                    def invert(u):
                        p = u % 2
                        dve.wait_ge(sums[p], at(i, u) + 1)
                        chain(nc.vector.tensor_tensor(inv[:, p:p + 1], total[:, p:p + 1], rest[:, p:p + 1], ALU.add))
                        nc.vector.sem_inc(sums_read[p], 1)
                        chain(nc.vector.reciprocal(inv[:, p:p + 1], inv[:, p:p + 1]))

                    def outputs(u):
                        b, h, p = u // H, u % H, u % 2
                        dve.wait_ge(pv_done[p], at(i, u) + 1)
                        nc.vector.tensor_scalar(out[:, b, h * HD:(h + 1) * HD], pO[:, 0:HD], inv[:, p:p + 1], None,
                                                ALU.mult).then_inc(o_done[p], 1)

                    def copy_out(b):
                        dve.wait_ge(y_turned[b], i + 1)
                        nc.vector.tensor_copy(yT[:, :, bass.ds((i * 2 + b) * P, P)], pY[:]).then_inc(y_copied, 1)

                    maxima(0)
                    for u in range(U):
                        if u:
                            invert(u - 1)
                        if u + 1 < U:
                            maxima(u + 1)
                        if u:
                            outputs(u - 1)
                        if u == H + 1:
                            copy_out(0)
                    invert(U - 1)
                    outputs(U - 1)
                    copy_out(1)
                    chain.close()



def prepare_recurrence(nc, name, ones64, rkv, lora_a, lora_b, k_k, gate_g2, kk, lora_in, g_dram):
    units = [(m, t0, n) for m in range(4) for t0, n in CHUNKS]
    with Stage(nc, name) as s:
        kvec, g2 = s.sb("kvec", [P, 4]), s.sb("g2", [96, 512])
        sq, rs = s.sb("sq", [P, 2, 512]), s.sb("rs", [P, 2, 512])
        hg, gout = s.sb("hg", [96, L]), s.sb("gout", [P, 2, L])
        ps, pg = s.ps("ps", [P, 2, 512]), s.ps("pg", [P, 2, 2, 512])
        loaded, scaled, squared, summed, clamped = (s.sem("loaded"), s.sem("scaled"), s.sem("squared"),
                                                    s.sem("summed"), s.sem("clamped"))
        rooted, keys_done, lora_done, chain_sem = s.sem("rooted"), s.sem("keys"), s.sem("lora"), s.sem("chain")
        g_ready, g_done, g_copied = s.sem("g_ready"), s.sem("g_done"), s.sem("g_copied")
        g_stored = s.slots("g_stored")
        with nc.Block() as block:
            @block.sync
            def _(sp):
                with nc.allow_non_contiguous_dma("a vector into columns"):
                    sp.dma_start(kvec[:], k_k.rearrange("(k p) -> p k", p=P)).then_inc(loaded, 16)
                sp.dma_start(g2[:], gate_g2).then_inc(loaded, 16)
                for m in range(4):
                    sp.wait_ge(g_copied, m + 1)
                    sp.dma_start(g_dram[m * P:(m + 1) * P, :], gout[:, m % 2]).then_inc(g_stored[m % 2], 16)
                for b in range(2):
                    sp.wait_ge(g_stored[b], 32)

            @block.scalar
            def _(act):
                nc.scalar.activation(hg[0:64, :], lora_a[64:128, 0:L], ACT.Sigmoid)
                nc.scalar.activation(hg[64:96, :], lora_b[0:32, 0:L], ACT.Sigmoid).then_inc(g_ready, 1)
                nc.scalar.activation(lora_in[0:32, :], lora_a[0:32, :], ACT.Tanh).then_inc(lora_done, 1)
                for q, (m, t0, n) in enumerate(units):
                    act.wait_ge(scaled, q + 1)
                    if q >= 2:
                        act.wait_ge(summed, q - 1)
                    nc.scalar.activation(sq[:, q % 2, 0:n], kk[:, m, t0:t0 + n], ACT.Square).then_inc(squared, 1)
                    act.wait_ge(clamped, q + 1)
                    nc.scalar.activation(rs[:, q % 2, 0:n], rs[:, q % 2, 0:n], ACT.Sqrt).then_inc(rooted, 1)
                for m in range(4):
                    act.wait_ge(g_done, m + 1)
                    if m >= 2:
                        act.wait_ge(g_stored[m % 2], 16)
                    nc.scalar.activation(gout[:, m % 2], pg[:, m % 2].rearrange("p c t -> p (c t)"), ACT.Copy
                                         ).then_inc(g_copied, 1)

            @block.tensor
            def _(pe):
                for q, (m, t0, n) in enumerate(units):
                    pe.wait_ge(squared, q + 1)
                    nc.tensor.matmul(ps[:, q % 2, 0:n], ones64, sq[:, q % 2, 0:n], start=True, stop=True
                                     ).then_inc(summed, 1)
                pe.wait_ge(g_ready, 1)
                pe.wait_ge(loaded, 32)
                for m in range(4):
                    if m >= 2:
                        pe.wait_ge(g_copied, m - 1)
                    for c in range(2):
                        mm = nc.tensor.matmul(pg[:, m % 2, c], g2[:, m * P:(m + 1) * P], hg[:, c * 512:(c + 1) * 512],
                                              start=True, stop=True)
                    mm.then_inc(g_done, 1)

            @block.vector
            def _(dve):
                chain = Chain(dve, chain_sem)
                nc.vector.tensor_copy(lora_in[32:64, :], lora_a[32:64, :])
                nc.vector.memset(lora_in[64:65, :], 1.0)
                dve.wait_ge(loaded, 32)
                for q, (m, t0, n) in enumerate(units):
                    nc.vector.tensor_scalar(kk[:, m, t0:t0 + n], rkv[:, 4 + m, t0:t0 + n], kvec[:, m:m + 1], None,
                                            ALU.mult).then_inc(scaled, 1)
                    dve.wait_ge(summed, q + 1)
                    nc.vector.tensor_scalar(rs[:, q % 2, 0:n], ps[:, q % 2, 0:n], 1e-24, None, ALU.max
                                            ).then_inc(clamped, 1)
                    dve.wait_ge(rooted, q + 1)
                    chain(nc.vector.reciprocal(rs[:, q % 2, 0:n], rs[:, q % 2, 0:n]))
                    nc.vector.tensor_tensor(kk[:, m, t0:t0 + n], kk[:, m, t0:t0 + n], rs[:, q % 2, 0:n], ALU.mult
                                            ).then_inc(keys_done, 1)


class Order:

    def __init__(self, names):
        self.names = names

    def at(self, i, *name):
        return i * len(self.names) + self.names.index(name) + 1

    def before(self, i):
        return i * len(self.names)


LEVELS = 6
RCH = 64
HALF_E = 0.5 * float(np.exp(-0.5))


def recurrence(nc, name, ident, masks, reset, lora_w, ka, rkv, kk, lora_in, S, y, turns, first_token, w):
    emit_y = y is not None
    cs = (0, 1)
    PE = Order([("z",)] + [e for c in cs for e in [("gb", c), ("gk", c), ("tb", c), ("tv", c), ("m0", c)] +
                           [(x, c, lv) for lv in range(1, LEVELS) for x in "tx"] +
                           [("rhs", c), ("u", c)] + [("y", c)] * emit_y + [("s", c)]])
    AC = Order([("tanh",), ("en",), ("exp",)] + [e for c in cs for e in [("tb", c), ("tv", c)] +
                                        [("t", c, lv) for lv in range(1, LEVELS)] + [("rhs", c), ("u", c)]])
    DV = Order([("cum",)] + [e for c in cs for e in [("kr", c), ("gb", c), ("gk", c), ("m0", c)] +
                             [("x", c, lv) for lv in range(1, LEVELS)] + [("y", c)] * emit_y + [("s", c)]])
    PO = Order([("ba",)] + [e for c in cs for e in [("bn", c), ("v", c)] + [("lv", c, lv) for lv in range(LEVELS)]])
    HALF = (slice(0, 64), slice(64, 128))
    dirs = (0, 1)
    with Stage(nc, name) as s:
        banks = [s.ps(f"ps{d}", [P, 4, 512]) for d in dirs]
        pe_done, act_done, dve_done, pool_done = (s.slots("pe"), s.slots("act"), s.slots("dve"), s.slots("pool"))
        dve_chain, pool_chain = s.slots("dve_chain"), s.sem("pool_chain")

        def tokens(i, d):
            return i * P + first_token if d == 0 else i * (-P) + ((turns - 1) * P + first_token)

        def col(d, c):
            return slice(RCH * c, RCH * c + RCH) if d == 0 else slice(RCH - RCH * c, 2 * RCH - RCH * c)

        def pairs(bank):
            return bank.rearrange("p (m i) -> p m i", i=P)

        with nc.Block() as block:
            @block.tensor
            def _(pe):
                with pe.Fori(0, turns) as i:
                    def done(d, ins):
                        ins.then_inc(pe_done[d], 1)

                    def products(d, bank, *terms):
                        for m in range(4):
                            for n, (left, right) in enumerate(terms):
                                mm = nc.tensor.matmul(banks[d][:, bank, m * P:(m + 1) * P], left[:, m], right[:, m],
                                                      start=(n == 0), stop=(n == len(terms) - 1))
                        return mm

                    def turned(d, bank, src):
                        for m in range(4):
                            tr = nc.tensor.transpose(banks[d][:, bank, m * P:(m + 1) * P], src[:, m], ident)
                        return tr

                    for d in dirs:
                        pe.wait_ge(dve_done[d], DV.before(i))
                        pe.wait_ge(act_done[d], AC.before(i))
                        for q in range(2):
                            for m in range(4):
                                mm = nc.tensor.matmul(banks[d][:, 2 + q, m * P:(m + 1) * P],
                                                      lora_w[0:65, d, q, m * P:(m + 1) * P],
                                                      lora_in[0:65, bass.ds(tokens(i, d), P)], start=True, stop=True)
                        done(d, mm)
                    for c in cs:
                        for d in dirs:
                            b = w[d]
                            pe.wait_ge(dve_done[d], DV.at(i, "kr", c))
                            pe.wait_ge(pool_done[d], PO.at(i, "bn", c))
                            if c:
                                pe.wait_ge(act_done[d], AC.at(i, "u", 0))
                            for q in range(2):
                                if q == 1:
                                    pe.wait_ge(act_done[d], AC.at(i, "tanh"))
                                    if c:
                                        pe.wait_ge(dve_done[d], DV.at(i, "s", 0))
                                for m in range(4):
                                    mm = nc.tensor.matmul(banks[d][:, 2 * q + m // 2, m % 2 * 256:m % 2 * 256 + 256],
                                                          b["bn"][:, q, m], b["kr"][:, m].rearrange("p q i -> p (q i)"),
                                                          start=True, stop=True)
                                done(d, mm)
                        for d in dirs:
                            b = w[d]
                            pe.wait_ge(dve_done[d], DV.at(i, "gb", c))
                            turned(d, 0, b["bn"][:, 0])
                            done(d, turned(d, 1, b["bn"][:, 1]))
                            pe.wait_ge(pool_done[d], PO.at(i, "v", c))
                            pe.wait_ge(dve_done[d], DV.at(i, "gk", c))
                            done(d, turned(d, 2, b["v"]))
                            pe.wait_ge(pool_done[d], PO.at(i, "lv", c, 0))
                            done(d, turned(d, 3, b["lv"][:, 0]))
                        for lv in range(1, LEVELS):
                            for d in dirs:
                                b = w[d]
                                pe.wait_ge(pool_done[d], PO.at(i, "lv", c, lv))
                                pe.wait_ge(dve_done[d], DV.at(i, "m0", c) if lv == 1 else DV.at(i, "x", c, lv - 1))
                                if lv == 1:
                                    pe.wait_ge(act_done[d], AC.at(i, "tv", c))
                                done(d, products(d, 0, (b["lv"][:, lv % 2], b["x"][:, 0])))
                            for d in dirs:
                                b = w[d]
                                pe.wait_ge(act_done[d], AC.at(i, "t", c, lv))
                                if lv < LEVELS - 1:
                                    products(d, 1, (b["x"][:, 1], b["t"]))
                                done(d, products(d, 2, (b["t"], b["x"][:, 1])))
                        for d in dirs:
                            b = w[d]
                            done(d, products(d, 0, (b["kr"][:, :, 0], S[:, d]), (b["an"][:, :, 0], b["tok"][:, 2])))
                        for d in dirs:
                            b = w[d]
                            pe.wait_ge(act_done[d], AC.at(i, "rhs", c))
                            pe.wait_ge(dve_done[d], DV.at(i, "x", c, LEVELS - 1))
                            done(d, products(d, 1, (b["x"][:, 1], b["t"])))
                        for d in dirs:
                            b = w[d]
                            pe.wait_ge(act_done[d], AC.at(i, "u", c))
                            u = b["x"][:, 0]
                            if emit_y:
                                done(d, products(d, 2, (S[:, d], b["kr"][:, :, 1]), (u, b["ab"][:, :, 1]),
                                                 (b["tok"][:, 2], b["an"][:, :, 1])))
                            done(d, products(d, 3, (b["tok"][:, 0], u), (b["tok"][:, 1], b["tok"][:, 2])))

            @block.scalar
            def _(act):
                with act.Fori(0, turns) as i:
                    for d in dirs:
                        b = w[d]
                        act.wait_ge(pe_done[d], PE.at(i, "z"))
                        nc.scalar.activation(b["lwa"], banks[d][:, 2:4].rearrange("p q (m t) -> p q m t", t=P),
                                             ACT.Tanh, scale=0.5).then_inc(act_done[d], 1)
                    for d in dirs:
                        b = w[d]
                        act.wait_ge(dve_done[d], DV.at(i, "cum"))
                        nc.scalar.activation(b["en"], b["e"][:, 0], ACT.Exp, scale=-1.0).then_inc(act_done[d], 1)
                        act.wait_ge(act_done[d], AC.at(i, "en"))
                        nc.scalar.activation(b["e"], b["e"], ACT.Exp).then_inc(act_done[d], 1)
                    for c in cs:
                        for d in dirs:
                            b = w[d]
                            act.wait_ge(pe_done[d], PE.at(i, "tb", c))
                            nc.scalar.activation(b["tok"][:, 0:2], banks[d][:, 0:2].rearrange(
                                "p q (m t) -> p q m t", t=P), ACT.Copy).then_inc(act_done[d], 1)
                            act.wait_ge(pe_done[d], PE.at(i, "tv", c))
                            nc.scalar.activation(b["tok"][:, 2], pairs(banks[d][:, 2]), ACT.Copy
                                                 ).then_inc(act_done[d], 1)
                        for lv in range(1, LEVELS):
                            for d in dirs:
                                act.wait_ge(pe_done[d], PE.at(i, "t", c, lv))
                                nc.scalar.activation(w[d]["t"], pairs(banks[d][:, 0]), ACT.Copy
                                                     ).then_inc(act_done[d], 1)
                        for d in dirs:
                            act.wait_ge(pe_done[d], PE.at(i, "rhs", c))
                            nc.scalar.activation(w[d]["t"], pairs(banks[d][:, 0]), ACT.Copy).then_inc(act_done[d], 1)
                        for d in dirs:
                            act.wait_ge(pe_done[d], PE.at(i, "u", c))
                            nc.scalar.activation(w[d]["x"][:, 0], pairs(banks[d][:, 1]), ACT.Copy, scale=-1.0
                                                 ).then_inc(act_done[d], 1)

            @block.vector
            def _(dve):
                with dve.Fori(0, turns) as i:
                    chains = [Chain(dve, dve_chain[d], i, 5) for d in dirs]
                    for d in dirs:
                        b = w[d]
                        dve.wait_ge(act_done[d], AC.at(i, "tanh"))
                        chains[d](nc.vector.tensor_scalar(b["lwa"][:, 0], b["lwa"][:, 0], -HALF_E, -HALF_E,
                                                          ALU.mult, ALU.add))
                        nc.vector.tensor_scalar(b["lwa"][:, 1], b["lwa"][:, 1], 0.5, 0.5, ALU.mult, ALU.add)
                        lw = b["lwa"][:, 0].rearrange("p m t -> p (m t)")
                        cum = b["e"][:, 0].rearrange("p m t -> p (m t)")
                        if d:
                            lw, cum = lw[:, ::-1], cum[:, ::-1]
                        chains[d](nc.vector.tensor_tensor_scan(cum, reset, lw, 0.0, ALU.mult, ALU.add))
                        nc.vector.tensor_tensor(b["e"][:, 1], b["e"][:, 0], b["lwa"][:, 0], ALU.subtract
                                                ).then_inc(dve_done[d], 1)
                    for c in cs:
                        for d in dirs:
                            b = w[d]
                            t = bass.ds(tokens(i, d) + col(d, c).start, RCH)
                            if c == 0:
                                dve.wait_ge(act_done[d], AC.at(i, "exp"))
                                chains[d](nc.vector.tensor_copy(b["end"], b["e"][:, 0, :, (RCH - 1 if d == 0 else 0)::RCH]))
                            for h in range(2):
                                nc.vector.tensor_tensor(b["kr"][HALF[h], :, 0, HALF[h]], kk[HALF[h], :, t],
                                                        b["e"][HALF[h], 1, :, col(d, c)], ALU.mult)
                                last = nc.vector.tensor_tensor(b["kr"][HALF[h], :, 1, HALF[h]],
                                                               rkv[HALF[h], 0:4, t],
                                                               b["e"][HALF[h], 0, :, col(d, c)], ALU.mult)
                            last.then_inc(dve_done[d], 1)
                        for d in dirs:
                            b = w[d]
                            for q, (x, to) in enumerate((("gb", "ab"), ("gk", "an"))):
                                dve.wait_ge(pe_done[d], PE.at(i, x, c))
                                nc.vector.tensor_tensor(
                                    b[to], banks[d][:, 2 * q:2 * q + 2].rearrange("p e (f q i) -> p (e f) (q i)", q=2, i=P),
                                    masks[:, d, 6:8].rearrange("p q i -> p (q i)").unsqueeze(1).to_broadcast([P, 4, 2 * P])
                                    , ALU.mult).then_inc(dve_done[d], 1)
                        for d in dirs:
                            b = w[d]
                            eye = ident.unsqueeze(1).to_broadcast([P, 4, P])
                            dve.wait_ge(pool_done[d], PO.at(i, "lv", c, 0))
                            nc.vector.scalar_tensor_tensor(b["x"][:, 1], b["lv"][:, 0], -1.0, eye, ALU.mult, ALU.add)
                            dve.wait_ge(pe_done[d], PE.at(i, "m0", c))
                            nc.vector.scalar_tensor_tensor(b["x"][:, 0], pairs(banks[d][:, 3]), -1.0, eye,
                                                           ALU.mult, ALU.add).then_inc(dve_done[d], 1)
                        for lv in range(1, LEVELS):
                            for d in dirs:
                                b = w[d]
                                dve.wait_ge(pe_done[d], PE.at(i, "x", c, lv))
                                q = 0 if lv < LEVELS - 1 else 1
                                nc.vector.tensor_tensor(
                                    b["x"][:, q:2].rearrange("p q m i -> p q (m i)"),
                                    b["x"][:, q:2].rearrange("p q m i -> p q (m i)"),
                                    banks[d][:, 1 + q:3], ALU.subtract).then_inc(dve_done[d], 1)
                        for d in dirs:
                            b = w[d]
                            t = bass.ds(tokens(i, d) + (col(d, c).start - first_token), RCH)
                            if emit_y:
                                dve.wait_ge(pe_done[d], PE.at(i, "y", c))
                                for h in range(2):
                                    out = y[HALF[h], :, t]
                                    last = nc.vector.tensor_tensor(out, out, pairs(banks[d][:, 2])[HALF[h], :, HALF[h]],
                                                                   ALU.add)
                                last.then_inc(dve_done[d], 1)
                            dve.wait_ge(pe_done[d], PE.at(i, "s", c))
                            chains[d](nc.vector.tensor_tensor(S[:, d], S[:, d], pairs(banks[d][:, 3]), ALU.add))
                            end = b["end"][:, :, (c if d == 0 else 1 - c)].unsqueeze(2).to_broadcast([P, 4, P])
                            nc.vector.tensor_tensor(S[:, d], S[:, d], end, ALU.mult).then_inc(dve_done[d], 1)
                    for x in chains:
                        x.close()

            @block.gpsimd
            def _(pool):
                with pool.Fori(0, turns) as i:
                    chain = Chain(pool, pool_chain, i, 22)

                    def event(d, ins, *name):
                        ins.then_inc(pool_done[d], 1)
                        pool.wait_ge(pool_done[d], PO.at(i, *name))

                    for d in dirs:
                        b = w[d]
                        t = bass.ds(tokens(i, d), P)
                        ba, kn = b["lwa"][:, 0], b["lwa"][:, 1]
                        pool.wait_ge(dve_done[d], DV.at(i, "cum"))
                        chain(nc.gpsimd.tensor_tensor(ba, kk[:, :, t], kn, ALU.mult))
                        chain(nc.gpsimd.tensor_tensor(kn, kn, ka[:, 0].unsqueeze(2).to_broadcast([P, 4, P]), ALU.mult))
                        chain(nc.gpsimd.tensor_tensor(kn, kn, ka[:, 1].unsqueeze(2).to_broadcast([P, 4, P]), ALU.add))
                        event(d, nc.gpsimd.tensor_tensor(kn, kn, rkv[:, 4:8, t], ALU.mult), "ba")
                    for c in cs:
                        for d in dirs:
                            b = w[d]
                            t = bass.ds(tokens(i, d) + col(d, c).start, RCH)
                            if c == 0:
                                pool.wait_ge(act_done[d], AC.at(i, "exp"))
                            else:
                                pool.wait_ge(pe_done[d], PE.at(i, "tv", 0))
                            for h, q in ((0, 0), (0, 1), (1, 0), (1, 1)):
                                ins = nc.gpsimd.tensor_tensor(b["bn"][HALF[h], q, :, HALF[h]],
                                                              b["lwa"][HALF[h], q, :, col(d, c)],
                                                              b["en"][HALF[h], :, col(d, c)], ALU.mult)
                                if h + q < 2:
                                    chain(ins)
                            event(d, ins, "bn", c)
                            for h in range(2):
                                ins = nc.gpsimd.tensor_copy(b["v"][HALF[h], :, HALF[h]], rkv[HALF[h], 8:12, t])
                                if h == 0:
                                    chain(ins)
                            event(d, ins, "v", c)
                        for lv in range(LEVELS):
                            for d in dirs:
                                b = w[d]
                                if lv == 0:
                                    pool.wait_ge(dve_done[d], DV.at(i, "gb", c))
                                elif lv == 2:
                                    pool.wait_ge(dve_done[d], DV.at(i, "m0", c))
                                elif lv > 2:
                                    pool.wait_ge(pe_done[d], PE.at(i, "t", c, lv - 2))
                                nc.gpsimd.tensor_tensor(b["lv"][:, lv % 2], b["ab"][:, :, 0],
                                                        masks[:, d, lv].unsqueeze(1).to_broadcast([P, 4, P]), ALU.mult
                                                        ).then_inc(pool_done[d], 1)
                        for d in dirs:
                            pool.wait_ge(pool_done[d], PO.at(i, "lv", c, LEVELS - 1))
                    chain.close()


def run_recurrences(nc, name, cst, ident, rkv, kk, lora_in, decay_w0, decay_w2, iclr_a0, iclr_a2, k_a, y):
    with Stage(nc, name) as s:
        masks = s.sb("masks", [P, 2, 8, P], mybir.dt.bfloat16)
        reset = s.sb("reset", [P, 512], mybir.dt.bfloat16)
        lora_w = s.sb("lora_w", [65, 2, 2, 512])
        ka = s.sb("ka", [P, 2, 4])
        S = s.sb("S", [P, 2, 4, P])
        w = []
        for d in range(2):
            t = {n: s.sb(f"{n}{d}", [P, *shape]) for n, shape in dict(
                lwa=[2, 4, P], e=[2, 4, P], en=[4, P], end=[4, 2], kr=[4, 2, P], bn=[2, 4, P], v=[4, P],
                ab=[4, 2, P], an=[4, 2, P], tok=[3, 4, P], lv=[2, 4, P], x=[2, 4, P], t=[4, P]).items()}
            w.append({n: x[:] for n, x in t.items()})
        with Stage(nc, name + "_init") as s2:
            masks32 = w[0]["ab"].rearrange("p m q i -> p (m q i)")[:, 0:512].rearrange("p (l i) -> p l i", i=64)
            ka_loaded, lora_loaded, mask_loaded = s2.sem("ka"), s2.sem("lora"), s2.slots("mask")
            zeroed, started = s2.sem("zeroed"), s2.sem("started")
            mask_read = s2.sem("mask_read")
            with nc.Block() as block:
                @block.gpsimd
                def _(pool):
                    nc.gpsimd.memset(lora_w[:], 0.0).then_inc(started, 1)
                    nc.gpsimd.memset(masks[:], 0.0).then_inc(started, 1)

                @block.sync
                def _(sp):
                    with nc.allow_non_contiguous_dma("a vector into columns"):
                        sp.dma_start(ka[:, 0], k_a.rearrange("(k p) -> p k", p=P)).then_inc(ka_loaded, 16)
                    sp.wait_ge(started, 2)
                    for d in range(2):
                        sp.dma_start(lora_w[0:32, d, 0], decay_w2[d]).then_inc(lora_loaded, 16)
                        sp.dma_start(lora_w[32:64, d, 1], iclr_a2[d]).then_inc(lora_loaded, 16)
                        sp.dma_start(lora_w[64:65, d, 0], decay_w0[d:d + 1]).then_inc(lora_loaded, 16)
                        sp.dma_start(lora_w[64:65, d, 1], iclr_a0[d:d + 1]).then_inc(lora_loaded, 16)
                    for d in range(2):
                        sp.wait_ge(mask_read, d)
                        sp.dma_start(masks32, cst["masks"][:, d]).then_inc(mask_loaded[d], 16)
                    sp.wait_ge(lora_loaded, 128)

                @block.vector
                def _(dve):
                    nc.vector.memset(reset[:], 1.0).then_inc(zeroed, 1)
                    dve.wait_ge(zeroed, 1)
                    nc.vector.memset(reset[:].rearrange("p (a t) -> p a t", t=RCH)[:, :, 0:1], 0.0)
                    nc.vector.memset(S[:], 0.0)
                    nc.vector.memset(y[:], 0.0)
                    for b in w:
                        for n in ("kr", "bn", "v"):
                            nc.vector.memset(b[n], 0.0)
                    dve.wait_ge(ka_loaded, 16)
                    nc.vector.tensor_scalar(ka[:, 1], ka[:, 0], -1.0, 1.0, ALU.mult, ALU.add)
                    dve.wait_ge(started, 2)
                    for d in range(2):
                        dve.wait_ge(mask_loaded[d], 16)
                        for h in range(2):
                            r = slice(64 * h, 64 * h + 64)
                            last = nc.vector.tensor_copy(masks[r, d, :, r], masks32[r])
                        last.then_inc(mask_read, 1)
        args = (ident, masks, reset[:], lora_w, ka, rkv, kk, lora_in, S)
        recurrence(nc, name + "_ctx", *args, None, C // P, L, w)
        recurrence(nc, name + "_lat", *args, y, L // P, 0, w)



def recurrence_outputs(nc, name, ones64, rkv, lora_in, iclr_a0, iclr_a2, k_a, r_k, lnx_w, lnx_b, g_dram, y, yr):
    units = [(m, c) for m in range(4) for c in range(2)]
    LNX_EPS = 1e-5 * 64
    with Stage(nc, name) as s:
        vec = s.sb("vec", [P, 6, 4])
        lora_w = s.sb("lora_w", [65, 2, 512])
        g = s.sb("g", [P, 2, 512])
        yc, sq, bon = s.sb("yc", [P, 2, 512]), s.sb("sq", [P, 2, 512]), s.sb("bon", [P, 2, 512])
        th, rs, yn = s.sb("th", [P, 2, 2, 512]), s.sb("rs", [P, 2, 512]), s.sb("yn", [P, 2, 512])
        pm, pv, pb, pa = s.ps("pm", [P, 512]), s.ps("pv", [P, 512]), s.ps("pb", [P, 512]), s.ps("pa", [P, 2, 512])
        loaded, zeroed, g_loaded, vec_done = s.sem("loaded"), s.sem("zeroed"), s.slots("g_loaded"), s.sem("vec")
        a_done, mean_done, var_done, bon_sum = s.sem("a"), s.sem("mean"), s.sem("var"), s.sem("bon_sum")
        tanh_done, squared, rooted, scaled = s.sem("tanh"), s.sem("squared"), s.sem("rooted"), s.sem("scaled")
        centred, bon_done, eps_done, yn_done, done = (s.sem("centred"), s.sem("bon"), s.sem("eps"), s.sem("yn"),
                                                      s.sem("done"))
        chain_sem = s.sem("chain")
        with nc.Block() as block:
            @block.gpsimd
            def _(pool):
                nc.gpsimd.memset(lora_w[:], 0.0).then_inc(zeroed, 1)

            @block.sync
            def _(sp):
                with nc.allow_non_contiguous_dma("vectors into columns"):
                    for j, v in enumerate((k_a, r_k.rearrange("h k -> (h k)"), lnx_w, lnx_b)):
                        sp.dma_start(vec[:, j], v.rearrange("(k p) -> p k", p=P)).then_inc(loaded, 16)
                sp.wait_ge(zeroed, 1)
                for d in range(2):
                    sp.dma_start(lora_w[32:64, d], iclr_a2[d]).then_inc(loaded, 16)
                    sp.dma_start(lora_w[64:65, d], iclr_a0[d:d + 1]).then_inc(loaded, 16)
                for q, (m, c) in enumerate(units):
                    if q >= 2:
                        sp.wait_ge(done, q - 1)
                    sp.dma_start(g[:, q % 2], g_dram[m * P:(m + 1) * P, c * 512:(c + 1) * 512]
                                 ).then_inc(g_loaded[q % 2], 16)

            @block.tensor
            def _(pe):
                pe.wait_ge(loaded, 128)
                for q, (m, c) in enumerate(units):
                    t = slice(c * 512, (c + 1) * 512)
                    if q:
                        pe.wait_ge(tanh_done, q)
                        pe.wait_ge(done, q)
                    for d in range(2):
                        mm = nc.tensor.matmul(pa[:, d], lora_w[0:65, d, m * P:(m + 1) * P], lora_in[0:65, t],
                                              start=True, stop=True)
                    mm.then_inc(a_done, 1)
                    nc.tensor.matmul(pm[:], ones64, y[:, m, t], start=True, stop=True).then_inc(mean_done, 1)
                    pe.wait_ge(squared, q + 1)
                    nc.tensor.matmul(pv[:], ones64, sq[:, q % 2], start=True, stop=True).then_inc(var_done, 1)
                    pe.wait_ge(bon_done, q + 1)
                    nc.tensor.matmul(pb[:], ones64, bon[:, q % 2], start=True, stop=True).then_inc(bon_sum, 1)

            @block.scalar
            def _(act):
                act.wait_ge(loaded, 128)
                for q, (m, c) in enumerate(units):
                    act.wait_ge(a_done, q + 1)
                    if q >= 2:
                        act.wait_ge(done, q - 1)
                    nc.scalar.activation(th[:, q % 2], pa[:], ACT.Tanh, scale=0.5).then_inc(tanh_done, 1)
                    act.wait_ge(centred, q + 1)
                    nc.scalar.activation(sq[:, q % 2], yc[:, q % 2], ACT.Square).then_inc(squared, 1)
                    act.wait_ge(eps_done, q + 1)
                    nc.scalar.activation(rs[:, q % 2], rs[:, q % 2], ACT.Sqrt).then_inc(rooted, 1)
                    act.wait_ge(yn_done, q + 1)
                    nc.scalar.activation(yn[:, q % 2], yn[:, q % 2], ACT.Identity, scale=vec[:, 2, m:m + 1],
                                         bias=vec[:, 3, m:m + 1]).then_inc(scaled, 1)

            @block.vector
            def _(dve):
                chain = Chain(dve, chain_sem)
                dve.wait_ge(loaded, 128)
                nc.vector.tensor_scalar(vec[:, 4], vec[:, 0], 0.5, None, ALU.mult).then_inc(vec_done, 1)
                nc.vector.tensor_scalar(vec[:, 5], vec[:, 0], -1.0, 2.0, ALU.mult, ALU.add).then_inc(vec_done, 1)
                dve.wait_ge(vec_done, 2)
                for q, (m, c) in enumerate(units):
                    p, t = q % 2, slice(c * 512, (c + 1) * 512)
                    dve.wait_ge(mean_done, q + 1)
                    nc.vector.scalar_tensor_tensor(yc[:, p], pm[:], -1.0 / HD, y[:, m, t], ALU.mult, ALU.add
                                                   ).then_inc(centred, 1)
                    dve.wait_ge(tanh_done, q + 1)
                    chain(nc.vector.tensor_tensor(th[:, p, 0], th[:, p, 0], th[:, p, 1], ALU.add))
                    chain(nc.vector.tensor_scalar(th[:, p, 0], th[:, p, 0], vec[:, 4, m:m + 1], vec[:, 5, m:m + 1],
                                                  ALU.mult, ALU.add))
                    chain(nc.vector.tensor_tensor(th[:, p, 0], th[:, p, 0], rkv[:, 4 + m, t], ALU.mult))
                    nc.vector.scalar_tensor_tensor(bon[:, p], th[:, p, 0], vec[:, 1, m:m + 1], rkv[:, m, t],
                                                   ALU.mult, ALU.mult).then_inc(bon_done, 1)
                    dve.wait_ge(var_done, q + 1)
                    nc.vector.tensor_scalar(rs[:, p], pv[:], 1.0 / HD, LNX_EPS, ALU.mult, ALU.add
                                            ).then_inc(eps_done, 1)
                    dve.wait_ge(rooted, q + 1)
                    chain(nc.vector.reciprocal(rs[:, p], rs[:, p]))
                    nc.vector.tensor_tensor(yn[:, p], yc[:, p], rs[:, p], ALU.mult).then_inc(yn_done, 1)
                    dve.wait_ge(bon_sum, q + 1)
                    chain(nc.vector.tensor_tensor(bon[:, p], pb[:], rkv[:, 8 + m, t], ALU.mult))
                    dve.wait_ge(scaled, q + 1)
                    chain(nc.vector.tensor_tensor(yn[:, p], yn[:, p], bon[:, p], ALU.add))
                    dve.wait_ge(g_loaded[p], 16 * (q // 2 + 1))
                    nc.vector.tensor_tensor(yr[:, m, t], yn[:, p], g[:, p], ALU.mult).then_inc(done, 1)



def project(nc, name, source, tiles, kt, rhs, spans, read_out, follow=None):
    with Stage(nc, name) as s:
        w = s.sb("w", [P, 2, kt, P])
        ps = s.ps("ps", [P, 2, len(spans), 512])
        w_full, ps_full, ps_free = s.slots("w_full"), s.slots("ps_full"), s.slots("ps_free")
        with nc.Block() as block:
            @block.sync
            def _(sp):
                load_weights(sp, tiles // 2, source, w, w_full, ps_full, len(spans))

            @block.tensor
            def _(pe):
                multiply_tiles(nc, pe, tiles // 2, w, rhs, kt, spans, ps, w_full, ps_free, ps_full)

            @block.vector
            def _(dve):
                with dve.Fori(0, tiles // 2) as i:
                    for b in range(2):
                        dve.wait_ge(ps_full[b], i * len(spans) + len(spans))
                        read_out(i * 2 + b, ps[:, b]).then_inc(ps_free[b], 1)

            if follow is not None:
                @block.scalar
                def _(act):
                    with act.Fori(0, tiles // 2) as i:
                        for b in range(2):
                            act.wait_ge(ps_free[b], i + 1)
                            follow(i * 2 + b)


def columns_of(w, kt=None):
    return lambda m: by_tiles(w)[:, :, bass.ds(m * P, P)]


def flat(ap):
    return ap.rearrange("p a t -> p (a t)")


def add_gated(nc, x, gate, tokens):
    def read_out(m, banks):
        own = flat(x[:, bass.ds(m, 1), 0:tokens])
        return nc.vector.scalar_tensor_tensor(own, flat(banks)[:, 0:tokens], gate[:, bass.ds(m, 1)], own,
                                              ALU.mult, ALU.add)
    return read_out


def merge_branches(nc, name, ya, yr, w_attn, w_rwkv, gates_dram, out):
    with Stage(nc, name) as s:
        w = s.sb("w", [P, 2, 2, 4, P])
        g = s.sb("g", [P, 2, 2, L])
        part = s.sb("part", [P, 2, L])
        ps = s.ps("ps", [P, 2, 2, 2, 512])
        w_full, g_full, ps_full, read, added = (s.slots("w_full"), s.slots("g_full"), s.slots("ps_full"),
                                                s.slots("read"), s.slots("added"))
        with nc.Block() as block:
            @block.sync
            def _(sp):
                with sp.Fori(0, KT // 2) as i:
                    for b in range(2):
                        m = i * 2 + b
                        sp.wait_ge(ps_full[b], i)
                        for j, mat in enumerate((w_attn, w_rwkv)):
                            sp.dma_start(w[:, b, j], by_tiles(mat)[:, :, bass.ds(m * P, P)]).then_inc(w_full[b], 16)
                        sp.wait_ge(read[b], i * 2)
                        for j in range(2):
                            sp.dma_start(g[:, b, j], gates_dram[bass.ds(m * P + j * D, P), :]).then_inc(g_full[b], 16)

            @block.tensor
            def _(pe):
                with pe.Fori(0, KT // 2) as i:
                    for b in range(2):
                        pe.wait_ge(w_full[b], i * 32 + 32)
                        pe.wait_ge(read[b], i * 2)
                        for j, rhs in enumerate((ya, yr)):
                            for c, (t0, n) in enumerate(LAT):
                                for k in range(4):
                                    mm = nc.tensor.matmul(ps[:, b, j, c], w[:, b, j, k], rhs[:, k, t0:t0 + n],
                                                          start=(k == 0), stop=(k == 3))
                        mm.then_inc(ps_full[b], 1)

            @block.vector
            def _(dve):
                with dve.Fori(0, KT // 2) as i:
                    for b in range(2):
                        own = flat(out[:, bass.ds(i * 2 + b, 1)])
                        dve.wait_ge(ps_full[b], i + 1)
                        dve.wait_ge(g_full[b], i * 32 + 32)
                        dve.wait_ge(added[b], i)
                        nc.vector.tensor_tensor(own, flat(ps[:, b, 0]), g[:, b, 0], ALU.mult).then_inc(read[b], 1)
                        nc.vector.tensor_tensor(part[:, b], flat(ps[:, b, 1]), g[:, b, 1], ALU.mult
                                                ).then_inc(read[b], 1)

            @block.gpsimd
            def _(pool):
                with pool.Fori(0, KT // 2) as i:
                    for b in range(2):
                        own = flat(out[:, bass.ds(i * 2 + b, 1)])
                        pool.wait_ge(read[b], i * 2 + 2)
                        nc.gpsimd.tensor_tensor(own, own, part[:, b], ALU.add).then_inc(added[b], 1)


def mlp(nc, name, hT, w_up, w_down, xT, gate):
    F = 4 * D
    for c, (t0, n) in enumerate(LAT):
        with ExitStack() as stack:
            hid = stack.enter_context(nc.sbuf_tensor(f"{name}_hid{c}", [P, F // P, n], F32))

            def relu(m, banks):
                return nc.vector.tensor_scalar(flat(hid[:, bass.ds(m, 1)]), flat(banks), 0.0, None, ALU.max)

            def square(m):
                own = flat(hid[:, bass.ds(m, 1)])
                return nc.scalar.activation(own, own, ACT.Square)

            project(nc, f"{name}_up{c}", columns_of(w_up), F // P, KT, hT[:, :, t0:t0 + n], [(0, n)], relu, square)
            project(nc, f"{name}_down{c}", columns_of(w_down), KT, F // P, hid, [(0, n)],
                    add_gated(nc, xT[:, :, t0:t0 + n], gate, n))



SGU_W, FNET_W, Q_LORA, KV_LORA, ROPE_W = 256, 256, 256, 128, 64
NOPE, VD, MH = 128, 128, 4
QK = NOPE + ROPE_W
MIX_F, MIX_Q = 512, 768


def project_mixers(nc, name, ones, hT, w_in, tokens, uT, vn, fT, pq, kv, kr):
    spans = [x for x in CHUNKS if x[0] < tokens]
    rows = tokens // P
    TILES = [(0, spans, uT[:, 0], ACT.Gelu_apprx_tanh), (P, spans, uT[:, 1], ACT.Gelu_apprx_tanh),
             (MIX_F, spans, fT[:, 0], ACT.Copy), (MIX_F + P, spans, fT[:, 1], ACT.Copy),
             (MIX_Q, spans, pq[:, 0], ACT.Copy), (MIX_Q + P, spans, pq[:, 1], ACT.Copy),
             (MIX_Q + Q_LORA, CHUNKS, kv, ACT.Copy), (MIX_Q + Q_LORA + KV_LORA, CHUNKS, kr, ACT.Copy)]
    with Stage(nc, name) as s:
        w = s.sb("w", [P, 2, KT, P])
        wv = s.sb("wv", [P, KT, SGU_W])
        sq = s.sb("sq", [P, 2, SGU_W])
        ss = s.sb("ss", [P, rows])
        ps, pv = s.ps("ps", [P, 2, 3, 512]), s.ps("pv", [P, 2, 512])
        w_full, v_loaded, mul_done, read = s.slots("w_full"), s.sem("v_loaded"), s.sem("mul"), s.sem("read")
        v_done, v_read, sums, eps_done, rooted, inv_done = (s.sem("v_done"), s.sem("v_read"), s.sem("sums"),
                                                            s.sem("eps"), s.sem("rooted"), s.sem("inv"))
        with nc.Block() as block:
            @block.sync
            def _(sp):
                for m, (c0, _, _, _) in enumerate(TILES):
                    if m >= 2:
                        sp.wait_ge(mul_done, m - 1)
                    if m < 7:
                        sp.dma_start(w[:, m % 2], by_tiles(w_in)[:, :, c0:c0 + P]).then_inc(w_full[m % 2], 16)
                    else:
                        for h in range(2):
                            sp.dma_start(w[:, m % 2, :, h * 64:h * 64 + 64], by_tiles(w_in)[:, :, c0:c0 + 64]
                                         ).then_inc(w_full[m % 2], 16)
                sp.dma_start(wv[:], by_tiles(w_in)[:, :, SGU_W:2 * SGU_W]).then_inc(v_loaded, 16)

            @block.tensor
            def _(pe):
                for m, (_, spn, _, _) in enumerate(TILES):
                    pe.wait_ge(w_full[m % 2], 16 * (m // 2 + 1) + (16 if m == 7 else 0))
                    if m >= 2:
                        pe.wait_ge(read, m - 1)
                    for c, (t0, n) in enumerate(spn):
                        for k in range(KT):
                            mm = nc.tensor.matmul(ps[:, m % 2, c, 0:n], w[:, m % 2, k], hT[:, k, t0:t0 + n],
                                                  start=(k == 0), stop=(k == KT - 1))
                    mm.then_inc(mul_done, 1)
                pe.wait_ge(v_loaded, 16)
                for t in range(rows):
                    if t >= 2:
                        pe.wait_ge(v_read, t - 1)
                    for k in range(KT):
                        mm = nc.tensor.matmul(pv[:, t % 2, 0:SGU_W], hT[:, k, t * P:(t + 1) * P], wv[:, k],
                                              start=(k == 0), stop=(k == KT - 1))
                    mm.then_inc(v_done, 1)

            @block.scalar
            def _(act):
                for m, (_, spn, dst, func) in enumerate(TILES):
                    act.wait_ge(mul_done, m + 1)
                    n = spn[-1][0] + spn[-1][1]
                    nc.scalar.activation(dst[:, 0:n], ps[:, m % 2].rearrange("p c t -> p (c t)")[:, 0:n], func
                                         ).then_inc(read, 1)
                for t in range(rows):
                    act.wait_ge(v_done, t + 1)
                    nc.scalar.activation(vn[:, t], pv[:, t % 2, 0:SGU_W], ACT.Gelu_apprx_tanh).then_inc(v_read, 1)
                for t in range(rows):
                    if t >= 2:
                        act.wait_ge(sums, t - 1)
                    else:
                        act.wait_ge(v_read, t + 1)
                    act.wait_ge(v_read, rows)
                    nc.scalar.activation(sq[:, t % 2], vn[:, t], ACT.Square, accum_out=ss[:, t:t + 1]
                                         ).then_inc(sums, 1)
                act.wait_ge(eps_done, 1)
                nc.scalar.activation(ss[:], ss[:], ACT.Sqrt).then_inc(rooted, 1)

            @block.vector
            def _(dve):
                dve.wait_ge(sums, rows)
                nc.vector.tensor_scalar(ss[:], ss[:], 1.0 / SGU_W, EPS, ALU.mult, ALU.add).then_inc(eps_done, 1)
                dve.wait_ge(rooted, 1)
                nc.vector.reciprocal(ss[:], ss[:]).then_inc(inv_done, 1)
                dve.wait_ge(inv_done, 1)
                for t in range(rows):
                    nc.vector.tensor_scalar(vn[:, t], vn[:, t], ss[:, t:t + 1], None, ALU.mult)


def gate_tokens(nc, name, ident, uT, vn, sgu_norm, w_sgu, b_sgu, tokens, mixT):
    rows = tokens // P
    with Stage(nc, name) as s:
        wr, wT = s.sb("wr", [P, 4, P]), s.sb("wT", [P, 4, P])
        norm, bias = s.sb("norm", [P, 2]), s.sb("bias", [P, 2, P])
        z = s.sb("z", [P, 2, 2, P])
        pT, pz = s.ps("pT", [P, 4, P]), s.ps("pz", [P, 2, 512])
        loaded, turned, copied, mixed, z_done, done = (s.sem("loaded"), s.sem("turned"), s.sem("copied"),
                                                       s.sem("mixed"), s.sem("z"), s.sem("done"))
        with nc.Block() as block:
            @block.sync
            def _(sp):
                sp.dma_start(wr[:], w_sgu.rearrange("h p q -> p h q")).then_inc(loaded, 16)
                with nc.allow_non_contiguous_dma("a vector into columns"):
                    sp.dma_start(norm[:], sgu_norm.rearrange("(k p) -> p k", p=P)).then_inc(loaded, 16)
                for h in range(4):
                    sp.dma_start(bias[h % 2 * 64:h % 2 * 64 + 64, h // 2], b_sgu[h].partition_broadcast(64)
                                 ).then_inc(loaded, 16)

            @block.tensor
            def _(pe):
                pe.wait_ge(loaded, 96)
                for h in range(4):
                    tr = nc.tensor.transpose(pT[:, h], wr[:, h], ident)
                tr.then_inc(turned, 1)
                pe.wait_ge(copied, 1)
                for t in range(rows):
                    if t >= 2:
                        pe.wait_ge(z_done, t - 1)
                    for h in range(4):
                        r = slice(h % 2 * 64, h % 2 * 64 + 64)
                        mm = nc.tensor.matmul(pz[r, t % 2, h // 2 * P:h // 2 * P + P], vn[:, t, h * 64:(h + 1) * 64],
                                              wT[:, h], start=True, stop=True)
                    mm.then_inc(mixed, 1)

            @block.scalar
            def _(act):
                act.wait_ge(turned, 1)
                nc.scalar.activation(wT[:], pT[:], ACT.Copy).then_inc(copied, 1)

            @block.vector
            def _(dve):
                dve.wait_ge(loaded, 96)
                for t in range(rows):
                    dve.wait_ge(mixed, t + 1)
                    for m in range(2):
                        last = nc.vector.scalar_tensor_tensor(z[:, t % 2, m], pz[:, t % 2, m * P:(m + 1) * P],
                                                              norm[:, m:m + 1], bias[:, m], ALU.mult, ALU.add)
                    last.then_inc(z_done, 1)
                    dve.wait_ge(z_done, t + 1)
                    nc.vector.tensor_tensor(mixT[:, 0:2, t * P:(t + 1) * P], z[:, t % 2],
                                            uT[:, :, t * P:(t + 1) * P], ALU.mult).then_inc(done, 1)


def fourier(nc, name, cst, fT, seqs, mixT):
    rows = sum(n for _, n, _ in seqs) // P
    steps = [(t0, n, sfx, t) for t0, n, sfx in seqs for t in range(n // P)]
    with Stage(nc, name) as s:
        d64 = s.sb("d64", [P, 2 * P])
        Z = s.sb("Z", [P, rows, 2, 2, P])
        dft = s.sb("dft", [P, 2, 2, L])
        pz, py = s.ps("pz", [P, 2, 512]), s.ps("py", [P, 4, 512])
        loaded, d_full = s.sem("loaded"), s.slots("d_full")
        z_done, z_read, used, y_read = s.sem("z_done"), s.sem("z_read"), s.sem("used"), s.sem("y_read")
        with nc.Block() as block:
            @block.sync
            def _(sp):
                sp.dma_start(d64[:], cst["dft64"]).then_inc(loaded, 16)
                for q, (_, n, sfx, t) in enumerate(steps):
                    if q >= 2:
                        sp.wait_ge(used, q - 1)
                    for j, x in enumerate(("dft_cos_", "dft_sin_")):
                        sp.dma_start(dft[:, q % 2, j, 0:n], cst[x + sfx][t * P:(t + 1) * P, :]
                                     ).then_inc(d_full[q % 2], 16)

            @block.tensor
            def _(pe):
                pe.wait_ge(loaded, 16)
                for t in range(rows):
                    if t >= 2:
                        pe.wait_ge(z_read, t - 1)
                    for m in range(2):
                        mm = nc.tensor.matmul(pz[:, t % 2, m * 2 * P:(m + 1) * 2 * P], fT[:, m, t * P:(t + 1) * P],
                                              d64[:], start=True, stop=True)
                    mm.then_inc(z_done, 1)
                pe.wait_ge(z_read, rows)
                for q, (t0, n, _, t) in enumerate(steps):
                    pe.wait_ge(d_full[q % 2], 32 * (q // 2 + 1))
                    if t == 0 and q:
                        pe.wait_ge(y_read, 1)
                    for m in range(2):
                        for c in range(0, n, 512):
                            for j in range(2):
                                w = min(512, n)
                                mm = nc.tensor.matmul(py[:, m * 2 + c // 512, 0:w], Z[:, t0 // P + t, m, j],
                                                      dft[:, q % 2, j, c:c + w], start=(t == 0 and j == 0),
                                                      stop=(t == n // P - 1 and j == 1))
                    mm.then_inc(used, 1)

            @block.scalar
            def _(act):
                for t in range(rows):
                    act.wait_ge(z_done, t + 1)
                    nc.scalar.activation(Z[:, t].rearrange("p m j c -> p (m j c)"), pz[:, t % 2], ACT.Copy
                                         ).then_inc(z_read, 1)

            @block.vector
            def _(dve):
                q = 0
                for t0, n, _ in seqs:
                    q += n // P
                    dve.wait_ge(used, q)
                    for m in range(2):
                        last = nc.vector.tensor_copy(
                            mixT[:, 2 + m, t0:t0 + n],
                            py[:, 2 * m:2 * m + 2].rearrange("p c t -> p (c t)")[:, 0:n])
                    last.then_inc(y_read, 1)



def latent_norm(nc, name, ones, x, tiles, width, vec, spans):
    units = [(t0, n) for t0, n in spans]
    with Stage(nc, name) as s:
        g = s.sb("g", [P, tiles])
        sq, rs = s.sb("sq", [P, tiles, 512]), s.sb("rs", [P, 512])
        ps = s.ps("ps", [P, 512])
        loaded, squared, summed, eps_done, rooted, done, chain_sem = (
            s.sem("loaded"), s.sem("squared"), s.sem("summed"), s.sem("eps"), s.sem("rooted"), s.sem("done"),
            s.sem("chain"))
        with nc.Block() as block:
            @block.sync
            def _(sp):
                with nc.allow_non_contiguous_dma("a vector into columns"):
                    sp.dma_start(g[:], vec.rearrange("(k p) -> p k", p=P)).then_inc(loaded, 16)

            @block.scalar
            def _(act):
                for q, (t0, n) in enumerate(units):
                    if q:
                        act.wait_ge(summed, q)
                    nc.scalar.activation(sq[:, :, 0:n], x[:, 0:tiles, t0:t0 + n], ACT.Square).then_inc(squared, 1)
                    act.wait_ge(eps_done, q + 1)
                    nc.scalar.activation(rs[:, 0:n], rs[:, 0:n], ACT.Sqrt).then_inc(rooted, 1)

            @block.tensor
            def _(pe):
                for q, (t0, n) in enumerate(units):
                    pe.wait_ge(squared, q + 1)
                    if q:
                        pe.wait_ge(eps_done, q)
                    for k in range(tiles):
                        mm = nc.tensor.matmul(ps[:, 0:n], ones, sq[:, k, 0:n], start=(k == 0), stop=(k == tiles - 1))
                    mm.then_inc(summed, 1)

            @block.vector
            def _(dve):
                chain = Chain(dve, chain_sem)
                dve.wait_ge(loaded, 16)
                for q, (t0, n) in enumerate(units):
                    dve.wait_ge(summed, q + 1)
                    if q:
                        dve.wait_ge(done, q)
                    nc.vector.tensor_scalar(rs[:, 0:n], ps[:, 0:n], 1.0 / width, EPS, ALU.mult, ALU.add
                                            ).then_inc(eps_done, 1)
                    dve.wait_ge(rooted, q + 1)
                    chain(nc.vector.reciprocal(rs[:, 0:n], rs[:, 0:n]))
                    for k in range(tiles):
                        own = x[:, k, t0:t0 + n]
                        last = nc.vector.scalar_tensor_tensor(own, own, g[:, k:k + 1], rs[:, 0:n], ALU.mult, ALU.mult)
                    last.then_inc(done, 1)


def heads_qk(nc, name, cst, ones, latent, kt, w_nope, w_rope, shared, norm, spans, nope, rope):
    units = [(t0, n) for t0, n in spans]
    W = 512
    with Stage(nc, name) as s:
        wn, wr = s.sb("wn", [P, kt, MH, P]), s.sb("wr", [P, kt, 2, P])
        g, gr = s.sb("g", [P, 1]), s.sb("gr", [P, 1])
        cos, sin, rot = s.sb("cos", [P, W]), s.sb("sin", [P, W]), s.sb("rot", [P, P])
        raw = s.sb("raw", [P, 2, W])
        sq, sqr = s.sb("sq", [P, MH, W]), s.sb("sqr", [P, 2, W])
        rs = s.sb("rs", [P, MH, W])
        pn, pr, psum = s.ps("pn", [P, MH, 512]), s.ps("pr", [P, 2, 512]), s.ps("psum", [P, 512])
        loaded, table_full = s.sem("loaded"), s.sem("table_full")
        nope_done, rope_done, copied, squared = s.sem("nope"), s.sem("rope"), s.sem("copied"), s.sem("squared")
        summed, eps_done, rooted, scaled, turned, done = (s.sem("summed"), s.sem("eps"), s.sem("rooted"),
                                                          s.sem("scaled"), s.sem("turned"), s.sem("done"))
        chain_sem = s.sem("chain")
        n_loads = 3 + MH + (4 if w_rope is not None else 0) + 1
        with nc.Block() as block:
            @block.sync
            def _(sp):
                sp.dma_start(rot[:], cst["rot2"]).then_inc(loaded, 16)
                with nc.allow_non_contiguous_dma("vectors into columns"):
                    sp.dma_start(g[:], norm[0:NOPE].rearrange("(p k) -> p k", k=1)).then_inc(loaded, 16)
                    for h in range(2):
                        sp.dma_start(gr[h * 64:h * 64 + 64], norm[NOPE:QK].rearrange("(p k) -> p k", k=1)
                                     ).then_inc(loaded, 16)
                for h in range(MH):
                    sp.dma_start(wn[:, :, h], w_nope(h)).then_inc(loaded, 16)
                if w_rope is not None:
                    for h in range(MH):
                        sp.dma_start(wr[:, :, h // 2, h % 2 * 64:h % 2 * 64 + 64], w_rope(h)).then_inc(loaded, 16)
                for q, (t0, n) in enumerate(units):
                    if t0 < L:
                        if q:
                            sp.wait_ge(done, q)
                        sp.dma_start(cos[:, 0:n], cst["cos2"][:, t0:t0 + n]).then_inc(table_full, 16)
                        sp.dma_start(sin[:, 0:n], cst["sin2"][:, t0:t0 + n]).then_inc(table_full, 16)

            @block.tensor
            def _(pe):
                pe.wait_ge(loaded, 16 * n_loads)
                for q, (t0, n) in enumerate(units):
                    if q:
                        pe.wait_ge(done, q)
                    for h in range(MH):
                        for k in range(kt):
                            mm = nc.tensor.matmul(pn[:, h, 0:n], wn[:, k, h], latent[:, k, t0:t0 + n],
                                                  start=(k == 0), stop=(k == kt - 1))
                    mm.then_inc(nope_done, 1)
                    if w_rope is not None:
                        for m in range(2):
                            for k in range(kt):
                                mm = nc.tensor.matmul(pr[:, m, 0:n], wr[:, k, m], latent[:, k, t0:t0 + n],
                                                      start=(k == 0), stop=(k == kt - 1))
                        mm.then_inc(rope_done, 1)
                    pe.wait_ge(squared, q + 1)
                    for h in range(MH):
                        if q or h:
                            pe.wait_ge(eps_done, q * MH + h)
                        r = slice(h % 2 * 64, h % 2 * 64 + 64)
                        nc.tensor.matmul(psum[:, 0:n], ones, sq[:, h, 0:n], start=True, stop=False)
                        nc.tensor.matmul(psum[:, 0:n], ones[r], sqr[r, h // 2, 0:n], start=False, stop=True
                                         ).then_inc(summed, 1)
                    if t0 < L:
                        pe.wait_ge(scaled, q + 1)
                        for m in range(2):
                            mm = nc.tensor.matmul(pr[:, m, 0:n], rot[:], raw[:, m, 0:n], start=True, stop=True)
                        mm.then_inc(turned, 1)

            @block.scalar
            def _(act):
                act.wait_ge(loaded, 16 * n_loads)
                for q, (t0, n) in enumerate(units):
                    if q:
                        act.wait_ge(done, q)
                    act.wait_ge(nope_done, q + 1)
                    nc.scalar.activation(sq[:, :, 0:n], pn[:, :, 0:n], ACT.Square)
                    if w_rope is not None:
                        act.wait_ge(rope_done, q + 1)
                        nc.scalar.activation(sqr[:, :, 0:n], pr[:, :, 0:n], ACT.Square).then_inc(squared, 1)
                        nc.scalar.activation(raw[:, :, 0:n], pr[:, :, 0:n], ACT.Copy, scale=gr[:, 0:1]
                                             ).then_inc(scaled, 1)
                    else:
                        for m in range(2):
                            sq_ins = nc.scalar.activation(sqr[:, m, 0:n], shared[:, t0:t0 + n], ACT.Square)
                            raw_ins = nc.scalar.activation(raw[:, m, 0:n], shared[:, t0:t0 + n], ACT.Copy,
                                                           scale=gr[:, 0:1])
                        sq_ins.then_inc(squared, 1)
                        raw_ins.then_inc(scaled, 1)
                    act.wait_ge(eps_done, (q + 1) * MH)
                    nc.scalar.activation(rs[:, :, 0:n], rs[:, :, 0:n], ACT.Sqrt).then_inc(rooted, 1)

            @block.vector
            def _(dve):
                chain = Chain(dve, chain_sem)
                dve.wait_ge(loaded, 16 * n_loads)
                tables = 0
                for q, (t0, n) in enumerate(units):
                    for h in range(MH):
                        dve.wait_ge(summed, q * MH + h + 1)
                        nc.vector.tensor_scalar(rs[:, h, 0:n], psum[:, 0:n], 1.0 / QK, EPS, ALU.mult, ALU.add
                                                ).then_inc(eps_done, 1)
                    dve.wait_ge(rooted, q + 1)
                    chain(nc.vector.reciprocal(rs[:, :, 0:n], rs[:, :, 0:n]))
                    for h in range(MH):
                        nc.vector.scalar_tensor_tensor(nope[:, h, t0:t0 + n], pn[:, h, 0:n], g[:, 0:1], rs[:, h, 0:n],
                                                       ALU.mult, ALU.mult)
                    dve.wait_ge(scaled, q + 1)
                    if t0 < L:
                        tables += 32
                        dve.wait_ge(table_full, tables)
                        dve.wait_ge(turned, q + 1)
                        both = lambda x: x[:, 0:n].unsqueeze(1).to_broadcast([P, 2, n])
                        chain(nc.vector.tensor_tensor(sqr[:, :, 0:n], pr[:, :, 0:n], both(sin), ALU.mult))
                        chain(nc.vector.tensor_tensor(raw[:, :, 0:n], raw[:, :, 0:n], both(cos), ALU.mult))
                        chain(nc.vector.tensor_tensor(raw[:, :, 0:n], raw[:, :, 0:n], sqr[:, :, 0:n], ALU.add))
                    for h in range(MH):
                        r = slice(h % 2 * 64, h % 2 * 64 + 64)
                        last = nc.vector.tensor_tensor(rope[r, h // 2, t0:t0 + n], raw[r, h // 2, 0:n], rs[r, h, 0:n],
                                                       ALU.mult)
                    last.then_inc(done, 1)


def values(nc, name, kv, w_ukv, v):
    with Stage(nc, name) as s:
        w = s.sb("w", [P, MH, VD])
        ps = s.ps("ps", [P, 2, 512])
        loaded, done, read = s.sem("loaded"), s.sem("done"), s.sem("read")
        with nc.Block() as block:
            @block.sync
            def _(sp):
                sp.dma_start(w[:], w_ukv.rearrange("p (h c) -> p h c", h=MH)[:, :, NOPE:]).then_inc(loaded, 16)

            @block.tensor
            def _(pe):
                pe.wait_ge(loaded, 16)
                for t in range(T // P):
                    if t >= 2:
                        pe.wait_ge(read, t - 1)
                    nc.tensor.matmul(ps[:, t % 2], kv[:, t * P:(t + 1) * P], w[:].rearrange("p h c -> p (h c)"),
                                     start=True, stop=True).then_inc(done, 1)

            @block.scalar
            def _(act):
                for t in range(T // P):
                    act.wait_ge(done, t + 1)
                    nc.scalar.activation(v[:, t], ps[:, t % 2], ACT.Copy).then_inc(read, 1)


def attend(nc, name, ident, q_nope, q_rope, k_nope, k_rope, v, q0, blocks, k0, mixT):
    NK = T - k0
    key_spans = [(c, min(512, NK - c)) for c in range(0, NK, 512)]
    nt = NK // P
    SPLIT = min(4, nt)
    TURNS, U = blocks // 2, 2 * MH
    SC = QK ** -0.5
    with Stage(nc, name) as s:
        qn, qr = s.sb("qn", [P, 2, MH, P]), s.sb("qr", [P, 2, 2, P])
        prob, probT = s.sb("prob", [P, 2, NK]), s.sb("probT", [P, nt, P])
        nmax, total, inv = s.sb("nmax", [P, 2]), s.sb("total", [P, 2]), s.sb("inv", [P, 2])
        out = s.sb("out", [P, 2, MH * VD])
        pS, pT = s.ps("pS", [P, 3 * 512]), s.ps("pT", [P, 12, P])
        pO, pY = s.ps("pO", [P, 512]), s.ps("pY", [P, MH, P])
        staged, turned_out = s.slots("staged"), s.slots("turned_out")
        s_full, max_done, sums, t_done = s.sem("s_full"), s.sem("max"), s.sem("sums"), s.sem("t_done")
        copied_a, copied_v, pv_done, o_done, y_copied = (s.sem("copied_a"), s.sem("copied_v"), s.sem("pv"),
                                                         s.sem("o"), s.sem("y_copied"))
        chain_sem = s.sem("chain")
        with nc.Block() as block:
            @block.gpsimd
            def _(pool):
                with pool.Fori(0, TURNS) as i:
                    for b in range(2):
                        t = bass.ds((i * 2 + b) * P + q0, P)
                        pool.wait_ge(turned_out[b], i)
                        nc.gpsimd.tensor_copy(qn[:, b], q_nope[:, :, t]).then_inc(staged[b], 1)
                        nc.gpsimd.tensor_copy(qr[:, b], q_rope[:, :, t]).then_inc(staged[b], 1)

            @block.tensor
            def _(pe):
                with pe.Fori(0, TURNS) as i:
                    def scores(u):
                        b, h = u // MH, u % MH
                        if h == 0:
                            pe.wait_ge(staged[b], i * 2 + 2)
                        pe.wait_ge(sums, i * U + u)
                        r = slice(h % 2 * 64, h % 2 * 64 + 64)
                        for c, n in key_spans:
                            k = slice(k0 + c, k0 + c + n)
                            nc.tensor.matmul(pS[:, c:c + n], qn[:, b, h], k_nope[:, h, k], start=True, stop=False)
                            mm = nc.tensor.matmul(pS[:, c:c + n], qr[r, b, h // 2], k_rope[r, h // 2, k],
                                                  start=False, stop=True)
                        mm.then_inc(s_full, 1)

                    def turn(u):
                        pe.wait_ge(sums, i * U + u + 1)
                        pe.wait_ge(copied_a, i * U + u)
                        pe.wait_ge(copied_v, i * U + u)
                        for j in range(nt):
                            tr = nc.tensor.transpose(pT[:, j], prob[:, u % 2, j * P:(j + 1) * P], ident)
                        tr.then_inc(t_done, 1)

                    def weigh(u):
                        h = u % MH
                        pe.wait_ge(copied_a, i * U + u + 1)
                        pe.wait_ge(copied_v, i * U + u + 1)
                        pe.wait_ge(o_done, i * U + u)
                        for j in range(nt):
                            mm = nc.tensor.matmul(pO[:, 0:VD], probT[:, j], v[:, k0 // P + j, h * VD:(h + 1) * VD],
                                                  start=(j == 0), stop=(j == nt - 1))
                        mm.then_inc(pv_done, 1)

                    def turn_out(b):
                        pe.wait_ge(o_done, i * U + (b + 1) * MH)
                        pe.wait_ge(y_copied, i * 2 + b)
                        for h in range(MH):
                            tr = nc.tensor.transpose(pY[:, h], out[:, b, h * VD:(h + 1) * VD], ident)
                        tr.then_inc(turned_out[b], 1)

                    for u in range(U):
                        scores(u)
                        if u:
                            weigh(u - 1)
                        if u == MH + 1:
                            turn_out(0)
                        turn(u)
                    weigh(U - 1)
                    turn_out(1)

            @block.scalar
            def _(act):
                with act.Fori(0, TURNS) as i:
                    for u in range(U):
                        p = u % 2
                        act.wait_ge(max_done, i * U + u + 1)
                        nc.scalar.activation(prob[:, p], pS[:, 0:NK], ACT.Exp, bias=nmax[:, p:p + 1], scale=SC,
                                             accum_out=total[:, p:p + 1]).then_inc(sums, 1)
                        act.wait_ge(t_done, i * U + u + 1)
                        act.wait_ge(pv_done, i * U + u)
                        if nt > SPLIT:
                            nc.scalar.activation(probT[:, SPLIT:nt], pT[:, SPLIT:nt], ACT.Copy).then_inc(copied_a, 1)
                        else:
                            nc.scalar.activation(nmax[:, p:p + 1], nmax[:, p:p + 1], ACT.Copy).then_inc(copied_a, 1)

            @block.vector
            def _(dve):
                with dve.Fori(0, TURNS) as i:
                    chain = Chain(dve, chain_sem, i, 2 * U)

                    def outputs(u):
                        b, h, p = u // MH, u % MH, u % 2
                        dve.wait_ge(pv_done, i * U + u + 1)
                        nc.vector.tensor_scalar(out[:, b, h * VD:(h + 1) * VD], pO[:, 0:VD], inv[:, p:p + 1], None,
                                                ALU.mult).then_inc(o_done, 1)

                    def copy_out(b):
                        dve.wait_ge(turned_out[b], i + 1)
                        nc.vector.tensor_copy(mixT[:, 4:8, bass.ds((i * 2 + b) * P + q0, P)], pY[:]
                                              ).then_inc(y_copied, 1)

                    for u in range(U):
                        p = u % 2
                        dve.wait_ge(s_full, i * U + u + 1)
                        chain(nc.vector.tensor_reduce(nmax[:, p:p + 1], pS[:, 0:NK], AX.X, ALU.max, negate=True))
                        nc.vector.tensor_scalar(nmax[:, p:p + 1], nmax[:, p:p + 1], SC, None, ALU.mult
                                                ).then_inc(max_done, 1)
                        if u:
                            outputs(u - 1)
                        if u == MH + 1:
                            copy_out(0)
                        dve.wait_ge(sums, i * U + u + 1)
                        chain(nc.vector.reciprocal(inv[:, p:p + 1], total[:, p:p + 1]))
                        dve.wait_ge(t_done, i * U + u + 1)
                        nc.vector.tensor_copy(probT[:, 0:SPLIT], pT[:, 0:SPLIT]).then_inc(copied_v, 1)
                    outputs(U - 1)
                    copy_out(1)
                    chain.close()



def col(mod, n, j=0):
    return mod[:, n * KT:(n + 1) * KT, j]


def first_mixers(nc, cst, ident, ones, a, scratch, mod):
    w_in = a["w_in"][0]
    c_rw = WQ + 2 * WKV

    def sb(stack, name, shape, dt=F32):
        return stack.enter_context(nc.sbuf_tensor(name, shape, dt))

    modulation(nc, "b1_mod", a["c"][0], a["c_ctx"], a["w_ada"][0], a["b_ada"][0], mod)
    with ExitStack() as recur:
        lora_in = sb(recur, "lora_in", [65, T])
        y = sb(recur, "y", [P, 4, L])
        rkv = sb(recur, "rkv", [P, 12, T])
        with ExitStack() as with_h:
            hT = sb(with_h, "hT", [P, KT, T])
            with ExitStack() as tmp:
                x0, c0 = sb(tmp, "x0", [P, KT, L]), sb(tmp, "c0", [P, KT, C])
                load_transposed(nc, "load_x", ident, a["x"][0], x0, L)
                load_transposed(nc, "load_ctx", ident, a["ctx"][0], c0, C)
                norm_modulate(nc, "norm1", ones, [(x0, 0, L, hT, col(mod, 0), col(mod, 1)),
                                                  (c0, L, C, hT, col(mod, 0, 1), col(mod, 1, 1))], a["norm1_g"][0])
            project_gates(nc, "gates", hT, w_in[:, c_rw + WRW:], scratch["gates"])
            qT, kT, v = rkv[:, 0:4, 0:L], rkv[:, 4], rkv[:, 5].rearrange("p (t w) -> p t w", w=WKV)
            kpad, vpad = rkv[:, 6], rkv[:, 7].rearrange("p (t w) -> p t w", w=WKV)
            project_qkv(nc, "qkv", cst, hT, w_in, qT, kT, v)
            window_attention(nc, "window", cst, ident, qT, kT, v, kpad, vpad, a["sink"][0], y)
            store_columns(nc, "store_ya", y[:], scratch["ya"])
            lora_a, lora_b = sb(with_h, "lora_a", [P, T]), sb(with_h, "lora_b", [32, T])
            project_rwkv(nc, "rkv", hT, w_in[:, c_rw:c_rw + WRW], a["conv_w"][0], rkv, lora_a, lora_b)
            with ExitStack() as o64:
                ones64 = sb(o64, "ones64", [P, P])
                load_matrix(nc, "load_ones64", cst["ones64"], ones64)
                kk = hT[:, 0:4]
                prepare_recurrence(nc, "keys", ones64[:], rkv, lora_a, lora_b, a["k_k"][0], a["gate_g2"][0], kk,
                                   lora_in, scratch["g"])
                store_columns(nc, "store_kk", kk, scratch["kk"])
        with ExitStack() as with_k:
            kk = sb(with_k, "kk", [P, 4, T])
            load_columns(nc, "load_kk", scratch["kk"], kk)
            run_recurrences(nc, "rec", cst, ident, rkv, kk, lora_in, a["decay_w0"][0], a["decay_w2"][0],
                            a["iclr_a0"][0], a["iclr_a2"][0], a["k_a"][0], y)
        with ExitStack() as o64:
            ones64 = sb(o64, "ones64b", [P, P])
            yr = sb(o64, "yr", [P, 4, L])
            load_matrix(nc, "load_ones64b", cst["ones64"], ones64)
            recurrence_outputs(nc, "rec_out", ones64[:], rkv, lora_in, a["iclr_a0"][0], a["iclr_a2"][0],
                               a["k_a"][0], a["r_k"][0], a["lnx_w"][0], a["lnx_b"][0], scratch["g"], y, yr)
            store_columns(nc, "store_yr", yr[:], scratch["yr"])


def first_rest(nc, ident, ones, a, scratch, mod, xT):
    def sb(stack, name, shape, dt=F32):
        return stack.enter_context(nc.sbuf_tensor(name, shape, dt))

    load_transposed(nc, "load_x2", ident, a["x"][0], xT, L)
    with ExitStack() as tmp:
        merged = sb(tmp, "merged", [P, KT, L])
        with ExitStack() as tmp2:
            ya, yr = sb(tmp2, "ya", [P, 4, L]), sb(tmp2, "yr2", [P, 4, L])
            load_columns(nc, "load_ya", scratch["ya"], ya)
            load_columns(nc, "load_yr", scratch["yr"], yr)
            merge_branches(nc, "merge", ya, yr, a["w_branch_attn"][0], a["w_branch_rwkv"][0], scratch["gates"],
                           merged)
        project(nc, "w_out", columns_of(a["w_out"][0]), KT, KT, merged, LAT, add_gated(nc, xT, col(mod, 2), L))
    with ExitStack() as tmp:
        h2 = sb(tmp, "h2", [P, KT, L])
        norm_modulate(nc, "norm2", ones, [(xT, 0, L, h2, col(mod, 3), col(mod, 4))], a["norm2_g"][0])
        mlp(nc, "mlp", h2, a["w_mlp_up"][0], a["w_mlp_down"][0], xT, col(mod, 5))
    norm_modulate(nc, "norm_f", ones, [(xT, 0, L, xT, None, None)], a["norm_f_g"])



E_N, FE = 16, 512
FT = FE // P


def store_rows(nc, name, ident, src, tokens, dram, zeroed_dram=None):
    rows = tokens // P
    with Stage(nc, name) as s:
        out = s.sb("out", [P, 2, D])
        zero = s.sb("zero", [P, D])
        ps = s.ps("ps", [P, 2, KT, P])
        turned, copied, stored = s.sem("turned"), s.sem("copied"), s.slots("stored")
        zero_set, zero_stored = s.sem("zero_set"), s.sem("zero_stored")
        with nc.Block() as block:
            @block.tensor
            def _(pe):
                for t in range(rows):
                    if t >= 2:
                        pe.wait_ge(copied, t - 1)
                    for k in range(KT):
                        tr = nc.tensor.transpose(ps[:, t % 2, k], src[:, k, t * P:(t + 1) * P], ident)
                    tr.then_inc(turned, 1)

            @block.scalar
            def _(act):
                for t in range(rows):
                    act.wait_ge(turned, t + 1)
                    if t >= 2:
                        act.wait_ge(stored[t % 2], 16 * (t // 2))
                    nc.scalar.activation(out[:, t % 2], ps[:, t % 2].rearrange("p k t -> p (k t)"), ACT.Copy
                                         ).then_inc(copied, 1)

            @block.vector
            def _(dve):
                nc.vector.memset(zero[:], 0.0).then_inc(zero_set, 1)

            @block.sync
            def _(sp):
                if zeroed_dram is not None:
                    sp.wait_ge(zero_set, 1)
                    for t in range(rows):
                        sp.dma_start(zeroed_dram[t * P:(t + 1) * P, :], zero[:]).then_inc(zero_stored, 16)
                for t in range(rows):
                    sp.wait_ge(copied, t + 1)
                    sp.dma_start(dram[t * P:(t + 1) * P, :], out[:, t % 2]).then_inc(stored[t % 2], 16)
                for b in range(2):
                    sp.wait_ge(stored[b], 16 * ((rows + 1 - b) // 2))
                if zeroed_dram is not None:
                    sp.wait_ge(zero_stored, 16 * rows)


def choose_tokens(nc, name, ident, hT, w_router, groups, idx, gain):
    rows = sum(g[1] for g in groups) // P
    N = rows * P
    CAP = max(g[2] for g in groups)
    with Stage(nc, name) as s:
        w = s.sb("w", [P, KT, E_N])
        aff = s.sb("aff", [P, rows, E_N])
        top, total = s.sb("top", [P, rows]), s.sb("total", [P, rows])
        affT = s.sb("affT", [E_N, N])
        best, where = s.sb("best", [E_N, len(groups), CAP]), s.sb("where", [E_N, len(groups), CAP], U32)
        wheref = s.sb("wheref", [E_N, len(groups), CAP])
        pl = s.ps("pl", [P, 512])
        pT = s.ps("pT", [P, 3 * 512])
        pB = s.ps("pB", [P, 512])
        w_loaded, logits, shifted, exped, aff_done = (s.sem("w"), s.sem("logits"), s.sem("shifted"), s.sem("exped"),
                                                      s.sem("aff"))
        turned, copied, chosen, turned_back, chain_sem = (s.sem("turned"), s.sem("copied"), s.sem("chosen"),
                                                          s.sem("turned_back"), s.sem("chain"))
        with nc.Block() as block:
            @block.sync
            def _(sp):
                sp.dma_start(w[:], by_tiles(w_router)).then_inc(w_loaded, 16)

            @block.tensor
            def _(pe):
                pe.wait_ge(w_loaded, 16)
                for t in range(rows):
                    for k in range(KT):
                        mm = nc.tensor.matmul(pl[:, t * E_N:(t + 1) * E_N], hT[:, k, t * P:(t + 1) * P], w[:, k],
                                              start=(k == 0), stop=(k == KT - 1))
                mm.then_inc(logits, 1)
                pe.wait_ge(aff_done, 1)
                for t in range(rows):
                    tr = nc.tensor.transpose(pT[0:E_N, t * P:(t + 1) * P], aff[:, t], ident)
                tr.then_inc(turned, 1)
                pe.wait_ge(chosen, 1)
                for n, (_, _, cap, _) in enumerate(groups):
                    for j, x in enumerate((best, wheref)):
                        o = (n * 2 + j) * E_N
                        tr = nc.tensor.transpose(pB[0:cap, o:o + E_N], x[:, n, 0:cap], ident[0:E_N, 0:E_N])
                tr.then_inc(turned_back, 1)

            @block.scalar
            def _(act):
                act.wait_ge(shifted, 1)
                nc.scalar.activation(aff[:], aff[:], ACT.Exp).then_inc(exped, 1)

            @block.vector
            def _(dve):
                chain = Chain(dve, chain_sem)
                wide = lambda x: x[:].unsqueeze(2).to_broadcast([P, rows, E_N])
                pl_v = pl[:, 0:rows * E_N].rearrange("p (t e) -> p t e", e=E_N)
                dve.wait_ge(logits, 1)
                chain(nc.vector.tensor_reduce(top[:], pl_v, AX.X, ALU.max))
                nc.vector.tensor_tensor(aff[:], pl_v, wide(top), ALU.subtract).then_inc(shifted, 1)
                dve.wait_ge(exped, 1)
                chain(nc.vector.tensor_reduce(total[:], aff[:], AX.X, ALU.add))
                chain(nc.vector.reciprocal(total[:], total[:]))
                nc.vector.tensor_tensor(aff[:], aff[:], wide(total), ALU.mult).then_inc(aff_done, 1)
                dve.wait_ge(turned, 1)
                chain(nc.vector.tensor_copy(affT[:], pT[0:E_N, 0:N]))
                for n, (t0, tokens, cap, _) in enumerate(groups):
                    own = affT[:, t0:t0 + tokens]
                    for r in range(0, cap, 8):
                        b8, w8 = best[:, n, r:r + 8], where[:, n, r:r + 8]
                        chain(nc.vector.max(b8, own))
                        chain(nc.vector.max_index(w8, b8, own))
                        chain(nc.vector.match_replace(own, b8, own, -1.0))
                    last = nc.vector.tensor_scalar(wheref[:, n, 0:cap], where[:, n, 0:cap], float(t0), None, ALU.add)
                    if n == len(groups) - 1:
                        last.then_inc(chosen, 1)
                    else:
                        chain(last)
                dve.wait_ge(turned_back, 1)
                for n, (_, _, cap, _) in enumerate(groups):
                    o = n * 2 * E_N
                    nc.vector.tensor_copy(gain[0:cap, n], pB[0:cap, o:o + E_N])
                    nc.vector.tensor_copy(idx[0:cap, n], pB[0:cap, o + E_N:o + 2 * E_N])


def run_experts(nc, name, ident, groups, idx, gain, h_dram, acc_dram, w_gate, w_up, w_down):
    caps = [g[2] for g in groups]
    offs = [sum(caps[:n]) for n in range(len(caps))]
    S = sum(caps)
    with Stage(nc, name) as s:
        wg, wu, wd = s.sb("wg", [P, 2, KT, FE]), s.sb("wu", [P, 2, KT, FE]), s.sb("wd", [P, 2, FT, D])
        own_idx = [s.sb(f"own_idx{n}", [cap, 2], U32) for n, cap in enumerate(caps)]
        xs = [s.sb(f"xs{n}", [cap, 2, D]) for n, cap in enumerate(caps)]
        ys = [s.sb(f"ys{n}", [cap, 2, D]) for n, cap in enumerate(caps)]
        xT = s.sb("xT", [P, 2, KT, S])
        hid, act_g = s.sb("hid", [P, 2, FT, S]), s.sb("act_g", [P, FT, S])
        pX = s.ps("pX", [P, 4, 512])
        pG, pU = s.ps("pG", [P, 2, 512]), s.ps("pU", [P, 2, 512])
        g_full, u_full, d_full = s.slots("g_full"), s.slots("u_full"), s.slots("d_full")
        idx_ready, gathered, x_turned, x_copied = (s.slots("idx"), s.slots("gathered"), s.slots("x_turned"),
                                                   s.slots("x_copied"))
        hid_mul, silu_done, hid_done, y_mul, y_read, added = (s.slots("hid_mul"), s.slots("silu"), s.slots("hid"),
                                                              s.slots("y_mul"), s.slots("y_read"), s.slots("added"))
        passed = s.sem("passed")
        NG = len(groups)

        def x_bank(k):
            return pX[:, k // 2, k % 2 * S:k % 2 * S + S]

        with nc.Block() as block:
            @block.sync
            def _(sp):
                with sp.Fori(0, E_N // 2) as i:
                    for b in range(2):
                        e = i * 2 + b
                        sp.wait_ge(hid_mul[b], i)
                        sp.dma_start(wg[:, b], w_gate[bass.ds(e, 1)].rearrange("a (k p) f -> p (a k) f", p=P)
                                     ).then_inc(g_full[b], 16)
                        sp.dma_start(wu[:, b], w_up[bass.ds(e, 1)].rearrange("a (k p) f -> p (a k) f", p=P)
                                     ).then_inc(u_full[b], 16)
                        sp.wait_ge(y_mul[b], i * NG)
                        sp.dma_start(wd[:, b], w_down[bass.ds(e, 1)].rearrange("a (k p) f -> p (a k) f", p=P)
                                     ).then_inc(d_full[b], 16)

            @block.gpsimd
            def _(pool):
                def gather(i, b):
                    e = bass.ds(i * 2 + b, 1)
                    for n, cap in enumerate(caps):
                        pool.wait_ge(x_turned[b], i)
                        nc.gpsimd.tensor_copy(own_idx[n][:, b:b + 1], idx[0:cap, n, e]).then_inc(idx_ready[b], 1)
                        pool.wait_ge(idx_ready[b], i * NG + n + 1)
                        pool.sem_inc(passed, 1)
                        pool.indirect_dma_start(
                            out=xs[n][:, b], out_offset=None, in_=h_dram,
                            in_offset=bass.IndirectOffsetOnAxis(ap=own_idx[n][:, b:b + 1], axis=0),
                            ).then_inc(gathered[b], 16)

                def scatter(i, b):
                    for n, cap in enumerate(caps):
                        pool.wait_ge(y_read[b], i * NG + n + 1)
                        pool.sem_inc(passed, 1)
                        pool.indirect_dma_start(
                            out=acc_dram, out_offset=bass.IndirectOffsetOnAxis(ap=own_idx[n][:, b:b + 1], axis=0),
                            in_=ys[n][:, b], in_offset=None, compute_op=ALU.add
                            ).then_inc(added[b], 16)
                        pool.wait_ge(added[b], i * (NG * 16) + (n + 1) * 16)

                with pool.Fori(0, E_N // 2) as i:
                    gather(i, 0)
                    gather(i, 1)
                    scatter(i, 0)
                    scatter(i, 1)

            @block.tensor
            def _(pe):
                with pe.Fori(0, E_N // 2) as i:
                    def turn(b):
                        pe.wait_ge(gathered[b], i * (NG * 16) + NG * 16)
                        pe.wait_ge(y_read[1 - b], i * NG + NG if b else i * NG)
                        for k in range(KT):
                            for n, cap in enumerate(caps):
                                tr = nc.tensor.transpose(x_bank(k)[:, offs[n]:offs[n] + cap],
                                                         xs[n][:, b, k * P:(k + 1) * P], ident[0:cap, 0:cap])
                        tr.then_inc(x_turned[b], 1)

                    def hidden(b):
                        pe.wait_ge(x_copied[b], i + 1)
                        pe.wait_ge(g_full[b], i * 16 + 16)
                        pe.wait_ge(hid_done[1 - b], i + 1 if b else i)
                        for w, full, ps in ((wg, g_full, pG), (wu, u_full, pU)):
                            pe.wait_ge(full[b], i * 16 + 16)
                            for f in range(FT):
                                for k in range(KT):
                                    mm = nc.tensor.matmul(ps[:, f // 2, f % 2 * S:f % 2 * S + S],
                                                          w[:, b, k, f * P:(f + 1) * P], xT[:, b, k],
                                                          start=(k == 0), stop=(k == KT - 1))
                        mm.then_inc(hid_mul[b], 1)

                    def down(b):
                        pe.wait_ge(hid_done[b], i + 1)
                        pe.wait_ge(d_full[b], i * 16 + 16)
                        for n, cap in enumerate(caps):
                            for c in range(2):
                                for f in range(FT):
                                    mm = nc.tensor.matmul(pX[0:cap, 2 * n + c], hid[:, b, f, offs[n]:offs[n] + cap],
                                                          wd[:, b, f, c * 512:(c + 1) * 512], start=(f == 0),
                                                          stop=(f == FT - 1))
                            mm.then_inc(y_mul[b], 1)

                    for b in range(2):
                        turn(b)
                        hidden(b)
                        down(b)

            @block.scalar
            def _(act):
                with act.Fori(0, E_N // 2) as i:
                    for b in range(2):
                        act.wait_ge(x_turned[b], i + 1)
                        for j in range(4):
                            cp = nc.scalar.activation(xT[:, b, 2 * j:2 * j + 2],
                                                      pX[:, j, 0:2 * S].rearrange("p (k t) -> p k t", k=2), ACT.Copy)
                        cp.then_inc(x_copied[b], 1)
                        act.wait_ge(hid_mul[b], i + 1)
                        act.wait_ge(hid_done[1 - b], i + 1 if b else i)
                        nc.scalar.activation(act_g[:].rearrange("p (a f) t -> p a (f t)", a=2), pG[:, :, 0:2 * S],
                                             ACT.Silu).then_inc(silu_done[b], 1)

            @block.vector
            def _(dve):
                with dve.Fori(0, E_N // 2) as i:
                    for b in range(2):
                        dve.wait_ge(silu_done[b], i + 1)
                        nc.vector.tensor_tensor(hid[:, b].rearrange("p (a f) t -> p a (f t)", a=2),
                                                act_g[:].rearrange("p (a f) t -> p a (f t)", a=2),
                                                pU[:, :, 0:2 * S], ALU.mult).then_inc(hid_done[b], 1)
                        for n, cap in enumerate(caps):
                            dve.wait_ge(y_mul[b], i * NG + n + 1)
                            dve.wait_ge(added[b], i * (NG * 16))
                            nc.vector.tensor_scalar(ys[n][:, b].rearrange("p (c d) -> p c d", c=2),
                                                    pX[0:cap, 2 * n:2 * n + 2],
                                                    gain[0:cap, n, bass.ds(i * 2 + b, 1)], None,
                                                    ALU.mult).then_inc(y_read[b], 1)


def add_rows(nc, name, ident, src, x, gate, tokens):
    TURNS = tokens // P // 2
    with Stage(nc, name) as s:
        rows = s.sb("rows", [P, 2, D])
        part = s.sb("part", [P, 2, KT, P])
        ps = s.ps("ps", [P, 2, KT, P])
        full, turned, read, added = s.slots("full"), s.slots("turned"), s.slots("read"), s.slots("added")
        with nc.Block() as block:
            @block.sync
            def _(sp):
                with sp.Fori(0, TURNS) as i:
                    for b in range(2):
                        sp.wait_ge(turned[b], i)
                        sp.dma_start(rows[:, b], src[bass.ds((i * 2 + b) * P, P), :]).then_inc(full[b], 16)

            @block.tensor
            def _(pe):
                with pe.Fori(0, TURNS) as i:
                    for b in range(2):
                        pe.wait_ge(full[b], i * 16 + 16)
                        pe.wait_ge(read[b], i)
                        for k in range(KT):
                            tr = nc.tensor.transpose(ps[:, b, k], rows[:, b, k * P:(k + 1) * P], ident)
                        tr.then_inc(turned[b], 1)

            @block.vector
            def _(dve):
                with dve.Fori(0, TURNS) as i:
                    for b in range(2):
                        dve.wait_ge(turned[b], i + 1)
                        dve.wait_ge(added[b], i)
                        nc.vector.tensor_tensor(part[:, b], ps[:, b], gate.unsqueeze(2).to_broadcast([P, KT, P]),
                                                ALU.mult).then_inc(read[b], 1)

            @block.gpsimd
            def _(pool):
                with pool.Fori(0, TURNS) as i:
                    for b in range(2):
                        pool.wait_ge(read[b], i + 1)
                        own = x[:, :, bass.ds((i * 2 + b) * P, P)]
                        nc.gpsimd.tensor_tensor(own, own, part[:, b], ALU.add).then_inc(added[b], 1)


def second_layer(nc, cst, ident, ones, a, scratch, layer, mod, xT, cT, last):
    nm = f"l{layer}_"
    tokens = L if last else T
    spans = [x for x in CHUNKS if x[0] < tokens]

    def sb(stack, name, shape, dt=F32):
        return stack.enter_context(nc.sbuf_tensor(nm + name, shape, dt))

    w_in, w_uq, w_ukv = a["w_in_2"][layer], a["w_uq_2"][layer], a["w_ukv_2"][layer]
    with ExitStack() as mixing:
        mixT = sb(mixing, "mixT", [P, KT, T])
        norm_modulate(nc, nm + "norm1", ones, [(xT, 0, L, mixT, col(mod, 0), col(mod, 1)),
                                               (cT, L, C, mixT, col(mod, 0, 1), col(mod, 1, 1))])
        pq, kv, kr = sb(mixing, "pq", [P, 2, T]), sb(mixing, "kv", [P, 1, T]), sb(mixing, "kr", [P, T])
        with ExitStack() as tmp:
            uT, fT, vn = sb(tmp, "uT", [P, 2, T]), sb(tmp, "fT", [P, 2, T]), sb(tmp, "vn", [P, T // P, SGU_W])
            project_mixers(nc, nm + "in", ones, mixT, w_in, tokens, uT, vn, fT, pq, kv[:, 0], kr)
            gate_tokens(nc, nm + "sgu", ident, uT, vn, a["sgu_norm_2"][layer], a["w_sgu_2"][layer],
                        a["b_sgu_2"][layer], tokens, mixT)
            fourier(nc, nm + "fnet", cst, fT, [(0, L, "l")] + ([] if last else [(L, C, "c")]), mixT)
        latent_norm(nc, nm + "qnorm", ones, pq, 2, Q_LORA, a["q_lora_norm_2"][layer], spans)
        latent_norm(nc, nm + "kvnorm", ones, kv, 1, KV_LORA, a["kv_lora_norm_2"][layer], CHUNKS)
        v = sb(mixing, "v", [P, T // P, MH * VD])
        values(nc, nm + "v", kv[:, 0], w_ukv, v)
        store = scratch["qk"]
        with ExitStack() as tmp:
            qn, qr = sb(tmp, "qn", [P, MH, T]), sb(tmp, "qr", [P, 2, T])
            uq = w_uq.rearrange("(k p) (h c) -> p k h c", p=P, h=MH)
            heads_qk(nc, nm + "q", cst, ones, pq, 2, lambda h: uq[:, :, h, 0:NOPE], lambda h: uq[:, :, h, NOPE:],
                     None, a["q_norm_2"][layer], spans, qn, qr)
            store_columns(nc, nm + "store_qn", qn[:, :, 0:tokens], store[0:MH * P, 0:tokens])
            store_columns(nc, nm + "store_qr", qr[:, :, 0:tokens], store[MH * P:, 0:tokens])
        kn, krope = sb(mixing, "kn", [P, MH, T]), sb(mixing, "krope", [P, 2, T])
        ukv = w_ukv.rearrange("(k p) (h c) -> p k h c", p=P, h=MH)
        heads_qk(nc, nm + "k", cst, ones, kv, 1, lambda h: ukv[:, :, h, 0:NOPE], None, kr, a["k_norm_2"][layer],
                 CHUNKS, kn, krope)
        with ExitStack() as tmp:
            qn, qr = sb(tmp, "qn2", [P, MH, tokens]), sb(tmp, "qr2", [P, 2, tokens])
            load_columns(nc, nm + "load_qn", store[0:MH * P, 0:tokens], qn)
            load_columns(nc, nm + "load_qr", store[MH * P:, 0:tokens], qr)
            attend(nc, nm + "att", ident, qn, qr, kn, krope, v, 0, L // P, 0, mixT)
            if not last:
                attend(nc, nm + "att_ctx", ident, qn, qr, kn, krope, v, L, C // P, L, mixT)
        w_out = columns_of(a["w_out_2"][layer])
        project(nc, nm + "w_out", w_out, KT, KT, mixT, LAT, add_gated(nc, xT, col(mod, 2), L))
        if not last:
            project(nc, nm + "w_out_ctx", w_out, KT, KT, mixT, CHUNKS[2:], add_gated(nc, cT, col(mod, 2, 1), C))
    groups = [(0, L, 2 * L // E_N, 0)] + ([] if last else [(L, C, 2 * C // E_N, 1)])
    with ExitStack() as moe:
        idx, gain = sb(moe, "idx", [P, len(groups), E_N], U32), sb(moe, "gain", [P, len(groups), E_N])
        with ExitStack() as tmp:
            h2 = sb(tmp, "h2", [P, KT, tokens])
            norm_modulate(nc, nm + "norm2", ones, [(xT, 0, L, h2, col(mod, 3), col(mod, 4))] + (
                [] if last else [(cT, L, C, h2, col(mod, 3, 1), col(mod, 4, 1))]))
            store_rows(nc, nm + "store_h", ident, h2, tokens, scratch["h"], scratch["acc"])
            choose_tokens(nc, nm + "choose", ident, h2, a["w_router_2"][layer], groups, idx, gain)
        run_experts(nc, nm + "experts", ident, groups, idx, gain, scratch["h"][0:tokens, :],
                    scratch["acc"][0:tokens, :],
                    a["w_gate_2"][layer], a["w_up_2"][layer], a["w_down_2"][layer])
    add_rows(nc, nm + "add", ident, scratch["acc"], xT, col(mod, 5), L)
    if not last:
        add_rows(nc, nm + "add_ctx", ident, scratch["acc"][L:, :], cT, col(mod, 5, 1), C)


def build(nc, a, cst, out):
    scratch = {name: nc.dram_tensor("s_" + name, shape, F32, kind="Internal").ap()
               for name, shape in (("gates", (2 * D, L)), ("g", (512, L)), ("ya", (512, L)), ("yr", (512, L)),
                                   ("kk", (512, T)), ("qk", (768, T)), ("h", (T, D)), ("acc", (T, D)))}
    with ExitStack() as stack:
        def sb(name, shape):
            return stack.enter_context(nc.sbuf_tensor(name, shape, F32))

        ident, ones, mod = sb("ident", [P, P]), sb("ones", [P, P]), sb("mod", [P, 6 * KT, 2])
        load_matrix(nc, "load_ident", cst["ident"], ident)
        load_matrix(nc, "load_ones", cst["ones"], ones)
        first_mixers(nc, cst, ident[:], ones[:], a, scratch, mod)
        xT = sb("xT", [P, KT, L])
        first_rest(nc, ident[:], ones[:], a, scratch, mod, xT)
        cT = sb("cT", [P, KT, C])
        load_transposed(nc, "load_ctx2", ident[:], a["ctx_2"][0], cT, C)
        for layer in range(2):
            modulation(nc, f"b2_mod{layer}", a["c_2"][0], a["c_ctx_2"], a["w_ada_2"][layer], a["b_ada_2"][layer],
                       mod)
            second_layer(nc, cst, ident[:], ones[:], a, scratch, layer, mod, xT, cT, layer == 1)
        store_rows(nc, "store_out", ident[:], xT, L, out)



def constants():
    f = np.float32
    out = {"ident": np.eye(P, dtype=f), "ones": np.ones((P, P), f)}
    out["ones64"] = np.kron(np.eye(2), np.ones((64, 64))).astype(f)
    pos = np.arange(L)
    row, col = pos // 64, pos % 64

    def rotation(half):
        r = np.zeros((P, P), f)
        for p in range(P):
            if p % (2 * half) < half:
                r[p + half, p] = -1.0
            else:
                r[p - half, p] = 1.0
        return r

    inv = (10000.0 ** (-np.arange(16) / 16.0)).astype(f)
    ang = np.concatenate([row[:, None].astype(f) * inv, col[:, None].astype(f) * inv], axis=1)
    ang1 = ang[:, np.arange(P) % 32].T
    out["cos1"], out["sin1"], out["rot1"] = np.cos(ang1).astype(f), np.sin(ang1).astype(f), rotation(32)
    p64 = np.arange(P) % 64
    ang2 = ang[:, (p64 // 32) * 16 + p64 % 16].T
    out["cos2"], out["sin2"], out["rot2"] = np.cos(ang2).astype(f), np.sin(ang2).astype(f), rotation(16)

    q, k = np.arange(P)[:, None], np.arange(P)[None, :]
    window = np.zeros((P, L // P, 2, P), f)
    window[:, :, 0][np.broadcast_to((k < q)[:, None], (P, L // P, P))] = NEG
    window[:, :, 1][np.broadcast_to((k > q)[:, None], (P, L // P, P))] = NEG
    window[:, 0, 0] = NEG
    window[:, -1, 1] = NEG
    out["window"] = window

    i, j = np.arange(64)[None, :], np.arange(64)[:, None]
    masks = np.zeros((2, 8, 64, 64), f)
    for lv in range(6):
        b = 1 << lv
        masks[0, lv] = (i // b % 2 == 1) & (j // b == i // b - 1)
    masks[0, 6], masks[0, 7] = j < i, j <= i
    masks[1] = masks[0].transpose(0, 2, 1)
    m = masks.transpose(2, 0, 1, 3)
    out["masks"] = np.concatenate([m, m], axis=0).copy()

    for nm, n in (("l", L), ("c", C)):
        a = 2 * np.pi * ((np.arange(n)[:, None] * np.arange(n)[None, :]) % n) / n
        out["dft_cos_" + nm] = (np.cos(a) / np.sqrt(n)).astype(f)
        out["dft_sin_" + nm] = (np.sin(a) / np.sqrt(n)).astype(f)
    a = 2 * np.pi * ((np.arange(64)[:, None] * np.arange(64)[None, :]) % 64) / 64
    out["dft64"] = np.concatenate([np.kron(np.eye(2), np.cos(a)), -np.kron(np.eye(2), np.sin(a))],
                                  axis=1).astype(f) / f(8)
    return out


_INS = ["x", "c", "ctx", "c_ctx", "w_ada", "b_ada", "norm1_g", "w_in", "sink", "conv_w", "decay_w0", "decay_w2",
        "iclr_a0", "iclr_a2", "gate_g2", "k_k", "k_a", "r_k", "lnx_w", "lnx_b", "w_branch_attn", "w_branch_rwkv",
        "w_out", "norm2_g", "w_mlp_up", "w_mlp_down", "norm_f_g", "c_2", "ctx_2", "c_ctx_2", "w_ada_2", "b_ada_2",
        "w_in_2", "sgu_norm_2", "w_sgu_2", "b_sgu_2", "q_lora_norm_2", "w_uq_2", "kv_lora_norm_2", "w_ukv_2",
        "q_norm_2", "k_norm_2", "w_out_2", "w_router_2", "w_gate_2", "w_up_2", "w_down_2"]


def kernel(**inputs):
    import numpy as _np
    import concourse.bacc as _bacc
    from concourse import mybir as _mybir
    from concourse.bass_utils import run_bass_kernel_spmd as _run

    nc = _bacc.Bacc("TRN2", target_bir_lowering=False, num_devices=1)
    arrays, a, cst = {}, {}, {}
    for group, names in ((a, _INS), (cst, None)):
        values = constants() if names is None else {name: inputs[name] for name in names}
        for name, value in values.items():
            full = ("in_" if names else "const_") + name + "_dram"
            arrays[full] = _np.ascontiguousarray(value)
            group[name] = nc.dram_tensor(full, arrays[full].shape, _mybir.dt.from_np(arrays[full].dtype),
                                         kind="ExternalInput").ap()
    out = nc.dram_tensor("out_0_dram", (1, L, D), _mybir.dt.float32, kind="ExternalOutput").ap()
    build(nc, a, cst, out[0])
    r = _run(nc, [arrays], core_ids=[0])
    return r.results[0]["out_0_dram"]
```

```python
from contextlib import ExitStack

import numpy as np
import concourse.bass as bass
from concourse import mybir

F32 = mybir.dt.float32
I32 = mybir.dt.int32
U32 = mybir.dt.uint32
F32R = mybir.dt.float32r
ALU = mybir.AluOpType
ACT = mybir.ActivationFunctionType
AX = mybir.AxisListType

P = 128
D = 1024
KT = D // P
L = 1024
C = 256
T = L + C
CHUNKS = [(0, 512), (512, 512), (1024, 256)]
LAT = CHUNKS[:2]
HD = 64
NQ = 8
WQ, WKV, WRW = 512, 128, 1696
EPS = 1e-6
NEG = -1.0e30


class Stage:

    def __init__(self, nc, name):
        self.nc, self.name, self.sems, self.stack = nc, name, [], ExitStack()

    def __enter__(self):
        self.stack.__enter__()
        return self

    def sb(self, name, shape, dt=F32):
        return self.stack.enter_context(self.nc.sbuf_tensor(f"{self.name}_{name}", shape, dt))

    def ps(self, name, shape, dt=F32):
        return self.stack.enter_context(self.nc.psum_tensor(f"{self.name}_{name}", shape, dt))

    def sem(self, name):
        self.sems.append(self.nc.alloc_semaphore(name=f"{self.name}_{name}"))
        return self.sems[-1]

    def slots(self, name, n=2):
        return [self.sem(f"{name}{b}") for b in range(n)]

    def __exit__(self, *e):
        if e[0] is None:
            self.nc.clear_and_free_semaphores(self.sems)
            self.nc.all_engine_barrier()
        return self.stack.__exit__(*e)


class Chain:

    def __init__(self, eng, sem, i=None, per=0):
        self.eng, self.sem, self.i, self.per, self.n = eng, sem, i, per, 0

    def __call__(self, ins):
        self.n += 1
        ins.then_inc(self.sem, 1)
        self.eng.wait_ge(self.sem, self.n if self.i is None else self.i * self.per + self.n)

    def close(self):
        assert self.i is None or self.n == self.per, f"{self.n} links, not {self.per}"


def by_tiles(ap):
    return ap.rearrange("(k p) m -> p k m", p=P)


def load_weights(sp, turns, source, w, w_full, ps_full, spans, first=0):
    with sp.Fori(0, turns) as i:
        for b in range(2):
            sp.wait_ge(ps_full[b], i * spans)
            sp.dma_start(w[:, b], source(i * 2 + b)).then_inc(w_full[b], 16)


def multiply_tiles(nc, pe, turns, w, rhs, kt, spans, ps, w_full, ps_free, ps_full):
    with pe.Fori(0, turns) as i:
        for b in range(2):
            pe.wait_ge(w_full[b], i * 16 + 16)
            pe.wait_ge(ps_free[b], i)
            for c, (t0, n) in enumerate(spans):
                for k in range(kt):
                    mm = nc.tensor.matmul(ps[:, b, c, 0:n], w[:, b, k], rhs[:, k, t0:t0 + n],
                                          start=(k == 0), stop=(k == kt - 1))
                mm.then_inc(ps_full[b], 1)



class SplitWeights:

    def __init__(self, nc, s, kt, ps_full, uses):
        self.nc, self.ps_full, self.uses = nc, ps_full, uses
        self.raw = s.sb("w", [P, 2, kt, P])
        self.hi, self.lo = s.sb("w_hi", [P, 2, kt, P], F32R), s.sb("w_lo", [P, 2, kt, P], F32R)
        self.passed = s.sem("w_passed")
        self.full, self.hi_done, self.split_done = s.slots("w_full"), s.slots("w_hi"), s.slots("w_split")

    def load(self, sp, b, ordinal, source):
        sp.wait_ge(self.split_done[b], ordinal)
        sp.dma_start(self.raw[:, b], source).then_inc(self.full[b], 16)

    def split(self, pool, b, ordinal):
        nc = self.nc
        pool.wait_ge(self.full[b], ordinal * 16 + 16)
        pool.wait_ge(self.ps_full[b], ordinal * self.uses)
        pool.sem_inc(self.passed, 1)
        nc.gpsimd.tensor_copy(self.hi[:, b], self.raw[:, b]).then_inc(self.hi_done[b], 1)
        pool.wait_ge(self.hi_done[b], ordinal + 1)
        nc.gpsimd.tensor_tensor(self.lo[:, b], self.raw[:, b], self.hi[:, b].bitcast(F32), ALU.subtract
                                ).then_inc(self.split_done[b], 1)

    def multiply(self, pe, b, ordinal, rhs, kt, spans, ps, rows=P):
        pe.wait_ge(self.split_done[b], ordinal + 1)
        for c, (t0, n) in enumerate(spans):
            for k in range(kt):
                for j, (w, x) in enumerate(((self.hi, rhs[0]), (self.hi, rhs[1]), (self.lo, rhs[0]))):
                    mm = self.nc.tensor.matmul(ps[0:rows, c, 0:n], w[:, b, k, 0:rows], x[:, k, t0:t0 + n],
                                               start=(k + j == 0), stop=(k == kt - 1 and j == 2))
        mm.then_inc(self.ps_full[b], 1)


def split_columns(nc, name, x, hi, lo):
    with Stage(nc, name) as s:
        hi_done = s.sem("hi")
        with nc.Block() as block:
            @block.scalar
            def _(act):
                for k in range(x.shape[1]):
                    nc.scalar.activation(hi[:, k], x[:, k], ACT.Copy).then_inc(hi_done, 1)

            @block.vector
            def _(dve):
                for k in range(x.shape[1]):
                    dve.wait_ge(hi_done, k + 1)
                    nc.vector.tensor_tensor(lo[:, k], x[:, k], hi[:, k].bitcast(F32), ALU.subtract)
    return hi, lo



def modulation(nc, name, ident, cond, cond_ctx, w_ada, b_ada, mod):
    NF = 6 * KT
    W, SLOTS = 512, 3
    TURNS = NF * P // W // SLOTS
    with Stage(nc, name) as s:
        cond_sb = s.sb("cond", [P, KT, 2])
        silu_sb = s.sb("silu", [P, KT, 2])
        bias = s.sb("bias", [P, NF, 2])
        w = s.sb("w", [P, SLOTS, KT, W])
        rows = s.sb("rows", [2, NF * P])
        ps = s.ps("ps", [P, SLOTS, 512])
        pt = s.ps("pt", [P, 512])
        small_loaded, silu_done, turned, bias_loaded = s.sem("small"), s.sem("silu"), s.sem("turned"), s.sem("bias")
        w_full, ps_full, ps_free = (s.slots("w_full", SLOTS), s.slots("ps_full", SLOTS), s.slots("ps_free", SLOTS))
        with nc.Block() as block:
            @block.sync
            def _(sp):
                with nc.allow_non_contiguous_dma("vectors into columns"):
                    for j, v in enumerate((cond, cond_ctx)):
                        sp.dma_start(cond_sb[:, :, j], v.rearrange("(k p) -> p k", p=P)).then_inc(small_loaded, 16)
                with sp.Fori(0, TURNS) as i:
                    for b in range(SLOTS):
                        sp.wait_ge(ps_full[b], i)
                        sp.dma_start(w[:, b], by_tiles(w_ada)[:, :, bass.ds((i * SLOTS + b) * W, W)]
                                     ).then_inc(w_full[b], 16)

            @block.scalar
            def _(act):
                act.wait_ge(small_loaded, 32)
                nc.scalar.activation(silu_sb[:], cond_sb[:], ACT.Silu).then_inc(silu_done, 1)
                with act.Fori(0, TURNS) as i:
                    for b in range(SLOTS):
                        act.wait_ge(ps_full[b], i + 1)
                        nc.scalar.activation(rows[:, bass.ds((i * SLOTS + b) * W, W)], ps[0:2, b], ACT.Copy
                                             ).then_inc(ps_free[b], 1)

            @block.tensor
            def _(pe):
                pe.wait_ge(silu_done, 1)
                with pe.Fori(0, TURNS) as i:
                    for b in range(SLOTS):
                        pe.wait_ge(w_full[b], i * 16 + 16)
                        pe.wait_ge(ps_free[b], i)
                        for k in range(KT):
                            mm = nc.tensor.matmul(ps[0:2, b], silu_sb[:, k], w[:, b, k], start=(k == 0),
                                                  stop=(k == KT - 1))
                        mm.then_inc(ps_full[b], 1)
                for b in range(SLOTS):
                    pe.wait_ge(ps_free[b], TURNS)
                for f in range(NF):
                    tr = nc.tensor.transpose(pt[:, 2 * f:2 * f + 2], rows[:, f * P:(f + 1) * P], ident[0:2, 0:2])
                tr.then_inc(turned, 1)

            @block.gpsimd
            def _(pool):
                with nc.allow_non_contiguous_dma("a vector into columns"):
                    for j in range(2):
                        pool.dma_start(bias[:, :, j], b_ada.rearrange("(k p) -> p k", p=P)).then_inc(bias_loaded, 16)

            @block.vector
            def _(dve):
                dve.wait_ge(bias_loaded, 32)
                dve.wait_ge(turned, 1)
                nc.vector.tensor_tensor(mod[:], pt[:, 0:2 * NF].rearrange("p (f j) -> p f j", j=2), bias[:], ALU.add)



def load_transposed(nc, name, ident, src, dst, tokens):
    TURNS = tokens // P // 2
    with Stage(nc, name) as s:
        rows = s.sb("rows", [P, 2, D])
        ps = s.ps("ps", [P, 2, KT, P])
        full, turned, free = s.slots("full"), s.slots("turned"), s.slots("free")
        with nc.Block() as block:
            @block.sync
            def _(sp):
                with sp.Fori(0, TURNS) as i:
                    for b in range(2):
                        sp.wait_ge(turned[b], i)
                        sp.dma_start(rows[:, b], src[bass.ds((i * 2 + b) * P, P), :]).then_inc(full[b], 16)

            @block.tensor
            def _(pe):
                with pe.Fori(0, TURNS) as i:
                    for b in range(2):
                        pe.wait_ge(full[b], i * 16 + 16)
                        pe.wait_ge(free[b], i)
                        for k in range(KT):
                            tr = nc.tensor.transpose(ps[:, b, k], rows[:, b, k * P:(k + 1) * P], ident)
                        tr.then_inc(turned[b], 1)

            @block.scalar
            def _(act):
                with act.Fori(0, TURNS) as i:
                    act.wait_ge(turned[0], i + 1)
                    nc.scalar.activation(dst[:, :, bass.ds(i * 2 * P, P)], ps[:, 0], ACT.Copy).then_inc(free[0], 1)

            @block.vector
            def _(dve):
                with dve.Fori(0, TURNS) as i:
                    dve.wait_ge(turned[1], i + 1)
                    nc.vector.tensor_copy(dst[:, :, bass.ds(i * 2 * P + P, P)], ps[:, 1]).then_inc(free[1], 1)



def norm_modulate(nc, name, ones, groups, g_vec=None):
    spans = [(n, c0, min(512, gr[2] - c0)) for n, gr in enumerate(groups) for c0 in range(0, gr[2], 512)]
    with Stage(nc, name) as s:
        g = s.sb("g", [P, KT])
        gain = s.sb("gain", [P, len(groups), KT])
        sq = s.sb("sq", [P, 2, 512])
        rstd = s.sb("rstd", [P, len(spans), 512])
        scaled = s.sb("scaled", [P, 2, 512])
        ps = s.ps("ps", [P, len(spans), 512])
        g_loaded, squared, summed, mean_done = s.sem("g"), s.sem("squared"), s.sem("summed"), s.sem("mean")
        rooted, gain_done = s.sem("rooted"), s.sem("gain")
        inv_done, scaled_done, out_done, chain_sem = s.sem("inv"), s.sem("scaled"), s.sem("out"), s.sem("chain")
        with nc.Block() as block:
            @block.sync
            def _(sp):
                if g_vec is not None:
                    with nc.allow_non_contiguous_dma("a vector into columns"):
                        sp.dma_start(g[:], g_vec.rearrange("(k p) -> p k", p=P)).then_inc(g_loaded, 16)

            @block.scalar
            def _(act):
                for m, (n, c0, w) in enumerate(spans):
                    for k in range(KT):
                        q = m * KT + k
                        if q >= 2:
                            act.wait_ge(summed, q - 1)
                        nc.scalar.activation(sq[:, q % 2, 0:w], groups[n][0][:, k, c0:c0 + w], ACT.Square
                                             ).then_inc(squared, 1)
                for m, (n, c0, w) in enumerate(spans):
                    act.wait_ge(mean_done, m + 1)
                    nc.scalar.activation(rstd[:, m, 0:w], rstd[:, m, 0:w], ACT.Sqrt).then_inc(rooted, 1)
                act.wait_ge(gain_done, len(groups))
                for m, (n, c0, w) in enumerate(spans):
                    _, t0, _, dst, shift, _ = groups[n]
                    for k in range(KT):
                        q = m * KT + k
                        act.wait_ge(scaled_done, q + 1)
                        nc.scalar.activation(dst[:, k, t0 + c0:t0 + c0 + w], scaled[:, q % 2, 0:w], ACT.Identity,
                                             scale=gain[:, n, k:k + 1],
                                             bias=0.0 if shift is None else shift[:, k:k + 1]).then_inc(out_done, 1)

            @block.tensor
            def _(pe):
                for m, (n, c0, w) in enumerate(spans):
                    for k in range(KT):
                        pe.wait_ge(squared, m * KT + k + 1)
                        nc.tensor.matmul(ps[:, m, 0:w], ones, sq[:, (m * KT + k) % 2, 0:w], start=(k == 0),
                                         stop=(k == KT - 1)).then_inc(summed, 1)

            @block.vector
            def _(dve):
                chain = Chain(dve, chain_sem)
                if g_vec is not None:
                    dve.wait_ge(g_loaded, 16)
                else:
                    chain(nc.vector.memset(g[:], 1.0))
                for n, gr in enumerate(groups):
                    if gr[5] is None:
                        nc.vector.tensor_copy(gain[:, n], g[:]).then_inc(gain_done, 1)
                    else:
                        nc.vector.scalar_tensor_tensor(gain[:, n], gr[5], 1.0, g[:], ALU.add, ALU.mult
                                                       ).then_inc(gain_done, 1)
                for m, (n, c0, w) in enumerate(spans):
                    dve.wait_ge(summed, (m + 1) * KT)
                    nc.vector.tensor_scalar(rstd[:, m, 0:w], ps[:, m, 0:w], 1.0 / D, EPS, ALU.mult, ALU.add
                                            ).then_inc(mean_done, 1)
                for m, (n, c0, w) in enumerate(spans):
                    dve.wait_ge(rooted, m + 1)
                    nc.vector.reciprocal(rstd[:, m, 0:w], rstd[:, m, 0:w]).then_inc(inv_done, 1)
                    dve.wait_ge(inv_done, m + 1)
                    for k in range(KT):
                        q = m * KT + k
                        if q >= 2:
                            dve.wait_ge(out_done, q - 1)
                        nc.vector.tensor_tensor(scaled[:, q % 2, 0:w], groups[n][0][:, k, c0:c0 + w],
                                                rstd[:, m, 0:w], ALU.mult).then_inc(scaled_done, 1)



def store_columns(nc, name, src, dram):
    with Stage(nc, name) as s:
        stored = s.sem("stored")
        with nc.Block() as block:
            @block.sync
            def _(sp):
                sp.dma_start(by_tiles(dram), src).then_inc(stored, 16)
                sp.wait_ge(stored, 16)


def load_columns(nc, name, dram, dst):
    with Stage(nc, name) as s:
        loaded = s.sem("loaded")
        with nc.Block() as block:
            @block.sync
            def _(sp):
                sp.dma_start(dst[:], by_tiles(dram)).then_inc(loaded, 16)
                sp.wait_ge(loaded, 16)


def load_matrix(nc, name, dram, dst):
    with Stage(nc, name) as s:
        loaded = s.sem("loaded")
        with nc.Block() as block:
            @block.sync
            def _(sp):
                sp.dma_start(dst[:], dram).then_inc(loaded, 16)
                sp.wait_ge(loaded, 16)



def project_qkv(nc, name, cst, hT, w_in, qT, kT, v):
    NT = 5
    with Stage(nc, name) as s:
        w = s.sb("w", [P, 2, KT, P])
        wv = s.sb("wv", [P, KT, WKV])
        cos, sin = s.sb("cos", [P, L]), s.sb("sin", [P, L])
        rot = s.sb("rot", [P, P])
        raw = s.sb("raw", [P, 2, T])
        part = s.sb("part", [P, 2, 512])
        ps = s.ps("ps", [P, 3, 512])
        pr = s.ps("pr", [P, 2, 512])
        pv = s.ps("pv", [P, 2, 512])
        loaded, w_full = s.sem("loaded"), s.slots("w_full")
        mul_done, raw_done, rot_done, rot_read = s.sem("mul"), s.sem("raw"), s.sem("rot"), s.sem("rot_read")
        cos_done, v_done, v_read, chain_sem = s.sem("cos"), s.sem("v"), s.sem("v_read"), s.sem("chain")
        halves = [(0, 512), (512, 512)]
        with nc.Block() as block:
            @block.sync
            def _(sp):
                sp.dma_start(cos[:], cst["cos1"]).then_inc(loaded, 16)
                sp.dma_start(sin[:], cst["sin1"]).then_inc(loaded, 16)
                sp.dma_start(rot[:], cst["rot1"]).then_inc(loaded, 16)
                sp.dma_start(wv[:], by_tiles(w_in)[:, :, WQ + WKV:WQ + 2 * WKV]).then_inc(loaded, 16)
                for m in range(NT):
                    if m >= 2:
                        sp.wait_ge(mul_done, m - 1)
                    if m < 4:
                        for h in range(2):
                            c0 = (m + 4 * h) * HD
                            sp.dma_start(w[:, m % 2, :, h * HD:(h + 1) * HD], by_tiles(w_in)[:, :, c0:c0 + HD]
                                         ).then_inc(w_full[m % 2], 16)
                    else:
                        sp.dma_start(w[:, m % 2], by_tiles(w_in)[:, :, WQ:WQ + WKV]).then_inc(w_full[m % 2], 16)

            @block.tensor
            def _(pe):
                need = [0, 0]

                def rotate(m):
                    pe.wait_ge(raw_done, m + 1)
                    for c, (t0, n) in enumerate(halves):
                        if 2 * m + c >= 2:
                            pe.wait_ge(rot_read, 2 * m + c - 1)
                        nc.tensor.matmul(pr[:, c], rot[:], raw[:, m % 2, t0:t0 + n], start=True, stop=True
                                         ).then_inc(rot_done, 1)

                pe.wait_ge(loaded, 64)
                for m in range(NT):
                    need[m % 2] += 32 if m < 4 else 16
                    pe.wait_ge(w_full[m % 2], need[m % 2])
                    if m:
                        pe.wait_ge(raw_done, m)
                    spans = LAT if m < 4 else CHUNKS
                    for c, (t0, n) in enumerate(spans):
                        for k in range(KT):
                            mm = nc.tensor.matmul(ps[:, c, 0:n], w[:, m % 2, k], hT[:, k, t0:t0 + n],
                                                  start=(k == 0), stop=(k == KT - 1))
                    mm.then_inc(mul_done, 1)
                    if m:
                        rotate(m - 1)
                rotate(NT - 1)
                for t in range(T // P):
                    if t >= 2:
                        pe.wait_ge(v_read, t - 1)
                    for k in range(KT):
                        mm = nc.tensor.matmul(pv[:, t % 2, 0:WKV], hT[:, k, t * P:(t + 1) * P], wv[:, k],
                                              start=(k == 0), stop=(k == KT - 1))
                    mm.then_inc(v_done, 1)

            @block.scalar
            def _(act):
                for m in range(NT):
                    act.wait_ge(mul_done, m + 1)
                    if m >= 2:
                        act.wait_ge(cos_done, 2 * (m - 1))
                    spans = LAT if m < 4 else CHUNKS
                    for t0, n in spans:
                        ev = nc.scalar.activation(raw[:, m % 2, t0:t0 + n], ps[:, t0 // 512, 0:n], ACT.Copy)
                    ev.then_inc(raw_done, 1)
                for t in range(T // P):
                    act.wait_ge(v_done, t + 1)
                    nc.scalar.activation(v[:, t], pv[:, t % 2, 0:WKV], ACT.Copy).then_inc(v_read, 1)

            @block.vector
            def _(dve):
                chain = Chain(dve, chain_sem)
                dve.wait_ge(loaded, 64)
                for m in range(NT):
                    dve.wait_ge(raw_done, m + 1)
                    for c, (t0, n) in enumerate(halves):
                        dst = qT[:, m, t0:t0 + n] if m < 4 else kT[:, t0:t0 + n]
                        dve.wait_ge(rot_done, 2 * m + c + 1)
                        chain(nc.vector.tensor_tensor(part[:, c], pr[:, c], sin[:, t0:t0 + n], ALU.mult))
                        nc.vector.sem_inc(rot_read, 1)
                        chain(nc.vector.tensor_tensor(dst, raw[:, m % 2, t0:t0 + n], cos[:, t0:t0 + n], ALU.mult))
                        nc.vector.tensor_tensor(dst, dst, part[:, c], ALU.add).then_inc(cos_done, 1)
                dve.wait_ge(cos_done, 2 * NT)
                nc.vector.tensor_copy(kT[:, L:T], raw[:, (NT - 1) % 2, L:T])


def project_gates(nc, name, hT, w_gl, gates_dram):
    NT = 2 * KT
    with Stage(nc, name) as s:
        w = s.sb("w", [P, 2, KT, P])
        out = s.sb("out", [P, 2, L])
        ps = s.ps("ps", [P, 2, 2, 512])
        w_full, ps_full, ps_free = s.slots("w_full"), s.slots("ps_full"), s.slots("ps_free")
        stored = s.slots("stored")
        with nc.Block() as block:
            @block.sync
            def _(sp):
                load_weights(sp, NT // 2, lambda m: by_tiles(w_gl)[:, :, bass.ds(m * P, P)], w, w_full, ps_full, 2)

            @block.tensor
            def _(pe):
                multiply_tiles(nc, pe, NT // 2, w, hT, KT, LAT, ps, w_full, ps_free, ps_full)

            @block.scalar
            def _(act):
                with act.Fori(0, NT // 2) as i:
                    for b in range(2):
                        act.wait_ge(ps_full[b], i * 2 + 2)
                        act.wait_ge(stored[b], i * 16)
                        nc.scalar.activation(out[:, b], ps[:, b].rearrange("p c t -> p (c t)"), ACT.Sigmoid
                                             ).then_inc(ps_free[b], 1)
                        act.wait_ge(ps_free[b], i + 1)
                        act.dma_start(gates_dram[bass.ds((i * 2 + b) * P, P), :], out[:, b]).then_inc(stored[b], 16)
                for b in range(2):
                    act.wait_ge(stored[b], NT // 2 * 16)


def project_rwkv(nc, name, hT, w_rw, conv_w, rkv, lora_a, lora_b):
    NT = 14
    with Stage(nc, name) as s:
        w = s.sb("w", [P, 2, KT, P])
        cw = s.sb("cw", [P, 3, NT])
        raw = s.sb("raw", [P, 2, T + 4])
        ps = s.ps("ps", [P, 2, 3, 512])
        cw_loaded, zeroed, tail_conv = s.sem("cw"), s.sem("zeroed"), s.sem("tail")
        w_full, ps_full, ps_free, conv_done = (s.slots("w_full"), s.slots("ps_full"), s.slots("ps_free"),
                                               s.slots("conv"))
        chain_sem = s.sem("chain")
        SEQS = [(1, 0, L), (L + 3, L, C)]
        with nc.Block() as block:
            @block.sync
            def _(sp):
                with nc.allow_non_contiguous_dma("vectors into columns"):
                    for j in range(3):
                        sp.dma_start(cw[:, j, 0:13], conv_w[j, 0:13 * P].rearrange("(k p) -> p k", p=P)
                                     ).then_inc(cw_loaded, 16)
                        sp.dma_start(cw[0:32, j, 13:14], conv_w[j, 13 * P:WRW].rearrange("(p k) -> p k", k=1)
                                     ).then_inc(cw_loaded, 16)
                load_weights(sp, 6, lambda m: by_tiles(w_rw)[:, :, bass.ds(m * P, P)], w, w_full, ps_full, 3)
                sp.wait_ge(ps_full[0], 18)
                sp.dma_start(w[:, 0], by_tiles(w_rw)[:, :, 12 * P:13 * P]).then_inc(w_full[0], 16)
                sp.wait_ge(ps_full[1], 18)
                sp.dma_start(w[:, 1, :, 0:32], by_tiles(w_rw)[:, :, 13 * P:WRW]).then_inc(w_full[1], 16)

            @block.tensor
            def _(pe):
                multiply_tiles(nc, pe, 6, w, hT, KT, CHUNKS, ps, w_full, ps_free, ps_full)
                for b, rows in ((0, P), (1, 32)):
                    pe.wait_ge(w_full[b], 7 * 16)
                    pe.wait_ge(ps_free[b], 6)
                    for c, (t0, n) in enumerate(CHUNKS):
                        for k in range(KT):
                            mm = nc.tensor.matmul(ps[0:rows, b, c, 0:n], w[:, b, k, 0:rows], hT[:, k, t0:t0 + n],
                                                  start=(k == 0), stop=(k == KT - 1))
                        mm.then_inc(ps_full[b], 1)

            def copy_out(act, b, rows):
                for (r0, t0, n) in ((1, 0, 512), (513, 512, 512), (L + 3, L, C)):
                    ev = nc.scalar.activation(raw[0:rows, b, r0:r0 + n], ps[0:rows, b, t0 // 512, 0:n], ACT.Copy)
                ev.then_inc(ps_free[b], 1)

            @block.scalar
            def _(act):
                act.wait_ge(zeroed, 1)
                with act.Fori(0, 6) as i:
                    for b in range(2):
                        act.wait_ge(ps_full[b], i * 3 + 3)
                        act.wait_ge(conv_done[b], i)
                        copy_out(act, b, P)
                for b, rows in ((0, P), (1, 32)):
                    act.wait_ge(ps_full[b], 21)
                    act.wait_ge(conv_done[b], 6)
                    copy_out(act, b, rows)

            def convolve(dve, chain, b, rows, dst, weight, done):
                for r0, t0, n in SEQS:
                    out = dst(t0, n)
                    chain(nc.vector.tensor_scalar(out, raw[0:rows, b, r0 - 1:r0 - 1 + n], weight(0), None, ALU.mult))
                    chain(nc.vector.scalar_tensor_tensor(out, raw[0:rows, b, r0:r0 + n], weight(1), out,
                                                         ALU.mult, ALU.add))
                    ins = nc.vector.scalar_tensor_tensor(out, raw[0:rows, b, r0 + 1:r0 + 1 + n], weight(2), out,
                                                         ALU.mult, ALU.add)
                ins.then_inc(done, 1)

            @block.vector
            def _(dve):
                nc.vector.memset(raw[:], 0.0).then_inc(zeroed, 1)
                dve.wait_ge(cw_loaded, 96)
                with dve.Fori(0, 6) as i:
                    chain = Chain(dve, chain_sem, i, 8)
                    for b in range(2):
                        dve.wait_ge(ps_free[b], i + 1)
                        m = i * 2 + b
                        convolve(dve, chain, b, P, lambda t0, n: rkv[:, bass.ds(m, 1), t0:t0 + n].rearrange(
                            "p a t -> p (a t)"), lambda j: cw[:, j, bass.ds(m, 1)], conv_done[b])
                    chain.close()
                chain = Chain(dve, chain_sem)
                chain.n = 48
                for b, rows, dst in ((0, P, lora_a), (1, 32, lora_b)):
                    dve.wait_ge(ps_free[b], 7)
                    convolve(dve, chain, b, rows, lambda t0, n: dst[0:rows, t0:t0 + n],
                             lambda j: cw[0:rows, j, 12 + b:13 + b], tail_conv)



def window_attention(nc, name, cst, ident, qT, kT, v, kpad, vpad, sink, yT):
    H = NQ
    SC = HD ** -0.5
    NK = C + 3 * P
    U = 2 * H
    TURNS = L // P // 2
    with Stage(nc, name) as s:
        qs, ks, vs = s.sb("qs", [P, 2, 4, P]), s.sb("ks", [P, 2, NK]), s.sb("vs", [P, 2, 3, WKV])
        window = s.sb("window", [P, L // P, 2, P])
        sk, nsk = s.sb("sk", [P, H]), s.sb("nsk", [P, H])
        prob, probT = s.sb("prob", [P, 2, NK]), s.sb("probT", [P, 2, 5, P])
        nmax, total, rest, inv = s.sb("nmax", [P, 2]), s.sb("total", [P, 2]), s.sb("rest", [P, 2]), s.sb("inv", [P, 2])
        nm = s.sb("nm", [P, 2])
        out = s.sb("out", [P, 2, H * HD])
        pS, pT = s.ps("pS", [P, 2, 1024]), s.ps("pT", [P, 8, P])
        pO, pY = s.ps("pO", [P, 512]), s.ps("pY", [P, 4, P])
        loaded, padded, ready = s.sem("loaded"), s.sem("padded"), s.sem("ready")
        staged = s.slots("staged")
        s_full, max_done = s.slots("s_full"), s.slots("max")
        t_done, t_copied, pv_done, sums = s.slots("t_done"), s.slots("t_copied"), s.slots("pv"), s.slots("sums")
        sums_read = s.slots("sums_read")
        o_done, y_turned, y_copied, chain_sem = s.slots("o"), s.slots("y_turned"), s.sem("y_copied"), s.sem("chain")

        def at(i, u):
            return i * (U // 2) + u // 2

        with nc.Block() as block:
            @block.sync
            def _(sp):
                sp.dma_start(window[:], cst["window"]).then_inc(loaded, 16)
                sp.dma_start(sk[:], sink.partition_broadcast(P)).then_inc(loaded, 16)

            @block.gpsimd
            def _(pool):
                for x in (kpad[:, 0:P], kpad[:, P + L:], vpad[:, 0], vpad[:, L // P + 1]):
                    nc.gpsimd.memset(x, 0.0).then_inc(padded, 1)
                nc.gpsimd.tensor_copy(kpad[:, P:P + L], kT[:, 0:L]).then_inc(padded, 1)
                nc.gpsimd.tensor_copy(vpad[:, 1:1 + L // P], v[:, 0:L // P]).then_inc(padded, 1)
                for b in range(2):
                    nc.gpsimd.tensor_copy(ks[:, b, 0:C], kT[:, L:T]).then_inc(padded, 1)
                pool.wait_ge(padded, 8)
                with pool.Fori(0, TURNS) as i:
                    for b in range(2):
                        n = i * 2 + b
                        pool.wait_ge(y_turned[b], i)
                        nc.gpsimd.tensor_copy(qs[:, b], qT[:, :, bass.ds(n * P, P)]).then_inc(staged[b], 1)
                        nc.gpsimd.tensor_copy(ks[:, b, C:NK], kpad[:, bass.ds(n * P, 3 * P)]).then_inc(staged[b], 1)
                        nc.gpsimd.tensor_copy(vs[:, b], vpad[:, bass.ds(n, 3)]).then_inc(staged[b], 1)

            @block.tensor
            def _(pe):
                with pe.Fori(0, TURNS) as i:
                    def scores(u):
                        b, h, p = u // H, u % H, u % 2
                        if h == 0:
                            pe.wait_ge(staged[b], i * 3 + 3)
                        pe.wait_ge(sums[p], at(i, u))
                        r = slice(h // 4 * 64, h // 4 * 64 + 64)
                        nc.tensor.matmul(pS[:, p, 0:512], qs[r, b, h % 4], ks[r, b, 0:512], start=True, stop=True)
                        nc.tensor.matmul(pS[:, p, 512:NK], qs[r, b, h % 4], ks[r, b, 512:NK], start=True, stop=True
                                         ).then_inc(s_full[p], 1)

                    def turn(u):
                        p = u % 2
                        pe.wait_ge(sums[p], at(i, u) + 1)
                        if u:
                            pe.wait_ge(t_copied[1 - p], at(i, u - 1) + 1)
                        else:
                            pe.wait_ge(t_copied[1], i * (U // 2))
                        for j in range(5):
                            tr = nc.tensor.transpose(pT[:, j], prob[:, p, j * P:(j + 1) * P], ident)
                        tr.then_inc(t_done[p], 1)

                    def values(u):
                        b, h, p = u // H, u % H, u % 2
                        pe.wait_ge(t_copied[p], at(i, u) + 1)
                        if u:
                            pe.wait_ge(o_done[1 - p], at(i, u - 1) + 1)
                        else:
                            pe.wait_ge(o_done[1], i * (U // 2))
                        g = h // 4 * 64
                        for j in range(5):
                            val = v[:, L // P + j, g:g + 64] if j < 2 else vs[:, b, j - 2, g:g + 64]
                            mm = nc.tensor.matmul(pO[:, 0:HD], probT[:, p, j], val, start=(j == 0), stop=(j == 4))
                        mm.then_inc(pv_done[p], 1)

                    def turn_out(b):
                        pe.wait_ge(o_done[0], at(i, b * H + H - 2) + 1)
                        pe.wait_ge(o_done[1], at(i, b * H + H - 1) + 1)
                        pe.wait_ge(y_copied, i * 2 + b)
                        for m in range(4):
                            tr = nc.tensor.transpose(pY[:, m], out[:, b, m * P:(m + 1) * P], ident)
                        tr.then_inc(y_turned[b], 1)

                    scores(0)
                    for u in range(U):
                        if u + 1 < U:
                            scores(u + 1)
                        turn(u)
                        if u:
                            values(u - 1)
                        if u == H + 1:
                            turn_out(0)
                    values(U - 1)
                    turn_out(1)

            @block.scalar
            def _(act):
                act.wait_ge(ready, 1)
                with act.Fori(0, TURNS) as i:
                    def exps(u):
                        h, p = u % H, u % 2
                        act.wait_ge(max_done[p], at(i, u) + 1)
                        act.wait_ge(t_done[p], at(i, u))
                        act.wait_ge(sums_read[p], at(i, u))
                        nc.scalar.activation(rest[:, p:p + 1], sk[:, h:h + 1], ACT.Exp, bias=nm[:, p:p + 1])
                        nc.scalar.activation(prob[:, p], pS[:, p, 0:NK], ACT.Exp, bias=nm[:, p:p + 1], scale=SC,
                                             accum_out=total[:, p:p + 1]).then_inc(sums[p], 1)

                    def copy(u):
                        p = u % 2
                        act.wait_ge(t_done[p], at(i, u) + 1)
                        act.wait_ge(pv_done[p], at(i, u))
                        nc.scalar.activation(probT[:, p], pT[:, 0:5], ACT.Copy).then_inc(t_copied[p], 1)

                    exps(0)
                    for u in range(U):
                        if u + 1 < U:
                            exps(u + 1)
                        copy(u)

            @block.vector
            def _(dve):
                dve.wait_ge(loaded, 32)
                nc.vector.tensor_scalar(nsk[:], sk[:], -1.0, None, ALU.mult).then_inc(ready, 1)
                dve.wait_ge(ready, 1)
                with dve.Fori(0, TURNS) as i:
                    chain = Chain(dve, chain_sem, i, 4 * U)

                    def maxima(u):
                        b, h, p = u // H, u % H, u % 2
                        dve.wait_ge(s_full[p], at(i, u) + 1)
                        sides = pS[:, p, C:C + 512].rearrange("p (a k) -> p a k", k=256)[:, :, 0:P]
                        chain(nc.vector.tensor_tensor(sides, sides, window[:, bass.ds(i * 2 + b, 1)].rearrange(
                            "p o a k -> p (o a) k"), ALU.add))
                        chain(nc.vector.tensor_reduce(nmax[:, p:p + 1], pS[:, p, 0:NK], AX.X, ALU.max, negate=True))
                        nc.vector.tensor_scalar(nm[:, p:p + 1], nmax[:, p:p + 1], SC, nsk[:, h:h + 1],
                                                ALU.mult, ALU.min).then_inc(max_done[p], 1)

                    def invert(u):
                        p = u % 2
                        dve.wait_ge(sums[p], at(i, u) + 1)
                        chain(nc.vector.tensor_tensor(inv[:, p:p + 1], total[:, p:p + 1], rest[:, p:p + 1], ALU.add))
                        nc.vector.sem_inc(sums_read[p], 1)
                        chain(nc.vector.reciprocal(inv[:, p:p + 1], inv[:, p:p + 1]))

                    def outputs(u):
                        b, h, p = u // H, u % H, u % 2
                        dve.wait_ge(pv_done[p], at(i, u) + 1)
                        nc.vector.tensor_scalar(out[:, b, h * HD:(h + 1) * HD], pO[:, 0:HD], inv[:, p:p + 1], None,
                                                ALU.mult).then_inc(o_done[p], 1)

                    def copy_out(b):
                        dve.wait_ge(y_turned[b], i + 1)
                        nc.vector.tensor_copy(yT[:, :, bass.ds((i * 2 + b) * P, P)], pY[:]).then_inc(y_copied, 1)

                    maxima(0)
                    for u in range(U):
                        if u:
                            invert(u - 1)
                        if u + 1 < U:
                            maxima(u + 1)
                        if u:
                            outputs(u - 1)
                        if u == H + 1:
                            copy_out(0)
                    invert(U - 1)
                    outputs(U - 1)
                    copy_out(1)
                    chain.close()



def prepare_recurrence(nc, name, ones64, rkv, lora_a, lora_b, k_k, gate_g2, kk, lora_in, g_dram):
    units = [(m, t0, n) for m in range(4) for t0, n in CHUNKS]
    with Stage(nc, name) as s:
        kvec, g2 = s.sb("kvec", [P, 4]), s.sb("g2", [96, 512])
        sq, rs = s.sb("sq", [P, 2, 512]), s.sb("rs", [P, 2, 512])
        hg, gout = s.sb("hg", [96, L]), s.sb("gout", [P, 2, L])
        ps, pg = s.ps("ps", [P, 2, 512]), s.ps("pg", [P, 2, 2, 512])
        loaded, scaled, squared, summed, clamped = (s.sem("loaded"), s.sem("scaled"), s.sem("squared"),
                                                    s.sem("summed"), s.sem("clamped"))
        rooted, keys_done, lora_done, chain_sem = s.sem("rooted"), s.sem("keys"), s.sem("lora"), s.sem("chain")
        g_ready, g_done, g_copied = s.sem("g_ready"), s.sem("g_done"), s.sem("g_copied")
        g_stored = s.slots("g_stored")
        with nc.Block() as block:
            @block.sync
            def _(sp):
                with nc.allow_non_contiguous_dma("a vector into columns"):
                    sp.dma_start(kvec[:], k_k.rearrange("(k p) -> p k", p=P)).then_inc(loaded, 16)
                sp.dma_start(g2[:], gate_g2).then_inc(loaded, 16)
                for m in range(4):
                    sp.wait_ge(g_copied, m + 1)
                    sp.dma_start(g_dram[m * P:(m + 1) * P, :], gout[:, m % 2]).then_inc(g_stored[m % 2], 16)
                for b in range(2):
                    sp.wait_ge(g_stored[b], 32)

            @block.scalar
            def _(act):
                nc.scalar.activation(hg[0:64, :], lora_a[64:128, 0:L], ACT.Sigmoid)
                nc.scalar.activation(hg[64:96, :], lora_b[0:32, 0:L], ACT.Sigmoid).then_inc(g_ready, 1)
                nc.scalar.activation(lora_in[0:32, :], lora_a[0:32, :], ACT.Tanh).then_inc(lora_done, 1)
                for q, (m, t0, n) in enumerate(units):
                    act.wait_ge(scaled, q + 1)
                    if q >= 2:
                        act.wait_ge(summed, q - 1)
                    nc.scalar.activation(sq[:, q % 2, 0:n], kk[:, m, t0:t0 + n], ACT.Square).then_inc(squared, 1)
                    act.wait_ge(clamped, q + 1)
                    nc.scalar.activation(rs[:, q % 2, 0:n], rs[:, q % 2, 0:n], ACT.Sqrt).then_inc(rooted, 1)
                for m in range(4):
                    act.wait_ge(g_done, m + 1)
                    if m >= 2:
                        act.wait_ge(g_stored[m % 2], 16)
                    nc.scalar.activation(gout[:, m % 2], pg[:, m % 2].rearrange("p c t -> p (c t)"), ACT.Copy
                                         ).then_inc(g_copied, 1)

            @block.tensor
            def _(pe):
                for q, (m, t0, n) in enumerate(units):
                    pe.wait_ge(squared, q + 1)
                    nc.tensor.matmul(ps[:, q % 2, 0:n], ones64, sq[:, q % 2, 0:n], start=True, stop=True
                                     ).then_inc(summed, 1)
                pe.wait_ge(g_ready, 1)
                pe.wait_ge(loaded, 32)
                for m in range(4):
                    if m >= 2:
                        pe.wait_ge(g_copied, m - 1)
                    for c in range(2):
                        mm = nc.tensor.matmul(pg[:, m % 2, c], g2[:, m * P:(m + 1) * P], hg[:, c * 512:(c + 1) * 512],
                                              start=True, stop=True)
                    mm.then_inc(g_done, 1)

            @block.vector
            def _(dve):
                chain = Chain(dve, chain_sem)
                nc.vector.tensor_copy(lora_in[32:64, :], lora_a[32:64, :])
                nc.vector.memset(lora_in[64:65, :], 1.0)
                dve.wait_ge(loaded, 32)
                for q, (m, t0, n) in enumerate(units):
                    nc.vector.tensor_scalar(kk[:, m, t0:t0 + n], rkv[:, 4 + m, t0:t0 + n], kvec[:, m:m + 1], None,
                                            ALU.mult).then_inc(scaled, 1)
                    dve.wait_ge(summed, q + 1)
                    nc.vector.tensor_scalar(rs[:, q % 2, 0:n], ps[:, q % 2, 0:n], 1e-24, None, ALU.max
                                            ).then_inc(clamped, 1)
                    dve.wait_ge(rooted, q + 1)
                    chain(nc.vector.reciprocal(rs[:, q % 2, 0:n], rs[:, q % 2, 0:n]))
                    nc.vector.tensor_tensor(kk[:, m, t0:t0 + n], kk[:, m, t0:t0 + n], rs[:, q % 2, 0:n], ALU.mult
                                            ).then_inc(keys_done, 1)


class Order:

    def __init__(self, names):
        self.names = names

    def at(self, i, *name, ahead=0):
        return i * len(self.names) + (ahead * len(self.names) + self.names.index(name) + 1)

    def before(self, i):
        return i * len(self.names)


LEVELS = 6
RCH = 64
HALF_E = 0.5 * float(np.exp(-0.5))


def recurrence(nc, name, ident, masks, reset, lora_w, ka, rkv, kk, lora_in, S, y, turns, first_token, w):
    emit_y = y is not None
    cs = (0, 1)
    PE = Order([e for c in cs for e in [("gb", c), ("gk", c), ("tb", c), ("tv", c), ("m0", c)] +
                           [(x, c, lv) for lv in range(1, LEVELS) for x in "tx"] +
                           [("rhs", c), ("u", c)] + [("y", c)] * emit_y + [("s", c)]])
    AC = Order([e for c in cs for e in [("tb", c), ("tv", c)] + [("t", c, lv) for lv in range(1, LEVELS)] + [("rhs", c), ("u", c)]])
    DV = Order([e for c in cs for e in [("kr", c), ("gb", c), ("gk", c), ("m0", c)] +
                             [("x", c, lv) for lv in range(1, LEVELS)] + [("y", c)] * emit_y + [("s", c)]])
    PO = Order([e for c in cs for e in [("bn", c), ("v", c)] + [("lv", c, lv) for lv in range(LEVELS)]])
    PPE, PAC, PDV, PPO = (Order([("z", 0), ("z", 1)]), Order([("tanh", 0), ("tanh", 1), ("en",), ("exp",)]),
                          Order([("cum",)]), Order([("ba",)]))
    AHEAD = ((2, 3), (3, 4))
    HALF = (slice(0, 64), slice(64, 128))
    dirs = (0, 1)
    with Stage(nc, name) as s:
        banks = [s.ps(f"ps{d}", [P, 4, 512]) for d in dirs]
        pe_done, act_done, dve_done, pool_done = (s.slots("pe"), s.slots("act"), s.slots("dve"), s.slots("pool"))
        pe_ahead, act_ahead, dve_ahead, pool_ahead = (s.slots("pe_ahead"), s.slots("act_ahead"),
                                                      s.slots("dve_ahead"), s.slots("pool_ahead"))
        dve_chain, pool_chain = s.slots("dve_chain"), s.sem("pool_chain")
        dve_chain_ahead, pool_chain_ahead = s.slots("dve_chain_ahead"), s.slots("pool_chain_ahead")

        def tokens(i, d, ahead=0):
            if d == 0:
                return i * P + (first_token + ahead * P)
            return i * (-P) + ((turns - 1 - ahead) * P + first_token)

        def all_turns(eng, prepare, turn):
            prepare()
            with eng.Fori(0, turns - 1) as i:
                turn(i, False)
            turn(turns - 1, True)

        def col(d, c):
            return slice(RCH * c, RCH * c + RCH) if d == 0 else slice(RCH - RCH * c, 2 * RCH - RCH * c)

        def pairs(bank):
            return bank.rearrange("p (m i) -> p m i", i=P)

        with nc.Block() as block:
            @block.tensor
            def _(pe):
                def lora(i, ahead, q):
                    for d in dirs:
                        if q:
                            pe.wait_ge(act_ahead[d], PAC.at(i, "tanh", 0, ahead=ahead))
                        for m in range(4):
                            mm = nc.tensor.matmul(banks[d][:, 3, m * P:(m + 1) * P],
                                                  lora_w[0:65, d, q, m * P:(m + 1) * P],
                                                  lora_in[0:65, bass.ds(tokens(i, d, ahead), P)],
                                                  start=True, stop=True)
                        mm.then_inc(pe_ahead[d], 1)

                def prepare():
                    for q in range(2):
                        lora(0, 0, q)

                def turn(i, final):
                    def done(d, ins):
                        ins.then_inc(pe_done[d], 1)

                    def products(d, bank, *terms):
                        for m in range(4):
                            for n, (left, right) in enumerate(terms):
                                mm = nc.tensor.matmul(banks[d][:, bank, m * P:(m + 1) * P], left[:, m], right[:, m],
                                                      start=(n == 0), stop=(n == len(terms) - 1))
                        return mm

                    def turned(d, bank, src):
                        for m in range(4):
                            tr = nc.tensor.transpose(banks[d][:, bank, m * P:(m + 1) * P], src[:, m], ident)
                        return tr

                    for c in cs:
                        for d in dirs:
                            b = w[d]
                            pe.wait_ge(dve_done[d], DV.at(i, "kr", c))
                            pe.wait_ge(pool_done[d], PO.at(i, "bn", c))
                            pe.wait_ge(act_done[d], AC.at(i, "u", 0) if c else AC.before(i))
                            for q in range(2):
                                if q == 1:
                                    pe.wait_ge(act_ahead[d], PAC.at(i, "tanh", 1))
                                    pe.wait_ge(dve_done[d], DV.at(i, "s", 0) if c else DV.before(i))
                                for m in range(4):
                                    mm = nc.tensor.matmul(banks[d][:, 2 * q + m // 2, m % 2 * 256:m % 2 * 256 + 256],
                                                          b["bn"][:, q, m], b["kr"][:, m].rearrange("p q i -> p (q i)"),
                                                          start=True, stop=True)
                                done(d, mm)
                        for d in dirs:
                            b = w[d]
                            pe.wait_ge(dve_done[d], DV.at(i, "gb", c))
                            turned(d, 0, b["bn"][:, 0])
                            done(d, turned(d, 1, b["bn"][:, 1]))
                            pe.wait_ge(pool_done[d], PO.at(i, "v", c))
                            pe.wait_ge(dve_done[d], DV.at(i, "gk", c))
                            done(d, turned(d, 2, b["v"]))
                            pe.wait_ge(pool_done[d], PO.at(i, "lv", c, 0))
                            done(d, turned(d, 3, b["lv"][:, 0]))
                        for lv in range(1, LEVELS):
                            for d in dirs:
                                b = w[d]
                                pe.wait_ge(pool_done[d], PO.at(i, "lv", c, lv))
                                pe.wait_ge(dve_done[d], DV.at(i, "m0", c) if lv == 1 else DV.at(i, "x", c, lv - 1))
                                if lv == 1:
                                    pe.wait_ge(act_done[d], AC.at(i, "tv", c))
                                done(d, products(d, 0, (b["lv"][:, lv % 2], b["x"][:, 0])))
                            for d in dirs:
                                b = w[d]
                                pe.wait_ge(act_done[d], AC.at(i, "t", c, lv))
                                if lv < LEVELS - 1:
                                    products(d, 1, (b["x"][:, 1], b["t"]))
                                done(d, products(d, 2, (b["t"], b["x"][:, 1])))
                            if c and lv <= 2 and not final:
                                lora(i, 1, lv - 1)
                        for d in dirs:
                            b = w[d]
                            done(d, products(d, 0, (b["kr"][:, :, 0], S[:, d]), (b["an"][:, :, 0], b["tok"][:, 2])))
                        for d in dirs:
                            b = w[d]
                            pe.wait_ge(act_done[d], AC.at(i, "rhs", c))
                            pe.wait_ge(dve_done[d], DV.at(i, "x", c, LEVELS - 1))
                            done(d, products(d, 1, (b["x"][:, 1], b["t"])))
                        for d in dirs:
                            b = w[d]
                            pe.wait_ge(act_done[d], AC.at(i, "u", c))
                            u = b["x"][:, 0]
                            if emit_y:
                                done(d, products(d, 2, (S[:, d], b["kr"][:, :, 1]), (u, b["ab"][:, :, 1]),
                                                 (b["tok"][:, 2], b["an"][:, :, 1])))
                            if c and not final:
                                pe.wait_ge(act_ahead[d], PAC.at(i, "tanh", 1, ahead=1))
                            done(d, products(d, 3, (b["tok"][:, 0], u), (b["tok"][:, 1], b["tok"][:, 2])))

                all_turns(pe, prepare, turn)

            @block.scalar
            def _(act):
                def tanh(i, ahead, q):
                    for d in dirs:
                        if ahead:
                            act.wait_ge(pool_done[d], PO.at(i, "bn", 1))
                        act.wait_ge(pe_ahead[d], PPE.at(i, "z", q, ahead=ahead))
                        nc.scalar.activation(w[d]["lwa"][:, q], pairs(banks[d][:, 3]), ACT.Tanh, scale=0.5
                                             ).then_inc(act_ahead[d], 1)

                def exps(i, ahead, d):
                    b = w[d]
                    act.wait_ge(dve_ahead[d], PDV.at(i, "cum", ahead=ahead))
                    nc.scalar.activation(b["en"], b["e"][:, 0], ACT.Exp, scale=-1.0).then_inc(act_ahead[d], 1)
                    act.wait_ge(act_ahead[d], PAC.at(i, "en", ahead=ahead))
                    nc.scalar.activation(b["e"], b["e"], ACT.Exp).then_inc(act_ahead[d], 1)

                def prepare():
                    for q in range(2):
                        tanh(0, 0, q)
                    for d in dirs:
                        exps(0, 0, d)

                def turn(i, final):
                    for c in cs:
                        for d in dirs:
                            b = w[d]
                            act.wait_ge(pe_done[d], PE.at(i, "tb", c))
                            nc.scalar.activation(b["tok"][:, 0:2], banks[d][:, 0:2].rearrange(
                                "p q (m t) -> p q m t", t=P), ACT.Copy).then_inc(act_done[d], 1)
                            act.wait_ge(pe_done[d], PE.at(i, "tv", c))
                            nc.scalar.activation(b["tok"][:, 2], pairs(banks[d][:, 2]), ACT.Copy
                                                 ).then_inc(act_done[d], 1)
                        for lv in range(1, LEVELS):
                            for d in dirs:
                                act.wait_ge(pe_done[d], PE.at(i, "t", c, lv))
                                nc.scalar.activation(w[d]["t"], pairs(banks[d][:, 0]), ACT.Copy
                                                     ).then_inc(act_done[d], 1)
                            if c and not final:
                                if lv in (2, 3):
                                    tanh(i, 1, lv - 2)
                                for d in dirs:
                                    if lv == AHEAD[d][1] + 1:
                                        exps(i, 1, d)
                        for d in dirs:
                            act.wait_ge(pe_done[d], PE.at(i, "rhs", c))
                            nc.scalar.activation(w[d]["t"], pairs(banks[d][:, 0]), ACT.Copy).then_inc(act_done[d], 1)
                        for d in dirs:
                            act.wait_ge(pe_done[d], PE.at(i, "u", c))
                            nc.scalar.activation(w[d]["x"][:, 0], pairs(banks[d][:, 1]), ACT.Copy, scale=-1.0
                                                 ).then_inc(act_done[d], 1)

                all_turns(act, prepare, turn)

            @block.vector
            def _(dve):
                def decays(i, ahead, d):
                    chain = Chain(dve, dve_chain_ahead[d], i, 2)
                    chain.n = 2 * ahead
                    b = w[d]
                    dve.wait_ge(act_ahead[d], PAC.at(i, "tanh", 1, ahead=ahead))
                    chain(nc.vector.tensor_scalar(b["lwa"][:, 0], b["lwa"][:, 0], -HALF_E, -HALF_E,
                                                  ALU.mult, ALU.add))
                    nc.vector.tensor_scalar(b["lwa"][:, 1], b["lwa"][:, 1], 0.5, 0.5, ALU.mult, ALU.add)
                    lw = b["lwa"][:, 0].rearrange("p m t -> p (m t)")
                    cum = b["e"][:, 0].rearrange("p m t -> p (m t)")
                    if d:
                        lw, cum = lw[:, ::-1], cum[:, ::-1]
                    chain(nc.vector.tensor_tensor_scan(cum, reset, lw, 0.0, ALU.mult, ALU.add))
                    nc.vector.tensor_tensor(b["e"][:, 1], b["e"][:, 0], b["lwa"][:, 0], ALU.subtract
                                            ).then_inc(dve_ahead[d], 1)

                def prepare():
                    for d in dirs:
                        decays(0, 0, d)

                def turn(i, final):
                    chains = [Chain(dve, dve_chain[d], i, 3) for d in dirs]
                    for c in cs:
                        for d in dirs:
                            b = w[d]
                            t = bass.ds(tokens(i, d) + col(d, c).start, RCH)
                            if c == 0:
                                dve.wait_ge(act_ahead[d], PAC.at(i, "exp"))
                                chains[d](nc.vector.tensor_copy(b["end"], b["e"][:, 0, :, (RCH - 1 if d == 0 else 0)::RCH]))
                            for h in range(2):
                                nc.vector.tensor_tensor(b["kr"][HALF[h], :, 0, HALF[h]], kk[HALF[h], :, t],
                                                        b["e"][HALF[h], 1, :, col(d, c)], ALU.mult)
                                last = nc.vector.tensor_tensor(b["kr"][HALF[h], :, 1, HALF[h]],
                                                               rkv[HALF[h], 0:4, t],
                                                               b["e"][HALF[h], 0, :, col(d, c)], ALU.mult)
                            last.then_inc(dve_done[d], 1)
                        for d in dirs:
                            b = w[d]
                            for q, (x, to) in enumerate((("gb", "ab"), ("gk", "an"))):
                                dve.wait_ge(pe_done[d], PE.at(i, x, c))
                                nc.vector.tensor_tensor(
                                    b[to], banks[d][:, 2 * q:2 * q + 2].rearrange("p e (f q i) -> p (e f) (q i)", q=2, i=P),
                                    masks[:, d, 6:8].rearrange("p q i -> p (q i)").unsqueeze(1).to_broadcast([P, 4, 2 * P])
                                    , ALU.mult).then_inc(dve_done[d], 1)
                        for d in dirs:
                            b = w[d]
                            eye = ident.unsqueeze(1).to_broadcast([P, 4, P])
                            dve.wait_ge(pool_done[d], PO.at(i, "lv", c, 0))
                            nc.vector.scalar_tensor_tensor(b["x"][:, 1], b["lv"][:, 0], -1.0, eye, ALU.mult, ALU.add)
                            dve.wait_ge(pe_done[d], PE.at(i, "m0", c))
                            nc.vector.scalar_tensor_tensor(b["x"][:, 0], pairs(banks[d][:, 3]), -1.0, eye,
                                                           ALU.mult, ALU.add).then_inc(dve_done[d], 1)
                        for lv in range(1, LEVELS):
                            for d in dirs:
                                b = w[d]
                                dve.wait_ge(pe_done[d], PE.at(i, "x", c, lv))
                                q = 0 if lv < LEVELS - 1 else 1
                                nc.vector.tensor_tensor(
                                    b["x"][:, q:2].rearrange("p q m i -> p q (m i)"),
                                    b["x"][:, q:2].rearrange("p q m i -> p q (m i)"),
                                    banks[d][:, 1 + q:3], ALU.subtract).then_inc(dve_done[d], 1)
                                if c and not final and lv == AHEAD[d][1]:
                                    decays(i, 1, d)
                        for d in dirs:
                            b = w[d]
                            t = bass.ds(tokens(i, d) + (col(d, c).start - first_token), RCH)
                            if emit_y:
                                dve.wait_ge(pe_done[d], PE.at(i, "y", c))
                                for h in range(2):
                                    out = y[HALF[h], :, t]
                                    last = nc.vector.tensor_tensor(out, out, pairs(banks[d][:, 2])[HALF[h], :, HALF[h]],
                                                                   ALU.add)
                                last.then_inc(dve_done[d], 1)
                            dve.wait_ge(pe_done[d], PE.at(i, "s", c))
                            chains[d](nc.vector.tensor_tensor(S[:, d], S[:, d], pairs(banks[d][:, 3]), ALU.add))
                            end = b["end"][:, :, (c if d == 0 else 1 - c)].unsqueeze(2).to_broadcast([P, 4, P])
                            nc.vector.tensor_tensor(S[:, d], S[:, d], end, ALU.mult).then_inc(dve_done[d], 1)
                    for x in chains:
                        x.close()

                all_turns(dve, prepare, turn)

            @block.gpsimd
            def _(pool):
                def gates(i, ahead, d):
                    chain = Chain(pool, pool_chain_ahead[d], i, 3)
                    chain.n = 3 * ahead
                    b = w[d]
                    t = bass.ds(tokens(i, d, ahead), P)
                    ba, kn = b["lwa"][:, 0], b["lwa"][:, 1]
                    pool.wait_ge(dve_ahead[d], PDV.at(i, "cum", ahead=ahead))
                    chain(nc.gpsimd.tensor_tensor(ba, kk[:, :, t], kn, ALU.mult))
                    chain(nc.gpsimd.tensor_tensor(kn, kn, ka[:, 0].unsqueeze(2).to_broadcast([P, 4, P]), ALU.mult))
                    chain(nc.gpsimd.tensor_tensor(kn, kn, ka[:, 1].unsqueeze(2).to_broadcast([P, 4, P]), ALU.add))
                    nc.gpsimd.tensor_tensor(kn, kn, rkv[:, 4:8, t], ALU.mult).then_inc(pool_ahead[d], 1)
                    pool.wait_ge(pool_ahead[d], PPO.at(i, "ba", ahead=ahead))

                def prepare():
                    for d in dirs:
                        gates(0, 0, d)

                def turn(i, final):
                    chain = Chain(pool, pool_chain, i, 16)

                    def event(d, ins, *name):
                        ins.then_inc(pool_done[d], 1)
                        pool.wait_ge(pool_done[d], PO.at(i, *name))

                    for c in cs:
                        for d in dirs:
                            b = w[d]
                            t = bass.ds(tokens(i, d) + col(d, c).start, RCH)
                            if c == 0:
                                pool.wait_ge(act_ahead[d], PAC.at(i, "exp"))
                            else:
                                pool.wait_ge(pe_done[d], PE.at(i, "tv", 0))
                            for h, q in ((0, 0), (0, 1), (1, 0), (1, 1)):
                                ins = nc.gpsimd.tensor_tensor(b["bn"][HALF[h], q, :, HALF[h]],
                                                              b["lwa"][HALF[h], q, :, col(d, c)],
                                                              b["en"][HALF[h], :, col(d, c)], ALU.mult)
                                if h + q < 2:
                                    chain(ins)
                            event(d, ins, "bn", c)
                            for h in range(2):
                                ins = nc.gpsimd.tensor_copy(b["v"][HALF[h], :, HALF[h]], rkv[HALF[h], 8:12, t])
                                if h == 0:
                                    chain(ins)
                            event(d, ins, "v", c)
                        for lv in range(LEVELS):
                            for d in dirs:
                                b = w[d]
                                if lv == 0:
                                    pool.wait_ge(dve_done[d], DV.at(i, "gb", c))
                                elif lv == 2:
                                    pool.wait_ge(dve_done[d], DV.at(i, "m0", c))
                                elif lv > 2:
                                    pool.wait_ge(pe_done[d], PE.at(i, "t", c, lv - 2))
                                nc.gpsimd.tensor_tensor(b["lv"][:, lv % 2], b["ab"][:, :, 0],
                                                        masks[:, d, lv].unsqueeze(1).to_broadcast([P, 4, P]), ALU.mult
                                                        ).then_inc(pool_done[d], 1)
                        for d in dirs:
                            pool.wait_ge(pool_done[d], PO.at(i, "lv", c, LEVELS - 1))
                        if c and not final:
                            for d in dirs:
                                gates(i, 1, d)
                    chain.close()

                all_turns(pool, prepare, turn)


def run_recurrences(nc, name, cst, ident, rkv, kk, lora_in, decay_w0, decay_w2, iclr_a0, iclr_a2, k_a, y):
    with Stage(nc, name) as s:
        masks = s.sb("masks", [P, 2, 8, P], mybir.dt.bfloat16)
        reset = s.sb("reset", [P, 512], mybir.dt.bfloat16)
        lora_w = s.sb("lora_w", [65, 2, 2, 512])
        ka = s.sb("ka", [P, 2, 4])
        S = s.sb("S", [P, 2, 4, P])
        w = []
        for d in range(2):
            t = {n: s.sb(f"{n}{d}", [P, *shape]) for n, shape in dict(
                lwa=[2, 4, P], e=[2, 4, P], en=[4, P], end=[4, 2], kr=[4, 2, P], bn=[2, 4, P], v=[4, P],
                ab=[4, 2, P], an=[4, 2, P], tok=[3, 4, P], lv=[2, 4, P], x=[2, 4, P], t=[4, P]).items()}
            w.append({n: x[:] for n, x in t.items()})
        with Stage(nc, name + "_init") as s2:
            masks32 = w[0]["ab"].rearrange("p m q i -> p (m q i)")[:, 0:512].rearrange("p (l i) -> p l i", i=64)
            ka_loaded, lora_loaded, mask_loaded = s2.sem("ka"), s2.sem("lora"), s2.slots("mask")
            zeroed, started = s2.sem("zeroed"), s2.sem("started")
            mask_read = s2.sem("mask_read")
            with nc.Block() as block:
                @block.gpsimd
                def _(pool):
                    nc.gpsimd.memset(lora_w[:], 0.0).then_inc(started, 1)
                    nc.gpsimd.memset(masks[:], 0.0).then_inc(started, 1)

                @block.sync
                def _(sp):
                    with nc.allow_non_contiguous_dma("a vector into columns"):
                        sp.dma_start(ka[:, 0], k_a.rearrange("(k p) -> p k", p=P)).then_inc(ka_loaded, 16)
                    sp.wait_ge(started, 2)
                    for d in range(2):
                        sp.dma_start(lora_w[0:32, d, 0], decay_w2[d]).then_inc(lora_loaded, 16)
                        sp.dma_start(lora_w[32:64, d, 1], iclr_a2[d]).then_inc(lora_loaded, 16)
                        sp.dma_start(lora_w[64:65, d, 0], decay_w0[d:d + 1]).then_inc(lora_loaded, 16)
                        sp.dma_start(lora_w[64:65, d, 1], iclr_a0[d:d + 1]).then_inc(lora_loaded, 16)
                    for d in range(2):
                        sp.wait_ge(mask_read, d)
                        sp.dma_start(masks32, cst["masks"][:, d]).then_inc(mask_loaded[d], 16)
                    sp.wait_ge(lora_loaded, 128)

                @block.vector
                def _(dve):
                    nc.vector.memset(reset[:], 1.0).then_inc(zeroed, 1)
                    dve.wait_ge(zeroed, 1)
                    nc.vector.memset(reset[:].rearrange("p (a t) -> p a t", t=RCH)[:, :, 0:1], 0.0)
                    nc.vector.memset(S[:], 0.0)
                    nc.vector.memset(y[:], 0.0)
                    for b in w:
                        for n in ("kr", "bn", "v"):
                            nc.vector.memset(b[n], 0.0)
                    dve.wait_ge(ka_loaded, 16)
                    nc.vector.tensor_scalar(ka[:, 1], ka[:, 0], -1.0, 1.0, ALU.mult, ALU.add)
                    dve.wait_ge(started, 2)
                    for d in range(2):
                        dve.wait_ge(mask_loaded[d], 16)
                        for h in range(2):
                            r = slice(64 * h, 64 * h + 64)
                            last = nc.vector.tensor_copy(masks[r, d, :, r], masks32[r])
                        last.then_inc(mask_read, 1)
        args = (ident, masks, reset[:], lora_w, ka, rkv, kk, lora_in, S)
        recurrence(nc, name + "_ctx", *args, None, C // P, L, w)
        recurrence(nc, name + "_lat", *args, y, L // P, 0, w)



def recurrence_outputs(nc, name, ones64, rkv, lora_in, iclr_a0, iclr_a2, k_a, r_k, lnx_w, lnx_b, g_dram, y, yr):
    units = [(m, c) for m in range(4) for c in range(2)]
    LNX_EPS = 1e-5 * 64
    with Stage(nc, name) as s:
        vec = s.sb("vec", [P, 6, 4])
        lora_w = s.sb("lora_w", [65, 2, 512])
        g = s.sb("g", [P, 2, 512])
        yc, sq, bon = s.sb("yc", [P, 2, 512]), s.sb("sq", [P, 2, 512]), s.sb("bon", [P, 2, 512])
        th, rs, yn = s.sb("th", [P, 2, 2, 512]), s.sb("rs", [P, 2, 512]), s.sb("yn", [P, 2, 512])
        pm, pv, pb, pa = s.ps("pm", [P, 512]), s.ps("pv", [P, 512]), s.ps("pb", [P, 512]), s.ps("pa", [P, 2, 512])
        loaded, zeroed, g_loaded, vec_done = s.sem("loaded"), s.sem("zeroed"), s.slots("g_loaded"), s.sem("vec")
        a_done, mean_done, var_done, bon_sum = s.sem("a"), s.sem("mean"), s.sem("var"), s.sem("bon_sum")
        tanh_done, squared, rooted, scaled = s.sem("tanh"), s.sem("squared"), s.sem("rooted"), s.sem("scaled")
        centred, bon_done, eps_done, yn_done, done = (s.sem("centred"), s.sem("bon"), s.sem("eps"), s.sem("yn"),
                                                      s.sem("done"))
        chain_sem = s.sem("chain")
        with nc.Block() as block:
            @block.gpsimd
            def _(pool):
                nc.gpsimd.memset(lora_w[:], 0.0).then_inc(zeroed, 1)

            @block.sync
            def _(sp):
                with nc.allow_non_contiguous_dma("vectors into columns"):
                    for j, v in enumerate((k_a, r_k.rearrange("h k -> (h k)"), lnx_w, lnx_b)):
                        sp.dma_start(vec[:, j], v.rearrange("(k p) -> p k", p=P)).then_inc(loaded, 16)
                sp.wait_ge(zeroed, 1)
                for d in range(2):
                    sp.dma_start(lora_w[32:64, d], iclr_a2[d]).then_inc(loaded, 16)
                    sp.dma_start(lora_w[64:65, d], iclr_a0[d:d + 1]).then_inc(loaded, 16)
                for q, (m, c) in enumerate(units):
                    if q >= 2:
                        sp.wait_ge(done, q - 1)
                    sp.dma_start(g[:, q % 2], g_dram[m * P:(m + 1) * P, c * 512:(c + 1) * 512]
                                 ).then_inc(g_loaded[q % 2], 16)

            @block.tensor
            def _(pe):
                pe.wait_ge(loaded, 128)
                for q, (m, c) in enumerate(units):
                    t = slice(c * 512, (c + 1) * 512)
                    if q:
                        pe.wait_ge(tanh_done, q)
                        pe.wait_ge(done, q)
                    for d in range(2):
                        mm = nc.tensor.matmul(pa[:, d], lora_w[0:65, d, m * P:(m + 1) * P], lora_in[0:65, t],
                                              start=True, stop=True)
                    mm.then_inc(a_done, 1)
                    nc.tensor.matmul(pm[:], ones64, y[:, m, t], start=True, stop=True).then_inc(mean_done, 1)
                    pe.wait_ge(squared, q + 1)
                    nc.tensor.matmul(pv[:], ones64, sq[:, q % 2], start=True, stop=True).then_inc(var_done, 1)
                    pe.wait_ge(bon_done, q + 1)
                    nc.tensor.matmul(pb[:], ones64, bon[:, q % 2], start=True, stop=True).then_inc(bon_sum, 1)

            @block.scalar
            def _(act):
                act.wait_ge(loaded, 128)
                for q, (m, c) in enumerate(units):
                    act.wait_ge(a_done, q + 1)
                    if q >= 2:
                        act.wait_ge(done, q - 1)
                    nc.scalar.activation(th[:, q % 2], pa[:], ACT.Tanh, scale=0.5).then_inc(tanh_done, 1)
                    act.wait_ge(centred, q + 1)
                    nc.scalar.activation(sq[:, q % 2], yc[:, q % 2], ACT.Square).then_inc(squared, 1)
                    act.wait_ge(eps_done, q + 1)
                    nc.scalar.activation(rs[:, q % 2], rs[:, q % 2], ACT.Sqrt).then_inc(rooted, 1)
                    act.wait_ge(yn_done, q + 1)
                    nc.scalar.activation(yn[:, q % 2], yn[:, q % 2], ACT.Identity, scale=vec[:, 2, m:m + 1],
                                         bias=vec[:, 3, m:m + 1]).then_inc(scaled, 1)

            @block.vector
            def _(dve):
                chain = Chain(dve, chain_sem)
                dve.wait_ge(loaded, 128)
                nc.vector.tensor_scalar(vec[:, 4], vec[:, 0], 0.5, None, ALU.mult).then_inc(vec_done, 1)
                nc.vector.tensor_scalar(vec[:, 5], vec[:, 0], -1.0, 2.0, ALU.mult, ALU.add).then_inc(vec_done, 1)
                dve.wait_ge(vec_done, 2)
                for q, (m, c) in enumerate(units):
                    p, t = q % 2, slice(c * 512, (c + 1) * 512)
                    dve.wait_ge(mean_done, q + 1)
                    nc.vector.scalar_tensor_tensor(yc[:, p], pm[:], -1.0 / HD, y[:, m, t], ALU.mult, ALU.add
                                                   ).then_inc(centred, 1)
                    dve.wait_ge(tanh_done, q + 1)
                    chain(nc.vector.tensor_tensor(th[:, p, 0], th[:, p, 0], th[:, p, 1], ALU.add))
                    chain(nc.vector.tensor_scalar(th[:, p, 0], th[:, p, 0], vec[:, 4, m:m + 1], vec[:, 5, m:m + 1],
                                                  ALU.mult, ALU.add))
                    chain(nc.vector.tensor_tensor(th[:, p, 0], th[:, p, 0], rkv[:, 4 + m, t], ALU.mult))
                    nc.vector.scalar_tensor_tensor(bon[:, p], th[:, p, 0], vec[:, 1, m:m + 1], rkv[:, m, t],
                                                   ALU.mult, ALU.mult).then_inc(bon_done, 1)
                    dve.wait_ge(var_done, q + 1)
                    nc.vector.tensor_scalar(rs[:, p], pv[:], 1.0 / HD, LNX_EPS, ALU.mult, ALU.add
                                            ).then_inc(eps_done, 1)
                    dve.wait_ge(rooted, q + 1)
                    chain(nc.vector.reciprocal(rs[:, p], rs[:, p]))
                    nc.vector.tensor_tensor(yn[:, p], yc[:, p], rs[:, p], ALU.mult).then_inc(yn_done, 1)
                    dve.wait_ge(bon_sum, q + 1)
                    chain(nc.vector.tensor_tensor(bon[:, p], pb[:], rkv[:, 8 + m, t], ALU.mult))
                    dve.wait_ge(scaled, q + 1)
                    chain(nc.vector.tensor_tensor(yn[:, p], yn[:, p], bon[:, p], ALU.add))
                    dve.wait_ge(g_loaded[p], 16 * (q // 2 + 1))
                    nc.vector.tensor_tensor(yr[:, m, t], yn[:, p], g[:, p], ALU.mult).then_inc(done, 1)



def project(nc, name, source, tiles, kt, rhs, spans, read_out):
    with Stage(nc, name) as s:
        ps = s.ps("ps", [P, 2, len(spans), 512])
        ps_full, ps_free = s.slots("ps_full"), s.slots("ps_free")
        w = SplitWeights(nc, s, kt, ps_full, 1)
        with nc.Block() as block:
            @block.sync
            def _(sp):
                with sp.Fori(0, tiles // 2) as i:
                    for b in range(2):
                        w.load(sp, b, i, source(i * 2 + b))

            @block.gpsimd
            def _(pool):
                with pool.Fori(0, tiles // 2) as i:
                    for b in range(2):
                        w.split(pool, b, i)

            @block.tensor
            def _(pe):
                with pe.Fori(0, tiles // 2) as i:
                    for b in range(2):
                        pe.wait_ge(ps_free[b], i)
                        w.multiply(pe, b, i, rhs, kt, spans, ps[:, b])

            @block.vector
            def _(dve):
                with dve.Fori(0, tiles // 2) as i:
                    for b in range(2):
                        dve.wait_ge(ps_full[b], i + 1)
                        read_out(i * 2 + b, ps[:, b]).then_inc(ps_free[b], 1)


def columns_of(w, kt=None):
    return lambda m: by_tiles(w)[:, :, bass.ds(m * P, P)]


def flat(ap):
    return ap.rearrange("p a t -> p (a t)")


def add_gated(nc, *parts):
    def read_out(m, banks):
        for x, gate, t0, n in parts:
            own = flat(x[:, bass.ds(m, 1), 0:n])
            last = nc.vector.scalar_tensor_tensor(own, flat(banks)[:, t0:t0 + n], gate[:, bass.ds(m, 1)], own,
                                                  ALU.mult, ALU.add)
        return last
    return read_out


def merge_branches(nc, name, ya, yr, w_attn, w_rwkv, gates_dram, out):
    with Stage(nc, name) as s:
        w = s.sb("w", [P, 2, 2, 4, P])
        g = s.sb("g", [P, 2, 2, L])
        part = s.sb("part", [P, 2, L])
        ps = s.ps("ps", [P, 2, 2, 2, 512])
        w_full, g_full, ps_full, read, added = (s.slots("w_full"), s.slots("g_full"), s.slots("ps_full"),
                                                s.slots("read"), s.slots("added"))
        with nc.Block() as block:
            @block.sync
            def _(sp):
                with sp.Fori(0, KT // 2) as i:
                    for b in range(2):
                        m = i * 2 + b
                        sp.wait_ge(ps_full[b], i)
                        for j, mat in enumerate((w_attn, w_rwkv)):
                            sp.dma_start(w[:, b, j], by_tiles(mat)[:, :, bass.ds(m * P, P)]).then_inc(w_full[b], 16)
                        sp.wait_ge(read[b], i * 2)
                        for j in range(2):
                            sp.dma_start(g[:, b, j], gates_dram[bass.ds(m * P + j * D, P), :]).then_inc(g_full[b], 16)

            @block.tensor
            def _(pe):
                with pe.Fori(0, KT // 2) as i:
                    for b in range(2):
                        pe.wait_ge(w_full[b], i * 32 + 32)
                        pe.wait_ge(read[b], i * 2)
                        for j, rhs in enumerate((ya, yr)):
                            for c, (t0, n) in enumerate(LAT):
                                for k in range(4):
                                    mm = nc.tensor.matmul(ps[:, b, j, c], w[:, b, j, k], rhs[:, k, t0:t0 + n],
                                                          start=(k == 0), stop=(k == 3))
                        mm.then_inc(ps_full[b], 1)

            @block.vector
            def _(dve):
                with dve.Fori(0, KT // 2) as i:
                    for b in range(2):
                        own = flat(out[:, bass.ds(i * 2 + b, 1)])
                        dve.wait_ge(ps_full[b], i + 1)
                        dve.wait_ge(g_full[b], i * 32 + 32)
                        dve.wait_ge(added[b], i)
                        nc.vector.tensor_tensor(own, flat(ps[:, b, 0]), g[:, b, 0], ALU.mult).then_inc(read[b], 1)
                        nc.vector.tensor_tensor(part[:, b], flat(ps[:, b, 1]), g[:, b, 1], ALU.mult
                                                ).then_inc(read[b], 1)

            @block.gpsimd
            def _(pool):
                with pool.Fori(0, KT // 2) as i:
                    for b in range(2):
                        own = flat(out[:, bass.ds(i * 2 + b, 1)])
                        pool.wait_ge(read[b], i * 2 + 2)
                        nc.gpsimd.tensor_tensor(own, own, part[:, b], ALU.add).then_inc(added[b], 1)


def mlp(nc, name, h, w_up, w_down, xT, gate):
    Q = 4
    HALF = KT // 2
    assert w_up.shape[1] == Q * D
    with Stage(nc, name) as s:
        hid = s.sb("hid_hi", [P, KT, L], F32R), s.sb("hid_lo", [P, KT, L], F32R)
        pos, sq = s.sb("pos", [P, 2, L]), s.sb("sq", [P, L])
        ps = s.ps("ps", [P, 2, 2, 512])
        ps_full, ps_free, hi_done = s.slots("ps_full"), s.slots("ps_free"), s.slots("hi")
        hid_done, squared = s.slots("hid"), s.slots("squared")
        w = SplitWeights(nc, s, KT, ps_full, 1)

        def tiles(eng, step_up, step_down):
            with eng.Fori(0, Q) as q:
                for step in (step_up, step_down):
                    with eng.Fori(0, HALF) as i:
                        for b in range(2):
                            step(b, q, i)

        def up_no(q, i):
            return q * (2 * HALF) + i

        def down_no(q, i):
            return q * (2 * HALF) + i + HALF

        with nc.Block() as block:
            @block.sync
            def _(sp):
                tiles(sp,
                      lambda b, q, i: w.load(sp, b, up_no(q, i), by_tiles(w_up)[
                          :, :, bass.ds(q * D + i * (2 * P) + b * P, P)]),
                      lambda b, q, i: w.load(sp, b, down_no(q, i), by_tiles(w_down)[
                          :, bass.ds(q * KT, KT), bass.ds(i * (2 * P) + b * P, P)]))

            @block.gpsimd
            def _(pool):
                tiles(pool, lambda b, q, i: w.split(pool, b, up_no(q, i)),
                      lambda b, q, i: w.split(pool, b, down_no(q, i)))

            @block.tensor
            def _(pe):
                def up(b, q, i):
                    pe.wait_ge(ps_free[b], up_no(q, i))
                    w.multiply(pe, b, up_no(q, i), h, KT, LAT, ps[:, b])

                def down(b, q, i):
                    pe.wait_ge(ps_free[b], down_no(q, i))
                    for j in range(2):
                        pe.wait_ge(hid_done[j], q * HALF + HALF)
                    w.multiply(pe, b, down_no(q, i), hid, KT, LAT, ps[:, b])

                tiles(pe, up, down)

            @block.scalar
            def _(act):
                with act.Fori(0, Q) as q:
                    with act.Fori(0, HALF) as i:
                        for b in range(2):
                            act.wait_ge(ps_free[b], up_no(q, i) + 1)
                            nc.scalar.activation(flat(hid[0][:, bass.ds(i * 2 + b, 1)]), pos[:, b], ACT.Square
                                                 ).then_inc(hi_done[b], 1)

            @block.vector
            def _(dve):
                def up(b, q, i):
                    dve.wait_ge(ps_full[b], up_no(q, i) + 1)
                    nc.vector.tensor_scalar(pos[:, b], flat(ps[:, b]), 0.0, None, ALU.max).then_inc(ps_free[b], 1)
                    dve.wait_ge(ps_free[b], up_no(q, i) + 1)
                    nc.vector.tensor_tensor(sq[:], pos[:, b], pos[:, b], ALU.mult).then_inc(squared[b], 1)
                    dve.wait_ge(squared[b], q * HALF + i + 1)
                    dve.wait_ge(hi_done[b], q * HALF + i + 1)
                    m = bass.ds(i * 2 + b, 1)
                    nc.vector.tensor_tensor(flat(hid[1][:, m]), sq[:], flat(hid[0][:, m]).bitcast(F32),
                                            ALU.subtract).then_inc(hid_done[b], 1)
                    dve.wait_ge(hid_done[b], q * HALF + i + 1)

                def down(b, q, i):
                    dve.wait_ge(ps_full[b], down_no(q, i) + 1)
                    add_gated(nc, (xT, gate, 0, L))(i * 2 + b, ps[:, b]).then_inc(ps_free[b], 1)

                tiles(dve, up, down)



SGU_W, FNET_W, Q_LORA, KV_LORA, ROPE_W = 256, 256, 256, 128, 64
NOPE, VD, MH = 128, 128, 4
QK = NOPE + ROPE_W
MIX_F, MIX_Q = 512, 768


def project_mixers(nc, name, ones, hT, w_in, tokens, uT, vn, fT, pq, kv, kr):
    spans = [x for x in CHUNKS if x[0] < tokens]
    rows = tokens // P
    TILES = [(0, spans, uT[:, 0], ACT.Gelu_apprx_tanh), (P, spans, uT[:, 1], ACT.Gelu_apprx_tanh),
             (MIX_F, spans, fT[:, 0], ACT.Copy), (MIX_F + P, spans, fT[:, 1], ACT.Copy),
             (MIX_Q, spans, pq[:, 0], ACT.Copy), (MIX_Q + P, spans, pq[:, 1], ACT.Copy),
             (MIX_Q + Q_LORA, CHUNKS, kv, ACT.Copy), (MIX_Q + Q_LORA + KV_LORA, CHUNKS, kr, ACT.Copy)]
    with Stage(nc, name) as s:
        w = s.sb("w", [P, 2, KT, P])
        wv = s.sb("wv", [P, KT, SGU_W])
        sq = s.sb("sq", [P, 2, SGU_W])
        ss = s.sb("ss", [P, rows])
        ps, pv = s.ps("ps", [P, 2, 3, 512]), s.ps("pv", [P, 2, 512])
        w_full, v_loaded, mul_done, read = s.slots("w_full"), s.sem("v_loaded"), s.sem("mul"), s.sem("read")
        v_done, v_read, sums, eps_done, rooted, inv_done = (s.sem("v_done"), s.sem("v_read"), s.sem("sums"),
                                                            s.sem("eps"), s.sem("rooted"), s.sem("inv"))
        with nc.Block() as block:
            @block.sync
            def _(sp):
                for m, (c0, _, _, _) in enumerate(TILES):
                    if m >= 2:
                        sp.wait_ge(mul_done, m - 1)
                    if m < 7:
                        sp.dma_start(w[:, m % 2], by_tiles(w_in)[:, :, c0:c0 + P]).then_inc(w_full[m % 2], 16)
                    else:
                        for h in range(2):
                            sp.dma_start(w[:, m % 2, :, h * 64:h * 64 + 64], by_tiles(w_in)[:, :, c0:c0 + 64]
                                         ).then_inc(w_full[m % 2], 16)
                sp.dma_start(wv[:], by_tiles(w_in)[:, :, SGU_W:2 * SGU_W]).then_inc(v_loaded, 16)

            @block.tensor
            def _(pe):
                for m, (_, spn, _, _) in enumerate(TILES):
                    pe.wait_ge(w_full[m % 2], 16 * (m // 2 + 1) + (16 if m == 7 else 0))
                    if m >= 2:
                        pe.wait_ge(read, m - 1)
                    for c, (t0, n) in enumerate(spn):
                        for k in range(KT):
                            mm = nc.tensor.matmul(ps[:, m % 2, c, 0:n], w[:, m % 2, k], hT[:, k, t0:t0 + n],
                                                  start=(k == 0), stop=(k == KT - 1))
                    mm.then_inc(mul_done, 1)
                pe.wait_ge(v_loaded, 16)
                for t in range(rows):
                    if t >= 2:
                        pe.wait_ge(v_read, t - 1)
                    for k in range(KT):
                        mm = nc.tensor.matmul(pv[:, t % 2, 0:SGU_W], hT[:, k, t * P:(t + 1) * P], wv[:, k],
                                              start=(k == 0), stop=(k == KT - 1))
                    mm.then_inc(v_done, 1)

            @block.scalar
            def _(act):
                for m, (_, spn, dst, func) in enumerate(TILES):
                    act.wait_ge(mul_done, m + 1)
                    n = spn[-1][0] + spn[-1][1]
                    nc.scalar.activation(dst[:, 0:n], ps[:, m % 2].rearrange("p c t -> p (c t)")[:, 0:n], func
                                         ).then_inc(read, 1)
                for t in range(rows):
                    act.wait_ge(v_done, t + 1)
                    nc.scalar.activation(vn[:, t], pv[:, t % 2, 0:SGU_W], ACT.Gelu_apprx_tanh).then_inc(v_read, 1)
                for t in range(rows):
                    if t >= 2:
                        act.wait_ge(sums, t - 1)
                    else:
                        act.wait_ge(v_read, t + 1)
                    act.wait_ge(v_read, rows)
                    nc.scalar.activation(sq[:, t % 2], vn[:, t], ACT.Square, accum_out=ss[:, t:t + 1]
                                         ).then_inc(sums, 1)
                act.wait_ge(eps_done, 1)
                nc.scalar.activation(ss[:], ss[:], ACT.Sqrt).then_inc(rooted, 1)

            @block.vector
            def _(dve):
                dve.wait_ge(sums, rows)
                nc.vector.tensor_scalar(ss[:], ss[:], 1.0 / SGU_W, EPS, ALU.mult, ALU.add).then_inc(eps_done, 1)
                dve.wait_ge(rooted, 1)
                nc.vector.reciprocal(ss[:], ss[:]).then_inc(inv_done, 1)
                dve.wait_ge(inv_done, 1)
                for t in range(rows):
                    nc.vector.tensor_scalar(vn[:, t], vn[:, t], ss[:, t:t + 1], None, ALU.mult)


def gate_tokens(nc, name, ident, uT, vn, sgu_norm, w_sgu, b_sgu, tokens, mixT):
    rows = tokens // P
    with Stage(nc, name) as s:
        wr, wT = s.sb("wr", [P, 4, P]), s.sb("wT", [P, 4, P])
        norm, bias = s.sb("norm", [P, 2]), s.sb("bias", [P, 2, P])
        z = s.sb("z", [P, 2, 2, P])
        pT, pz = s.ps("pT", [P, 4, P]), s.ps("pz", [P, 2, 512])
        loaded, turned, copied, mixed, z_done, done = (s.sem("loaded"), s.sem("turned"), s.sem("copied"),
                                                       s.sem("mixed"), s.sem("z"), s.sem("done"))
        with nc.Block() as block:
            @block.sync
            def _(sp):
                sp.dma_start(wr[:], w_sgu.rearrange("h p q -> p h q")).then_inc(loaded, 16)
                with nc.allow_non_contiguous_dma("a vector into columns"):
                    sp.dma_start(norm[:], sgu_norm.rearrange("(k p) -> p k", p=P)).then_inc(loaded, 16)
                for h in range(4):
                    sp.dma_start(bias[h % 2 * 64:h % 2 * 64 + 64, h // 2], b_sgu[h].partition_broadcast(64)
                                 ).then_inc(loaded, 16)

            @block.tensor
            def _(pe):
                pe.wait_ge(loaded, 96)
                for h in range(4):
                    tr = nc.tensor.transpose(pT[:, h], wr[:, h], ident)
                tr.then_inc(turned, 1)
                pe.wait_ge(copied, 1)
                for t in range(rows):
                    if t >= 2:
                        pe.wait_ge(z_done, t - 1)
                    for h in range(4):
                        r = slice(h % 2 * 64, h % 2 * 64 + 64)
                        mm = nc.tensor.matmul(pz[r, t % 2, h // 2 * P:h // 2 * P + P], vn[:, t, h * 64:(h + 1) * 64],
                                              wT[:, h], start=True, stop=True)
                    mm.then_inc(mixed, 1)

            @block.scalar
            def _(act):
                act.wait_ge(turned, 1)
                nc.scalar.activation(wT[:], pT[:], ACT.Copy).then_inc(copied, 1)

            @block.vector
            def _(dve):
                dve.wait_ge(loaded, 96)
                for t in range(rows):
                    dve.wait_ge(mixed, t + 1)
                    for m in range(2):
                        last = nc.vector.scalar_tensor_tensor(z[:, t % 2, m], pz[:, t % 2, m * P:(m + 1) * P],
                                                              norm[:, m:m + 1], bias[:, m], ALU.mult, ALU.add)
                    last.then_inc(z_done, 1)
                    dve.wait_ge(z_done, t + 1)
                    nc.vector.tensor_tensor(mixT[:, 0:2, t * P:(t + 1) * P], z[:, t % 2],
                                            uT[:, :, t * P:(t + 1) * P], ALU.mult).then_inc(done, 1)


def fourier(nc, name, cst, fT, seqs, mixT):
    rows = sum(n for _, n, _ in seqs) // P
    steps = [(t0, n, sfx, t) for t0, n, sfx in seqs for t in range(n // P)]
    with Stage(nc, name) as s:
        d64 = s.sb("d64", [P, 2 * P])
        Z = s.sb("Z", [P, rows, 2, 2, P])
        dft = s.sb("dft", [P, 2, 2, L])
        pz, py = s.ps("pz", [P, 2, 512]), s.ps("py", [P, 4, 512])
        loaded, d_full = s.sem("loaded"), s.slots("d_full")
        z_done, z_read, used, y_read = s.sem("z_done"), s.sem("z_read"), s.sem("used"), s.sem("y_read")
        with nc.Block() as block:
            @block.sync
            def _(sp):
                sp.dma_start(d64[:], cst["dft64"]).then_inc(loaded, 16)
                for q, (_, n, sfx, t) in enumerate(steps):
                    if q >= 2:
                        sp.wait_ge(used, q - 1)
                    for j, x in enumerate(("dft_cos_", "dft_sin_")):
                        sp.dma_start(dft[:, q % 2, j, 0:n], cst[x + sfx][t * P:(t + 1) * P, :]
                                     ).then_inc(d_full[q % 2], 16)

            @block.tensor
            def _(pe):
                pe.wait_ge(loaded, 16)
                for t in range(rows):
                    if t >= 2:
                        pe.wait_ge(z_read, t - 1)
                    for m in range(2):
                        mm = nc.tensor.matmul(pz[:, t % 2, m * 2 * P:(m + 1) * 2 * P], fT[:, m, t * P:(t + 1) * P],
                                              d64[:], start=True, stop=True)
                    mm.then_inc(z_done, 1)
                pe.wait_ge(z_read, rows)
                for q, (t0, n, _, t) in enumerate(steps):
                    pe.wait_ge(d_full[q % 2], 32 * (q // 2 + 1))
                    if t == 0 and q:
                        pe.wait_ge(y_read, 1)
                    for m in range(2):
                        for c in range(0, n, 512):
                            for j in range(2):
                                w = min(512, n)
                                mm = nc.tensor.matmul(py[:, m * 2 + c // 512, 0:w], Z[:, t0 // P + t, m, j],
                                                      dft[:, q % 2, j, c:c + w], start=(t == 0 and j == 0),
                                                      stop=(t == n // P - 1 and j == 1))
                    mm.then_inc(used, 1)

            @block.scalar
            def _(act):
                for t in range(rows):
                    act.wait_ge(z_done, t + 1)
                    nc.scalar.activation(Z[:, t].rearrange("p m j c -> p (m j c)"), pz[:, t % 2], ACT.Copy
                                         ).then_inc(z_read, 1)

            @block.vector
            def _(dve):
                q = 0
                for t0, n, _ in seqs:
                    q += n // P
                    dve.wait_ge(used, q)
                    for m in range(2):
                        last = nc.vector.tensor_copy(
                            mixT[:, 2 + m, t0:t0 + n],
                            py[:, 2 * m:2 * m + 2].rearrange("p c t -> p (c t)")[:, 0:n])
                    last.then_inc(y_read, 1)



def latent_norm(nc, name, ones, x, tiles, width, vec, spans):
    units = [(t0, n) for t0, n in spans]
    with Stage(nc, name) as s:
        g = s.sb("g", [P, tiles])
        sq, rs = s.sb("sq", [P, tiles, 512]), s.sb("rs", [P, 512])
        ps = s.ps("ps", [P, 512])
        loaded, squared, summed, eps_done, rooted, done, chain_sem = (
            s.sem("loaded"), s.sem("squared"), s.sem("summed"), s.sem("eps"), s.sem("rooted"), s.sem("done"),
            s.sem("chain"))
        with nc.Block() as block:
            @block.sync
            def _(sp):
                with nc.allow_non_contiguous_dma("a vector into columns"):
                    sp.dma_start(g[:], vec.rearrange("(k p) -> p k", p=P)).then_inc(loaded, 16)

            @block.scalar
            def _(act):
                for q, (t0, n) in enumerate(units):
                    if q:
                        act.wait_ge(summed, q)
                    nc.scalar.activation(sq[:, :, 0:n], x[:, 0:tiles, t0:t0 + n], ACT.Square).then_inc(squared, 1)
                    act.wait_ge(eps_done, q + 1)
                    nc.scalar.activation(rs[:, 0:n], rs[:, 0:n], ACT.Sqrt).then_inc(rooted, 1)

            @block.tensor
            def _(pe):
                for q, (t0, n) in enumerate(units):
                    pe.wait_ge(squared, q + 1)
                    if q:
                        pe.wait_ge(eps_done, q)
                    for k in range(tiles):
                        mm = nc.tensor.matmul(ps[:, 0:n], ones, sq[:, k, 0:n], start=(k == 0), stop=(k == tiles - 1))
                    mm.then_inc(summed, 1)

            @block.vector
            def _(dve):
                chain = Chain(dve, chain_sem)
                dve.wait_ge(loaded, 16)
                for q, (t0, n) in enumerate(units):
                    dve.wait_ge(summed, q + 1)
                    if q:
                        dve.wait_ge(done, q)
                    nc.vector.tensor_scalar(rs[:, 0:n], ps[:, 0:n], 1.0 / width, EPS, ALU.mult, ALU.add
                                            ).then_inc(eps_done, 1)
                    dve.wait_ge(rooted, q + 1)
                    chain(nc.vector.reciprocal(rs[:, 0:n], rs[:, 0:n]))
                    for k in range(tiles):
                        own = x[:, k, t0:t0 + n]
                        last = nc.vector.scalar_tensor_tensor(own, own, g[:, k:k + 1], rs[:, 0:n], ALU.mult, ALU.mult)
                    last.then_inc(done, 1)


def heads_qk(nc, name, cst, ones, latent, kt, w_nope, w_rope, shared, norm, spans, nope, rope, spare):
    units = [(t0, n, m) for t0, n in spans for m in range(MH // 2)]
    NU = len(units)
    W = 512
    turning = [u for u, (t0, _, _) in enumerate(units) if t0 < L]
    with Stage(nc, name) as s:
        wn, wr = s.sb("wn", [P, kt, MH, P]), s.sb("wr", [P, kt, 2, P])
        g, gr = s.sb("g", [P, 1]), s.sb("gr", [P, 1])
        cos, sin, rot = s.sb("cos", [P, W]), s.sb("sin", [P, W]), s.sb("rot", [P, P])
        raw, side = s.sb("raw", [P, 2, W]), s.sb("side", [P, 2, W])
        sqr = s.sb("sqr", [P, 2, W])
        sq, rs = (spare[:, j * 4 * W:(j + 1) * 4 * W].rearrange("p (a b t) -> p a b t", a=2, b=2) for j in range(2))
        pn, pr, psum = s.ps("pn", [P, 2, 2, 512]), s.ps("pr", [P, 2, 512]), s.ps("psum", [P, 2, 512])
        loaded, table_full = s.sem("loaded"), s.slots("table_full")
        nope_done, rope_done, squared = s.sem("nope"), s.sem("rope"), s.sem("squared")
        summed, eps_done, rooted, scaled, turned, done = (s.sem("summed"), s.sem("eps"), s.sem("rooted"),
                                                          s.sem("scaled"), s.sem("turned"), s.sem("done"))
        inv_done, side_done, rope_out = s.sem("inv"), s.sem("side"), s.sem("rope_out")
        chain_sem = s.sem("chain")
        n_loads = 3 + MH + (4 if w_rope is not None else 0) + 1
        with nc.Block() as block:
            @block.sync
            def _(sp):
                sp.dma_start(rot[:], cst["rot2"]).then_inc(loaded, 16)
                with nc.allow_non_contiguous_dma("vectors into columns"):
                    sp.dma_start(g[:], norm[0:NOPE].rearrange("(p k) -> p k", k=1)).then_inc(loaded, 16)
                    for h in range(2):
                        sp.dma_start(gr[h * 64:h * 64 + 64], norm[NOPE:QK].rearrange("(p k) -> p k", k=1)
                                     ).then_inc(loaded, 16)
                for h in range(MH):
                    sp.dma_start(wn[:, :, h], w_nope(h)).then_inc(loaded, 16)
                if w_rope is not None:
                    for h in range(MH):
                        sp.dma_start(wr[:, :, h // 2, h % 2 * 64:h % 2 * 64 + 64], w_rope(h)).then_inc(loaded, 16)
                for u in turning[::2]:
                    t0, n, _ = units[u]
                    if u:
                        sp.wait_ge(side_done, u)
                        sp.wait_ge(rope_out, u)
                    for j, (x, table) in enumerate(((cos, "cos2"), (sin, "sin2"))):
                        sp.dma_start(x[:, 0:n], cst[table][:, t0:t0 + n]).then_inc(table_full[j], 16)

            @block.tensor
            def _(pe):
                pe.wait_ge(loaded, 16 * n_loads)

                def project_unit(u):
                    t0, n, m = units[u]
                    if u >= 2:
                        pe.wait_ge(done, u - 1)
                        pe.wait_ge(scaled, u - 1)
                        if u - 2 in turning:
                            pe.wait_ge(side_done, u - 1)
                    for h in range(2):
                        for k in range(kt):
                            mm = nc.tensor.matmul(pn[:, u % 2, h, 0:n], wn[:, k, 2 * m + h], latent[:, k, t0:t0 + n],
                                                  start=(k == 0), stop=(k == kt - 1))
                    mm.then_inc(nope_done, 1)
                    if w_rope is not None:
                        for k in range(kt):
                            mm = nc.tensor.matmul(pr[:, u % 2, 0:n], wr[:, k, m], latent[:, k, t0:t0 + n],
                                                  start=(k == 0), stop=(k == kt - 1))
                        mm.then_inc(rope_done, 1)

                for u in range(2):
                    project_unit(u)
                for u, (t0, n, m) in enumerate(units):
                    if u >= 2:
                        project_unit(u)
                    pe.wait_ge(squared, u + 1)
                    if u:
                        pe.wait_ge(eps_done, u)
                    for h in range(2):
                        r = slice(h * 64, h * 64 + 64)
                        nc.tensor.matmul(psum[:, h, 0:n], ones, sq[:, u % 2, h, 0:n], start=True, stop=False)
                        mm = nc.tensor.matmul(psum[:, h, 0:n], ones[r], sqr[r, u % 2, 0:n], start=False, stop=True)
                    mm.then_inc(summed, 1)
                    if u in turning:
                        pe.wait_ge(scaled, u + 1)
                        nc.tensor.matmul(pr[:, u % 2, 0:n], rot[:], raw[:, u % 2, 0:n], start=True, stop=True
                                         ).then_inc(turned, 1)

            @block.scalar
            def _(act):
                act.wait_ge(loaded, 16 * n_loads)

                def square(u):
                    t0, n, m = units[u]
                    act.wait_ge(nope_done, u + 1)
                    if u >= 2:
                        act.wait_ge(summed, u - 1)
                        act.wait_ge(rope_out, u - 1)
                    nc.scalar.activation(sq[:, u % 2, :, 0:n], pn[:, u % 2, :, 0:n], ACT.Square)
                    if w_rope is not None:
                        act.wait_ge(rope_done, u + 1)
                    src = pr[:, u % 2, 0:n] if w_rope is not None else shared[:, t0:t0 + n]
                    nc.scalar.activation(sqr[:, u % 2, 0:n], src, ACT.Square).then_inc(squared, 1)
                    nc.scalar.activation(raw[:, u % 2, 0:n], src, ACT.Copy, scale=gr[:, 0:1]).then_inc(scaled, 1)

                for u in range(2):
                    square(u)
                for u, (t0, n, m) in enumerate(units):
                    if u >= 2:
                        square(u)
                    act.wait_ge(eps_done, u + 1)
                    nc.scalar.activation(rs[:, u % 2, :, 0:n], rs[:, u % 2, :, 0:n], ACT.Sqrt).then_inc(rooted, 1)

            @block.vector
            def _(dve):
                dve.wait_ge(loaded, 16 * n_loads)
                def add_eps(u):
                    _, n, _ = units[u]
                    dve.wait_ge(summed, u + 1)
                    if u >= 2:
                        dve.wait_ge(rope_out, u - 1)
                        dve.wait_ge(done, u - 1)
                    nc.vector.tensor_scalar(rs[:, u % 2, :, 0:n], psum[:, :, 0:n], 1.0 / QK, EPS, ALU.mult, ALU.add
                                            ).then_inc(eps_done, 1)

                for u in range(2):
                    add_eps(u)
                for u, (t0, n, m) in enumerate(units):
                    dve.wait_ge(rooted, u + 1)
                    nc.vector.reciprocal(rs[:, u % 2, :, 0:n], rs[:, u % 2, :, 0:n]).then_inc(inv_done, 1)
                    if u in turning:
                        dve.wait_ge(table_full[1], 16 * (u // 2 + 1))
                        dve.wait_ge(turned, u + 1)
                        if u >= 2:
                            dve.wait_ge(rope_out, u - 1)
                        nc.vector.tensor_tensor(side[:, u % 2, 0:n], pr[:, u % 2, 0:n], sin[:, 0:n], ALU.mult
                                                ).then_inc(side_done, 1)
                    dve.wait_ge(inv_done, u + 1)
                    nc.vector.scalar_tensor_tensor(nope[:, 2 * m:2 * m + 2, t0:t0 + n], pn[:, u % 2, :, 0:n],
                                                   g[:, 0:1], rs[:, u % 2, :, 0:n], ALU.mult, ALU.mult
                                                   ).then_inc(done, 1)
                    if 2 <= u + 1 < NU:
                        add_eps(u + 1)

            @block.gpsimd
            def _(pool):
                chain = Chain(pool, chain_sem)
                for u, (t0, n, m) in enumerate(units):
                    own = raw[:, u % 2, 0:n]
                    pool.wait_ge(scaled, u + 1)
                    if u in turning:
                        pool.wait_ge(table_full[0], 16 * (u // 2 + 1))
                        pool.wait_ge(turned, u + 1)
                        chain(nc.gpsimd.tensor_tensor(own, own, cos[:, 0:n], ALU.mult))
                        pool.wait_ge(side_done, u + 1)
                        chain(nc.gpsimd.tensor_tensor(own, own, side[:, u % 2, 0:n], ALU.add))
                    pool.wait_ge(inv_done, u + 1)
                    for h in range(2):
                        r = slice(h * 64, h * 64 + 64)
                        ins = nc.gpsimd.tensor_tensor(rope[r, m, t0:t0 + n], raw[r, u % 2, 0:n], rs[r, u % 2, h, 0:n],
                                                      ALU.mult)
                        if h == 0:
                            chain(ins)
                    ins.then_inc(rope_out, 1)
                    pool.wait_ge(rope_out, u + 1)


def values(nc, name, kv, w_ukv, v):
    with Stage(nc, name) as s:
        w = s.sb("w", [P, MH, VD])
        ps = s.ps("ps", [P, 2, 512])
        loaded, done, read = s.sem("loaded"), s.sem("done"), s.sem("read")
        with nc.Block() as block:
            @block.sync
            def _(sp):
                sp.dma_start(w[:], w_ukv.rearrange("p (h c) -> p h c", h=MH)[:, :, NOPE:]).then_inc(loaded, 16)

            @block.tensor
            def _(pe):
                pe.wait_ge(loaded, 16)
                for t in range(T // P):
                    if t >= 2:
                        pe.wait_ge(read, t - 1)
                    nc.tensor.matmul(ps[:, t % 2], kv[:, t * P:(t + 1) * P], w[:].rearrange("p h c -> p (h c)"),
                                     start=True, stop=True).then_inc(done, 1)

            @block.scalar
            def _(act):
                for t in range(T // P):
                    act.wait_ge(done, t + 1)
                    nc.scalar.activation(v[:, t], ps[:, t % 2], ACT.Copy).then_inc(read, 1)


def attend(nc, name, ident, q_nope, q_rope, k_nope, k_rope, v, q0, blocks, k0, mixT):
    NK = T - k0
    key_spans = [(c, min(512, NK - c)) for c in range(0, NK, 512)]
    nt = NK // P
    SPLIT = min(4, nt)
    TURNS, U = blocks // 2, 2 * MH
    SC = QK ** -0.5
    with Stage(nc, name) as s:
        qn, qr = s.sb("qn", [P, 2, MH, P]), s.sb("qr", [P, 2, 2, P])
        prob, probT = s.sb("prob", [P, 2, NK]), s.sb("probT", [P, nt, P])
        nmax, total, inv = s.sb("nmax", [P, 2]), s.sb("total", [P, 2]), s.sb("inv", [P, 2])
        out = s.sb("out", [P, 2, MH * VD])
        pS, pT = s.ps("pS", [P, 3 * 512]), s.ps("pT", [P, 12, P])
        pO, pY = s.ps("pO", [P, 512]), s.ps("pY", [P, MH, P])
        staged, turned_out = s.slots("staged"), s.slots("turned_out")
        s_full, max_done, sums, t_done = s.sem("s_full"), s.sem("max"), s.sem("sums"), s.sem("t_done")
        copied_a, copied_v, pv_done, o_done, y_copied = (s.sem("copied_a"), s.sem("copied_v"), s.sem("pv"),
                                                         s.sem("o"), s.sem("y_copied"))
        chain_sem = s.sem("chain")
        with nc.Block() as block:
            @block.gpsimd
            def _(pool):
                with pool.Fori(0, TURNS) as i:
                    for b in range(2):
                        t = bass.ds((i * 2 + b) * P + q0, P)
                        pool.wait_ge(turned_out[b], i)
                        nc.gpsimd.tensor_copy(qn[:, b], q_nope[:, :, t]).then_inc(staged[b], 1)
                        nc.gpsimd.tensor_copy(qr[:, b], q_rope[:, :, t]).then_inc(staged[b], 1)

            @block.tensor
            def _(pe):
                with pe.Fori(0, TURNS) as i:
                    def scores(u):
                        b, h = u // MH, u % MH
                        if h == 0:
                            pe.wait_ge(staged[b], i * 2 + 2)
                        pe.wait_ge(sums, i * U + u)
                        r = slice(h % 2 * 64, h % 2 * 64 + 64)
                        for c, n in key_spans:
                            k = slice(k0 + c, k0 + c + n)
                            nc.tensor.matmul(pS[:, c:c + n], qn[:, b, h], k_nope[:, h, k], start=True, stop=False)
                            mm = nc.tensor.matmul(pS[:, c:c + n], qr[r, b, h // 2], k_rope[r, h // 2, k],
                                                  start=False, stop=True)
                        mm.then_inc(s_full, 1)

                    def turn(u):
                        pe.wait_ge(sums, i * U + u + 1)
                        pe.wait_ge(copied_a, i * U + u)
                        pe.wait_ge(copied_v, i * U + u)
                        for j in range(nt):
                            tr = nc.tensor.transpose(pT[:, j], prob[:, u % 2, j * P:(j + 1) * P], ident)
                        tr.then_inc(t_done, 1)

                    def weigh(u):
                        h = u % MH
                        pe.wait_ge(copied_a, i * U + u + 1)
                        pe.wait_ge(copied_v, i * U + u + 1)
                        pe.wait_ge(o_done, i * U + u)
                        for j in range(nt):
                            mm = nc.tensor.matmul(pO[:, 0:VD], probT[:, j], v[:, k0 // P + j, h * VD:(h + 1) * VD],
                                                  start=(j == 0), stop=(j == nt - 1))
                        mm.then_inc(pv_done, 1)

                    def turn_out(b):
                        pe.wait_ge(o_done, i * U + (b + 1) * MH)
                        pe.wait_ge(y_copied, i * 2 + b)
                        for h in range(MH):
                            tr = nc.tensor.transpose(pY[:, h], out[:, b, h * VD:(h + 1) * VD], ident)
                        tr.then_inc(turned_out[b], 1)

                    for u in range(U):
                        scores(u)
                        if u:
                            weigh(u - 1)
                        if u == MH + 1:
                            turn_out(0)
                        turn(u)
                    weigh(U - 1)
                    turn_out(1)

            @block.scalar
            def _(act):
                with act.Fori(0, TURNS) as i:
                    for u in range(U):
                        p = u % 2
                        act.wait_ge(max_done, i * U + u + 1)
                        nc.scalar.activation(prob[:, p], pS[:, 0:NK], ACT.Exp, bias=nmax[:, p:p + 1], scale=SC,
                                             accum_out=total[:, p:p + 1]).then_inc(sums, 1)
                        act.wait_ge(t_done, i * U + u + 1)
                        act.wait_ge(pv_done, i * U + u)
                        if nt > SPLIT:
                            nc.scalar.activation(probT[:, SPLIT:nt], pT[:, SPLIT:nt], ACT.Copy).then_inc(copied_a, 1)
                        else:
                            nc.scalar.activation(nmax[:, p:p + 1], nmax[:, p:p + 1], ACT.Copy).then_inc(copied_a, 1)

            @block.vector
            def _(dve):
                with dve.Fori(0, TURNS) as i:
                    chain = Chain(dve, chain_sem, i, 2 * U)

                    def outputs(u):
                        b, h, p = u // MH, u % MH, u % 2
                        dve.wait_ge(pv_done, i * U + u + 1)
                        nc.vector.tensor_scalar(out[:, b, h * VD:(h + 1) * VD], pO[:, 0:VD], inv[:, p:p + 1], None,
                                                ALU.mult).then_inc(o_done, 1)

                    def copy_out(b):
                        dve.wait_ge(turned_out[b], i + 1)
                        nc.vector.tensor_copy(mixT[:, 4:8, bass.ds((i * 2 + b) * P + q0, P)], pY[:]
                                              ).then_inc(y_copied, 1)

                    for u in range(U):
                        p = u % 2
                        dve.wait_ge(s_full, i * U + u + 1)
                        chain(nc.vector.tensor_reduce(nmax[:, p:p + 1], pS[:, 0:NK], AX.X, ALU.max, negate=True))
                        nc.vector.tensor_scalar(nmax[:, p:p + 1], nmax[:, p:p + 1], SC, None, ALU.mult
                                                ).then_inc(max_done, 1)
                        if u:
                            outputs(u - 1)
                        if u == MH + 1:
                            copy_out(0)
                        dve.wait_ge(sums, i * U + u + 1)
                        chain(nc.vector.reciprocal(inv[:, p:p + 1], total[:, p:p + 1]))
                        dve.wait_ge(t_done, i * U + u + 1)
                        nc.vector.tensor_copy(probT[:, 0:SPLIT], pT[:, 0:SPLIT]).then_inc(copied_v, 1)
                    outputs(U - 1)
                    copy_out(1)
                    chain.close()



def col(mod, n, j=0):
    return mod[:, n * KT:(n + 1) * KT, j]


def first_mixers(nc, cst, ident, ones, a, scratch, mod):
    w_in = a["w_in"][0]
    c_rw = WQ + 2 * WKV

    def sb(stack, name, shape, dt=F32):
        return stack.enter_context(nc.sbuf_tensor(name, shape, dt))

    modulation(nc, "b1_mod", ident, a["c"][0], a["c_ctx"], a["w_ada"][0], a["b_ada"][0], mod)
    with ExitStack() as recur:
        lora_in = sb(recur, "lora_in", [65, T])
        y = sb(recur, "y", [P, 4, L])
        rkv = sb(recur, "rkv", [P, 12, T])
        with ExitStack() as with_h:
            hT = sb(with_h, "hT", [P, KT, T])
            with ExitStack() as tmp:
                x0, c0 = sb(tmp, "x0", [P, KT, L]), sb(tmp, "c0", [P, KT, C])
                load_transposed(nc, "load_x", ident, a["x"][0], x0, L)
                load_transposed(nc, "load_ctx", ident, a["ctx"][0], c0, C)
                norm_modulate(nc, "norm1", ones, [(x0, 0, L, hT, col(mod, 0), col(mod, 1)),
                                                  (c0, L, C, hT, col(mod, 0, 1), col(mod, 1, 1))], a["norm1_g"][0])
            project_gates(nc, "gates", hT, w_in[:, c_rw + WRW:], scratch["gates"])
            qT, kT, v = rkv[:, 0:4, 0:L], rkv[:, 4], rkv[:, 5].rearrange("p (t w) -> p t w", w=WKV)
            kpad, vpad = rkv[:, 6], rkv[:, 7].rearrange("p (t w) -> p t w", w=WKV)
            project_qkv(nc, "qkv", cst, hT, w_in, qT, kT, v)
            window_attention(nc, "window", cst, ident, qT, kT, v, kpad, vpad, a["sink"][0], y)
            store_columns(nc, "store_ya", y[:], scratch["ya"])
            lora_a, lora_b = sb(with_h, "lora_a", [P, T]), sb(with_h, "lora_b", [32, T])
            project_rwkv(nc, "rkv", hT, w_in[:, c_rw:c_rw + WRW], a["conv_w"][0], rkv, lora_a, lora_b)
            with ExitStack() as o64:
                ones64 = sb(o64, "ones64", [P, P])
                load_matrix(nc, "load_ones64", cst["ones64"], ones64)
                kk = hT[:, 0:4]
                prepare_recurrence(nc, "keys", ones64[:], rkv, lora_a, lora_b, a["k_k"][0], a["gate_g2"][0], kk,
                                   lora_in, scratch["g"])
                store_columns(nc, "store_kk", kk, scratch["kk"])
        with ExitStack() as with_k:
            kk = sb(with_k, "kk", [P, 4, T])
            load_columns(nc, "load_kk", scratch["kk"], kk)
            run_recurrences(nc, "rec", cst, ident, rkv, kk, lora_in, a["decay_w0"][0], a["decay_w2"][0],
                            a["iclr_a0"][0], a["iclr_a2"][0], a["k_a"][0], y)
        with ExitStack() as o64:
            ones64 = sb(o64, "ones64b", [P, P])
            yr = sb(o64, "yr", [P, 4, L])
            load_matrix(nc, "load_ones64b", cst["ones64"], ones64)
            recurrence_outputs(nc, "rec_out", ones64[:], rkv, lora_in, a["iclr_a0"][0], a["iclr_a2"][0],
                               a["k_a"][0], a["r_k"][0], a["lnx_w"][0], a["lnx_b"][0], scratch["g"], y, yr)
            store_columns(nc, "store_yr", yr[:], scratch["yr"])


def first_rest(nc, ident, ones, a, scratch, mod, xT):
    def sb(stack, name, shape, dt=F32):
        return stack.enter_context(nc.sbuf_tensor(name, shape, dt))

    load_transposed(nc, "load_x2", ident, a["x"][0], xT, L)
    with ExitStack() as tmp:
        merged = sb(tmp, "merged", [P, KT, L])
        with ExitStack() as tmp2:
            ya, yr = sb(tmp2, "ya", [P, 4, L]), sb(tmp2, "yr2", [P, 4, L])
            load_columns(nc, "load_ya", scratch["ya"], ya)
            load_columns(nc, "load_yr", scratch["yr"], yr)
            merge_branches(nc, "merge", ya, yr, a["w_branch_attn"][0], a["w_branch_rwkv"][0], scratch["gates"],
                           merged)
        hi, lo = sb(tmp, "merged_hi", [P, KT, L], F32R), sb(tmp, "merged_lo", [P, KT, L], F32R)
        project(nc, "w_out", columns_of(a["w_out"][0]), KT, KT, split_columns(nc, "split_merged", merged, hi, lo),
                LAT, add_gated(nc, (xT, col(mod, 2), 0, L)))
    with ExitStack() as tmp:
        hi, lo = sb(tmp, "h2_hi", [P, KT, L], F32R), sb(tmp, "h2_lo", [P, KT, L], F32R)
        with ExitStack() as tmp2:
            h2 = sb(tmp2, "h2", [P, KT, L])
            norm_modulate(nc, "norm2", ones, [(xT, 0, L, h2, col(mod, 3), col(mod, 4))], a["norm2_g"][0])
            split_columns(nc, "split_h2", h2, hi, lo)
        mlp(nc, "mlp", (hi, lo), a["w_mlp_up"][0], a["w_mlp_down"][0], xT, col(mod, 5))
    norm_modulate(nc, "norm_f", ones, [(xT, 0, L, xT, None, None)], a["norm_f_g"])



E_N, FE = 16, 512
FT = FE // P


def store_rows(nc, name, ident, src, tokens, dram, zeroed_dram=None):
    rows = tokens // P
    with Stage(nc, name) as s:
        out = s.sb("out", [P, 2, D])
        zero = s.sb("zero", [P, D])
        ps = s.ps("ps", [P, 2, KT, P])
        turned, copied, stored = s.sem("turned"), s.sem("copied"), s.slots("stored")
        zero_set, zero_stored = s.sem("zero_set"), s.sem("zero_stored")
        with nc.Block() as block:
            @block.tensor
            def _(pe):
                for t in range(rows):
                    if t >= 2:
                        pe.wait_ge(copied, t - 1)
                    for k in range(KT):
                        tr = nc.tensor.transpose(ps[:, t % 2, k], src[:, k, t * P:(t + 1) * P], ident)
                    tr.then_inc(turned, 1)

            @block.scalar
            def _(act):
                for t in range(rows):
                    act.wait_ge(turned, t + 1)
                    if t >= 2:
                        act.wait_ge(stored[t % 2], 16 * (t // 2))
                    nc.scalar.activation(out[:, t % 2], ps[:, t % 2].rearrange("p k t -> p (k t)"), ACT.Copy
                                         ).then_inc(copied, 1)

            @block.vector
            def _(dve):
                nc.vector.memset(zero[:], 0.0).then_inc(zero_set, 1)

            @block.sync
            def _(sp):
                if zeroed_dram is not None:
                    sp.wait_ge(zero_set, 1)
                    for t in range(rows):
                        sp.dma_start(zeroed_dram[t * P:(t + 1) * P, :], zero[:]).then_inc(zero_stored, 16)
                for t in range(rows):
                    sp.wait_ge(copied, t + 1)
                    sp.dma_start(dram[t * P:(t + 1) * P, :], out[:, t % 2]).then_inc(stored[t % 2], 16)
                for b in range(2):
                    sp.wait_ge(stored[b], 16 * ((rows + 1 - b) // 2))
                if zeroed_dram is not None:
                    sp.wait_ge(zero_stored, 16 * rows)


def choose_tokens(nc, name, ident, hT, w_router, groups, idx, gain):
    rows = sum(g[1] for g in groups) // P
    N = rows * P
    CAP = max(g[2] for g in groups)
    with Stage(nc, name) as s:
        w = s.sb("w", [P, KT, E_N])
        aff = s.sb("aff", [P, rows, E_N])
        top, total = s.sb("top", [P, rows]), s.sb("total", [P, rows])
        affT = s.sb("affT", [E_N, N])
        best, where = s.sb("best", [E_N, len(groups), CAP]), s.sb("where", [E_N, len(groups), CAP], U32)
        wheref = s.sb("wheref", [E_N, len(groups), CAP])
        pl = s.ps("pl", [P, 512])
        pT = s.ps("pT", [P, 3 * 512])
        pB = s.ps("pB", [P, 512])
        w_loaded, logits, shifted, exped, aff_done = (s.sem("w"), s.sem("logits"), s.sem("shifted"), s.sem("exped"),
                                                      s.sem("aff"))
        turned, copied, chosen, turned_back, chain_sem = (s.sem("turned"), s.sem("copied"), s.sem("chosen"),
                                                          s.sem("turned_back"), s.sem("chain"))
        with nc.Block() as block:
            @block.sync
            def _(sp):
                sp.dma_start(w[:], by_tiles(w_router)).then_inc(w_loaded, 16)

            @block.tensor
            def _(pe):
                pe.wait_ge(w_loaded, 16)
                for t in range(rows):
                    for k in range(KT):
                        mm = nc.tensor.matmul(pl[:, t * E_N:(t + 1) * E_N], hT[:, k, t * P:(t + 1) * P], w[:, k],
                                              start=(k == 0), stop=(k == KT - 1))
                mm.then_inc(logits, 1)
                pe.wait_ge(aff_done, 1)
                for t in range(rows):
                    tr = nc.tensor.transpose(pT[0:E_N, t * P:(t + 1) * P], aff[:, t], ident)
                tr.then_inc(turned, 1)
                pe.wait_ge(chosen, 1)
                for n, (_, _, cap, _) in enumerate(groups):
                    for j, x in enumerate((best, wheref)):
                        o = (n * 2 + j) * E_N
                        tr = nc.tensor.transpose(pB[0:cap, o:o + E_N], x[:, n, 0:cap], ident[0:E_N, 0:E_N])
                tr.then_inc(turned_back, 1)

            @block.scalar
            def _(act):
                act.wait_ge(shifted, 1)
                nc.scalar.activation(aff[:], aff[:], ACT.Exp).then_inc(exped, 1)

            @block.vector
            def _(dve):
                chain = Chain(dve, chain_sem)
                wide = lambda x: x[:].unsqueeze(2).to_broadcast([P, rows, E_N])
                pl_v = pl[:, 0:rows * E_N].rearrange("p (t e) -> p t e", e=E_N)
                dve.wait_ge(logits, 1)
                chain(nc.vector.tensor_reduce(top[:], pl_v, AX.X, ALU.max))
                nc.vector.tensor_tensor(aff[:], pl_v, wide(top), ALU.subtract).then_inc(shifted, 1)
                dve.wait_ge(exped, 1)
                chain(nc.vector.tensor_reduce(total[:], aff[:], AX.X, ALU.add))
                chain(nc.vector.reciprocal(total[:], total[:]))
                nc.vector.tensor_tensor(aff[:], aff[:], wide(total), ALU.mult).then_inc(aff_done, 1)
                dve.wait_ge(turned, 1)
                chain(nc.vector.tensor_copy(affT[:], pT[0:E_N, 0:N]))
                for n, (t0, tokens, cap, _) in enumerate(groups):
                    own = affT[:, t0:t0 + tokens]
                    for r in range(0, cap, 8):
                        b8, w8 = best[:, n, r:r + 8], where[:, n, r:r + 8]
                        chain(nc.vector.max(b8, own))
                        chain(nc.vector.max_index(w8, b8, own))
                        chain(nc.vector.match_replace(own, b8, own, -1.0))
                    last = nc.vector.tensor_scalar(wheref[:, n, 0:cap], where[:, n, 0:cap], float(t0), None, ALU.add)
                    if n == len(groups) - 1:
                        last.then_inc(chosen, 1)
                    else:
                        chain(last)
                dve.wait_ge(turned_back, 1)
                for n, (_, _, cap, _) in enumerate(groups):
                    o = n * 2 * E_N
                    nc.vector.tensor_copy(gain[0:cap, n], pB[0:cap, o:o + E_N])
                    nc.vector.tensor_copy(idx[0:cap, n], pB[0:cap, o + E_N:o + 2 * E_N])


def run_experts(nc, name, ident, groups, idx, gain, h_dram, acc_dram, w_gate, w_up, w_down):
    caps = [g[2] for g in groups]
    offs = [sum(caps[:n]) for n in range(len(caps))]
    S = sum(caps)
    NG = len(groups)
    PAIRS = E_N // 2 - 1
    UNITS = [(n, c) for n in range(NG) for c in range(2)]
    U = len(UNITS)
    with Stage(nc, name) as s:
        wg, wu, wd = s.sb("wg", [P, 2, KT, FE]), s.sb("wu", [P, 2, KT, FE]), s.sb("wd", [P, 2, FT, D])
        own_idx = [s.sb(f"own_idx{n}", [cap, 2], U32) for n, cap in enumerate(caps)]
        xs = [s.sb(f"xs{n}", [cap, 2, D]) for n, cap in enumerate(caps)]
        ys = [s.sb(f"ys{n}", [cap, 2, D]) for n, cap in enumerate(caps)]
        xT = s.sb("xT", [P, 2, KT, S])
        hid, act_g = s.sb("hid", [P, 2, FT, S]), s.sb("act_g", [P, FT, S])
        pX, pY = s.ps("pX", [P, 2, 512]), s.ps("pY", [P, 2, 512])
        pG, pU = s.ps("pG", [P, 2, 512]), s.ps("pU", [P, 2, 512])
        g_full, u_full, d_full = s.slots("g_full"), s.slots("u_full"), s.slots("d_full")
        idx_ready, gathered, x_turned, x_copied = (s.slots("idx"), s.slots("gathered"), s.slots("x_turned"),
                                                   s.slots("x_copied"))
        hid_mul, silu_done, hid_done, y_mul, y_read, added = (s.slots("hid_mul"), s.slots("silu"), s.slots("hid"),
                                                              s.slots("y_mul"), s.slots("y_read"), s.slots("added"))
        passed = s.sem("passed")
        with nc.Block() as block:
            @block.sync
            def _(sp):
                with sp.Fori(0, E_N // 2) as i:
                    for b in range(2):
                        e = i * 2 + b
                        sp.wait_ge(hid_mul[b], i)
                        sp.dma_start(wg[:, b], w_gate[bass.ds(e, 1)].rearrange("a (k p) f -> p (a k) f", p=P)
                                     ).then_inc(g_full[b], 16)
                        sp.dma_start(wu[:, b], w_up[bass.ds(e, 1)].rearrange("a (k p) f -> p (a k) f", p=P)
                                     ).then_inc(u_full[b], 16)
                        sp.wait_ge(y_mul[b], i * U)
                        sp.dma_start(wd[:, b], w_down[bass.ds(e, 1)].rearrange("a (k p) f -> p (a k) f", p=P)
                                     ).then_inc(d_full[b], 16)

            @block.gpsimd
            def _(pool):
                def gather(b, m):
                    for n, cap in enumerate(caps):
                        if n == 0 and not isinstance(m, int):
                            pool.wait_ge(x_turned[b], m * 2)
                        nc.gpsimd.tensor_copy(own_idx[n][:, b:b + 1], idx[0:cap, n, bass.ds(m * 2 + b, 1)]
                                              ).then_inc(idx_ready[b], 1)
                        pool.wait_ge(idx_ready[b], m * NG + (n + 1))
                        pool.sem_inc(passed, 1)
                        pool.indirect_dma_start(
                            out=xs[n][:, b], out_offset=None, in_=h_dram,
                            in_offset=bass.IndirectOffsetOnAxis(ap=own_idx[n][:, b:b + 1], axis=0),
                            ).then_inc(gathered[b], 16)

                def scatter(b, m):
                    for n, cap in enumerate(caps):
                        pool.wait_ge(y_read[b], m * U + 2 * (n + 1))
                        pool.sem_inc(passed, 1)
                        pool.indirect_dma_start(
                            out=acc_dram, out_offset=bass.IndirectOffsetOnAxis(ap=own_idx[n][:, b:b + 1], axis=0),
                            in_=ys[n][:, b], in_offset=None, compute_op=ALU.add
                            ).then_inc(added[b], 16)
                        pool.wait_ge(added[b], m * (NG * 16) + (n + 1) * 16)

                for b in range(2):
                    gather(b, 0)
                with pool.Fori(0, PAIRS) as i:
                    for b in range(2):
                        scatter(b, i)
                        gather(b, i + 1)
                for b in range(2):
                    scatter(b, PAIRS)

            @block.tensor
            def _(pe):
                def turn(b, m, half):
                    if half == 0:
                        pe.wait_ge(gathered[b], m * (NG * 16) + NG * 16)
                    else:
                        pe.wait_ge(x_copied[b], m * 2 + 1)
                    for j in range(4):
                        k = 4 * half + j
                        for n, cap in enumerate(caps):
                            o = j % 2 * S + offs[n]
                            tr = nc.tensor.transpose(pX[:, j // 2, o:o + cap], xs[n][:, b, k * P:(k + 1) * P],
                                                     ident[0:cap, 0:cap])
                    tr.then_inc(x_turned[b], 1)

                def hidden(b, m):
                    pe.wait_ge(x_copied[b], m * 2 + 2)
                    for w, full, ps in ((wg, g_full, pG), (wu, u_full, pU)):
                        pe.wait_ge(full[b], m * 16 + 16)
                        for f in range(FT):
                            for k in range(KT):
                                mm = nc.tensor.matmul(ps[:, f // 2, f % 2 * S:f % 2 * S + S],
                                                      w[:, b, k, f * P:(f + 1) * P], xT[:, b, k],
                                                      start=(k == 0), stop=(k == KT - 1))
                    mm.then_inc(hid_mul[b], 1)

                def down(b, m, units):
                    pe.wait_ge(hid_done[b], m + 1)
                    pe.wait_ge(d_full[b], m * 16 + 16)
                    for u in units:
                        n, c = UNITS[u]
                        if u >= 2:
                            pe.wait_ge(y_read[b], m * U + (u - 1))
                        elif b or not isinstance(m, int):
                            pe.wait_ge(y_read[1 - b], (m + b) * U)
                        for f in range(FT):
                            mm = nc.tensor.matmul(pY[0:caps[n], c], hid[:, b, f, offs[n]:offs[n] + caps[n]],
                                                  wd[:, b, f, c * 512:(c + 1) * 512], start=(f == 0),
                                                  stop=(f == FT - 1))
                        mm.then_inc(y_mul[b], 1)

                def step(b, m, i):
                    turn(b, m, 0)
                    down(1 - b, i, range(U // 2))
                    turn(b, m, 1)
                    down(1 - b, i, range(U // 2, U))
                    hidden(b, m)

                turn(0, 0, 0)
                turn(0, 0, 1)
                hidden(0, 0)
                with pe.Fori(0, PAIRS) as i:
                    step(1, i, i)
                    step(0, i + 1, i)
                step(1, PAIRS, PAIRS)
                down(1, PAIRS, range(U))

            @block.scalar
            def _(act):
                with act.Fori(0, E_N // 2) as i:
                    for b in range(2):
                        for half in range(2):
                            act.wait_ge(x_turned[b], i * 2 + (half + 1))
                            for j in range(2):
                                k = 4 * half + 2 * j
                                cp = nc.scalar.activation(xT[:, b, k:k + 2], pX[:, j, 0:2 * S].rearrange(
                                    "p (k t) -> p k t", k=2), ACT.Copy)
                            cp.then_inc(x_copied[b], 1)
                        act.wait_ge(hid_mul[b], i + 1)
                        nc.scalar.activation(act_g[:].rearrange("p (a f) t -> p a (f t)", a=2), pG[:, :, 0:2 * S],
                                             ACT.Silu).then_inc(silu_done[b], 1)

            @block.vector
            def _(dve):
                with dve.Fori(0, E_N // 2) as i:
                    for b in range(2):
                        dve.wait_ge(silu_done[b], i + 1)
                        nc.vector.tensor_tensor(hid[:, b].rearrange("p (a f) t -> p a (f t)", a=2),
                                                act_g[:].rearrange("p (a f) t -> p a (f t)", a=2),
                                                pU[:, :, 0:2 * S], ALU.mult).then_inc(hid_done[b], 1)
                        dve.wait_ge(added[b], i * (NG * 16))
                        for u, (n, c) in enumerate(UNITS):
                            dve.wait_ge(y_mul[b], i * U + (u + 1))
                            nc.vector.tensor_scalar(ys[n][:, b, c * 512:(c + 1) * 512], pY[0:caps[n], c],
                                                    gain[0:caps[n], n, bass.ds(i * 2 + b, 1)], None,
                                                    ALU.mult).then_inc(y_read[b], 1)


def add_rows(nc, name, ident, src, x, gate, tokens):
    TURNS = tokens // P // 2
    with Stage(nc, name) as s:
        rows = s.sb("rows", [P, 2, D])
        part = s.sb("part", [P, 2, KT, P])
        ps = s.ps("ps", [P, 2, KT, P])
        full, turned, read, added = s.slots("full"), s.slots("turned"), s.slots("read"), s.slots("added")
        with nc.Block() as block:
            @block.sync
            def _(sp):
                with sp.Fori(0, TURNS) as i:
                    for b in range(2):
                        sp.wait_ge(turned[b], i)
                        sp.dma_start(rows[:, b], src[bass.ds((i * 2 + b) * P, P), :]).then_inc(full[b], 16)

            @block.tensor
            def _(pe):
                with pe.Fori(0, TURNS) as i:
                    for b in range(2):
                        pe.wait_ge(full[b], i * 16 + 16)
                        pe.wait_ge(read[b], i)
                        for k in range(KT):
                            tr = nc.tensor.transpose(ps[:, b, k], rows[:, b, k * P:(k + 1) * P], ident)
                        tr.then_inc(turned[b], 1)

            @block.vector
            def _(dve):
                with dve.Fori(0, TURNS) as i:
                    for b in range(2):
                        dve.wait_ge(turned[b], i + 1)
                        dve.wait_ge(added[b], i)
                        nc.vector.tensor_tensor(part[:, b], ps[:, b], gate.unsqueeze(2).to_broadcast([P, KT, P]),
                                                ALU.mult).then_inc(read[b], 1)

            @block.gpsimd
            def _(pool):
                with pool.Fori(0, TURNS) as i:
                    for b in range(2):
                        pool.wait_ge(read[b], i + 1)
                        own = x[:, :, bass.ds((i * 2 + b) * P, P)]
                        nc.gpsimd.tensor_tensor(own, own, part[:, b], ALU.add).then_inc(added[b], 1)


def second_layer(nc, cst, ident, ones, a, scratch, layer, mod, xT, cT, last):
    nm = f"l{layer}_"
    tokens = L if last else T
    spans = [x for x in CHUNKS if x[0] < tokens]

    def sb(stack, name, shape, dt=F32):
        return stack.enter_context(nc.sbuf_tensor(nm + name, shape, dt))

    w_in, w_uq, w_ukv = a["w_in_2"][layer], a["w_uq_2"][layer], a["w_ukv_2"][layer]
    with ExitStack() as mixing:
        mixT = sb(mixing, "mixT", [P, KT, T])
        norm_modulate(nc, nm + "norm1", ones, [(xT, 0, L, mixT, col(mod, 0), col(mod, 1)),
                                               (cT, L, C, mixT, col(mod, 0, 1), col(mod, 1, 1))])
        inner = mixing.enter_context(ExitStack())
        pq, kvr = sb(inner, "pq", [P, 2, T]), sb(inner, "kvr", [P, 2, T])
        kv, kr = kvr[:, 0:1], kvr[:, 1]
        with ExitStack() as tmp:
            uT, fT, vn = sb(tmp, "uT", [P, 2, T]), sb(tmp, "fT", [P, 2, T]), sb(tmp, "vn", [P, T // P, SGU_W])
            project_mixers(nc, nm + "in", ones, mixT, w_in, tokens, uT, vn, fT, pq, kv[:, 0], kr)
            gate_tokens(nc, nm + "sgu", ident, uT, vn, a["sgu_norm_2"][layer], a["w_sgu_2"][layer],
                        a["b_sgu_2"][layer], tokens, mixT)
            fourier(nc, nm + "fnet", cst, fT, [(0, L, "l")] + ([] if last else [(L, C, "c")]), mixT)
        latent_norm(nc, nm + "qnorm", ones, pq, 2, Q_LORA, a["q_lora_norm_2"][layer], spans)
        latent_norm(nc, nm + "kvnorm", ones, kv, 1, KV_LORA, a["kv_lora_norm_2"][layer], CHUNKS)
        v = sb(inner, "v", [P, T // P, MH * VD])
        values(nc, nm + "v", kv[:, 0], w_ukv, v)
        spare = flat(mixT[:, 4:8])
        kn, krope = sb(inner, "kn", [P, MH, T]), sb(inner, "krope", [P, 2, T])
        ukv = w_ukv.rearrange("(k p) (h c) -> p k h c", p=P, h=MH)
        heads_qk(nc, nm + "k", cst, ones, kv, 1, lambda h: ukv[:, :, h, 0:NOPE], None, kr, a["k_norm_2"][layer],
                 CHUNKS, kn, krope, spare)
        qn, qr = sb(inner, "qn", [P, MH, T]), kvr
        uq = w_uq.rearrange("(k p) (h c) -> p k h c", p=P, h=MH)
        heads_qk(nc, nm + "q", cst, ones, pq, 2, lambda h: uq[:, :, h, 0:NOPE], lambda h: uq[:, :, h, NOPE:],
                 None, a["q_norm_2"][layer], spans, qn, qr, spare)
        attend(nc, nm + "att", ident, qn, qr, kn, krope, v, 0, L // P, 0, mixT)
        if not last:
            attend(nc, nm + "att_ctx", ident, qn, qr, kn, krope, v, L, C // P, L, mixT)
        inner.close()
        hi, lo = sb(mixing, "mix_hi", [P, KT, tokens], F32R), sb(mixing, "mix_lo", [P, KT, tokens], F32R)
        parts = [(xT, col(mod, 2), 0, L)] + ([] if last else [(cT, col(mod, 2, 1), L, C)])
        project(nc, nm + "w_out", columns_of(a["w_out_2"][layer]), KT, KT,
                split_columns(nc, nm + "split_mix", mixT[:, :, 0:tokens], hi, lo), spans, add_gated(nc, *parts))
    groups = [(0, L, 2 * L // E_N, 0)] + ([] if last else [(L, C, 2 * C // E_N, 1)])
    with ExitStack() as moe:
        idx, gain = sb(moe, "idx", [P, len(groups), E_N], U32), sb(moe, "gain", [P, len(groups), E_N])
        with ExitStack() as tmp:
            h2 = sb(tmp, "h2", [P, KT, tokens])
            norm_modulate(nc, nm + "norm2", ones, [(xT, 0, L, h2, col(mod, 3), col(mod, 4))] + (
                [] if last else [(cT, L, C, h2, col(mod, 3, 1), col(mod, 4, 1))]))
            store_rows(nc, nm + "store_h", ident, h2, tokens, scratch["h"], scratch["acc"])
            choose_tokens(nc, nm + "choose", ident, h2, a["w_router_2"][layer], groups, idx, gain)
        run_experts(nc, nm + "experts", ident, groups, idx, gain, scratch["h"][0:tokens, :],
                    scratch["acc"][0:tokens, :],
                    a["w_gate_2"][layer], a["w_up_2"][layer], a["w_down_2"][layer])
    add_rows(nc, nm + "add", ident, scratch["acc"], xT, col(mod, 5), L)
    if not last:
        add_rows(nc, nm + "add_ctx", ident, scratch["acc"][L:, :], cT, col(mod, 5, 1), C)


def build(nc, a, cst, out):
    scratch = {name: nc.dram_tensor("s_" + name, shape, F32, kind="Internal").ap()
               for name, shape in (("gates", (2 * D, L)), ("g", (512, L)), ("ya", (512, L)), ("yr", (512, L)),
                                   ("kk", (512, T)), ("h", (T, D)), ("acc", (T, D)))}
    with ExitStack() as stack:
        def sb(name, shape):
            return stack.enter_context(nc.sbuf_tensor(name, shape, F32))

        ident, ones, mod = sb("ident", [P, P]), sb("ones", [P, P]), sb("mod", [P, 6 * KT, 2])
        load_matrix(nc, "load_ident", cst["ident"], ident)
        load_matrix(nc, "load_ones", cst["ones"], ones)
        first_mixers(nc, cst, ident[:], ones[:], a, scratch, mod)
        xT = sb("xT", [P, KT, L])
        first_rest(nc, ident[:], ones[:], a, scratch, mod, xT)
        cT = sb("cT", [P, KT, C])
        load_transposed(nc, "load_ctx2", ident[:], a["ctx_2"][0], cT, C)
        for layer in range(2):
            modulation(nc, f"b2_mod{layer}", ident[:], a["c_2"][0], a["c_ctx_2"], a["w_ada_2"][layer], a["b_ada_2"][layer],
                       mod)
            second_layer(nc, cst, ident[:], ones[:], a, scratch, layer, mod, xT, cT, layer == 1)
        store_rows(nc, "store_out", ident[:], xT, L, out)



def constants():
    f = np.float32
    out = {"ident": np.eye(P, dtype=f), "ones": np.ones((P, P), f)}
    out["ones64"] = np.kron(np.eye(2), np.ones((64, 64))).astype(f)
    pos = np.arange(L)
    row, col = pos // 64, pos % 64

    def rotation(half):
        r = np.zeros((P, P), f)
        for p in range(P):
            if p % (2 * half) < half:
                r[p + half, p] = -1.0
            else:
                r[p - half, p] = 1.0
        return r

    inv = (10000.0 ** (-np.arange(16) / 16.0)).astype(f)
    ang = np.concatenate([row[:, None].astype(f) * inv, col[:, None].astype(f) * inv], axis=1)
    ang1 = ang[:, np.arange(P) % 32].T
    out["cos1"], out["sin1"], out["rot1"] = np.cos(ang1).astype(f), np.sin(ang1).astype(f), rotation(32)
    p64 = np.arange(P) % 64
    ang2 = ang[:, (p64 // 32) * 16 + p64 % 16].T
    out["cos2"], out["sin2"], out["rot2"] = np.cos(ang2).astype(f), np.sin(ang2).astype(f), rotation(16)

    q, k = np.arange(P)[:, None], np.arange(P)[None, :]
    window = np.zeros((P, L // P, 2, P), f)
    window[:, :, 0][np.broadcast_to((k < q)[:, None], (P, L // P, P))] = NEG
    window[:, :, 1][np.broadcast_to((k > q)[:, None], (P, L // P, P))] = NEG
    window[:, 0, 0] = NEG
    window[:, -1, 1] = NEG
    out["window"] = window

    i, j = np.arange(64)[None, :], np.arange(64)[:, None]
    masks = np.zeros((2, 8, 64, 64), f)
    for lv in range(6):
        b = 1 << lv
        masks[0, lv] = (i // b % 2 == 1) & (j // b == i // b - 1)
    masks[0, 6], masks[0, 7] = j < i, j <= i
    masks[1] = masks[0].transpose(0, 2, 1)
    m = masks.transpose(2, 0, 1, 3)
    out["masks"] = np.concatenate([m, m], axis=0).copy()

    for nm, n in (("l", L), ("c", C)):
        a = 2 * np.pi * ((np.arange(n)[:, None] * np.arange(n)[None, :]) % n) / n
        out["dft_cos_" + nm] = (np.cos(a) / np.sqrt(n)).astype(f)
        out["dft_sin_" + nm] = (np.sin(a) / np.sqrt(n)).astype(f)
    a = 2 * np.pi * ((np.arange(64)[:, None] * np.arange(64)[None, :]) % 64) / 64
    out["dft64"] = np.concatenate([np.kron(np.eye(2), np.cos(a)), -np.kron(np.eye(2), np.sin(a))],
                                  axis=1).astype(f) / f(8)
    return out


_INS = ["x", "c", "ctx", "c_ctx", "w_ada", "b_ada", "norm1_g", "w_in", "sink", "conv_w", "decay_w0", "decay_w2",
        "iclr_a0", "iclr_a2", "gate_g2", "k_k", "k_a", "r_k", "lnx_w", "lnx_b", "w_branch_attn", "w_branch_rwkv",
        "w_out", "norm2_g", "w_mlp_up", "w_mlp_down", "norm_f_g", "c_2", "ctx_2", "c_ctx_2", "w_ada_2", "b_ada_2",
        "w_in_2", "sgu_norm_2", "w_sgu_2", "b_sgu_2", "q_lora_norm_2", "w_uq_2", "kv_lora_norm_2", "w_ukv_2",
        "q_norm_2", "k_norm_2", "w_out_2", "w_router_2", "w_gate_2", "w_up_2", "w_down_2"]


def kernel(**inputs):
    import numpy as _np
    import concourse.bacc as _bacc
    from concourse import mybir as _mybir
    from concourse.bass_utils import run_bass_kernel_spmd as _run

    nc = _bacc.Bacc("TRN2", target_bir_lowering=False, num_devices=1)
    arrays, a, cst = {}, {}, {}
    for group, names in ((a, _INS), (cst, None)):
        values = constants() if names is None else {name: inputs[name] for name in names}
        for name, value in values.items():
            full = ("in_" if names else "const_") + name + "_dram"
            arrays[full] = _np.ascontiguousarray(value)
            group[name] = nc.dram_tensor(full, arrays[full].shape, _mybir.dt.from_np(arrays[full].dtype),
                                         kind="ExternalInput").ap()
    out = nc.dram_tensor("out_0_dram", (1, L, D), _mybir.dt.float32, kind="ExternalOutput").ap()
    build(nc, a, cst, out[0])
    r = _run(nc, [arrays], core_ids=[0])
    return r.results[0]["out_0_dram"]
```

```python
from contextlib import ExitStack

import numpy as np
import concourse.bass as bass
from concourse import mybir

F32 = mybir.dt.float32
I32 = mybir.dt.int32
U32 = mybir.dt.uint32
F32R = mybir.dt.float32r
ALU = mybir.AluOpType
ACT = mybir.ActivationFunctionType
AX = mybir.AxisListType

P = 128
D = 1024
KT = D // P
L = 1024
C = 256
T = L + C
CHUNKS = [(0, 512), (512, 512), (1024, 256)]
LAT = CHUNKS[:2]
HD = 64
NQ = 8
WQ, WKV, WRW = 512, 128, 1696
EPS = 1e-6
NEG = -1.0e30


class Stage:

    def __init__(self, nc, name):
        self.nc, self.name, self.sems, self.stack = nc, name, [], ExitStack()

    def __enter__(self):
        self.stack.__enter__()
        return self

    def sb(self, name, shape, dt=F32):
        return self.stack.enter_context(self.nc.sbuf_tensor(f"{self.name}_{name}", shape, dt))

    def ps(self, name, shape, dt=F32):
        return self.stack.enter_context(self.nc.psum_tensor(f"{self.name}_{name}", shape, dt))

    def sem(self, name):
        self.sems.append(self.nc.alloc_semaphore(name=f"{self.name}_{name}"))
        return self.sems[-1]

    def slots(self, name, n=2):
        return [self.sem(f"{name}{b}") for b in range(n)]

    def __exit__(self, *e):
        if e[0] is None:
            self.nc.clear_and_free_semaphores(self.sems)
            self.nc.all_engine_barrier()
        return self.stack.__exit__(*e)


class Chain:

    def __init__(self, eng, sem, i=None, per=0):
        self.eng, self.sem, self.i, self.per, self.n = eng, sem, i, per, 0

    def __call__(self, ins):
        self.n += 1
        ins.then_inc(self.sem, 1)
        self.eng.wait_ge(self.sem, self.n if self.i is None else self.i * self.per + self.n)

    def close(self):
        assert self.i is None or self.n == self.per, f"{self.n} links, not {self.per}"


def by_tiles(ap):
    return ap.rearrange("(k p) m -> p k m", p=P)



class SplitWeights:

    def __init__(self, nc, s, kt, ps_full, uses):
        self.nc, self.ps_full, self.uses = nc, ps_full, uses
        self.raw = s.sb("w", [P, 2, kt, P])
        self.hi, self.lo = s.sb("w_hi", [P, 2, kt, P], F32R), s.sb("w_lo", [P, 2, kt, P], F32R)
        self.passed = s.sem("w_passed")
        self.full, self.hi_done, self.split_done = s.slots("w_full"), s.slots("w_hi"), s.slots("w_split")

    def load(self, sp, b, ordinal, source):
        sp.wait_ge(self.split_done[b], ordinal)
        sp.dma_start(self.raw[:, b], source).then_inc(self.full[b], 16)

    def split(self, pool, b, ordinal, full=None):
        nc = self.nc
        pool.wait_ge(self.full[b], ordinal * 16 + 16 if full is None else full)
        pool.wait_ge(self.ps_full[b], ordinal * self.uses)
        pool.sem_inc(self.passed, 1)
        nc.gpsimd.tensor_copy(self.hi[:, b], self.raw[:, b]).then_inc(self.hi_done[b], 1)
        pool.wait_ge(self.hi_done[b], ordinal + 1)
        nc.gpsimd.tensor_tensor(self.lo[:, b], self.raw[:, b], self.hi[:, b].bitcast(F32), ALU.subtract
                                ).then_inc(self.split_done[b], 1)

    def multiply(self, pe, b, ordinal, rhs, kt, spans, ps, rows=P):
        pe.wait_ge(self.split_done[b], ordinal + 1)
        for c, (t0, n) in enumerate(spans):
            for k in range(kt):
                for j, (w, x) in enumerate(((self.hi, rhs[0]), (self.hi, rhs[1]), (self.lo, rhs[0]))):
                    mm = self.nc.tensor.matmul(ps[0:rows, c, 0:n], w[:, b, k, 0:rows], x[:, k, t0:t0 + n],
                                               start=(k + j == 0), stop=(k == kt - 1 and j == 2))
        mm.then_inc(self.ps_full[b], 1)


def split_columns(nc, name, x, hi, lo):
    with Stage(nc, name) as s:
        hi_done = s.sem("hi")
        with nc.Block() as block:
            @block.scalar
            def _(act):
                for k in range(x.shape[1]):
                    nc.scalar.activation(hi[:, k], x[:, k], ACT.Copy).then_inc(hi_done, 1)

            @block.vector
            def _(dve):
                for k in range(x.shape[1]):
                    dve.wait_ge(hi_done, k + 1)
                    nc.vector.tensor_tensor(lo[:, k], x[:, k], hi[:, k].bitcast(F32), ALU.subtract)
    return hi, lo



class Modulation:

    W = 512
    STEPS = 6 * D // W

    def __init__(self, nc, s, ident, conds, w_ada, b_ada, mod, banks, pt):
        self.nc, self.ident, self.conds, self.w_ada, self.b_ada = nc, ident, conds, w_ada, b_ada
        self.mod, self.banks, self.pt, self.slots = mod, banks, pt, len(banks)
        self.cond_sb, self.silu_sb = s.sb("cond", [P, KT, 2]), s.sb("silu_sb", [P, KT, 2])
        self.bias = s.sb("bias", [P, 6 * KT, 2])
        self.w = s.sb("w_ada", [P, self.slots, KT, self.W])
        self.rows = s.sb("mod_rows", [2, 6 * D])
        self.small_loaded, self.silu_done, self.turned = s.sem("mod_small"), s.sem("mod_silu"), s.sem("mod_turned")
        self.w_full, self.ps_full, self.ps_free = (s.slots("mod_w", self.slots), s.slots("mod_ps_full", self.slots),
                                                   s.slots("mod_ps_free", self.slots))

    def load_small(self, eng):
        with self.nc.allow_non_contiguous_dma("vectors into columns"):
            for j, v in enumerate(self.conds):
                eng.dma_start(self.cond_sb[:, :, j], v.rearrange("(k p) -> p k", p=P)).then_inc(self.small_loaded, 16)
            for j in range(2):
                eng.dma_start(self.bias[:, :, j], self.b_ada.rearrange("(k p) -> p k", p=P)
                              ).then_inc(self.small_loaded, 16)

    def load(self, eng):
        with eng.Fori(0, self.STEPS // self.slots) as i:
            for b in range(self.slots):
                eng.wait_ge(self.ps_full[b], i)
                eng.dma_start(self.w[:, b], by_tiles(self.w_ada)[:, :, bass.ds((i * self.slots + b) * self.W, self.W)]
                              ).then_inc(self.w_full[b], 16)

    def silu(self, act):
        act.wait_ge(self.small_loaded, 64)
        self.nc.scalar.activation(self.silu_sb[:], self.cond_sb[:], ACT.Silu).then_inc(self.silu_done, 1)

    def multiply(self, pe, b, i):
        if isinstance(i, int) and i == 0:
            pe.wait_ge(self.silu_done, 1)
        else:
            pe.wait_ge(self.ps_free[b], i)
        pe.wait_ge(self.w_full[b], i * 16 + 16)
        for k in range(KT):
            mm = self.nc.tensor.matmul(self.banks[b][0:2, :], self.silu_sb[:, k], self.w[:, b, k], start=(k == 0),
                                       stop=(k == KT - 1))
        mm.then_inc(self.ps_full[b], 1)

    def read_out(self, act, b, i):
        act.wait_ge(self.ps_full[b], i + 1)
        self.nc.scalar.activation(self.rows[:, bass.ds((i * self.slots + b) * self.W, self.W)], self.banks[b][0:2, :],
                                  ACT.Copy).then_inc(self.ps_free[b], 1)

    def turn(self, pe):
        for b in range(self.slots):
            pe.wait_ge(self.ps_free[b], self.STEPS // self.slots)
        for f in range(6 * KT):
            tr = self.nc.tensor.transpose(self.pt[:, 2 * f:2 * f + 2], self.rows[:, f * P:(f + 1) * P],
                                          self.ident[0:2, 0:2])
        tr.then_inc(self.turned, 1)

    def add_bias(self, dve):
        dve.wait_ge(self.small_loaded, 64)
        dve.wait_ge(self.turned, 1)
        self.nc.vector.tensor_tensor(self.mod[:], self.pt[:, 0:12 * KT].rearrange("p (f j) -> p f j", j=2),
                                     self.bias[:], ALU.add)


def modulation(nc, name, ident, conds, w_ada, b_ada, mod):
    with Stage(nc, name) as s:
        ps, pt = s.ps("ps", [P, 3, 512]), s.ps("pt", [P, 512])
        m = Modulation(nc, s, ident, conds, w_ada, b_ada, mod, [ps[:, b] for b in range(3)], pt)
        with nc.Block() as block:
            @block.sync
            def _(sp):
                m.load_small(sp)
                m.load(sp)

            @block.scalar
            def _(act):
                m.silu(act)
                with act.Fori(0, m.STEPS // m.slots) as i:
                    for b in range(m.slots):
                        m.read_out(act, b, i)

            @block.tensor
            def _(pe):
                pe.wait_ge(m.silu_done, 1)
                with pe.Fori(0, m.STEPS // m.slots) as i:
                    for b in range(m.slots):
                        m.multiply(pe, b, i)
                m.turn(pe)

            @block.vector
            def _(dve):
                m.add_bias(dve)



def load_transposed(nc, name, ident, src, dst, tokens, beside=()):
    TURNS = tokens // P // 2
    with Stage(nc, name) as s:
        rows = s.sb("rows", [P, 2, D])
        ps = s.ps("ps", [P, 2, KT, P])
        full, turned, free = s.slots("full"), s.slots("turned"), s.slots("free")
        others_loaded = s.sem("others_loaded")
        with nc.Block() as block:
            @block.sync
            def _(sp):
                with sp.Fori(0, TURNS) as i:
                    for b in range(2):
                        sp.wait_ge(turned[b], i)
                        sp.dma_start(rows[:, b], src[bass.ds((i * 2 + b) * P, P), :]).then_inc(full[b], 16)

            @block.gpsimd
            def _(pool):
                for to, dram in beside:
                    pool.dma_start(to, dram).then_inc(others_loaded, 16)
                if beside:
                    pool.wait_ge(others_loaded, 16 * len(beside))

            @block.tensor
            def _(pe):
                with pe.Fori(0, TURNS) as i:
                    for b in range(2):
                        pe.wait_ge(full[b], i * 16 + 16)
                        pe.wait_ge(free[b], i)
                        for k in range(KT):
                            tr = nc.tensor.transpose(ps[:, b, k], rows[:, b, k * P:(k + 1) * P], ident)
                        tr.then_inc(turned[b], 1)

            @block.scalar
            def _(act):
                with act.Fori(0, TURNS) as i:
                    act.wait_ge(turned[0], i + 1)
                    nc.scalar.activation(dst[:, :, bass.ds(i * 2 * P, P)], ps[:, 0], ACT.Copy).then_inc(free[0], 1)

            @block.vector
            def _(dve):
                with dve.Fori(0, TURNS) as i:
                    dve.wait_ge(turned[1], i + 1)
                    nc.vector.tensor_copy(dst[:, :, bass.ds(i * 2 * P + P, P)], ps[:, 1]).then_inc(free[1], 1)



def norm_modulate(nc, name, ones, groups, g_vec=None):
    spans = [(n, c0, min(512, gr[2] - c0)) for n, gr in enumerate(groups) for c0 in range(0, gr[2], 512)]
    with Stage(nc, name) as s:
        g = s.sb("g", [P, KT])
        gain = s.sb("gain", [P, len(groups), KT])
        sq = s.sb("sq", [P, 2, 512])
        rstd = s.sb("rstd", [P, len(spans), 512])
        scaled = s.sb("scaled", [P, 2, 512])
        split = isinstance(groups[0][3], tuple)
        whole = s.sb("whole", [P, 2, 512]) if split else None
        hi_done, lo_done = s.sem("hi"), s.sem("lo")
        ps = s.ps("ps", [P, len(spans), 512])
        g_loaded, squared, summed, mean_done = s.sem("g"), s.sem("squared"), s.sem("summed"), s.sem("mean")
        rooted, gain_done = s.sem("rooted"), s.sem("gain")
        inv_done, scaled_done, out_done, chain_sem = s.sem("inv"), s.sem("scaled"), s.sem("out"), s.sem("chain")
        with nc.Block() as block:
            @block.sync
            def _(sp):
                if g_vec is not None:
                    with nc.allow_non_contiguous_dma("a vector into columns"):
                        sp.dma_start(g[:], g_vec.rearrange("(k p) -> p k", p=P)).then_inc(g_loaded, 16)

            @block.scalar
            def _(act):
                for m, (n, c0, w) in enumerate(spans):
                    for k in range(KT):
                        q = m * KT + k
                        if q >= 2:
                            act.wait_ge(summed, q - 1)
                        nc.scalar.activation(sq[:, q % 2, 0:w], groups[n][0][:, k, c0:c0 + w], ACT.Square
                                             ).then_inc(squared, 1)
                for m, (n, c0, w) in enumerate(spans):
                    act.wait_ge(mean_done, m + 1)
                    nc.scalar.activation(rstd[:, m, 0:w], rstd[:, m, 0:w], ACT.Sqrt).then_inc(rooted, 1)
                act.wait_ge(gain_done, len(groups))
                for m, (n, c0, w) in enumerate(spans):
                    _, t0, _, dst, shift, _ = groups[n]
                    for k in range(KT):
                        q = m * KT + k
                        act.wait_ge(scaled_done, q + 1)
                        if split and q >= 2:
                            act.wait_ge(lo_done, q - 1)
                        out = whole[:, q % 2, 0:w] if split else dst[:, k, t0 + c0:t0 + c0 + w]
                        for x, sem in ((out, out_done),) + (((dst[0][:, k, t0 + c0:t0 + c0 + w], hi_done),) if split else ()):
                            nc.scalar.activation(x, scaled[:, q % 2, 0:w], ACT.Identity,
                                                 scale=gain[:, n, k:k + 1],
                                                 bias=0.0 if shift is None else shift[:, k:k + 1]).then_inc(sem, 1)

            @block.tensor
            def _(pe):
                for m, (n, c0, w) in enumerate(spans):
                    for k in range(KT):
                        pe.wait_ge(squared, m * KT + k + 1)
                        nc.tensor.matmul(ps[:, m, 0:w], ones, sq[:, (m * KT + k) % 2, 0:w], start=(k == 0),
                                         stop=(k == KT - 1)).then_inc(summed, 1)

            @block.vector
            def _(dve):
                chain = Chain(dve, chain_sem)
                if g_vec is not None:
                    dve.wait_ge(g_loaded, 16)
                else:
                    chain(nc.vector.memset(g[:], 1.0))
                for n, gr in enumerate(groups):
                    if gr[5] is None:
                        nc.vector.tensor_copy(gain[:, n], g[:]).then_inc(gain_done, 1)
                    else:
                        nc.vector.scalar_tensor_tensor(gain[:, n], gr[5], 1.0, g[:], ALU.add, ALU.mult
                                                       ).then_inc(gain_done, 1)
                for m, (n, c0, w) in enumerate(spans):
                    dve.wait_ge(summed, (m + 1) * KT)
                    nc.vector.tensor_scalar(rstd[:, m, 0:w], ps[:, m, 0:w], 1.0 / D, EPS, ALU.mult, ALU.add
                                            ).then_inc(mean_done, 1)

                def rest(q):
                    n, c0, w = spans[q // KT]
                    t = slice(groups[n][1] + c0, groups[n][1] + c0 + w)
                    hi, lo = groups[n][3]
                    dve.wait_ge(hi_done, q + 1)
                    nc.vector.tensor_tensor(lo[:, q % KT, t], whole[:, q % 2, 0:w], hi[:, q % KT, t].bitcast(F32),
                                            ALU.subtract).then_inc(lo_done, 1)

                for m, (n, c0, w) in enumerate(spans):
                    dve.wait_ge(rooted, m + 1)
                    nc.vector.reciprocal(rstd[:, m, 0:w], rstd[:, m, 0:w]).then_inc(inv_done, 1)
                    dve.wait_ge(inv_done, m + 1)
                    for k in range(KT):
                        q = m * KT + k
                        if q >= 2:
                            dve.wait_ge(hi_done if split else out_done, q - 1)
                        nc.vector.tensor_tensor(scaled[:, q % 2, 0:w], groups[n][0][:, k, c0:c0 + w],
                                                rstd[:, m, 0:w], ALU.mult).then_inc(scaled_done, 1)
                        if split and q:
                            rest(q - 1)
                if split:
                    rest(len(spans) * KT - 1)



def store_columns(nc, name, src, dram):
    with Stage(nc, name) as s:
        stored = s.sem("stored")
        with nc.Block() as block:
            @block.sync
            def _(sp):
                sp.dma_start(by_tiles(dram), src).then_inc(stored, 16)
                sp.wait_ge(stored, 16)


def load_matrix(nc, name, dram, dst):
    with Stage(nc, name) as s:
        loaded = s.sem("loaded")
        with nc.Block() as block:
            @block.sync
            def _(sp):
                sp.dma_start(dst[:], dram).then_inc(loaded, 16)
                sp.wait_ge(loaded, 16)



def project_qkv(nc, name, cst, ident, h, w_in, qT, kT, v, spare):
    NT = 6
    with Stage(nc, name) as s:
        cos, sin = spare[:, 0:L], spare[:, L:2 * L]
        rot = s.sb("rot", [P, P])
        raw = s.sb("raw", [P, 2, T])
        part = s.sb("part", [P, 2, 512])
        ps = s.ps("ps", [P, 3, 512])
        pr = s.ps("pr", [P, 2, 512])
        pv = s.ps("pv", [P, 2, 512])
        loaded, mul_done = s.sem("loaded"), s.slots("mul")
        w = SplitWeights(nc, s, KT, mul_done, 1)
        raw_done, rot_done, rot_read = s.sem("raw"), s.sem("rot"), s.sem("rot_read")
        cos_done, v_done, v_read, chain_sem = s.sem("cos"), s.sem("v"), s.sem("v_read"), s.sem("chain")
        halves = [(0, 512), (512, 512)]
        with nc.Block() as block:
            @block.sync
            def _(sp):
                sp.dma_start(cos[:], cst["cos1"]).then_inc(loaded, 16)
                sp.dma_start(sin[:], cst["sin1"]).then_inc(loaded, 16)
                sp.dma_start(rot[:], cst["rot1"]).then_inc(loaded, 16)
                for m in range(NT):
                    if m < 4:
                        sp.wait_ge(w.split_done[m % 2], m // 2)
                        for h_no in range(2):
                            c0 = (m + 4 * h_no) * HD
                            sp.dma_start(w.raw[:, m % 2, :, h_no * HD:(h_no + 1) * HD], by_tiles(w_in)[:, :, c0:c0 + HD]
                                         ).then_inc(w.full[m % 2], 16)
                    else:
                        w.load(sp, m % 2, m // 2, by_tiles(w_in)[:, :, WQ + (m - 4) * WKV:WQ + (m - 3) * WKV])

            @block.gpsimd
            def _(pool):
                for m in range(NT):
                    w.split(pool, m % 2, m // 2, full=32 * (m // 2 + 1) if m < 4 else 80)

            @block.tensor
            def _(pe):
                def rotate(m):
                    pe.wait_ge(raw_done, m + 1)
                    for c, (t0, n) in enumerate(halves):
                        if 2 * m + c >= 2:
                            pe.wait_ge(rot_read, 2 * m + c - 1)
                        nc.tensor.matmul(pr[:, c], rot[:], raw[:, m % 2, t0:t0 + n], start=True, stop=True
                                         ).then_inc(rot_done, 1)

                pe.wait_ge(loaded, 48)
                for m in range(NT):
                    if m:
                        pe.wait_ge(raw_done, m)
                    w.multiply(pe, m % 2, m // 2, h, KT, LAT if m < 4 else CHUNKS, ps)
                    if m:
                        rotate(m - 1)
                pe.wait_ge(raw_done, NT)
                for t in range(T // P):
                    if t >= 2:
                        pe.wait_ge(v_read, t - 1)
                    nc.tensor.transpose(pv[:, t % 2, 0:WKV], raw[:, (NT - 1) % 2, t * P:(t + 1) * P], ident
                                        ).then_inc(v_done, 1)

            @block.scalar
            def _(act):
                for m in range(NT):
                    act.wait_ge(mul_done[m % 2], m // 2 + 1)
                    if m >= 2:
                        act.wait_ge(cos_done, 2 * (m - 1))
                    spans = LAT if m < 4 else CHUNKS
                    for t0, n in spans:
                        ev = nc.scalar.activation(raw[:, m % 2, t0:t0 + n], ps[:, t0 // 512, 0:n], ACT.Copy)
                    ev.then_inc(raw_done, 1)
                for t in range(T // P):
                    act.wait_ge(v_done, t + 1)
                    nc.scalar.activation(v[:, t], pv[:, t % 2, 0:WKV], ACT.Copy).then_inc(v_read, 1)

            @block.vector
            def _(dve):
                chain = Chain(dve, chain_sem)
                dve.wait_ge(loaded, 48)
                for m in range(NT - 1):
                    dve.wait_ge(raw_done, m + 1)
                    for c, (t0, n) in enumerate(halves):
                        dst = qT[:, m, t0:t0 + n] if m < 4 else kT[:, t0:t0 + n]
                        dve.wait_ge(rot_done, 2 * m + c + 1)
                        chain(nc.vector.tensor_tensor(part[:, c], pr[:, c], sin[:, t0:t0 + n], ALU.mult))
                        nc.vector.sem_inc(rot_read, 1)
                        chain(nc.vector.tensor_tensor(dst, raw[:, m % 2, t0:t0 + n], cos[:, t0:t0 + n], ALU.mult))
                        nc.vector.tensor_tensor(dst, dst, part[:, c], ALU.add).then_inc(cos_done, 1)
                dve.wait_ge(cos_done, 2 * (NT - 1))
                nc.vector.tensor_copy(kT[:, L:T], raw[:, (NT - 2) % 2, L:T])


def project_gates(nc, name, h, w_gl, gates_dram):
    NT = 2 * KT
    with Stage(nc, name) as s:
        out = s.sb("out", [P, 2, L])
        ps = s.ps("ps", [P, 2, 2, 512])
        ps_full, ps_free, stored = s.slots("ps_full"), s.slots("ps_free"), s.slots("stored")
        w = SplitWeights(nc, s, KT, ps_full, 1)
        with nc.Block() as block:
            @block.sync
            def _(sp):
                with sp.Fori(0, NT // 2) as i:
                    for b in range(2):
                        w.load(sp, b, i, by_tiles(w_gl)[:, :, bass.ds(i * (2 * P) + b * P, P)])

            @block.gpsimd
            def _(pool):
                with pool.Fori(0, NT // 2) as i:
                    for b in range(2):
                        w.split(pool, b, i)

            @block.tensor
            def _(pe):
                with pe.Fori(0, NT // 2) as i:
                    for b in range(2):
                        pe.wait_ge(ps_free[b], i)
                        w.multiply(pe, b, i, h, KT, LAT, ps[:, b])

            @block.scalar
            def _(act):
                with act.Fori(0, NT // 2) as i:
                    for b in range(2):
                        act.wait_ge(ps_full[b], i + 1)
                        act.wait_ge(stored[b], i * 16)
                        nc.scalar.activation(out[:, b], ps[:, b].rearrange("p c t -> p (c t)"), ACT.Sigmoid
                                             ).then_inc(ps_free[b], 1)
                        act.wait_ge(ps_free[b], i + 1)
                        act.dma_start(gates_dram[bass.ds((i * 2 + b) * P, P), :], out[:, b]).then_inc(stored[b], 16)
                for b in range(2):
                    act.wait_ge(stored[b], NT // 2 * 16)


def project_rwkv(nc, name, h, w_rw, conv_w, rkv, lora_a, lora_b):
    NT = 14
    with Stage(nc, name) as s:
        cw = s.sb("cw", [P, 3, NT])
        raw = s.sb("raw", [P, 2, T + 4])
        ps = s.ps("ps", [P, 2, 3, 512])
        cw_loaded, zeroed, tail_conv = s.sem("cw"), s.sem("zeroed"), s.sem("tail")
        ps_full, ps_free, conv_done = s.slots("ps_full"), s.slots("ps_free"), s.slots("conv")
        w = SplitWeights(nc, s, KT, ps_full, 1)
        chain_sem = s.sem("chain")
        SEQS = [(1, 0, L), (L + 3, L, C)]
        with nc.Block() as block:
            @block.sync
            def _(sp):
                with nc.allow_non_contiguous_dma("vectors into columns"):
                    for j in range(3):
                        sp.dma_start(cw[:, j, 0:13], conv_w[j, 0:13 * P].rearrange("(k p) -> p k", p=P)
                                     ).then_inc(cw_loaded, 16)
                        sp.dma_start(cw[0:32, j, 13:14], conv_w[j, 13 * P:WRW].rearrange("(p k) -> p k", k=1)
                                     ).then_inc(cw_loaded, 16)
                with sp.Fori(0, 6) as i:
                    for b in range(2):
                        w.load(sp, b, i, by_tiles(w_rw)[:, :, bass.ds(i * (2 * P) + b * P, P)])
                w.load(sp, 0, 6, by_tiles(w_rw)[:, :, 12 * P:13 * P])
                sp.wait_ge(w.split_done[1], 6)
                sp.dma_start(w.raw[:, 1, :, 0:32], by_tiles(w_rw)[:, :, 13 * P:WRW]).then_inc(w.full[1], 16)

            @block.gpsimd
            def _(pool):
                with pool.Fori(0, 7) as i:
                    for b in range(2):
                        w.split(pool, b, i)

            @block.tensor
            def _(pe):
                with pe.Fori(0, 6) as i:
                    for b in range(2):
                        pe.wait_ge(ps_free[b], i)
                        w.multiply(pe, b, i, h, KT, CHUNKS, ps[:, b])
                for b, rows in ((0, P), (1, 32)):
                    pe.wait_ge(ps_free[b], 6)
                    w.multiply(pe, b, 6, h, KT, CHUNKS, ps[:, b], rows)

            def copy_out(act, b, rows):
                for (r0, t0, n) in ((1, 0, 512), (513, 512, 512), (L + 3, L, C)):
                    ev = nc.scalar.activation(raw[0:rows, b, r0:r0 + n], ps[0:rows, b, t0 // 512, 0:n], ACT.Copy)
                ev.then_inc(ps_free[b], 1)

            @block.scalar
            def _(act):
                act.wait_ge(zeroed, 1)
                with act.Fori(0, 6) as i:
                    for b in range(2):
                        act.wait_ge(ps_full[b], i + 1)
                        act.wait_ge(conv_done[b], i)
                        copy_out(act, b, P)
                for b, rows in ((0, P), (1, 32)):
                    act.wait_ge(ps_full[b], 7)
                    act.wait_ge(conv_done[b], 6)
                    copy_out(act, b, rows)

            def convolve(dve, chain, b, rows, dst, weight, done):
                for r0, t0, n in SEQS:
                    out = dst(t0, n)
                    chain(nc.vector.tensor_scalar(out, raw[0:rows, b, r0 - 1:r0 - 1 + n], weight(0), None, ALU.mult))
                    chain(nc.vector.scalar_tensor_tensor(out, raw[0:rows, b, r0:r0 + n], weight(1), out,
                                                         ALU.mult, ALU.add))
                    ins = nc.vector.scalar_tensor_tensor(out, raw[0:rows, b, r0 + 1:r0 + 1 + n], weight(2), out,
                                                         ALU.mult, ALU.add)
                ins.then_inc(done, 1)

            @block.vector
            def _(dve):
                nc.vector.memset(raw[:], 0.0).then_inc(zeroed, 1)
                dve.wait_ge(cw_loaded, 96)
                with dve.Fori(0, 6) as i:
                    chain = Chain(dve, chain_sem, i, 8)
                    for b in range(2):
                        dve.wait_ge(ps_free[b], i + 1)
                        m = i * 2 + b
                        convolve(dve, chain, b, P, lambda t0, n: rkv[:, bass.ds(m, 1), t0:t0 + n].rearrange(
                            "p a t -> p (a t)"), lambda j: cw[:, j, bass.ds(m, 1)], conv_done[b])
                    chain.close()
                chain = Chain(dve, chain_sem)
                chain.n = 48
                for b, rows, dst in ((0, P, lora_a), (1, 32, lora_b)):
                    dve.wait_ge(ps_free[b], 7)
                    convolve(dve, chain, b, rows, lambda t0, n: dst[0:rows, t0:t0 + n],
                             lambda j: cw[0:rows, j, 12 + b:13 + b], tail_conv)



def window_attention(nc, name, cst, ident, qT, kT, v, kpad, vpad, sink, yT):
    H = NQ
    SC = HD ** -0.5
    NK = C + 3 * P
    U = 2 * H
    TURNS = L // P // 2
    with Stage(nc, name) as s:
        qs, ks, vs = s.sb("qs", [P, 2, 4, P]), s.sb("ks", [P, 2, NK]), s.sb("vs", [P, 2, 3, WKV])
        window = s.sb("window", [P, L // P, 2, P])
        sk, nsk = s.sb("sk", [P, H]), s.sb("nsk", [P, H])
        prob, probT = s.sb("prob", [P, 2, NK]), s.sb("probT", [P, 2, 5, P])
        nmax, total, rest, inv = s.sb("nmax", [P, 2]), s.sb("total", [P, 2]), s.sb("rest", [P, 2]), s.sb("inv", [P, 2])
        nm = s.sb("nm", [P, 2])
        pS, pT = s.ps("pS", [P, 2, 1024]), s.ps("pT", [P, 8, P])
        pO = s.ps("pO", [P, 512])
        loaded, padded, ready = s.sem("loaded"), s.sem("padded"), s.sem("ready")
        staged = s.slots("staged")
        s_full, max_done = s.slots("s_full"), s.slots("max")
        t_done, t_copied, pv_done, sums = s.slots("t_done"), s.slots("t_copied"), s.slots("pv"), s.slots("sums")
        sums_read = s.slots("sums_read")
        o_done, block_done, normed, chain_sem = s.slots("o"), s.slots("block_done"), s.slots("normed"), s.sem("chain")

        def at(i, u):
            return i * (U // 2) + u // 2

        with nc.Block() as block:
            @block.sync
            def _(sp):
                sp.dma_start(window[:], cst["window"]).then_inc(loaded, 16)
                sp.dma_start(sk[:], sink.partition_broadcast(P)).then_inc(loaded, 16)

            @block.gpsimd
            def _(pool):
                for x in (kpad[:, 0:P], kpad[:, P + L:], vpad[:, 0], vpad[:, L // P + 1]):
                    nc.gpsimd.memset(x, 0.0).then_inc(padded, 1)
                nc.gpsimd.tensor_copy(kpad[:, P:P + L], kT[:, 0:L]).then_inc(padded, 1)
                nc.gpsimd.tensor_copy(vpad[:, 1:1 + L // P], v[:, 0:L // P]).then_inc(padded, 1)
                for b in range(2):
                    nc.gpsimd.tensor_copy(ks[:, b, 0:C], kT[:, L:T]).then_inc(padded, 1)
                pool.wait_ge(padded, 8)
                with pool.Fori(0, TURNS) as i:
                    for b in range(2):
                        n = i * 2 + b
                        pool.wait_ge(block_done[b], i)
                        nc.gpsimd.tensor_copy(qs[:, b], qT[:, :, bass.ds(n * P, P)]).then_inc(staged[b], 1)
                        nc.gpsimd.tensor_copy(ks[:, b, C:NK], kpad[:, bass.ds(n * P, 3 * P)]).then_inc(staged[b], 1)
                        nc.gpsimd.tensor_copy(vs[:, b], vpad[:, bass.ds(n, 3)]).then_inc(staged[b], 1)

            @block.tensor
            def _(pe):
                with pe.Fori(0, TURNS) as i:
                    def scores(u):
                        b, h, p = u // H, u % H, u % 2
                        if h == 0:
                            pe.wait_ge(staged[b], i * 3 + 3)
                        pe.wait_ge(sums[p], at(i, u))
                        r = slice(h // 4 * 64, h // 4 * 64 + 64)
                        nc.tensor.matmul(pS[:, p, 0:512], qs[r, b, h % 4], ks[r, b, 0:512], start=True, stop=True)
                        nc.tensor.matmul(pS[:, p, 512:NK], qs[r, b, h % 4], ks[r, b, 512:NK], start=True, stop=True
                                         ).then_inc(s_full[p], 1)

                    def turn(u):
                        p = u % 2
                        pe.wait_ge(normed[p], at(i, u) + 1)
                        if u:
                            pe.wait_ge(t_copied[1 - p], at(i, u - 1) + 1)
                        else:
                            pe.wait_ge(t_copied[1], i * (U // 2))
                        for j in range(5):
                            tr = nc.tensor.transpose(pT[:, j], prob[:, p, j * P:(j + 1) * P], ident)
                        tr.then_inc(t_done[p], 1)

                    def values(u):
                        b, h, p = u // H, u % H, u % 2
                        pe.wait_ge(t_copied[p], at(i, u) + 1)
                        if u:
                            pe.wait_ge(o_done[1 - p], at(i, u - 1) + 1)
                        else:
                            pe.wait_ge(o_done[1], i * (U // 2))
                        g = h // 4 * 64
                        for j in range(5):
                            val = v[:, L // P + j, g:g + 64] if j < 2 else vs[:, b, j - 2, g:g + 64]
                            mm = nc.tensor.matmul(pO[0:HD, 0:P], val, probT[:, p, j], start=(j == 0), stop=(j == 4))
                        mm.then_inc(pv_done[p], 1)

                    scores(0)
                    for u in range(U):
                        if u + 1 < U:
                            scores(u + 1)
                        turn(u)
                        if u:
                            values(u - 1)
                    values(U - 1)

            @block.scalar
            def _(act):
                act.wait_ge(ready, 1)
                with act.Fori(0, TURNS) as i:
                    def exps(u):
                        h, p = u % H, u % 2
                        act.wait_ge(max_done[p], at(i, u) + 1)
                        act.wait_ge(t_done[p], at(i, u))
                        act.wait_ge(sums_read[p], at(i, u))
                        nc.scalar.activation(rest[:, p:p + 1], sk[:, h:h + 1], ACT.Exp, bias=nm[:, p:p + 1])
                        nc.scalar.activation(prob[:, p], pS[:, p, 0:NK], ACT.Exp, bias=nm[:, p:p + 1], scale=SC,
                                             accum_out=total[:, p:p + 1]).then_inc(sums[p], 1)

                    def copy(u):
                        p = u % 2
                        act.wait_ge(t_done[p], at(i, u) + 1)
                        act.wait_ge(pv_done[p], at(i, u))
                        nc.scalar.activation(probT[:, p], pT[:, 0:5], ACT.Copy).then_inc(t_copied[p], 1)

                    exps(0)
                    for u in range(U):
                        if u + 1 < U:
                            exps(u + 1)
                        copy(u)

            @block.vector
            def _(dve):
                dve.wait_ge(loaded, 32)
                nc.vector.tensor_scalar(nsk[:], sk[:], -1.0, None, ALU.mult).then_inc(ready, 1)
                dve.wait_ge(ready, 1)
                with dve.Fori(0, TURNS) as i:
                    chain = Chain(dve, chain_sem, i, 4 * U)

                    def maxima(u):
                        b, h, p = u // H, u % H, u % 2
                        dve.wait_ge(s_full[p], at(i, u) + 1)
                        sides = pS[:, p, C:C + 512].rearrange("p (a k) -> p a k", k=256)[:, :, 0:P]
                        chain(nc.vector.tensor_tensor(sides, sides, window[:, bass.ds(i * 2 + b, 1)].rearrange(
                            "p o a k -> p (o a) k"), ALU.add))
                        chain(nc.vector.tensor_reduce(nmax[:, p:p + 1], pS[:, p, 0:NK], AX.X, ALU.max, negate=True))
                        nc.vector.tensor_scalar(nm[:, p:p + 1], nmax[:, p:p + 1], SC, nsk[:, h:h + 1],
                                                ALU.mult, ALU.min).then_inc(max_done[p], 1)

                    def invert(u):
                        p = u % 2
                        dve.wait_ge(sums[p], at(i, u) + 1)
                        chain(nc.vector.tensor_tensor(inv[:, p:p + 1], total[:, p:p + 1], rest[:, p:p + 1], ALU.add))
                        nc.vector.sem_inc(sums_read[p], 1)
                        chain(nc.vector.reciprocal(inv[:, p:p + 1], inv[:, p:p + 1]))
                        nc.vector.tensor_scalar(prob[:, p], prob[:, p], inv[:, p:p + 1], None, ALU.mult
                                                ).then_inc(normed[p], 1)

                    def outputs(u):
                        b, h, p = u // H, u % H, u % 2
                        dve.wait_ge(pv_done[p], at(i, u) + 1)
                        nc.vector.tensor_copy(yT[h % 2 * HD:(h % 2 + 1) * HD, h // 2, bass.ds((i * 2 + b) * P, P)],
                                              pO[0:HD, 0:P]).then_inc(o_done[p], 1)
                        if h == H - 1:
                            dve.wait_ge(o_done[p], at(i, u) + 1)
                            nc.vector.sem_inc(block_done[b], 1)

                    maxima(0)
                    for u in range(U):
                        invert(u)
                        if u + 1 < U:
                            maxima(u + 1)
                        if u:
                            outputs(u - 1)
                    outputs(U - 1)
                    chain.close()



def prepare_recurrence(nc, name, cst, rkv, lora_a, lora_b, k_k, gate_g2, kk_dram, lora_in, g_dram):
    units = [(m, t0, n) for m in range(4) for t0, n in CHUNKS]
    with Stage(nc, name) as s:
        kvec, g2 = s.sb("kvec", [P, 4]), s.sb("g2", [96, 512])
        kk, ones64, kk_stored = s.sb("kk", [P, 4, T]), s.sb("ones64", [P, P]), s.sem("kk_stored")
        sq, rs = s.sb("sq", [P, 2, 512]), s.sb("rs", [P, 2, 512])
        hg, gout = s.sb("hg", [96, L]), s.sb("gout", [P, 2, L])
        ps, pg = s.ps("ps", [P, 2, 512]), s.ps("pg", [P, 2, 2, 512])
        loaded, scaled, squared, summed, clamped = (s.sem("loaded"), s.sem("scaled"), s.sem("squared"),
                                                    s.sem("summed"), s.sem("clamped"))
        rooted, keys_done, lora_done, chain_sem = s.sem("rooted"), s.sem("keys"), s.sem("lora"), s.sem("chain")
        g_ready, g_done, g_copied = s.sem("g_ready"), s.sem("g_done"), s.sem("g_copied")
        g_stored = s.slots("g_stored")
        with nc.Block() as block:
            @block.sync
            def _(sp):
                with nc.allow_non_contiguous_dma("a vector into columns"):
                    sp.dma_start(kvec[:], k_k.rearrange("(k p) -> p k", p=P)).then_inc(loaded, 16)
                sp.dma_start(g2[:], gate_g2).then_inc(loaded, 16)
                sp.dma_start(ones64[:], cst["ones64"]).then_inc(loaded, 16)
                for m in range(4):
                    sp.wait_ge(keys_done, (m + 1) * len(CHUNKS))
                    sp.dma_start(by_tiles(kk_dram)[:, m], kk[:, m]).then_inc(kk_stored, 16)
                for m in range(4):
                    sp.wait_ge(g_copied, m + 1)
                    sp.dma_start(g_dram[m * P:(m + 1) * P, :], gout[:, m % 2]).then_inc(g_stored[m % 2], 16)
                for b in range(2):
                    sp.wait_ge(g_stored[b], 32)
                sp.wait_ge(kk_stored, 64)

            @block.scalar
            def _(act):
                nc.scalar.activation(hg[0:64, :], lora_a[64:128, 0:L], ACT.Sigmoid)
                nc.scalar.activation(hg[64:96, :], lora_b[0:32, 0:L], ACT.Sigmoid).then_inc(g_ready, 1)
                nc.scalar.activation(lora_in[0:32, :], lora_a[0:32, :], ACT.Tanh).then_inc(lora_done, 1)
                for q, (m, t0, n) in enumerate(units):
                    act.wait_ge(scaled, q + 1)
                    if q >= 2:
                        act.wait_ge(summed, q - 1)
                    nc.scalar.activation(sq[:, q % 2, 0:n], kk[:, m, t0:t0 + n], ACT.Square).then_inc(squared, 1)
                    act.wait_ge(clamped, q + 1)
                    nc.scalar.activation(rs[:, q % 2, 0:n], rs[:, q % 2, 0:n], ACT.Sqrt).then_inc(rooted, 1)
                for m in range(4):
                    act.wait_ge(g_done, m + 1)
                    if m >= 2:
                        act.wait_ge(g_stored[m % 2], 16)
                    nc.scalar.activation(gout[:, m % 2], pg[:, m % 2].rearrange("p c t -> p (c t)"), ACT.Copy
                                         ).then_inc(g_copied, 1)

            @block.tensor
            def _(pe):
                pe.wait_ge(loaded, 48)
                for q, (m, t0, n) in enumerate(units):
                    pe.wait_ge(squared, q + 1)
                    nc.tensor.matmul(ps[:, q % 2, 0:n], ones64[:], sq[:, q % 2, 0:n], start=True, stop=True
                                     ).then_inc(summed, 1)
                pe.wait_ge(g_ready, 1)
                for m in range(4):
                    if m >= 2:
                        pe.wait_ge(g_copied, m - 1)
                    for c in range(2):
                        mm = nc.tensor.matmul(pg[:, m % 2, c], g2[:, m * P:(m + 1) * P], hg[:, c * 512:(c + 1) * 512],
                                              start=True, stop=True)
                    mm.then_inc(g_done, 1)

            @block.vector
            def _(dve):
                chain = Chain(dve, chain_sem)
                nc.vector.tensor_copy(lora_in[32:64, :], lora_a[32:64, :])
                nc.vector.memset(lora_in[64:65, :], 1.0)
                dve.wait_ge(loaded, 48)

                def scale(q):
                    m, t0, n = units[q]
                    nc.vector.tensor_scalar(kk[:, m, t0:t0 + n], rkv[:, 4 + m, t0:t0 + n], kvec[:, m:m + 1], None,
                                            ALU.mult).then_inc(scaled, 1)

                def clamp(q):
                    dve.wait_ge(summed, q + 1)
                    if q >= 2:
                        dve.wait_ge(keys_done, q - 1)
                    n = units[q][2]
                    nc.vector.tensor_scalar(rs[:, q % 2, 0:n], ps[:, q % 2, 0:n], 1e-24, None, ALU.max
                                            ).then_inc(clamped, 1)

                scale(0)
                clamp(0)
                for q, (m, t0, n) in enumerate(units):
                    if q + 1 < len(units):
                        scale(q + 1)
                    dve.wait_ge(rooted, q + 1)
                    chain(nc.vector.reciprocal(rs[:, q % 2, 0:n], rs[:, q % 2, 0:n]))
                    if q + 1 < len(units):
                        clamp(q + 1)
                    nc.vector.tensor_tensor(kk[:, m, t0:t0 + n], kk[:, m, t0:t0 + n], rs[:, q % 2, 0:n], ALU.mult
                                            ).then_inc(keys_done, 1)


class Order:

    def __init__(self, names):
        self.names = names

    def at(self, i, *name, ahead=0):
        return i * len(self.names) + (ahead * len(self.names) + self.names.index(name) + 1)

    def before(self, i):
        return i * len(self.names)


LEVELS = 6
RCH = 64
HALF_E = 0.5 * float(np.exp(-0.5))


def recurrence(nc, name, ident, masks, reset, lora_w, ka, rkv, kk, lora_in, S, y, turns, first_token, w):
    emit_y = y is not None
    cs = (0, 1)
    PE = Order([e for c in cs for e in [("gb", c), ("gk", c), ("tb", c), ("tv", c), ("m0", c)] +
                           [(x, c, lv) for lv in range(1, LEVELS) for x in "tx"] +
                           [("rhs", c), ("u", c)] + [("y", c)] * emit_y + [("s", c)]])
    AC = Order([e for c in cs for e in [("tb", c), ("tv", c)] + [("t", c, lv) for lv in range(1, LEVELS)] + [("rhs", c), ("u", c)]])
    DV = Order([e for c in cs for e in [("kr", c), ("gb", c), ("gk", c), ("m0", c)] +
                             [("x", c, lv) for lv in range(1, LEVELS)] + [("y", c)] * emit_y + [("s", c)]])
    PO = Order([e for c in cs for e in [("bn", c), ("v", c)] + [("lv", c, lv) for lv in range(LEVELS)]])
    PPE, PAC, PDV, PPO = (Order([("z", 0), ("z", 1)]), Order([("tanh", 0), ("tanh", 1), ("en",), ("exp",)]),
                          Order([("cum",)]), Order([("ba",)]))
    AHEAD = ((2, 3), (3, 4))
    HALF = (slice(0, 64), slice(64, 128))
    dirs = (0, 1)
    with Stage(nc, name) as s:
        banks = [s.ps(f"ps{d}", [P, 4, 512]) for d in dirs]
        pe_done, act_done, dve_done, pool_done = (s.slots("pe"), s.slots("act"), s.slots("dve"), s.slots("pool"))
        pe_ahead, act_ahead, dve_ahead, pool_ahead = (s.slots("pe_ahead"), s.slots("act_ahead"),
                                                      s.slots("dve_ahead"), s.slots("pool_ahead"))
        dve_chain, pool_chain = s.slots("dve_chain"), s.sem("pool_chain")
        dve_chain_ahead, pool_chain_ahead = s.slots("dve_chain_ahead"), s.slots("pool_chain_ahead")

        def tokens(i, d, ahead=0):
            if d == 0:
                return i * P + (first_token + ahead * P)
            return i * (-P) + ((turns - 1 - ahead) * P + first_token)

        def all_turns(eng, prepare, turn):
            prepare()
            with eng.Fori(0, turns - 1) as i:
                turn(i, False)
            turn(turns - 1, True)

        def col(d, c):
            return slice(RCH * c, RCH * c + RCH) if d == 0 else slice(RCH - RCH * c, 2 * RCH - RCH * c)

        def pairs(bank):
            return bank.rearrange("p (m i) -> p m i", i=P)

        with nc.Block() as block:
            @block.tensor
            def _(pe):
                def lora(i, ahead, q):
                    for d in dirs:
                        if q:
                            pe.wait_ge(act_ahead[d], PAC.at(i, "tanh", 0, ahead=ahead))
                        for m in range(4):
                            mm = nc.tensor.matmul(banks[d][:, 3, m * P:(m + 1) * P],
                                                  lora_w[0:65, d, q, m * P:(m + 1) * P],
                                                  lora_in[0:65, bass.ds(tokens(i, d, ahead), P)],
                                                  start=True, stop=True)
                        mm.then_inc(pe_ahead[d], 1)

                def prepare():
                    for q in range(2):
                        lora(0, 0, q)

                def turn(i, final):
                    def done(d, ins):
                        ins.then_inc(pe_done[d], 1)

                    def products(d, bank, *terms):
                        for m in range(4):
                            for n, (left, right) in enumerate(terms):
                                mm = nc.tensor.matmul(banks[d][:, bank, m * P:(m + 1) * P], left[:, m], right[:, m],
                                                      start=(n == 0), stop=(n == len(terms) - 1))
                        return mm

                    def turned(d, bank, src):
                        for m in range(4):
                            tr = nc.tensor.transpose(banks[d][:, bank, m * P:(m + 1) * P], src[:, m], ident)
                        return tr

                    for c in cs:
                        for d in dirs:
                            b = w[d]
                            pe.wait_ge(dve_done[d], DV.at(i, "kr", c))
                            pe.wait_ge(pool_done[d], PO.at(i, "bn", c))
                            pe.wait_ge(act_done[d], AC.at(i, "u", 0) if c else AC.before(i))
                            for q in range(2):
                                if q == 1:
                                    pe.wait_ge(act_ahead[d], PAC.at(i, "tanh", 1))
                                    pe.wait_ge(dve_done[d], DV.at(i, "s", 0) if c else DV.before(i))
                                for m in range(4):
                                    mm = nc.tensor.matmul(banks[d][:, 2 * q + m // 2, m % 2 * 256:m % 2 * 256 + 256],
                                                          b["bn"][:, q, m], b["kr"][:, m].rearrange("p q i -> p (q i)"),
                                                          start=True, stop=True)
                                done(d, mm)
                        for d in dirs:
                            b = w[d]
                            pe.wait_ge(dve_done[d], DV.at(i, "gb", c))
                            turned(d, 0, b["bn"][:, 0])
                            done(d, turned(d, 1, b["bn"][:, 1]))
                            pe.wait_ge(pool_done[d], PO.at(i, "v", c))
                            pe.wait_ge(dve_done[d], DV.at(i, "gk", c))
                            done(d, turned(d, 2, b["v"]))
                            pe.wait_ge(pool_done[d], PO.at(i, "lv", c, 0))
                            done(d, turned(d, 3, b["lv"][:, 0]))
                        for lv in range(1, LEVELS):
                            for d in dirs:
                                b = w[d]
                                pe.wait_ge(pool_done[d], PO.at(i, "lv", c, lv))
                                pe.wait_ge(dve_done[d], DV.at(i, "m0", c) if lv == 1 else DV.at(i, "x", c, lv - 1))
                                if lv == 1:
                                    pe.wait_ge(act_done[d], AC.at(i, "tv", c))
                                done(d, products(d, 0, (b["lv"][:, lv % 2], b["x"][:, 0])))
                            for d in dirs:
                                b = w[d]
                                pe.wait_ge(act_done[d], AC.at(i, "t", c, lv))
                                if lv < LEVELS - 1:
                                    products(d, 1, (b["x"][:, 1], b["t"]))
                                done(d, products(d, 2, (b["t"], b["x"][:, 1])))
                            if c and lv <= 2 and not final:
                                lora(i, 1, lv - 1)
                        for d in dirs:
                            b = w[d]
                            done(d, products(d, 0, (b["kr"][:, :, 0], S[:, d]), (b["an"][:, :, 0], b["tok"][:, 2])))
                        for d in dirs:
                            b = w[d]
                            pe.wait_ge(act_done[d], AC.at(i, "rhs", c))
                            pe.wait_ge(dve_done[d], DV.at(i, "x", c, LEVELS - 1))
                            done(d, products(d, 1, (b["x"][:, 1], b["t"])))
                        for d in dirs:
                            b = w[d]
                            pe.wait_ge(act_done[d], AC.at(i, "u", c))
                            u = b["x"][:, 0]
                            if emit_y:
                                done(d, products(d, 2, (S[:, d], b["kr"][:, :, 1]), (u, b["ab"][:, :, 1]),
                                                 (b["tok"][:, 2], b["an"][:, :, 1])))
                            if c and not final:
                                pe.wait_ge(act_ahead[d], PAC.at(i, "tanh", 1, ahead=1))
                            done(d, products(d, 3, (b["tok"][:, 0], u), (b["tok"][:, 1], b["tok"][:, 2])))

                all_turns(pe, prepare, turn)

            @block.scalar
            def _(act):
                def tanh(i, ahead, q):
                    for d in dirs:
                        if ahead:
                            act.wait_ge(pool_done[d], PO.at(i, "bn", 1))
                        act.wait_ge(pe_ahead[d], PPE.at(i, "z", q, ahead=ahead))
                        nc.scalar.activation(w[d]["lwa"][:, q], pairs(banks[d][:, 3]), ACT.Tanh, scale=0.5
                                             ).then_inc(act_ahead[d], 1)

                def exps(i, ahead, d):
                    b = w[d]
                    act.wait_ge(dve_ahead[d], PDV.at(i, "cum", ahead=ahead))
                    nc.scalar.activation(b["en"], b["e"][:, 0], ACT.Exp, scale=-1.0).then_inc(act_ahead[d], 1)
                    act.wait_ge(act_ahead[d], PAC.at(i, "en", ahead=ahead))
                    nc.scalar.activation(b["e"], b["e"], ACT.Exp).then_inc(act_ahead[d], 1)

                def prepare():
                    for q in range(2):
                        tanh(0, 0, q)
                    for d in dirs:
                        exps(0, 0, d)

                def turn(i, final):
                    for c in cs:
                        for d in dirs:
                            b = w[d]
                            act.wait_ge(pe_done[d], PE.at(i, "tb", c))
                            nc.scalar.activation(b["tok"][:, 0:2], banks[d][:, 0:2].rearrange(
                                "p q (m t) -> p q m t", t=P), ACT.Copy).then_inc(act_done[d], 1)
                            act.wait_ge(pe_done[d], PE.at(i, "tv", c))
                            nc.scalar.activation(b["tok"][:, 2], pairs(banks[d][:, 2]), ACT.Copy
                                                 ).then_inc(act_done[d], 1)
                        for lv in range(1, LEVELS):
                            for d in dirs:
                                act.wait_ge(pe_done[d], PE.at(i, "t", c, lv))
                                nc.scalar.activation(w[d]["t"], pairs(banks[d][:, 0]), ACT.Copy
                                                     ).then_inc(act_done[d], 1)
                            if c and not final:
                                if lv in (2, 3):
                                    tanh(i, 1, lv - 2)
                                for d in dirs:
                                    if lv == AHEAD[d][1] + 1:
                                        exps(i, 1, d)
                        for d in dirs:
                            act.wait_ge(pe_done[d], PE.at(i, "rhs", c))
                            nc.scalar.activation(w[d]["t"], pairs(banks[d][:, 0]), ACT.Copy).then_inc(act_done[d], 1)
                        for d in dirs:
                            act.wait_ge(pe_done[d], PE.at(i, "u", c))
                            nc.scalar.activation(w[d]["x"][:, 0], pairs(banks[d][:, 1]), ACT.Copy, scale=-1.0
                                                 ).then_inc(act_done[d], 1)

                all_turns(act, prepare, turn)

            @block.vector
            def _(dve):
                def decays(i, ahead, d):
                    chain = Chain(dve, dve_chain_ahead[d], i, 2)
                    chain.n = 2 * ahead
                    b = w[d]
                    dve.wait_ge(act_ahead[d], PAC.at(i, "tanh", 1, ahead=ahead))
                    chain(nc.vector.tensor_scalar(b["lwa"][:, 0], b["lwa"][:, 0], -HALF_E, -HALF_E,
                                                  ALU.mult, ALU.add))
                    nc.vector.tensor_scalar(b["lwa"][:, 1], b["lwa"][:, 1], 0.5, 0.5, ALU.mult, ALU.add)
                    lw = b["lwa"][:, 0].rearrange("p m t -> p (m t)")
                    cum = b["e"][:, 0].rearrange("p m t -> p (m t)")
                    if d:
                        lw, cum = lw[:, ::-1], cum[:, ::-1]
                    chain(nc.vector.tensor_tensor_scan(cum, reset, lw, 0.0, ALU.mult, ALU.add))
                    nc.vector.tensor_tensor(b["e"][:, 1], b["e"][:, 0], b["lwa"][:, 0], ALU.subtract
                                            ).then_inc(dve_ahead[d], 1)

                def prepare():
                    for d in dirs:
                        decays(0, 0, d)

                def turn(i, final):
                    chains = [Chain(dve, dve_chain[d], i, 3) for d in dirs]
                    for c in cs:
                        for d in dirs:
                            b = w[d]
                            t = bass.ds(tokens(i, d) + col(d, c).start, RCH)
                            if c == 0:
                                dve.wait_ge(act_ahead[d], PAC.at(i, "exp"))
                                chains[d](nc.vector.tensor_copy(b["end"], b["e"][:, 0, :, (RCH - 1 if d == 0 else 0)::RCH]))
                            for h in range(2):
                                nc.vector.tensor_tensor(b["kr"][HALF[h], :, 0, HALF[h]], kk[HALF[h], :, t],
                                                        b["e"][HALF[h], 1, :, col(d, c)], ALU.mult)
                                last = nc.vector.tensor_tensor(b["kr"][HALF[h], :, 1, HALF[h]],
                                                               rkv[HALF[h], 0:4, t],
                                                               b["e"][HALF[h], 0, :, col(d, c)], ALU.mult)
                            last.then_inc(dve_done[d], 1)
                        for d in dirs:
                            b = w[d]
                            for q, (x, to) in enumerate((("gb", "ab"), ("gk", "an"))):
                                dve.wait_ge(pe_done[d], PE.at(i, x, c))
                                nc.vector.tensor_tensor(
                                    b[to], banks[d][:, 2 * q:2 * q + 2].rearrange("p e (f q i) -> p (e f) (q i)", q=2, i=P),
                                    masks[:, d, 6:8].rearrange("p q i -> p (q i)").unsqueeze(1).to_broadcast([P, 4, 2 * P])
                                    , ALU.mult).then_inc(dve_done[d], 1)
                        for d in dirs:
                            b = w[d]
                            eye = ident.unsqueeze(1).to_broadcast([P, 4, P])
                            dve.wait_ge(pool_done[d], PO.at(i, "lv", c, 0))
                            nc.vector.scalar_tensor_tensor(b["x"][:, 1], b["lv"][:, 0], -1.0, eye, ALU.mult, ALU.add)
                            dve.wait_ge(pe_done[d], PE.at(i, "m0", c))
                            nc.vector.scalar_tensor_tensor(b["x"][:, 0], pairs(banks[d][:, 3]), -1.0, eye,
                                                           ALU.mult, ALU.add).then_inc(dve_done[d], 1)
                        for lv in range(1, LEVELS):
                            for d in dirs:
                                b = w[d]
                                dve.wait_ge(pe_done[d], PE.at(i, "x", c, lv))
                                q = 0 if lv < LEVELS - 1 else 1
                                nc.vector.tensor_tensor(
                                    b["x"][:, q:2].rearrange("p q m i -> p q (m i)"),
                                    b["x"][:, q:2].rearrange("p q m i -> p q (m i)"),
                                    banks[d][:, 1 + q:3], ALU.subtract).then_inc(dve_done[d], 1)
                                if c and not final and lv == AHEAD[d][1]:
                                    decays(i, 1, d)
                        for d in dirs:
                            b = w[d]
                            t = bass.ds(tokens(i, d) + (col(d, c).start - first_token), RCH)
                            if emit_y:
                                dve.wait_ge(pe_done[d], PE.at(i, "y", c))
                                for h in range(2):
                                    out = y[HALF[h], :, t]
                                    last = nc.vector.tensor_tensor(out, out, pairs(banks[d][:, 2])[HALF[h], :, HALF[h]],
                                                                   ALU.add)
                                last.then_inc(dve_done[d], 1)
                            dve.wait_ge(pe_done[d], PE.at(i, "s", c))
                            chains[d](nc.vector.tensor_tensor(S[:, d], S[:, d], pairs(banks[d][:, 3]), ALU.add))
                            end = b["end"][:, :, (c if d == 0 else 1 - c)].unsqueeze(2).to_broadcast([P, 4, P])
                            nc.vector.tensor_tensor(S[:, d], S[:, d], end, ALU.mult).then_inc(dve_done[d], 1)
                    for x in chains:
                        x.close()

                all_turns(dve, prepare, turn)

            @block.gpsimd
            def _(pool):
                def gates(i, ahead, d):
                    chain = Chain(pool, pool_chain_ahead[d], i, 3)
                    chain.n = 3 * ahead
                    b = w[d]
                    t = bass.ds(tokens(i, d, ahead), P)
                    ba, kn = b["lwa"][:, 0], b["lwa"][:, 1]
                    pool.wait_ge(dve_ahead[d], PDV.at(i, "cum", ahead=ahead))
                    chain(nc.gpsimd.tensor_tensor(ba, kk[:, :, t], kn, ALU.mult))
                    chain(nc.gpsimd.tensor_tensor(kn, kn, ka[:, 0].unsqueeze(2).to_broadcast([P, 4, P]), ALU.mult))
                    chain(nc.gpsimd.tensor_tensor(kn, kn, ka[:, 1].unsqueeze(2).to_broadcast([P, 4, P]), ALU.add))
                    nc.gpsimd.tensor_tensor(kn, kn, rkv[:, 4:8, t], ALU.mult).then_inc(pool_ahead[d], 1)
                    pool.wait_ge(pool_ahead[d], PPO.at(i, "ba", ahead=ahead))

                def prepare():
                    for d in dirs:
                        gates(0, 0, d)

                def turn(i, final):
                    chain = Chain(pool, pool_chain, i, 16)

                    def event(d, ins, *name):
                        ins.then_inc(pool_done[d], 1)
                        pool.wait_ge(pool_done[d], PO.at(i, *name))

                    for c in cs:
                        for d in dirs:
                            b = w[d]
                            t = bass.ds(tokens(i, d) + col(d, c).start, RCH)
                            if c == 0:
                                pool.wait_ge(act_ahead[d], PAC.at(i, "exp"))
                            else:
                                pool.wait_ge(pe_done[d], PE.at(i, "tv", 0))
                            for h, q in ((0, 0), (0, 1), (1, 0), (1, 1)):
                                ins = nc.gpsimd.tensor_tensor(b["bn"][HALF[h], q, :, HALF[h]],
                                                              b["lwa"][HALF[h], q, :, col(d, c)],
                                                              b["en"][HALF[h], :, col(d, c)], ALU.mult)
                                if h + q < 2:
                                    chain(ins)
                            event(d, ins, "bn", c)
                            for h in range(2):
                                ins = nc.gpsimd.tensor_copy(b["v"][HALF[h], :, HALF[h]], rkv[HALF[h], 8:12, t])
                                if h == 0:
                                    chain(ins)
                            event(d, ins, "v", c)
                        for lv in range(LEVELS):
                            for d in dirs:
                                b = w[d]
                                if lv == 0:
                                    pool.wait_ge(dve_done[d], DV.at(i, "gb", c))
                                elif lv == 2:
                                    pool.wait_ge(dve_done[d], DV.at(i, "m0", c))
                                elif lv > 2:
                                    pool.wait_ge(pe_done[d], PE.at(i, "t", c, lv - 2))
                                nc.gpsimd.tensor_tensor(b["lv"][:, lv % 2], b["ab"][:, :, 0],
                                                        masks[:, d, lv].unsqueeze(1).to_broadcast([P, 4, P]), ALU.mult
                                                        ).then_inc(pool_done[d], 1)
                        for d in dirs:
                            pool.wait_ge(pool_done[d], PO.at(i, "lv", c, LEVELS - 1))
                        if c and not final:
                            for d in dirs:
                                gates(i, 1, d)
                    chain.close()

                all_turns(pool, prepare, turn)


def run_recurrences(nc, name, cst, ident, rkv, kk, kk_dram, lora_in, decay_w0, decay_w2, iclr_a0, iclr_a2, k_a, y):
    with Stage(nc, name) as s:
        masks = s.sb("masks", [P, 2, 8, P], mybir.dt.bfloat16)
        reset = s.sb("reset", [P, 512], mybir.dt.bfloat16)
        lora_w = s.sb("lora_w", [65, 2, 2, 512])
        ka = s.sb("ka", [P, 2, 4])
        S = s.sb("S", [P, 2, 4, P])
        w = []
        for d in range(2):
            t = {n: s.sb(f"{n}{d}", [P, *shape]) for n, shape in dict(
                lwa=[2, 4, P], e=[2, 4, P], en=[4, P], end=[4, 2], kr=[4, 2, P], bn=[2, 4, P], v=[4, P],
                ab=[4, 2, P], an=[4, 2, P], tok=[3, 4, P], lv=[2, 4, P], x=[2, 4, P], t=[4, P]).items()}
            w.append({n: x[:] for n, x in t.items()})
        with Stage(nc, name + "_init") as s2:
            masks32 = w[0]["ab"].rearrange("p m q i -> p (m q i)")[:, 0:512].rearrange("p (l i) -> p l i", i=64)
            ka_loaded, lora_loaded, mask_loaded = s2.sem("ka"), s2.sem("lora"), s2.slots("mask")
            zeroed, started = s2.sem("zeroed"), s2.sem("started")
            mask_read, kk_loaded = s2.sem("mask_read"), s2.sem("kk_loaded")
            with nc.Block() as block:
                @block.gpsimd
                def _(pool):
                    nc.gpsimd.memset(lora_w[:], 0.0).then_inc(started, 1)
                    nc.gpsimd.memset(masks[:], 0.0).then_inc(started, 1)

                @block.sync
                def _(sp):
                    with nc.allow_non_contiguous_dma("a vector into columns"):
                        sp.dma_start(ka[:, 0], k_a.rearrange("(k p) -> p k", p=P)).then_inc(ka_loaded, 16)
                    sp.dma_start(kk[:], by_tiles(kk_dram)).then_inc(kk_loaded, 16)
                    sp.wait_ge(started, 2)
                    for d in range(2):
                        sp.dma_start(lora_w[0:32, d, 0], decay_w2[d]).then_inc(lora_loaded, 16)
                        sp.dma_start(lora_w[32:64, d, 1], iclr_a2[d]).then_inc(lora_loaded, 16)
                        sp.dma_start(lora_w[64:65, d, 0], decay_w0[d:d + 1]).then_inc(lora_loaded, 16)
                        sp.dma_start(lora_w[64:65, d, 1], iclr_a0[d:d + 1]).then_inc(lora_loaded, 16)
                    for d in range(2):
                        sp.wait_ge(mask_read, d)
                        sp.dma_start(masks32, cst["masks"][:, d]).then_inc(mask_loaded[d], 16)
                    sp.wait_ge(lora_loaded, 128)
                    sp.wait_ge(kk_loaded, 16)

                @block.vector
                def _(dve):
                    nc.vector.memset(reset[:], 1.0).then_inc(zeroed, 1)
                    dve.wait_ge(zeroed, 1)
                    nc.vector.memset(reset[:].rearrange("p (a t) -> p a t", t=RCH)[:, :, 0:1], 0.0)
                    nc.vector.memset(S[:], 0.0)
                    nc.vector.memset(y[:], 0.0)
                    for b in w:
                        for n in ("kr", "bn", "v"):
                            nc.vector.memset(b[n], 0.0)
                    dve.wait_ge(ka_loaded, 16)
                    nc.vector.tensor_scalar(ka[:, 1], ka[:, 0], -1.0, 1.0, ALU.mult, ALU.add)
                    dve.wait_ge(started, 2)
                    for d in range(2):
                        dve.wait_ge(mask_loaded[d], 16)
                        for h in range(2):
                            r = slice(64 * h, 64 * h + 64)
                            last = nc.vector.tensor_copy(masks[r, d, :, r], masks32[r])
                        last.then_inc(mask_read, 1)
        args = (ident, masks, reset[:], lora_w, ka, rkv, kk, lora_in, S)
        recurrence(nc, name + "_ctx", *args, None, C // P, L, w)
        recurrence(nc, name + "_lat", *args, y, L // P, 0, w)



def recurrence_outputs(nc, name, cst, rkv, lora_in, iclr_a0, iclr_a2, k_a, r_k, lnx_w, lnx_b, g_dram, y, yr_dram,
                       beside):
    units = [(m, c) for m in range(4) for c in range(2)]
    LNX_EPS = 1e-5 * 64
    with Stage(nc, name) as s:
        vec = s.sb("vec", [P, 6, 4])
        lora_w = s.sb("lora_w", [65, 2, 512])
        g = s.sb("g", [P, 2, 512])
        yc, sq, bon = s.sb("yc", [P, 2, 512]), s.sb("sq", [P, 2, 512]), s.sb("bon", [P, 2, 512])
        th, rs, yn = s.sb("th", [P, 2, 2, 512]), s.sb("rs", [P, 2, 512]), s.sb("yn", [P, 2, 512])
        pm, pv, pb, pa = s.ps("pm", [P, 512]), s.ps("pv", [P, 512]), s.ps("pb", [P, 512]), s.ps("pa", [P, 2, 512])
        loaded, zeroed, g_loaded, vec_done = s.sem("loaded"), s.sem("zeroed"), s.slots("g_loaded"), s.sem("vec")
        a_done, mean_done, var_done, bon_sum = s.sem("a"), s.sem("mean"), s.sem("var"), s.sem("bon_sum")
        tanh_done, squared, rooted, scaled = s.sem("tanh"), s.sem("squared"), s.sem("rooted"), s.sem("scaled")
        centred, bon_done, eps_done, yn_done, done = (s.sem("centred"), s.sem("bon"), s.sem("eps"), s.sem("yn"),
                                                      s.sem("done"))
        chain_sem = s.sem("chain")
        yr, ones64, yr_stored = s.sb("yr", [P, 2, 512]), s.sb("ones64", [P, P]), s.slots("yr_stored")
        px, py = s.ps("px", [P, 2, 512]), s.ps("py", [P, 512])
        side = beside(s, [px[:, b] for b in range(2)], py)

        def side_steps(q):
            return [(e % 2, e // 2) for e in range(q * side.STEPS // len(units), (q + 1) * side.STEPS // len(units))]

        with nc.Block() as block:
            @block.gpsimd
            def _(pool):
                nc.gpsimd.memset(lora_w[:], 0.0).then_inc(zeroed, 1)
                side.load_small(pool)
                side.load(pool)

            @block.sync
            def _(sp):
                with nc.allow_non_contiguous_dma("vectors into columns"):
                    for j, v in enumerate((k_a, r_k.rearrange("h k -> (h k)"), lnx_w, lnx_b)):
                        sp.dma_start(vec[:, j], v.rearrange("(k p) -> p k", p=P)).then_inc(loaded, 16)
                sp.dma_start(ones64[:], cst["ones64"]).then_inc(loaded, 16)
                sp.wait_ge(zeroed, 1)
                for d in range(2):
                    sp.dma_start(lora_w[32:64, d], iclr_a2[d]).then_inc(loaded, 16)
                    sp.dma_start(lora_w[64:65, d], iclr_a0[d:d + 1]).then_inc(loaded, 16)

                def part(dram, q):
                    m, c = units[q]
                    return dram[m * P:(m + 1) * P, c * 512:(c + 1) * 512]

                for q in range(len(units) + 2):
                    if q >= 2:
                        sp.wait_ge(done, q - 1)
                        sp.dma_start(part(yr_dram, q - 2), yr[:, q % 2]).then_inc(yr_stored[q % 2], 16)
                    if q < len(units):
                        sp.dma_start(g[:, q % 2], part(g_dram, q)).then_inc(g_loaded[q % 2], 16)
                for b in range(2):
                    sp.wait_ge(yr_stored[b], 16 * (len(units) // 2))

            @block.tensor
            def _(pe):
                pe.wait_ge(loaded, 144)
                for q, (m, c) in enumerate(units):
                    t = slice(c * 512, (c + 1) * 512)
                    if q:
                        pe.wait_ge(tanh_done, q)
                        pe.wait_ge(done, q)
                    for d in range(2):
                        mm = nc.tensor.matmul(pa[:, d], lora_w[0:65, d, m * P:(m + 1) * P], lora_in[0:65, t],
                                              start=True, stop=True)
                    mm.then_inc(a_done, 1)
                    nc.tensor.matmul(pm[:], ones64[:], y[:, m, t], start=True, stop=True).then_inc(mean_done, 1)
                    pe.wait_ge(squared, q + 1)
                    nc.tensor.matmul(pv[:], ones64[:], sq[:, q % 2], start=True, stop=True).then_inc(var_done, 1)
                    pe.wait_ge(bon_done, q + 1)
                    nc.tensor.matmul(pb[:], ones64[:], bon[:, q % 2], start=True, stop=True).then_inc(bon_sum, 1)
                    for b, i in side_steps(q):
                        side.multiply(pe, b, i)
                side.turn(pe)

            @block.scalar
            def _(act):
                act.wait_ge(loaded, 144)
                side.silu(act)
                for q, (m, c) in enumerate(units):
                    if q:
                        for b, i in side_steps(q - 1):
                            side.read_out(act, b, i)
                    act.wait_ge(a_done, q + 1)
                    if q >= 2:
                        act.wait_ge(done, q - 1)
                    nc.scalar.activation(th[:, q % 2], pa[:], ACT.Tanh, scale=0.5).then_inc(tanh_done, 1)
                    act.wait_ge(centred, q + 1)
                    nc.scalar.activation(sq[:, q % 2], yc[:, q % 2], ACT.Square).then_inc(squared, 1)
                    act.wait_ge(eps_done, q + 1)
                    nc.scalar.activation(rs[:, q % 2], rs[:, q % 2], ACT.Sqrt).then_inc(rooted, 1)
                    act.wait_ge(yn_done, q + 1)
                    nc.scalar.activation(yn[:, q % 2], yn[:, q % 2], ACT.Identity, scale=vec[:, 2, m:m + 1],
                                         bias=vec[:, 3, m:m + 1]).then_inc(scaled, 1)
                for b, i in side_steps(len(units) - 1):
                    side.read_out(act, b, i)

            @block.vector
            def _(dve):
                chain = Chain(dve, chain_sem)
                dve.wait_ge(loaded, 144)
                nc.vector.tensor_scalar(vec[:, 4], vec[:, 0], 0.5, None, ALU.mult).then_inc(vec_done, 1)
                nc.vector.tensor_scalar(vec[:, 5], vec[:, 0], -1.0, 2.0, ALU.mult, ALU.add).then_inc(vec_done, 1)
                dve.wait_ge(vec_done, 2)
                for q, (m, c) in enumerate(units):
                    p, t = q % 2, slice(c * 512, (c + 1) * 512)
                    dve.wait_ge(mean_done, q + 1)
                    nc.vector.scalar_tensor_tensor(yc[:, p], pm[:], -1.0 / HD, y[:, m, t], ALU.mult, ALU.add
                                                   ).then_inc(centred, 1)
                    dve.wait_ge(tanh_done, q + 1)
                    chain(nc.vector.tensor_tensor(th[:, p, 0], th[:, p, 0], th[:, p, 1], ALU.add))
                    chain(nc.vector.tensor_scalar(th[:, p, 0], th[:, p, 0], vec[:, 4, m:m + 1], vec[:, 5, m:m + 1],
                                                  ALU.mult, ALU.add))
                    chain(nc.vector.tensor_tensor(th[:, p, 0], th[:, p, 0], rkv[:, 4 + m, t], ALU.mult))
                    nc.vector.scalar_tensor_tensor(bon[:, p], th[:, p, 0], vec[:, 1, m:m + 1], rkv[:, m, t],
                                                   ALU.mult, ALU.mult).then_inc(bon_done, 1)
                    dve.wait_ge(var_done, q + 1)
                    nc.vector.tensor_scalar(rs[:, p], pv[:], 1.0 / HD, LNX_EPS, ALU.mult, ALU.add
                                            ).then_inc(eps_done, 1)
                    dve.wait_ge(rooted, q + 1)
                    chain(nc.vector.reciprocal(rs[:, p], rs[:, p]))
                    nc.vector.tensor_tensor(yn[:, p], yc[:, p], rs[:, p], ALU.mult).then_inc(yn_done, 1)
                    dve.wait_ge(bon_sum, q + 1)
                    chain(nc.vector.tensor_tensor(bon[:, p], pb[:], rkv[:, 8 + m, t], ALU.mult))
                    dve.wait_ge(scaled, q + 1)
                    chain(nc.vector.tensor_tensor(yn[:, p], yn[:, p], bon[:, p], ALU.add))
                    dve.wait_ge(g_loaded[p], 16 * (q // 2 + 1))
                    if q >= 2:
                        dve.wait_ge(yr_stored[p], 16 * (q // 2))
                    nc.vector.tensor_tensor(yr[:, p], yn[:, p], g[:, p], ALU.mult).then_inc(done, 1)
                side.add_bias(dve)



def project(nc, name, source, tiles, kt, rhs, spans, read_out):
    with Stage(nc, name) as s:
        ps = s.ps("ps", [P, 2, len(spans), 512])
        ps_full, ps_free = s.slots("ps_full"), s.slots("ps_free")
        w = SplitWeights(nc, s, kt, ps_full, 1)
        with nc.Block() as block:
            @block.sync
            def _(sp):
                with sp.Fori(0, tiles // 2) as i:
                    for b in range(2):
                        w.load(sp, b, i, source(i * 2 + b))

            @block.gpsimd
            def _(pool):
                with pool.Fori(0, tiles // 2) as i:
                    for b in range(2):
                        w.split(pool, b, i)

            @block.tensor
            def _(pe):
                with pe.Fori(0, tiles // 2) as i:
                    for b in range(2):
                        pe.wait_ge(ps_free[b], i)
                        w.multiply(pe, b, i, rhs, kt, spans, ps[:, b])

            @block.vector
            def _(dve):
                with dve.Fori(0, tiles // 2) as i:
                    for b in range(2):
                        dve.wait_ge(ps_full[b], i + 1)
                        read_out(i * 2 + b, ps[:, b]).then_inc(ps_free[b], 1)


def columns_of(w, kt=None):
    return lambda m: by_tiles(w)[:, :, bass.ds(m * P, P)]


def flat(ap):
    return ap.rearrange("p a t -> p (a t)")


def add_gated(nc, *parts):
    def read_out(m, banks):
        for x, gate, t0, n in parts:
            own = flat(x[:, bass.ds(m, 1), 0:n])
            last = nc.vector.scalar_tensor_tensor(own, flat(banks)[:, t0:t0 + n], gate[:, bass.ds(m, 1)], own,
                                                  ALU.mult, ALU.add)
        return last
    return read_out


def merge_branches(nc, name, ya, yr, w_attn, w_rwkv, gates_dram, out):
    with Stage(nc, name) as s:
        w = s.sb("w", [P, 2, 2, 4, P])
        g = s.sb("g", [P, 2, 2, L])
        part = s.sb("part", [P, 2, L])
        ps = s.ps("ps", [P, 2, 2, 2, 512])
        w_full, g_full, ps_full, read, added = (s.slots("w_full"), s.slots("g_full"), s.slots("ps_full"),
                                                s.slots("read"), s.slots("added"))
        with nc.Block() as block:
            @block.sync
            def _(sp):
                with sp.Fori(0, KT // 2) as i:
                    for b in range(2):
                        m = i * 2 + b
                        sp.wait_ge(ps_full[b], i)
                        for j, mat in enumerate((w_attn, w_rwkv)):
                            sp.dma_start(w[:, b, j], by_tiles(mat)[:, :, bass.ds(m * P, P)]).then_inc(w_full[b], 16)
                        sp.wait_ge(read[b], i * 2)
                        for j in range(2):
                            sp.dma_start(g[:, b, j], gates_dram[bass.ds(m * P + j * D, P), :]).then_inc(g_full[b], 16)

            @block.tensor
            def _(pe):
                with pe.Fori(0, KT // 2) as i:
                    for b in range(2):
                        pe.wait_ge(w_full[b], i * 32 + 32)
                        pe.wait_ge(read[b], i * 2)
                        for j, rhs in enumerate((ya, yr)):
                            for c, (t0, n) in enumerate(LAT):
                                for k in range(4):
                                    mm = nc.tensor.matmul(ps[:, b, j, c], w[:, b, j, k], rhs[:, k, t0:t0 + n],
                                                          start=(k == 0), stop=(k == 3))
                        mm.then_inc(ps_full[b], 1)

            @block.vector
            def _(dve):
                with dve.Fori(0, KT // 2) as i:
                    for b in range(2):
                        own = flat(out[:, bass.ds(i * 2 + b, 1)])
                        dve.wait_ge(ps_full[b], i + 1)
                        dve.wait_ge(g_full[b], i * 32 + 32)
                        dve.wait_ge(added[b], i)
                        nc.vector.tensor_tensor(own, flat(ps[:, b, 0]), g[:, b, 0], ALU.mult).then_inc(read[b], 1)
                        nc.vector.tensor_tensor(part[:, b], flat(ps[:, b, 1]), g[:, b, 1], ALU.mult
                                                ).then_inc(read[b], 1)

            @block.gpsimd
            def _(pool):
                with pool.Fori(0, KT // 2) as i:
                    for b in range(2):
                        own = flat(out[:, bass.ds(i * 2 + b, 1)])
                        pool.wait_ge(read[b], i * 2 + 2)
                        nc.gpsimd.tensor_tensor(own, own, part[:, b], ALU.add).then_inc(added[b], 1)


def mlp(nc, name, h, w_up, w_down, xT, gate):
    Q = 4
    HALF = KT // 2
    assert w_up.shape[1] == Q * D
    with Stage(nc, name) as s:
        hid = s.sb("hid_hi", [P, KT, L], F32R), s.sb("hid_lo", [P, KT, L], F32R)
        pos, sq = s.sb("pos", [P, 2, L]), s.sb("sq", [P, L])
        ps = s.ps("ps", [P, 2, 2, 512])
        ps_full, ps_free, hi_done = s.slots("ps_full"), s.slots("ps_free"), s.slots("hi")
        hid_done, squared = s.slots("hid"), s.slots("squared")
        w = SplitWeights(nc, s, KT, ps_full, 1)

        def tiles(eng, step_up, step_down):
            with eng.Fori(0, Q) as q:
                for step in (step_up, step_down):
                    with eng.Fori(0, HALF) as i:
                        for b in range(2):
                            step(b, q, i)

        def up_no(q, i):
            return q * (2 * HALF) + i

        def down_no(q, i):
            return q * (2 * HALF) + i + HALF

        with nc.Block() as block:
            @block.sync
            def _(sp):
                tiles(sp,
                      lambda b, q, i: w.load(sp, b, up_no(q, i), by_tiles(w_up)[
                          :, :, bass.ds(q * D + i * (2 * P) + b * P, P)]),
                      lambda b, q, i: w.load(sp, b, down_no(q, i), by_tiles(w_down)[
                          :, bass.ds(q * KT, KT), bass.ds(i * (2 * P) + b * P, P)]))

            @block.gpsimd
            def _(pool):
                tiles(pool, lambda b, q, i: w.split(pool, b, up_no(q, i)),
                      lambda b, q, i: w.split(pool, b, down_no(q, i)))

            @block.tensor
            def _(pe):
                def up(b, q, i):
                    pe.wait_ge(ps_free[b], up_no(q, i))
                    w.multiply(pe, b, up_no(q, i), h, KT, LAT, ps[:, b])

                def down(b, q, i):
                    pe.wait_ge(ps_free[b], down_no(q, i))
                    for j in range(2):
                        pe.wait_ge(hid_done[j], q * HALF + HALF)
                    w.multiply(pe, b, down_no(q, i), hid, KT, LAT, ps[:, b])

                tiles(pe, up, down)

            @block.scalar
            def _(act):
                with act.Fori(0, Q) as q:
                    with act.Fori(0, HALF) as i:
                        for b in range(2):
                            act.wait_ge(ps_free[b], up_no(q, i) + 1)
                            nc.scalar.activation(flat(hid[0][:, bass.ds(i * 2 + b, 1)]), pos[:, b], ACT.Square
                                                 ).then_inc(hi_done[b], 1)

            @block.vector
            def _(dve):
                def up(b, q, i):
                    dve.wait_ge(ps_full[b], up_no(q, i) + 1)
                    nc.vector.tensor_scalar(pos[:, b], flat(ps[:, b]), 0.0, None, ALU.max).then_inc(ps_free[b], 1)
                    dve.wait_ge(ps_free[b], up_no(q, i) + 1)
                    nc.vector.tensor_tensor(sq[:], pos[:, b], pos[:, b], ALU.mult).then_inc(squared[b], 1)
                    dve.wait_ge(squared[b], q * HALF + i + 1)
                    dve.wait_ge(hi_done[b], q * HALF + i + 1)
                    m = bass.ds(i * 2 + b, 1)
                    nc.vector.tensor_tensor(flat(hid[1][:, m]), sq[:], flat(hid[0][:, m]).bitcast(F32),
                                            ALU.subtract).then_inc(hid_done[b], 1)
                    dve.wait_ge(hid_done[b], q * HALF + i + 1)

                def down(b, q, i):
                    dve.wait_ge(ps_full[b], down_no(q, i) + 1)
                    add_gated(nc, (xT, gate, 0, L))(i * 2 + b, ps[:, b]).then_inc(ps_free[b], 1)

                tiles(dve, up, down)



SGU_W, FNET_W, Q_LORA, KV_LORA, ROPE_W = 256, 256, 256, 128, 64
NOPE, VD, MH = 128, 128, 4
QK = NOPE + ROPE_W
MIX_F, MIX_Q = 512, 768


def project_mixers(nc, name, ones, hT, w_in, tokens, uT, vn, fT, pq, kv, kr):
    spans = [x for x in CHUNKS if x[0] < tokens]
    rows = tokens // P
    TILES = [(0, spans, uT[:, 0], ACT.Gelu_apprx_tanh), (P, spans, uT[:, 1], ACT.Gelu_apprx_tanh),
             (MIX_F, spans, fT[:, 0], ACT.Copy), (MIX_F + P, spans, fT[:, 1], ACT.Copy),
             (MIX_Q, spans, pq[:, 0], ACT.Copy), (MIX_Q + P, spans, pq[:, 1], ACT.Copy),
             (MIX_Q + Q_LORA, CHUNKS, kv, ACT.Copy), (MIX_Q + Q_LORA + KV_LORA, CHUNKS, kr, ACT.Copy)]
    with Stage(nc, name) as s:
        w = s.sb("w", [P, 2, KT, P])
        wv = s.sb("wv", [P, KT, SGU_W])
        sq = s.sb("sq", [P, 2, SGU_W])
        ss = s.sb("ss", [P, rows])
        ps, pv = s.ps("ps", [P, 2, 3, 512]), s.ps("pv", [P, 2, 512])
        w_full, v_loaded, mul_done, read = s.slots("w_full"), s.sem("v_loaded"), s.sem("mul"), s.sem("read")
        v_done, v_read, sums, eps_done, rooted, inv_done = (s.sem("v_done"), s.sem("v_read"), s.sem("sums"),
                                                            s.sem("eps"), s.sem("rooted"), s.sem("inv"))
        with nc.Block() as block:
            @block.sync
            def _(sp):
                for m, (c0, _, _, _) in enumerate(TILES):
                    if m >= 2:
                        sp.wait_ge(mul_done, m - 1)
                    if m < 7:
                        sp.dma_start(w[:, m % 2], by_tiles(w_in)[:, :, c0:c0 + P]).then_inc(w_full[m % 2], 16)
                    else:
                        for h in range(2):
                            sp.dma_start(w[:, m % 2, :, h * 64:h * 64 + 64], by_tiles(w_in)[:, :, c0:c0 + 64]
                                         ).then_inc(w_full[m % 2], 16)
                sp.dma_start(wv[:], by_tiles(w_in)[:, :, SGU_W:2 * SGU_W]).then_inc(v_loaded, 16)

            @block.tensor
            def _(pe):
                for m, (_, spn, _, _) in enumerate(TILES):
                    pe.wait_ge(w_full[m % 2], 16 * (m // 2 + 1) + (16 if m == 7 else 0))
                    if m >= 2:
                        pe.wait_ge(read, m - 1)
                    for c, (t0, n) in enumerate(spn):
                        for k in range(KT):
                            mm = nc.tensor.matmul(ps[:, m % 2, c, 0:n], w[:, m % 2, k], hT[:, k, t0:t0 + n],
                                                  start=(k == 0), stop=(k == KT - 1))
                    mm.then_inc(mul_done, 1)
                pe.wait_ge(v_loaded, 16)
                for t in range(rows):
                    if t >= 2:
                        pe.wait_ge(v_read, t - 1)
                    for k in range(KT):
                        mm = nc.tensor.matmul(pv[:, t % 2, 0:SGU_W], hT[:, k, t * P:(t + 1) * P], wv[:, k],
                                              start=(k == 0), stop=(k == KT - 1))
                    mm.then_inc(v_done, 1)

            @block.scalar
            def _(act):
                for m, (_, spn, dst, func) in enumerate(TILES):
                    act.wait_ge(mul_done, m + 1)
                    n = spn[-1][0] + spn[-1][1]
                    nc.scalar.activation(dst[:, 0:n], ps[:, m % 2].rearrange("p c t -> p (c t)")[:, 0:n], func
                                         ).then_inc(read, 1)
                for t in range(rows):
                    act.wait_ge(v_done, t + 1)
                    nc.scalar.activation(vn[:, t], pv[:, t % 2, 0:SGU_W], ACT.Gelu_apprx_tanh).then_inc(v_read, 1)
                for t in range(rows):
                    if t >= 2:
                        act.wait_ge(sums, t - 1)
                    else:
                        act.wait_ge(v_read, t + 1)
                    act.wait_ge(v_read, rows)
                    nc.scalar.activation(sq[:, t % 2], vn[:, t], ACT.Square, accum_out=ss[:, t:t + 1]
                                         ).then_inc(sums, 1)
                act.wait_ge(eps_done, 1)
                nc.scalar.activation(ss[:], ss[:], ACT.Sqrt).then_inc(rooted, 1)

            @block.vector
            def _(dve):
                dve.wait_ge(sums, rows)
                nc.vector.tensor_scalar(ss[:], ss[:], 1.0 / SGU_W, EPS, ALU.mult, ALU.add).then_inc(eps_done, 1)
                dve.wait_ge(rooted, 1)
                nc.vector.reciprocal(ss[:], ss[:]).then_inc(inv_done, 1)
                dve.wait_ge(inv_done, 1)
                for t in range(rows):
                    nc.vector.tensor_scalar(vn[:, t], vn[:, t], ss[:, t:t + 1], None, ALU.mult)


def gate_tokens(nc, name, ident, uT, vn, sgu_norm, w_sgu, b_sgu, tokens, mixT):
    rows = tokens // P
    with Stage(nc, name) as s:
        wr, wT = s.sb("wr", [P, 4, P]), s.sb("wT", [P, 4, P])
        norm, bias = s.sb("norm", [P, 2]), s.sb("bias", [P, 2, P])
        z = s.sb("z", [P, 2, 2, P])
        pT, pz = s.ps("pT", [P, 4, P]), s.ps("pz", [P, 2, 512])
        loaded, turned, copied, mixed, z_done, done = (s.sem("loaded"), s.sem("turned"), s.sem("copied"),
                                                       s.sem("mixed"), s.sem("z"), s.sem("done"))
        with nc.Block() as block:
            @block.sync
            def _(sp):
                sp.dma_start(wr[:], w_sgu.rearrange("h p q -> p h q")).then_inc(loaded, 16)
                with nc.allow_non_contiguous_dma("a vector into columns"):
                    sp.dma_start(norm[:], sgu_norm.rearrange("(k p) -> p k", p=P)).then_inc(loaded, 16)
                for h in range(4):
                    sp.dma_start(bias[h % 2 * 64:h % 2 * 64 + 64, h // 2], b_sgu[h].partition_broadcast(64)
                                 ).then_inc(loaded, 16)

            @block.tensor
            def _(pe):
                pe.wait_ge(loaded, 96)
                for h in range(4):
                    tr = nc.tensor.transpose(pT[:, h], wr[:, h], ident)
                tr.then_inc(turned, 1)
                pe.wait_ge(copied, 1)
                for t in range(rows):
                    if t >= 2:
                        pe.wait_ge(z_done, t - 1)
                    for h in range(4):
                        r = slice(h % 2 * 64, h % 2 * 64 + 64)
                        mm = nc.tensor.matmul(pz[r, t % 2, h // 2 * P:h // 2 * P + P], vn[:, t, h * 64:(h + 1) * 64],
                                              wT[:, h], start=True, stop=True)
                    mm.then_inc(mixed, 1)

            @block.scalar
            def _(act):
                act.wait_ge(turned, 1)
                nc.scalar.activation(wT[:], pT[:], ACT.Copy).then_inc(copied, 1)

            @block.vector
            def _(dve):
                dve.wait_ge(loaded, 96)
                for t in range(rows):
                    dve.wait_ge(mixed, t + 1)
                    for m in range(2):
                        last = nc.vector.scalar_tensor_tensor(z[:, t % 2, m], pz[:, t % 2, m * P:(m + 1) * P],
                                                              norm[:, m:m + 1], bias[:, m], ALU.mult, ALU.add)
                    last.then_inc(z_done, 1)
                    dve.wait_ge(z_done, t + 1)
                    nc.vector.tensor_tensor(mixT[:, 0:2, t * P:(t + 1) * P], z[:, t % 2],
                                            uT[:, :, t * P:(t + 1) * P], ALU.mult).then_inc(done, 1)


def fourier(nc, name, cst, fT, seqs, mixT):
    rows = sum(n for _, n, _ in seqs) // P
    steps = [(t0, n, sfx, t) for t0, n, sfx in seqs for t in range(n // P)]
    with Stage(nc, name) as s:
        d64 = s.sb("d64", [P, 2 * P])
        Z = s.sb("Z", [P, rows, 2, 2, P])
        dft = s.sb("dft", [P, 2, 2, L])
        pz, py = s.ps("pz", [P, 2, 512]), s.ps("py", [P, 4, 512])
        loaded, d_full = s.sem("loaded"), s.slots("d_full")
        z_done, z_read, used, y_read = s.sem("z_done"), s.sem("z_read"), s.sem("used"), s.sem("y_read")
        with nc.Block() as block:
            @block.sync
            def _(sp):
                sp.dma_start(d64[:], cst["dft64"]).then_inc(loaded, 16)
                for q, (_, n, sfx, t) in enumerate(steps):
                    if q >= 2:
                        sp.wait_ge(used, q - 1)
                    for j, x in enumerate(("dft_cos_", "dft_sin_")):
                        sp.dma_start(dft[:, q % 2, j, 0:n], cst[x + sfx][t * P:(t + 1) * P, :]
                                     ).then_inc(d_full[q % 2], 16)

            @block.tensor
            def _(pe):
                pe.wait_ge(loaded, 16)
                for t in range(rows):
                    if t >= 2:
                        pe.wait_ge(z_read, t - 1)
                    for m in range(2):
                        mm = nc.tensor.matmul(pz[:, t % 2, m * 2 * P:(m + 1) * 2 * P], fT[:, m, t * P:(t + 1) * P],
                                              d64[:], start=True, stop=True)
                    mm.then_inc(z_done, 1)
                pe.wait_ge(z_read, rows)
                for q, (t0, n, _, t) in enumerate(steps):
                    pe.wait_ge(d_full[q % 2], 32 * (q // 2 + 1))
                    if t == 0 and q:
                        pe.wait_ge(y_read, 1)
                    for m in range(2):
                        for c in range(0, n, 512):
                            for j in range(2):
                                w = min(512, n)
                                mm = nc.tensor.matmul(py[:, m * 2 + c // 512, 0:w], Z[:, t0 // P + t, m, j],
                                                      dft[:, q % 2, j, c:c + w], start=(t == 0 and j == 0),
                                                      stop=(t == n // P - 1 and j == 1))
                    mm.then_inc(used, 1)

            @block.scalar
            def _(act):
                for t in range(rows):
                    act.wait_ge(z_done, t + 1)
                    nc.scalar.activation(Z[:, t].rearrange("p m j c -> p (m j c)"), pz[:, t % 2], ACT.Copy
                                         ).then_inc(z_read, 1)

            @block.vector
            def _(dve):
                q = 0
                for t0, n, _ in seqs:
                    q += n // P
                    dve.wait_ge(used, q)
                    for m in range(2):
                        last = nc.vector.tensor_copy(
                            mixT[:, 2 + m, t0:t0 + n],
                            py[:, 2 * m:2 * m + 2].rearrange("p c t -> p (c t)")[:, 0:n])
                    last.then_inc(y_read, 1)



def latent_norm(nc, name, ones, x, tiles, width, vec, spans):
    units = [(t0, n) for t0, n in spans]
    with Stage(nc, name) as s:
        g = s.sb("g", [P, tiles])
        sq, rs = s.sb("sq", [P, tiles, 512]), s.sb("rs", [P, 512])
        ps = s.ps("ps", [P, 512])
        loaded, squared, summed, eps_done, rooted, done, chain_sem = (
            s.sem("loaded"), s.sem("squared"), s.sem("summed"), s.sem("eps"), s.sem("rooted"), s.sem("done"),
            s.sem("chain"))
        with nc.Block() as block:
            @block.sync
            def _(sp):
                with nc.allow_non_contiguous_dma("a vector into columns"):
                    sp.dma_start(g[:], vec.rearrange("(k p) -> p k", p=P)).then_inc(loaded, 16)

            @block.scalar
            def _(act):
                for q, (t0, n) in enumerate(units):
                    if q:
                        act.wait_ge(summed, q)
                    nc.scalar.activation(sq[:, :, 0:n], x[:, 0:tiles, t0:t0 + n], ACT.Square).then_inc(squared, 1)
                    act.wait_ge(eps_done, q + 1)
                    nc.scalar.activation(rs[:, 0:n], rs[:, 0:n], ACT.Sqrt).then_inc(rooted, 1)

            @block.tensor
            def _(pe):
                for q, (t0, n) in enumerate(units):
                    pe.wait_ge(squared, q + 1)
                    if q:
                        pe.wait_ge(eps_done, q)
                    for k in range(tiles):
                        mm = nc.tensor.matmul(ps[:, 0:n], ones, sq[:, k, 0:n], start=(k == 0), stop=(k == tiles - 1))
                    mm.then_inc(summed, 1)

            @block.vector
            def _(dve):
                chain = Chain(dve, chain_sem)
                dve.wait_ge(loaded, 16)
                for q, (t0, n) in enumerate(units):
                    dve.wait_ge(summed, q + 1)
                    if q:
                        dve.wait_ge(done, q)
                    nc.vector.tensor_scalar(rs[:, 0:n], ps[:, 0:n], 1.0 / width, EPS, ALU.mult, ALU.add
                                            ).then_inc(eps_done, 1)
                    dve.wait_ge(rooted, q + 1)
                    chain(nc.vector.reciprocal(rs[:, 0:n], rs[:, 0:n]))
                    for k in range(tiles):
                        own = x[:, k, t0:t0 + n]
                        last = nc.vector.scalar_tensor_tensor(own, own, g[:, k:k + 1], rs[:, 0:n], ALU.mult, ALU.mult)
                    last.then_inc(done, 1)


def heads_qk(nc, name, cst, ones, latent, kt, w_nope, w_rope, shared, norm, spans, nope, rope, spare):
    units = [(t0, n, m) for t0, n in spans for m in range(MH // 2)]
    NU = len(units)
    W = 512
    turning = [u for u, (t0, _, _) in enumerate(units) if t0 < L]
    with Stage(nc, name) as s:
        wn, wr = s.sb("wn", [P, kt, MH, P]), s.sb("wr", [P, kt, 2, P])
        g, gr = s.sb("g", [P, 1]), s.sb("gr", [P, 1])
        cos, sin, rot = s.sb("cos", [P, W]), s.sb("sin", [P, W]), s.sb("rot", [P, P])
        raw, side = s.sb("raw", [P, 2, W]), s.sb("side", [P, 2, W])
        sqr = s.sb("sqr", [P, 2, W])
        sq, rs = (spare[:, j * 4 * W:(j + 1) * 4 * W].rearrange("p (a b t) -> p a b t", a=2, b=2) for j in range(2))
        pn, pr, psum = s.ps("pn", [P, 2, 2, 512]), s.ps("pr", [P, 2, 512]), s.ps("psum", [P, 2, 512])
        loaded, table_full = s.sem("loaded"), s.slots("table_full")
        nope_done, rope_done, squared = s.sem("nope"), s.sem("rope"), s.sem("squared")
        summed, eps_done, rooted, scaled, turned, done = (s.sem("summed"), s.sem("eps"), s.sem("rooted"),
                                                          s.sem("scaled"), s.sem("turned"), s.sem("done"))
        inv_done, side_done, rope_out = s.sem("inv"), s.sem("side"), s.sem("rope_out")
        chain_sem = s.sem("chain")
        n_loads = 3 + MH + (4 if w_rope is not None else 0) + 1
        with nc.Block() as block:
            @block.sync
            def _(sp):
                sp.dma_start(rot[:], cst["rot2"]).then_inc(loaded, 16)
                with nc.allow_non_contiguous_dma("vectors into columns"):
                    sp.dma_start(g[:], norm[0:NOPE].rearrange("(p k) -> p k", k=1)).then_inc(loaded, 16)
                    for h in range(2):
                        sp.dma_start(gr[h * 64:h * 64 + 64], norm[NOPE:QK].rearrange("(p k) -> p k", k=1)
                                     ).then_inc(loaded, 16)
                for h in range(MH):
                    sp.dma_start(wn[:, :, h], w_nope(h)).then_inc(loaded, 16)
                if w_rope is not None:
                    for h in range(MH):
                        sp.dma_start(wr[:, :, h // 2, h % 2 * 64:h % 2 * 64 + 64], w_rope(h)).then_inc(loaded, 16)
                for u in turning[::2]:
                    t0, n, _ = units[u]
                    if u:
                        sp.wait_ge(side_done, u)
                        sp.wait_ge(rope_out, u)
                    for j, (x, table) in enumerate(((cos, "cos2"), (sin, "sin2"))):
                        sp.dma_start(x[:, 0:n], cst[table][:, t0:t0 + n]).then_inc(table_full[j], 16)

            @block.tensor
            def _(pe):
                pe.wait_ge(loaded, 16 * n_loads)

                def project_unit(u):
                    t0, n, m = units[u]
                    if u >= 2:
                        pe.wait_ge(done, u - 1)
                        pe.wait_ge(scaled, u - 1)
                        if u - 2 in turning:
                            pe.wait_ge(side_done, u - 1)
                    for h in range(2):
                        for k in range(kt):
                            mm = nc.tensor.matmul(pn[:, u % 2, h, 0:n], wn[:, k, 2 * m + h], latent[:, k, t0:t0 + n],
                                                  start=(k == 0), stop=(k == kt - 1))
                    mm.then_inc(nope_done, 1)
                    if w_rope is not None:
                        for k in range(kt):
                            mm = nc.tensor.matmul(pr[:, u % 2, 0:n], wr[:, k, m], latent[:, k, t0:t0 + n],
                                                  start=(k == 0), stop=(k == kt - 1))
                        mm.then_inc(rope_done, 1)

                for u in range(2):
                    project_unit(u)
                for u, (t0, n, m) in enumerate(units):
                    if u >= 2:
                        project_unit(u)
                    pe.wait_ge(squared, u + 1)
                    if u:
                        pe.wait_ge(eps_done, u)
                    for h in range(2):
                        r = slice(h * 64, h * 64 + 64)
                        nc.tensor.matmul(psum[:, h, 0:n], ones, sq[:, u % 2, h, 0:n], start=True, stop=False)
                        mm = nc.tensor.matmul(psum[:, h, 0:n], ones[r], sqr[r, u % 2, 0:n], start=False, stop=True)
                    mm.then_inc(summed, 1)
                    if u in turning:
                        pe.wait_ge(scaled, u + 1)
                        nc.tensor.matmul(pr[:, u % 2, 0:n], rot[:], raw[:, u % 2, 0:n], start=True, stop=True
                                         ).then_inc(turned, 1)

            @block.scalar
            def _(act):
                act.wait_ge(loaded, 16 * n_loads)

                def square(u):
                    t0, n, m = units[u]
                    act.wait_ge(nope_done, u + 1)
                    if u >= 2:
                        act.wait_ge(summed, u - 1)
                        act.wait_ge(rope_out, u - 1)
                    nc.scalar.activation(sq[:, u % 2, :, 0:n], pn[:, u % 2, :, 0:n], ACT.Square)
                    if w_rope is not None:
                        act.wait_ge(rope_done, u + 1)
                    src = pr[:, u % 2, 0:n] if w_rope is not None else shared[:, t0:t0 + n]
                    nc.scalar.activation(sqr[:, u % 2, 0:n], src, ACT.Square).then_inc(squared, 1)
                    nc.scalar.activation(raw[:, u % 2, 0:n], src, ACT.Copy, scale=gr[:, 0:1]).then_inc(scaled, 1)

                for u in range(2):
                    square(u)
                for u, (t0, n, m) in enumerate(units):
                    if u >= 2:
                        square(u)
                    act.wait_ge(eps_done, u + 1)
                    nc.scalar.activation(rs[:, u % 2, :, 0:n], rs[:, u % 2, :, 0:n], ACT.Sqrt).then_inc(rooted, 1)

            @block.vector
            def _(dve):
                dve.wait_ge(loaded, 16 * n_loads)
                def add_eps(u):
                    _, n, _ = units[u]
                    dve.wait_ge(summed, u + 1)
                    if u >= 2:
                        dve.wait_ge(rope_out, u - 1)
                        dve.wait_ge(done, u - 1)
                    nc.vector.tensor_scalar(rs[:, u % 2, :, 0:n], psum[:, :, 0:n], 1.0 / QK, EPS, ALU.mult, ALU.add
                                            ).then_inc(eps_done, 1)

                for u in range(2):
                    add_eps(u)
                for u, (t0, n, m) in enumerate(units):
                    dve.wait_ge(rooted, u + 1)
                    nc.vector.reciprocal(rs[:, u % 2, :, 0:n], rs[:, u % 2, :, 0:n]).then_inc(inv_done, 1)
                    if u in turning:
                        dve.wait_ge(table_full[1], 16 * (u // 2 + 1))
                        dve.wait_ge(turned, u + 1)
                        if u >= 2:
                            dve.wait_ge(rope_out, u - 1)
                        nc.vector.tensor_tensor(side[:, u % 2, 0:n], pr[:, u % 2, 0:n], sin[:, 0:n], ALU.mult
                                                ).then_inc(side_done, 1)
                    dve.wait_ge(inv_done, u + 1)
                    nc.vector.scalar_tensor_tensor(nope[:, 2 * m:2 * m + 2, t0:t0 + n], pn[:, u % 2, :, 0:n],
                                                   g[:, 0:1], rs[:, u % 2, :, 0:n], ALU.mult, ALU.mult
                                                   ).then_inc(done, 1)
                    if 2 <= u + 1 < NU:
                        add_eps(u + 1)

            @block.gpsimd
            def _(pool):
                chain = Chain(pool, chain_sem)
                for u, (t0, n, m) in enumerate(units):
                    own = raw[:, u % 2, 0:n]
                    pool.wait_ge(scaled, u + 1)
                    if u in turning:
                        pool.wait_ge(table_full[0], 16 * (u // 2 + 1))
                        pool.wait_ge(turned, u + 1)
                        chain(nc.gpsimd.tensor_tensor(own, own, cos[:, 0:n], ALU.mult))
                        pool.wait_ge(side_done, u + 1)
                        chain(nc.gpsimd.tensor_tensor(own, own, side[:, u % 2, 0:n], ALU.add))
                    pool.wait_ge(inv_done, u + 1)
                    for h in range(2):
                        r = slice(h * 64, h * 64 + 64)
                        ins = nc.gpsimd.tensor_tensor(rope[r, m, t0:t0 + n], raw[r, u % 2, 0:n], rs[r, u % 2, h, 0:n],
                                                      ALU.mult)
                        if h == 0:
                            chain(ins)
                    ins.then_inc(rope_out, 1)
                    pool.wait_ge(rope_out, u + 1)


def values(nc, name, kv, w_ukv, v):
    with Stage(nc, name) as s:
        w = s.sb("w", [P, MH, VD])
        ps = s.ps("ps", [P, 2, 512])
        loaded, done, read = s.sem("loaded"), s.sem("done"), s.sem("read")
        with nc.Block() as block:
            @block.sync
            def _(sp):
                sp.dma_start(w[:], w_ukv.rearrange("p (h c) -> p h c", h=MH)[:, :, NOPE:]).then_inc(loaded, 16)

            @block.tensor
            def _(pe):
                pe.wait_ge(loaded, 16)
                for t in range(T // P):
                    if t >= 2:
                        pe.wait_ge(read, t - 1)
                    nc.tensor.matmul(ps[:, t % 2], kv[:, t * P:(t + 1) * P], w[:].rearrange("p h c -> p (h c)"),
                                     start=True, stop=True).then_inc(done, 1)

            @block.scalar
            def _(act):
                for t in range(T // P):
                    act.wait_ge(done, t + 1)
                    nc.scalar.activation(v[:, t], ps[:, t % 2], ACT.Copy).then_inc(read, 1)


def attend(nc, name, ident, q_nope, q_rope, k_nope, k_rope, v, q0, blocks, k0, mixT):
    NK = T - k0
    key_spans = [(c, min(512, NK - c)) for c in range(0, NK, 512)]
    nt = NK // P
    SPLIT = min(4, nt)
    TURNS, U = blocks // 2, 2 * MH
    SC = QK ** -0.5
    with Stage(nc, name) as s:
        qn, qr = s.sb("qn", [P, 2, MH, P]), s.sb("qr", [P, 2, 2, P])
        prob, probT = s.sb("prob", [P, 2, NK]), s.sb("probT", [P, nt, P])
        nmax, total, inv = s.sb("nmax", [P, 2]), s.sb("total", [P, 2]), s.sb("inv", [P, 2])
        out = s.sb("out", [P, 2, MH * VD])
        pS, pT = s.ps("pS", [P, 3 * 512]), s.ps("pT", [P, 12, P])
        pO, pY = s.ps("pO", [P, 512]), s.ps("pY", [P, MH, P])
        staged, turned_out = s.slots("staged"), s.slots("turned_out")
        lead = s.sb("lead", [P, 2])
        LEAD = key_spans[-1][0]
        lead_full = s.sem("lead_full")
        s_full, max_done, sums, t_done = s.sem("s_full"), s.sem("max"), s.sem("sums"), s.sem("t_done")
        copied_a, copied_v, pv_done, o_done, y_copied = (s.sem("copied_a"), s.sem("copied_v"), s.sem("pv"),
                                                         s.sem("o"), s.sem("y_copied"))
        chain_sem = s.sem("chain")
        with nc.Block() as block:
            @block.gpsimd
            def _(pool):
                with pool.Fori(0, TURNS) as i:
                    for b in range(2):
                        t = bass.ds((i * 2 + b) * P + q0, P)
                        pool.wait_ge(turned_out[b], i)
                        nc.gpsimd.tensor_copy(qn[:, b], q_nope[:, :, t]).then_inc(staged[b], 1)
                        nc.gpsimd.tensor_copy(qr[:, b], q_rope[:, :, t]).then_inc(staged[b], 1)

            @block.tensor
            def _(pe):
                with pe.Fori(0, TURNS) as i:
                    def scores(u):
                        b, h = u // MH, u % MH
                        if h == 0:
                            pe.wait_ge(staged[b], i * 2 + 2)
                        pe.wait_ge(sums, i * U + u)
                        r = slice(h % 2 * 64, h % 2 * 64 + 64)
                        for c, n in key_spans:
                            k = slice(k0 + c, k0 + c + n)
                            nc.tensor.matmul(pS[:, c:c + n], qn[:, b, h], k_nope[:, h, k], start=True, stop=False)
                            mm = nc.tensor.matmul(pS[:, c:c + n], qr[r, b, h // 2], k_rope[r, h // 2, k],
                                                  start=False, stop=True)
                            if c + n == LEAD:
                                mm.then_inc(lead_full, 1)
                        mm.then_inc(s_full, 1)

                    def turn(u):
                        pe.wait_ge(sums, i * U + u + 1)
                        pe.wait_ge(copied_a, i * U + u)
                        pe.wait_ge(copied_v, i * U + u)
                        for j in range(nt):
                            tr = nc.tensor.transpose(pT[:, j], prob[:, u % 2, j * P:(j + 1) * P], ident)
                        tr.then_inc(t_done, 1)

                    def weigh(u):
                        h = u % MH
                        pe.wait_ge(copied_a, i * U + u + 1)
                        pe.wait_ge(copied_v, i * U + u + 1)
                        pe.wait_ge(o_done, i * U + u)
                        for j in range(nt):
                            mm = nc.tensor.matmul(pO[:, 0:VD], probT[:, j], v[:, k0 // P + j, h * VD:(h + 1) * VD],
                                                  start=(j == 0), stop=(j == nt - 1))
                        mm.then_inc(pv_done, 1)

                    def turn_out(b):
                        pe.wait_ge(o_done, i * U + (b + 1) * MH)
                        pe.wait_ge(y_copied, i * 2 + b)
                        for h in range(MH):
                            tr = nc.tensor.transpose(pY[:, h], out[:, b, h * VD:(h + 1) * VD], ident)
                        tr.then_inc(turned_out[b], 1)

                    for u in range(U):
                        scores(u)
                        if u:
                            weigh(u - 1)
                        if u == MH + 1:
                            turn_out(0)
                        turn(u)
                    weigh(U - 1)
                    turn_out(1)

            @block.scalar
            def _(act):
                with act.Fori(0, TURNS) as i:
                    for u in range(U):
                        p = u % 2
                        act.wait_ge(max_done, i * U + u + 1)
                        nc.scalar.activation(prob[:, p], pS[:, 0:NK], ACT.Exp, bias=nmax[:, p:p + 1], scale=SC,
                                             accum_out=total[:, p:p + 1]).then_inc(sums, 1)
                        act.wait_ge(t_done, i * U + u + 1)
                        act.wait_ge(pv_done, i * U + u)
                        if nt > SPLIT:
                            nc.scalar.activation(probT[:, SPLIT:nt], pT[:, SPLIT:nt], ACT.Copy).then_inc(copied_a, 1)
                        else:
                            nc.scalar.activation(nmax[:, p:p + 1], nmax[:, p:p + 1], ACT.Copy).then_inc(copied_a, 1)

            @block.vector
            def _(dve):
                with dve.Fori(0, TURNS) as i:
                    chain = Chain(dve, chain_sem, i, (3 if LEAD else 2) * U)

                    def outputs(u):
                        b, h, p = u // MH, u % MH, u % 2
                        dve.wait_ge(pv_done, i * U + u + 1)
                        nc.vector.tensor_scalar(out[:, b, h * VD:(h + 1) * VD], pO[:, 0:VD], inv[:, p:p + 1], None,
                                                ALU.mult).then_inc(o_done, 1)

                    def copy_out(b):
                        dve.wait_ge(turned_out[b], i + 1)
                        nc.vector.tensor_copy(mixT[:, 4:8, bass.ds((i * 2 + b) * P + q0, P)], pY[:]
                                              ).then_inc(y_copied, 1)

                    for u in range(U):
                        p = u % 2
                        if LEAD:
                            dve.wait_ge(lead_full, i * U + u + 1)
                            chain(nc.vector.tensor_reduce(lead[:, p:p + 1], pS[:, 0:LEAD], AX.X, ALU.max, negate=True))
                        dve.wait_ge(s_full, i * U + u + 1)
                        chain(nc.vector.tensor_reduce(nmax[:, p:p + 1], pS[:, LEAD:NK], AX.X, ALU.max, negate=True))
                        if LEAD:
                            nc.vector.tensor_scalar(nmax[:, p:p + 1], nmax[:, p:p + 1], lead[:, p:p + 1], SC, ALU.min,
                                                    ALU.mult).then_inc(max_done, 1)
                        else:
                            nc.vector.tensor_scalar(nmax[:, p:p + 1], nmax[:, p:p + 1], SC, None, ALU.mult
                                                    ).then_inc(max_done, 1)
                        if u:
                            outputs(u - 1)
                        if u == MH + 1:
                            copy_out(0)
                        dve.wait_ge(sums, i * U + u + 1)
                        chain(nc.vector.reciprocal(inv[:, p:p + 1], total[:, p:p + 1]))
                        dve.wait_ge(t_done, i * U + u + 1)
                        nc.vector.tensor_copy(probT[:, 0:SPLIT], pT[:, 0:SPLIT]).then_inc(copied_v, 1)
                    outputs(U - 1)
                    copy_out(1)
                    chain.close()



def col(mod, n, j=0):
    return mod[:, n * KT:(n + 1) * KT, j]


def first_mixers(nc, cst, ident, ones, a, scratch, mod, next_mod):
    w_in = a["w_in"][0]
    c_rw = WQ + 2 * WKV

    def sb(stack, name, shape, dt=F32):
        return stack.enter_context(nc.sbuf_tensor(name, shape, dt))

    modulation(nc, "b1_mod", ident, (a["c"][0], a["c_ctx"]), a["w_ada"][0], a["b_ada"][0], mod)
    with ExitStack() as recur:
        lora_in = sb(recur, "lora_in", [65, T])
        y = sb(recur, "y", [P, 4, L])
        rkv = sb(recur, "rkv", [P, 12, T])
        with ExitStack() as with_h:
            lora_a, lora_b = flat(y[:])[:, 0:T], flat(y[:])[0:32, T:2 * T]
            h = sb(with_h, "h_hi", [P, KT, T], F32R), sb(with_h, "h_lo", [P, KT, T], F32R)
            x0 = flat(rkv[:])[:, 0:KT * L].rearrange("p (k t) -> p k t", k=KT)
            c0 = flat(rkv[:])[:, KT * L:KT * T].rearrange("p (k t) -> p k t", k=KT)
            load_transposed(nc, "load_x", ident, a["x"][0], x0, L)
            load_transposed(nc, "load_ctx", ident, a["ctx"][0], c0, C)
            norm_modulate(nc, "norm1", ones, [(x0, 0, L, h, col(mod, 0), col(mod, 1)),
                                              (c0, L, C, h, col(mod, 0, 1), col(mod, 1, 1))], a["norm1_g"][0])
            project_gates(nc, "gates", h, w_in[:, c_rw + WRW:], scratch["gates"])
            qT, kT, v = rkv[:, 0:4, 0:L], rkv[:, 4], rkv[:, 5].rearrange("p (t w) -> p t w", w=WKV)
            kpad, vpad = rkv[:, 6], rkv[:, 7].rearrange("p (t w) -> p t w", w=WKV)
            project_qkv(nc, "qkv", cst, ident, h, w_in, qT, kT, v, flat(y[:]))
            window_attention(nc, "window", cst, ident, qT, kT, v, kpad, vpad, a["sink"][0], y)
            store_columns(nc, "store_ya", y[:], scratch["ya"])
            project_rwkv(nc, "rkv", h, w_in[:, c_rw:c_rw + WRW], a["conv_w"][0], rkv, lora_a, lora_b)
        prepare_recurrence(nc, "keys", cst, rkv, lora_a, lora_b, a["k_k"][0], a["gate_g2"][0], scratch["kk"],
                           lora_in, scratch["g"])
        with ExitStack() as with_k:
            kk = sb(with_k, "kk", [P, 4, T])
            run_recurrences(nc, "rec", cst, ident, rkv, kk, scratch["kk"], lora_in, a["decay_w0"][0], a["decay_w2"][0],
                            a["iclr_a0"][0], a["iclr_a2"][0], a["k_a"][0], y)
        recurrence_outputs(nc, "rec_out", cst, rkv, lora_in, a["iclr_a0"][0], a["iclr_a2"][0], a["k_a"][0],
                           a["r_k"][0], a["lnx_w"][0], a["lnx_b"][0], scratch["g"], y, scratch["yr"],
                           lambda *args: Modulation(nc, args[0], ident, (a["c_2"][0], a["c_ctx_2"]), a["w_ada_2"][0],
                                                    a["b_ada_2"][0], next_mod, *args[1:]))


def first_rest(nc, ident, ones, a, scratch, mod, xT):
    def sb(stack, name, shape, dt=F32):
        return stack.enter_context(nc.sbuf_tensor(name, shape, dt))

    with ExitStack() as tmp:
        merged = sb(tmp, "merged", [P, KT, L])
        with ExitStack() as tmp2:
            ya, yr = sb(tmp2, "ya", [P, 4, L]), sb(tmp2, "yr2", [P, 4, L])
            load_transposed(nc, "load_x2", ident, a["x"][0], xT, L,
                            ((ya[:], by_tiles(scratch["ya"])), (yr[:], by_tiles(scratch["yr"]))))
            merge_branches(nc, "merge", ya, yr, a["w_branch_attn"][0], a["w_branch_rwkv"][0], scratch["gates"],
                           merged)
        hi, lo = sb(tmp, "merged_hi", [P, KT, L], F32R), sb(tmp, "merged_lo", [P, KT, L], F32R)
        project(nc, "w_out", columns_of(a["w_out"][0]), KT, KT, split_columns(nc, "split_merged", merged, hi, lo),
                LAT, add_gated(nc, (xT, col(mod, 2), 0, L)))
    with ExitStack() as tmp:
        hi, lo = sb(tmp, "h2_hi", [P, KT, L], F32R), sb(tmp, "h2_lo", [P, KT, L], F32R)
        norm_modulate(nc, "norm2", ones, [(xT, 0, L, (hi, lo), col(mod, 3), col(mod, 4))], a["norm2_g"][0])
        mlp(nc, "mlp", (hi, lo), a["w_mlp_up"][0], a["w_mlp_down"][0], xT, col(mod, 5))
    norm_modulate(nc, "norm_f", ones, [(xT, 0, L, xT, None, None)], a["norm_f_g"])



E_N, FE = 16, 512
FT = FE // P


def store_rows(nc, name, ident, src, tokens, dram):
    rows = tokens // P
    with Stage(nc, name) as s:
        out = s.sb("out", [P, 2, D])
        ps = s.ps("ps", [P, 2, KT, P])
        turned, copied, stored = s.sem("turned"), s.sem("copied"), s.slots("stored")
        with nc.Block() as block:
            @block.tensor
            def _(pe):
                for t in range(rows):
                    if t >= 2:
                        pe.wait_ge(copied, t - 1)
                    for k in range(KT):
                        tr = nc.tensor.transpose(ps[:, t % 2, k], src[:, k, t * P:(t + 1) * P], ident)
                    tr.then_inc(turned, 1)

            @block.scalar
            def _(act):
                for t in range(rows):
                    act.wait_ge(turned, t + 1)
                    if t >= 2:
                        act.wait_ge(stored[t % 2], 16 * (t // 2))
                    nc.scalar.activation(out[:, t % 2], ps[:, t % 2].rearrange("p k t -> p (k t)"), ACT.Copy
                                         ).then_inc(copied, 1)

            @block.sync
            def _(sp):
                for t in range(rows):
                    sp.wait_ge(copied, t + 1)
                    sp.dma_start(dram[t * P:(t + 1) * P, :], out[:, t % 2]).then_inc(stored[t % 2], 16)
                for b in range(2):
                    sp.wait_ge(stored[b], 16 * ((rows + 1 - b) // 2))


def choose_tokens(nc, name, ident, hT, w_router, groups, idx, gain, h_dram, acc_dram, beside=None):
    rows = sum(g[1] for g in groups) // P
    N = rows * P
    CAP = max(g[2] for g in groups)
    with Stage(nc, name) as s:
        w = s.sb("w", [P, KT, E_N])
        aff = s.sb("aff", [P, rows, E_N])
        top, total = s.sb("top", [P, rows]), s.sb("total", [P, rows])
        affT = s.sb("affT", [E_N, N])
        best, where = s.sb("best", [E_N, len(groups), CAP]), s.sb("where", [E_N, len(groups), CAP], U32)
        wheref = s.sb("wheref", [E_N, len(groups), CAP])
        out, zero = s.sb("out", [P, 2, D]), s.sb("zero", [P, D])
        pl = s.ps("pl", [P, 512])
        pT = s.ps("pT", [P, 3 * 512])
        ps = s.ps("ps", [P, 2, KT, P])
        row_turned, row_copied, row_stored = s.sem("row_turned"), s.sem("row_copied"), s.slots("row_stored")
        zero_set, zero_stored = s.sem("zero_set"), s.sem("zero_stored")
        banks = ps[:].rearrange("p a k t -> p (a k t)").rearrange("p (a t) -> p a t", t=512)
        side = None if beside is None else beside(s, [pT[:, b * 512:(b + 1) * 512] for b in range(3)], banks[:, 3])
        aff_copied = s.sem("aff_copied")

        def side_steps(t):
            if side is None:
                return []
            return [(e % 3, e // 3) for e in range(t * side.STEPS // rows, (t + 1) * side.STEPS // rows)]
        w_loaded, logits, shifted, exped, aff_done = (s.sem("w"), s.sem("logits"), s.sem("shifted"), s.sem("exped"),
                                                      s.sem("aff"))
        turned, copied, chosen, turned_back, chain_sem = (s.sem("turned"), s.sem("copied"), s.sem("chosen"),
                                                          s.sem("turned_back"), s.sem("chain"))
        with nc.Block() as block:
            @block.sync
            def _(sp):
                sp.dma_start(w[:], by_tiles(w_router)).then_inc(w_loaded, 16)
                sp.wait_ge(zero_set, 1)
                for t in range(rows):
                    sp.dma_start(acc_dram[t * P:(t + 1) * P, :], zero[:]).then_inc(zero_stored, 16)
                for t in range(rows):
                    sp.wait_ge(row_copied, t + 1)
                    sp.dma_start(h_dram[t * P:(t + 1) * P, :], out[:, t % 2]).then_inc(row_stored[t % 2], 16)
                for b in range(2):
                    sp.wait_ge(row_stored[b], 16 * ((rows + 1 - b) // 2))
                sp.wait_ge(zero_stored, 16 * rows)

            @block.gpsimd
            def _(pool):
                nc.gpsimd.memset(zero[:], 0.0).then_inc(zero_set, 1)
                if side is not None:
                    side.load_small(pool)
                    side.load(pool)

            @block.tensor
            def _(pe):
                pe.wait_ge(w_loaded, 16)
                for t in range(rows):
                    for k in range(KT):
                        mm = nc.tensor.matmul(pl[:, t * E_N:(t + 1) * E_N], hT[:, k, t * P:(t + 1) * P], w[:, k],
                                              start=(k == 0), stop=(k == KT - 1))
                mm.then_inc(logits, 1)
                pe.wait_ge(aff_done, 1)
                for t in range(rows):
                    tr = nc.tensor.transpose(pT[0:E_N, t * P:(t + 1) * P], aff[:, t], ident)
                tr.then_inc(turned, 1)
                for t in range(rows):
                    if t >= 2:
                        pe.wait_ge(row_copied, t - 1)
                    for k in range(KT):
                        tr = nc.tensor.transpose(ps[:, t % 2, k], hT[:, k, t * P:(t + 1) * P], ident)
                    tr.then_inc(row_turned, 1)
                    if t == 0 and side is not None:
                        pe.wait_ge(aff_copied, 1)
                    for b, i in side_steps(t):
                        side.multiply(pe, b, i)
                if side is not None:
                    pe.wait_ge(row_copied, rows)
                    side.turn(pe)
                pe.wait_ge(chosen, 1)
                for n, (_, _, cap, _) in enumerate(groups):
                    for j, x in enumerate((best, wheref)):
                        o = (n * 2 + j) * E_N
                        tr = nc.tensor.transpose(pl[0:cap, o:o + E_N], x[:, n, 0:cap], ident[0:E_N, 0:E_N])
                tr.then_inc(turned_back, 1)

            @block.scalar
            def _(act):
                act.wait_ge(shifted, 1)
                nc.scalar.activation(aff[:], aff[:], ACT.Exp).then_inc(exped, 1)
                if side is not None:
                    side.silu(act)
                for t in range(rows):
                    act.wait_ge(row_turned, t + 1)
                    if t >= 2:
                        act.wait_ge(row_stored[t % 2], 16 * (t // 2))
                    nc.scalar.activation(out[:, t % 2], ps[:, t % 2].rearrange("p k t -> p (k t)"), ACT.Copy
                                         ).then_inc(row_copied, 1)
                    for b, i in side_steps(t):
                        side.read_out(act, b, i)

            @block.vector
            def _(dve):
                chain = Chain(dve, chain_sem)
                wide = lambda x: x[:].unsqueeze(2).to_broadcast([P, rows, E_N])
                pl_v = pl[:, 0:rows * E_N].rearrange("p (t e) -> p t e", e=E_N)
                dve.wait_ge(logits, 1)
                chain(nc.vector.tensor_reduce(top[:], pl_v, AX.X, ALU.max))
                nc.vector.tensor_tensor(aff[:], pl_v, wide(top), ALU.subtract).then_inc(shifted, 1)
                dve.wait_ge(exped, 1)
                chain(nc.vector.tensor_reduce(total[:], aff[:], AX.X, ALU.add))
                chain(nc.vector.reciprocal(total[:], total[:]))
                nc.vector.tensor_tensor(aff[:], aff[:], wide(total), ALU.mult).then_inc(aff_done, 1)
                dve.wait_ge(turned, 1)
                nc.vector.tensor_copy(affT[:], pT[0:E_N, 0:N]).then_inc(aff_copied, 1)
                dve.wait_ge(aff_copied, 1)
                for n, (t0, tokens, cap, _) in enumerate(groups):
                    own = affT[:, t0:t0 + tokens]
                    for r in range(0, cap, 8):
                        b8, w8 = best[:, n, r:r + 8], where[:, n, r:r + 8]
                        chain(nc.vector.max(b8, own))
                        chain(nc.vector.max_index(w8, b8, own))
                        chain(nc.vector.match_replace(own, b8, own, -1.0))
                    last = nc.vector.tensor_scalar(wheref[:, n, 0:cap], where[:, n, 0:cap], float(t0), None, ALU.add)
                    if n == len(groups) - 1:
                        last.then_inc(chosen, 1)
                    else:
                        chain(last)
                dve.wait_ge(turned_back, 1)
                for n, (_, _, cap, _) in enumerate(groups):
                    o = n * 2 * E_N
                    nc.vector.tensor_copy(gain[0:cap, n], pl[0:cap, o:o + E_N])
                    nc.vector.tensor_copy(idx[0:cap, n], pl[0:cap, o + E_N:o + 2 * E_N])
                if side is not None:
                    side.add_bias(dve)


def run_experts(nc, name, ident, groups, idx, gain, h_dram, acc_dram, w_gate, w_up, w_down):
    caps = [g[2] for g in groups]
    offs = [sum(caps[:n]) for n in range(len(caps))]
    S = sum(caps)
    NG = len(groups)
    PAIRS = E_N // 2 - 1
    UNITS = [(n, c) for n in range(NG) for c in range(2)]
    U = len(UNITS)
    with Stage(nc, name) as s:
        wg, wu, wd = s.sb("wg", [P, 2, KT, FE]), s.sb("wu", [P, 2, KT, FE]), s.sb("wd", [P, 2, FT, D])
        own_idx = [s.sb(f"own_idx{n}", [cap, 2], U32) for n, cap in enumerate(caps)]
        xs = [s.sb(f"xs{n}", [cap, 2, D]) for n, cap in enumerate(caps)]
        ys = [s.sb(f"ys{n}", [cap, 2, D]) for n, cap in enumerate(caps)]
        xT = s.sb("xT", [P, 2, KT, S])
        hid, act_g = s.sb("hid", [P, 2, FT, S]), s.sb("act_g", [P, FT, S])
        pX, pY = s.ps("pX", [P, 2, 512]), s.ps("pY", [P, 2, 512])
        pG, pU = s.ps("pG", [P, 2, 512]), s.ps("pU", [P, 2, 512])
        g_full, u_full, d_full = s.slots("g_full"), s.slots("u_full"), s.slots("d_full")
        idx_ready, gathered, x_turned, x_copied = (s.slots("idx"), s.slots("gathered"), s.slots("x_turned"),
                                                   s.slots("x_copied"))
        hid_mul, silu_done, hid_done, y_mul, y_read, added = (s.slots("hid_mul"), s.slots("silu"), s.slots("hid"),
                                                              s.slots("y_mul"), s.slots("y_read"), s.slots("added"))
        passed = s.sem("passed")
        with nc.Block() as block:
            @block.sync
            def _(sp):
                with sp.Fori(0, E_N // 2) as i:
                    for b in range(2):
                        e = i * 2 + b
                        sp.wait_ge(hid_mul[b], i)
                        sp.dma_start(wg[:, b], w_gate[bass.ds(e, 1)].rearrange("a (k p) f -> p (a k) f", p=P)
                                     ).then_inc(g_full[b], 16)
                        sp.dma_start(wu[:, b], w_up[bass.ds(e, 1)].rearrange("a (k p) f -> p (a k) f", p=P)
                                     ).then_inc(u_full[b], 16)
                        sp.wait_ge(y_mul[b], i * U)
                        sp.dma_start(wd[:, b], w_down[bass.ds(e, 1)].rearrange("a (k p) f -> p (a k) f", p=P)
                                     ).then_inc(d_full[b], 16)

            @block.gpsimd
            def _(pool):
                def gather(b, m):
                    for n, cap in enumerate(caps):
                        if n == 0 and not isinstance(m, int):
                            pool.wait_ge(x_turned[b], m * 2)
                        nc.gpsimd.tensor_copy(own_idx[n][:, b:b + 1], idx[0:cap, n, bass.ds(m * 2 + b, 1)]
                                              ).then_inc(idx_ready[b], 1)
                        pool.wait_ge(idx_ready[b], m * NG + (n + 1))
                        pool.sem_inc(passed, 1)
                        pool.indirect_dma_start(
                            out=xs[n][:, b], out_offset=None, in_=h_dram,
                            in_offset=bass.IndirectOffsetOnAxis(ap=own_idx[n][:, b:b + 1], axis=0),
                            ).then_inc(gathered[b], 16)

                def scatter(b, m):
                    for n, cap in enumerate(caps):
                        pool.wait_ge(y_read[b], m * U + 2 * (n + 1))
                        pool.sem_inc(passed, 1)
                        pool.indirect_dma_start(
                            out=acc_dram, out_offset=bass.IndirectOffsetOnAxis(ap=own_idx[n][:, b:b + 1], axis=0),
                            in_=ys[n][:, b], in_offset=None, compute_op=ALU.add
                            ).then_inc(added[b], 16)
                        pool.wait_ge(added[b], m * (NG * 16) + (n + 1) * 16)

                for b in range(2):
                    gather(b, 0)
                with pool.Fori(0, PAIRS) as i:
                    for b in range(2):
                        scatter(b, i)
                        gather(b, i + 1)
                for b in range(2):
                    scatter(b, PAIRS)

            @block.tensor
            def _(pe):
                def turn(b, m, half):
                    if half == 0:
                        pe.wait_ge(gathered[b], m * (NG * 16) + NG * 16)
                    else:
                        pe.wait_ge(x_copied[b], m * 2 + 1)
                    for j in range(4):
                        k = 4 * half + j
                        for n, cap in enumerate(caps):
                            o = j % 2 * S + offs[n]
                            tr = nc.tensor.transpose(pX[:, j // 2, o:o + cap], xs[n][:, b, k * P:(k + 1) * P],
                                                     ident[0:cap, 0:cap])
                    tr.then_inc(x_turned[b], 1)

                def hidden(b, m):
                    pe.wait_ge(x_copied[b], m * 2 + 2)
                    for w, full, ps in ((wg, g_full, pG), (wu, u_full, pU)):
                        pe.wait_ge(full[b], m * 16 + 16)
                        for f in range(FT):
                            for k in range(KT):
                                mm = nc.tensor.matmul(ps[:, f // 2, f % 2 * S:f % 2 * S + S],
                                                      w[:, b, k, f * P:(f + 1) * P], xT[:, b, k],
                                                      start=(k == 0), stop=(k == KT - 1))
                    mm.then_inc(hid_mul[b], 1)

                def down(b, m, units):
                    pe.wait_ge(hid_done[b], m + 1)
                    pe.wait_ge(d_full[b], m * 16 + 16)
                    for u in units:
                        n, c = UNITS[u]
                        if u >= 2:
                            pe.wait_ge(y_read[b], m * U + (u - 1))
                        elif b or not isinstance(m, int):
                            pe.wait_ge(y_read[1 - b], (m + b) * U)
                        for f in range(FT):
                            mm = nc.tensor.matmul(pY[0:caps[n], c], hid[:, b, f, offs[n]:offs[n] + caps[n]],
                                                  wd[:, b, f, c * 512:(c + 1) * 512], start=(f == 0),
                                                  stop=(f == FT - 1))
                        mm.then_inc(y_mul[b], 1)

                def step(b, m, i):
                    turn(b, m, 0)
                    down(1 - b, i, range(U // 2))
                    turn(b, m, 1)
                    down(1 - b, i, range(U // 2, U))
                    hidden(b, m)

                turn(0, 0, 0)
                turn(0, 0, 1)
                hidden(0, 0)
                with pe.Fori(0, PAIRS) as i:
                    step(1, i, i)
                    step(0, i + 1, i)
                step(1, PAIRS, PAIRS)
                down(1, PAIRS, range(U))

            @block.scalar
            def _(act):
                with act.Fori(0, E_N // 2) as i:
                    for b in range(2):
                        for half in range(2):
                            act.wait_ge(x_turned[b], i * 2 + (half + 1))
                            for j in range(2):
                                k = 4 * half + 2 * j
                                cp = nc.scalar.activation(xT[:, b, k:k + 2], pX[:, j, 0:2 * S].rearrange(
                                    "p (k t) -> p k t", k=2), ACT.Copy)
                            cp.then_inc(x_copied[b], 1)
                        act.wait_ge(hid_mul[b], i + 1)
                        nc.scalar.activation(act_g[:].rearrange("p (a f) t -> p a (f t)", a=2), pG[:, :, 0:2 * S],
                                             ACT.Silu).then_inc(silu_done[b], 1)

            @block.vector
            def _(dve):
                with dve.Fori(0, E_N // 2) as i:
                    for b in range(2):
                        dve.wait_ge(silu_done[b], i + 1)
                        nc.vector.tensor_tensor(hid[:, b].rearrange("p (a f) t -> p a (f t)", a=2),
                                                act_g[:].rearrange("p (a f) t -> p a (f t)", a=2),
                                                pU[:, :, 0:2 * S], ALU.mult).then_inc(hid_done[b], 1)
                        dve.wait_ge(added[b], i * (NG * 16))
                        for u, (n, c) in enumerate(UNITS):
                            dve.wait_ge(y_mul[b], i * U + (u + 1))
                            nc.vector.tensor_scalar(ys[n][:, b, c * 512:(c + 1) * 512], pY[0:caps[n], c],
                                                    gain[0:caps[n], n, bass.ds(i * 2 + b, 1)], None,
                                                    ALU.mult).then_inc(y_read[b], 1)


def add_rows(nc, name, ident, src, x, gate, tokens):
    TURNS = tokens // P // 2
    with Stage(nc, name) as s:
        rows = s.sb("rows", [P, 2, D])
        part = s.sb("part", [P, 2, KT, P])
        ps = s.ps("ps", [P, 2, KT, P])
        full, turned, read, added = s.slots("full"), s.slots("turned"), s.slots("read"), s.slots("added")
        with nc.Block() as block:
            @block.sync
            def _(sp):
                with sp.Fori(0, TURNS) as i:
                    for b in range(2):
                        sp.wait_ge(turned[b], i)
                        sp.dma_start(rows[:, b], src[bass.ds((i * 2 + b) * P, P), :]).then_inc(full[b], 16)

            @block.tensor
            def _(pe):
                with pe.Fori(0, TURNS) as i:
                    for b in range(2):
                        pe.wait_ge(full[b], i * 16 + 16)
                        pe.wait_ge(read[b], i)
                        for k in range(KT):
                            tr = nc.tensor.transpose(ps[:, b, k], rows[:, b, k * P:(k + 1) * P], ident)
                        tr.then_inc(turned[b], 1)

            @block.vector
            def _(dve):
                with dve.Fori(0, TURNS) as i:
                    for b in range(2):
                        dve.wait_ge(turned[b], i + 1)
                        dve.wait_ge(added[b], i)
                        nc.vector.tensor_tensor(part[:, b], ps[:, b], gate.unsqueeze(2).to_broadcast([P, KT, P]),
                                                ALU.mult).then_inc(read[b], 1)

            @block.gpsimd
            def _(pool):
                with pool.Fori(0, TURNS) as i:
                    for b in range(2):
                        pool.wait_ge(read[b], i + 1)
                        own = x[:, :, bass.ds((i * 2 + b) * P, P)]
                        nc.gpsimd.tensor_tensor(own, own, part[:, b], ALU.add).then_inc(added[b], 1)


def second_layer(nc, cst, ident, ones, a, scratch, layer, mod, next_mod, xT, cT):
    last = next_mod is None
    nm = f"l{layer}_"
    tokens = L if last else T
    spans = [x for x in CHUNKS if x[0] < tokens]

    def sb(stack, name, shape, dt=F32):
        return stack.enter_context(nc.sbuf_tensor(nm + name, shape, dt))

    w_in, w_uq, w_ukv = a["w_in_2"][layer], a["w_uq_2"][layer], a["w_ukv_2"][layer]
    with ExitStack() as mixing:
        mixT = sb(mixing, "mixT", [P, KT, T])
        norm_modulate(nc, nm + "norm1", ones, [(xT, 0, L, mixT, col(mod, 0), col(mod, 1)),
                                               (cT, L, C, mixT, col(mod, 0, 1), col(mod, 1, 1))])
        inner = mixing.enter_context(ExitStack())
        pq, kvr = sb(inner, "pq", [P, 2, T]), sb(inner, "kvr", [P, 2, T])
        kv, kr = kvr[:, 0:1], kvr[:, 1]
        with ExitStack() as tmp:
            uT, fT, vn = sb(tmp, "uT", [P, 2, T]), sb(tmp, "fT", [P, 2, T]), sb(tmp, "vn", [P, T // P, SGU_W])
            project_mixers(nc, nm + "in", ones, mixT, w_in, tokens, uT, vn, fT, pq, kv[:, 0], kr)
            gate_tokens(nc, nm + "sgu", ident, uT, vn, a["sgu_norm_2"][layer], a["w_sgu_2"][layer],
                        a["b_sgu_2"][layer], tokens, mixT)
            fourier(nc, nm + "fnet", cst, fT, [(0, L, "l")] + ([] if last else [(L, C, "c")]), mixT)
        latent_norm(nc, nm + "qnorm", ones, pq, 2, Q_LORA, a["q_lora_norm_2"][layer], spans)
        latent_norm(nc, nm + "kvnorm", ones, kv, 1, KV_LORA, a["kv_lora_norm_2"][layer], CHUNKS)
        v = sb(inner, "v", [P, T // P, MH * VD])
        values(nc, nm + "v", kv[:, 0], w_ukv, v)
        spare = flat(mixT[:, 4:8])
        kn, krope = sb(inner, "kn", [P, MH, T]), sb(inner, "krope", [P, 2, T])
        ukv = w_ukv.rearrange("(k p) (h c) -> p k h c", p=P, h=MH)
        heads_qk(nc, nm + "k", cst, ones, kv, 1, lambda h: ukv[:, :, h, 0:NOPE], None, kr, a["k_norm_2"][layer],
                 CHUNKS, kn, krope, spare)
        qn, qr = sb(inner, "qn", [P, MH, T]), kvr
        uq = w_uq.rearrange("(k p) (h c) -> p k h c", p=P, h=MH)
        heads_qk(nc, nm + "q", cst, ones, pq, 2, lambda h: uq[:, :, h, 0:NOPE], lambda h: uq[:, :, h, NOPE:],
                 None, a["q_norm_2"][layer], spans, qn, qr, spare)
        attend(nc, nm + "att", ident, qn, qr, kn, krope, v, 0, L // P, 0, mixT)
        if not last:
            attend(nc, nm + "att_ctx", ident, qn, qr, kn, krope, v, L, C // P, L, mixT)
        inner.close()
        hi, lo = sb(mixing, "mix_hi", [P, KT, tokens], F32R), sb(mixing, "mix_lo", [P, KT, tokens], F32R)
        parts = [(xT, col(mod, 2), 0, L)] + ([] if last else [(cT, col(mod, 2, 1), L, C)])
        project(nc, nm + "w_out", columns_of(a["w_out_2"][layer]), KT, KT,
                split_columns(nc, nm + "split_mix", mixT[:, :, 0:tokens], hi, lo), spans, add_gated(nc, *parts))
    groups = [(0, L, 2 * L // E_N, 0)] + ([] if last else [(L, C, 2 * C // E_N, 1)])
    with ExitStack() as moe:
        idx, gain = sb(moe, "idx", [P, len(groups), E_N], U32), sb(moe, "gain", [P, len(groups), E_N])
        with ExitStack() as tmp:
            h2 = sb(tmp, "h2", [P, KT, tokens])
            norm_modulate(nc, nm + "norm2", ones, [(xT, 0, L, h2, col(mod, 3), col(mod, 4))] + (
                [] if last else [(cT, L, C, h2, col(mod, 3, 1), col(mod, 4, 1))]))
            choose_tokens(nc, nm + "choose", ident, h2, a["w_router_2"][layer], groups, idx, gain,
                          scratch["h"], scratch["acc"], None if last else lambda *args: Modulation(
                              nc, args[0], ident, (a["c_2"][0], a["c_ctx_2"]), a["w_ada_2"][layer + 1],
                              a["b_ada_2"][layer + 1], next_mod, *args[1:]))
        run_experts(nc, nm + "experts", ident, groups, idx, gain, scratch["h"][0:tokens, :],
                    scratch["acc"][0:tokens, :],
                    a["w_gate_2"][layer], a["w_up_2"][layer], a["w_down_2"][layer])
    add_rows(nc, nm + "add", ident, scratch["acc"], xT, col(mod, 5), L)
    if not last:
        add_rows(nc, nm + "add_ctx", ident, scratch["acc"][L:, :], cT, col(mod, 5, 1), C)


def build(nc, a, cst, out):
    scratch = {name: nc.dram_tensor("s_" + name, shape, F32, kind="Internal").ap()
               for name, shape in (("gates", (2 * D, L)), ("g", (512, L)), ("ya", (512, L)), ("yr", (512, L)),
                                   ("kk", (512, T)), ("h", (T, D)), ("acc", (T, D)))}
    with ExitStack() as stack:
        def sb(name, shape):
            return stack.enter_context(nc.sbuf_tensor(name, shape, F32))

        ident, ones = sb("ident", [P, P]), sb("ones", [P, P])
        mod, mods = sb("mod", [P, 6 * KT, 2]), [sb("mod2_0", [P, 6 * KT, 2])]
        load_matrix(nc, "load_ident", cst["ident"], ident)
        load_matrix(nc, "load_ones", cst["ones"], ones)
        first_mixers(nc, cst, ident[:], ones[:], a, scratch, mod, mods[0])
        mods.append(sb("mod2_1", [P, 6 * KT, 2]))
        xT = sb("xT", [P, KT, L])
        first_rest(nc, ident[:], ones[:], a, scratch, mod, xT)
        cT = sb("cT", [P, KT, C])
        load_transposed(nc, "load_ctx2", ident[:], a["ctx_2"][0], cT, C)
        for layer in range(2):
            second_layer(nc, cst, ident[:], ones[:], a, scratch, layer, mods[layer], (mods + [None])[layer + 1], xT,
                         cT)
        store_rows(nc, "store_out", ident[:], xT, L, out)



def constants():
    f = np.float32
    out = {"ident": np.eye(P, dtype=f), "ones": np.ones((P, P), f)}
    out["ones64"] = np.kron(np.eye(2), np.ones((64, 64))).astype(f)
    pos = np.arange(L)
    row, col = pos // 64, pos % 64

    def rotation(half):
        r = np.zeros((P, P), f)
        for p in range(P):
            if p % (2 * half) < half:
                r[p + half, p] = -1.0
            else:
                r[p - half, p] = 1.0
        return r

    inv = (10000.0 ** (-np.arange(16) / 16.0)).astype(f)
    ang = np.concatenate([row[:, None].astype(f) * inv, col[:, None].astype(f) * inv], axis=1)
    ang1 = ang[:, np.arange(P) % 32].T
    out["cos1"], out["sin1"], out["rot1"] = np.cos(ang1).astype(f), np.sin(ang1).astype(f), rotation(32)
    p64 = np.arange(P) % 64
    ang2 = ang[:, (p64 // 32) * 16 + p64 % 16].T
    out["cos2"], out["sin2"], out["rot2"] = np.cos(ang2).astype(f), np.sin(ang2).astype(f), rotation(16)

    q, k = np.arange(P)[:, None], np.arange(P)[None, :]
    window = np.zeros((P, L // P, 2, P), f)
    window[:, :, 0][np.broadcast_to((k < q)[:, None], (P, L // P, P))] = NEG
    window[:, :, 1][np.broadcast_to((k > q)[:, None], (P, L // P, P))] = NEG
    window[:, 0, 0] = NEG
    window[:, -1, 1] = NEG
    out["window"] = window

    i, j = np.arange(64)[None, :], np.arange(64)[:, None]
    masks = np.zeros((2, 8, 64, 64), f)
    for lv in range(6):
        b = 1 << lv
        masks[0, lv] = (i // b % 2 == 1) & (j // b == i // b - 1)
    masks[0, 6], masks[0, 7] = j < i, j <= i
    masks[1] = masks[0].transpose(0, 2, 1)
    m = masks.transpose(2, 0, 1, 3)
    out["masks"] = np.concatenate([m, m], axis=0).copy()

    for nm, n in (("l", L), ("c", C)):
        a = 2 * np.pi * ((np.arange(n)[:, None] * np.arange(n)[None, :]) % n) / n
        out["dft_cos_" + nm] = (np.cos(a) / np.sqrt(n)).astype(f)
        out["dft_sin_" + nm] = (np.sin(a) / np.sqrt(n)).astype(f)
    a = 2 * np.pi * ((np.arange(64)[:, None] * np.arange(64)[None, :]) % 64) / 64
    out["dft64"] = np.concatenate([np.kron(np.eye(2), np.cos(a)), -np.kron(np.eye(2), np.sin(a))],
                                  axis=1).astype(f) / f(8)
    return out


_INS = ["x", "c", "ctx", "c_ctx", "w_ada", "b_ada", "norm1_g", "w_in", "sink", "conv_w", "decay_w0", "decay_w2",
        "iclr_a0", "iclr_a2", "gate_g2", "k_k", "k_a", "r_k", "lnx_w", "lnx_b", "w_branch_attn", "w_branch_rwkv",
        "w_out", "norm2_g", "w_mlp_up", "w_mlp_down", "norm_f_g", "c_2", "ctx_2", "c_ctx_2", "w_ada_2", "b_ada_2",
        "w_in_2", "sgu_norm_2", "w_sgu_2", "b_sgu_2", "q_lora_norm_2", "w_uq_2", "kv_lora_norm_2", "w_ukv_2",
        "q_norm_2", "k_norm_2", "w_out_2", "w_router_2", "w_gate_2", "w_up_2", "w_down_2"]


def kernel(**inputs):
    import numpy as _np
    import concourse.bacc as _bacc
    from concourse import mybir as _mybir
    from concourse.bass_utils import run_bass_kernel_spmd as _run

    nc = _bacc.Bacc("TRN2", target_bir_lowering=False, num_devices=1)
    arrays, a, cst = {}, {}, {}
    for group, names in ((a, _INS), (cst, None)):
        values = constants() if names is None else {name: inputs[name] for name in names}
        for name, value in values.items():
            full = ("in_" if names else "const_") + name + "_dram"
            arrays[full] = _np.ascontiguousarray(value)
            group[name] = nc.dram_tensor(full, arrays[full].shape, _mybir.dt.from_np(arrays[full].dtype),
                                         kind="ExternalInput").ap()
    out = nc.dram_tensor("out_0_dram", (1, L, D), _mybir.dt.float32, kind="ExternalOutput").ap()
    build(nc, a, cst, out[0])
    r = _run(nc, [arrays], core_ids=[0])
    return r.results[0]["out_0_dram"]
```
